# Optimizing a Trainium2 kernel written in Bass

```python
import math
import jax
import jax.numpy as jnp
from jax import lax
import numpy as np
import jax, jax.numpy as jnp

D_MODEL = 1024
BATCH = 1
SEQ = 1024
DEPTH = 1

CHUNK = 64
NORM_EPS = 1e-6

HG_HEADS = 4
HG_DK = 128
HG_DV = 128
HG_KEY = HG_HEADS * HG_DK
HG_VAL = HG_HEADS * HG_DV

GLA_HEADS = 4
GLA_DK = 64
GLA_DV = 128
GLA_KEY = GLA_HEADS * GLA_DK
GLA_VAL = GLA_HEADS * GLA_DV
GLA_RANK = 16
GLA_TAU = 16.0

ML_HEADS = 4
ML_DK = 64
ML_DV = 128
ML_KEY = ML_HEADS * ML_DK
ML_VAL = ML_HEADS * ML_DV
CONV_K = 4

D_MIX = HG_VAL + GLA_VAL + ML_VAL

SEGMENTS = (
    ("hg_q", HG_KEY), ("hg_f", HG_KEY), ("hg_i", HG_VAL), ("hg_z", HG_VAL),
    ("gla_q", GLA_KEY), ("gla_k", GLA_KEY), ("gla_v", GLA_VAL), ("gla_a", GLA_RANK), ("gla_z", GLA_VAL),
    ("ml_q", ML_KEY), ("ml_k", ML_KEY), ("ml_v", ML_VAL), ("ml_i", ML_HEADS), ("ml_f", ML_HEADS),
    ("ml_o", ML_VAL), ("ml_z", ML_VAL),
)
N_IN = (3 * HG_KEY + HG_VAL) - HG_KEY + HG_VAL + (2 * GLA_KEY + 2 * GLA_VAL + GLA_RANK) + (2 * ML_KEY + 3 * ML_VAL + 2 * ML_HEADS)


def _segment_offsets():
    offs = {}
    start = 0
    for name, width in SEGMENTS:
        offs[name] = (start, start + width)
        start += width
    return offs

def _split_columns(proj):
    return {name: proj[..., s:e] for name, (s, e) in _segment_offsets().items()}

def _rmsnorm(x, w):
    xf = x.astype(jnp.float32)
    y = xf * lax.rsqrt(jnp.mean(xf * xf, axis=-1, keepdims=True) + NORM_EPS)
    return (y * w.astype(jnp.float32)).astype(x.dtype)

def _heads(a, n_heads):
    b, t, _ = a.shape
    return a.reshape(b, t, n_heads, -1).transpose(0, 2, 1, 3).astype(jnp.float32)

def _to_chunks(a, n_chunks):
    a = a.reshape(a.shape[:2] + (n_chunks, CHUNK) + a.shape[3:])
    return jnp.moveaxis(a, 2, 0)

def _from_chunks(a):
    a = jnp.moveaxis(a, 0, 2)
    return a.reshape(a.shape[:2] + (a.shape[2] * a.shape[3],) + a.shape[4:])

def _causal_conv(a, w, bias):
    k = w.shape[0]
    y = lax.conv_general_dilated(a, w[:, None, :].astype(a.dtype), window_strides=(1,), padding=[(k - 1, 0)],
                                 dimension_numbers=("NWC", "WIO", "NWC"), feature_group_count=a.shape[-1])
    return y + bias.astype(a.dtype)

def _chunk_gated_linear_attention(q, k, v, log_g):
    bsz, nh, seq, dk = q.shape
    dv = v.shape[-1]
    nc = seq // CHUNK
    causal = jnp.tril(jnp.ones((CHUNK, CHUNK), dtype=bool))[None, None, :, :, None]

    def step(state, inp):
        qc, kc, vc, gc = inp
        b = jnp.cumsum(gc, axis=2)
        dec = jnp.exp(jnp.where(causal, b[:, :, :, None, :] - b[:, :, None, :, :], -jnp.inf))
        att = jnp.einsum("bhtd,bhsd,bhtsd->bhts", qc, kc, dec)
        out = jnp.einsum("bhts,bhsv->bhtv", att, vc) + jnp.einsum("bhtd,bhdv->bhtv", qc * jnp.exp(b), state)
        b_last = b[:, :, -1:, :]
        state = jnp.exp(b_last[:, :, 0, :, None]) * state + jnp.einsum("bhsd,bhsv->bhdv", kc * jnp.exp(b_last - b), vc)
        return state, out

    s0 = jnp.zeros((bsz, nh, dk, dv), jnp.float32)
    _, out = lax.scan(step, s0, (_to_chunks(q, nc), _to_chunks(k, nc), _to_chunks(v, nc), _to_chunks(log_g, nc)))
    return _from_chunks(out)

def _chunk_mlstm(q, k, v, i_pre, log_f):
    bsz, nh, seq, dk = q.shape
    dv = v.shape[-1]
    nc = seq // CHUNK
    causal = jnp.tril(jnp.ones((CHUNK, CHUNK), dtype=bool))[None, None]

    def step(carry, inp):
        c_st, n_st, m_st = carry
        qc, kc, vc, ic, fc = inp
        b = jnp.cumsum(fc, axis=-1)
        d = jnp.where(causal, b[..., :, None] - b[..., None, :] + ic[..., None, :], -jnp.inf)
        m_t = jnp.maximum(b + m_st[..., None], jnp.max(d, axis=-1))
        w = jnp.exp(d - m_t[..., None])
        inter = jnp.exp(b + m_st[..., None] - m_t)
        s = jnp.einsum("bhtd,bhsd->bhts", qc, kc) * w
        num = inter[..., None] * jnp.einsum("bhtd,bhdv->bhtv", qc, c_st) + jnp.einsum("bhts,bhsv->bhtv", s, vc)
        den = inter * jnp.einsum("bhtd,bhd->bht", qc, n_st) + jnp.sum(s, axis=-1)
        h = num / jnp.maximum(jnp.abs(den), jnp.exp(-m_t))[..., None]
        m_new = m_t[..., -1]
        wk = jnp.exp(b[..., -1:] - b + ic - m_new[..., None])
        scale = jnp.exp(b[..., -1] + m_st - m_new)
        c_st = scale[..., None, None] * c_st + jnp.einsum("bhs,bhsd,bhsv->bhdv", wk, kc, vc)
        n_st = scale[..., None] * n_st + jnp.einsum("bhs,bhsd->bhd", wk, kc)
        return (c_st, n_st, m_new), h

    carry0 = (jnp.zeros((bsz, nh, dk, dv), jnp.float32), jnp.zeros((bsz, nh, dk), jnp.float32),
              jnp.zeros((bsz, nh), jnp.float32))
    _, h = lax.scan(step, carry0, (_to_chunks(q, nc), _to_chunks(k, nc), _to_chunks(v, nc),
                                   _to_chunks(i_pre, nc), _to_chunks(log_f, nc)))
    return _from_chunks(h)

def _gated_head_norm(o, z, w):
    bsz, nh, seq, dv = o.shape
    of = o.transpose(0, 2, 1, 3)
    of = of * lax.rsqrt(jnp.mean(of * of, axis=-1, keepdims=True) + NORM_EPS)
    of = of.reshape(bsz, seq, nh * dv) * w.astype(jnp.float32)
    return (of * jax.nn.silu(z.astype(jnp.float32))).astype(z.dtype)

def _hgrn2_branch(parts, lb):
    q = jax.nn.silu(_heads(parts["hg_q"], HG_HEADS))
    lb = lb.reshape(HG_HEADS, 1, HG_DK)
    f = lb + (1.0 - lb) * jax.nn.sigmoid(_heads(parts["hg_f"], HG_HEADS))
    i = _heads(parts["hg_i"], HG_HEADS)
    return _chunk_gated_linear_attention(q, 1.0 - f, i, jnp.log(f))

def _gla_branch(parts, w_a2, b_a2):
    q = _heads(parts["gla_q"], GLA_HEADS) * (GLA_DK ** -0.5)
    k = _heads(parts["gla_k"], GLA_HEADS)
    v = _heads(parts["gla_v"], GLA_HEADS)
    a = parts["gla_a"] @ w_a2 + b_a2
    log_alpha = jax.nn.log_sigmoid(_heads(a, GLA_HEADS)) / GLA_TAU
    return _chunk_gated_linear_attention(q, k, v, log_alpha)

def _mlstm_branch(parts, conv_w, conv_b):
    qk = jax.nn.silu(_causal_conv(jnp.concatenate([parts["ml_q"], parts["ml_k"]], axis=-1), conv_w, conv_b))
    q = _heads(qk[..., :ML_KEY], ML_HEADS) * (ML_DK ** -0.5)
    k = _heads(qk[..., ML_KEY:], ML_HEADS)
    v = _heads(parts["ml_v"], ML_HEADS)
    i_pre = parts["ml_i"].astype(jnp.float32).transpose(0, 2, 1)
    log_f = jax.nn.log_sigmoid(parts["ml_f"].astype(jnp.float32).transpose(0, 2, 1))
    h = _chunk_mlstm(q, k, v, i_pre, log_f)
    return h * jax.nn.sigmoid(_heads(parts["ml_o"], ML_HEADS))

def first_inputs(seed: int = 0) -> dict:
    key = jax.random.key(seed)
    ks = jax.random.split(key, 16)
    nrm = jax.random.normal
    x = nrm(ks[0], (BATCH, SEQ, D_MODEL), jnp.float32)
    norm_w = 1.0 + 0.02 * nrm(ks[1], (DEPTH, D_MODEL), jnp.float32)
    w_in = nrm(ks[2], (DEPTH, D_MODEL, N_IN), jnp.float32) * (D_MODEL ** -0.5)
    b_in = 0.02 * nrm(ks[3], (DEPTH, N_IN), jnp.float32)
    f_start, f_end = _segment_offsets()["ml_f"]
    b_in = b_in.at[:, f_start:f_end].add(jnp.linspace(3.0, 6.0, ML_HEADS, dtype=jnp.float32))
    hg_lb_logits = 0.1 * nrm(ks[4], (DEPTH, HG_KEY), jnp.float32)
    hg_norm_w = 1.0 + 0.02 * nrm(ks[5], (DEPTH, HG_VAL), jnp.float32)
    gla_w_a2 = nrm(ks[6], (DEPTH, GLA_RANK, GLA_KEY), jnp.float32) * (GLA_RANK ** -0.5)
    gla_b_a2 = 0.02 * nrm(ks[7], (DEPTH, GLA_KEY), jnp.float32)
    gla_norm_w = 1.0 + 0.02 * nrm(ks[8], (DEPTH, GLA_VAL), jnp.float32)
    ml_conv_w = nrm(ks[9], (DEPTH, CONV_K, 2 * ML_KEY), jnp.float32) * (CONV_K ** -0.5)
    ml_conv_b = 0.02 * nrm(ks[10], (DEPTH, 2 * ML_KEY), jnp.float32)
    ml_norm_w = 1.0 + 0.02 * nrm(ks[11], (DEPTH, ML_VAL), jnp.float32)
    w_out = nrm(ks[12], (DEPTH, D_MIX, D_MODEL), jnp.float32) * (D_MIX ** -0.5) * 0.5
    final_norm_w = 1.0 + 0.02 * nrm(ks[13], (D_MODEL,), jnp.float32)
    return {"x": x, "norm_w": norm_w, "w_in": w_in, "b_in": b_in, "hg_lb_logits": hg_lb_logits,
            "hg_norm_w": hg_norm_w, "gla_w_a2": gla_w_a2, "gla_b_a2": gla_b_a2, "gla_norm_w": gla_norm_w,
            "ml_conv_w": ml_conv_w, "ml_conv_b": ml_conv_b, "ml_norm_w": ml_norm_w, "w_out": w_out,
            "final_norm_w": final_norm_w}

def first_block(x, norm_w, w_in, b_in, hg_lb_logits, hg_norm_w, gla_w_a2, gla_b_a2, gla_norm_w,
              ml_conv_w, ml_conv_b, ml_norm_w, w_out, final_norm_w):
    p = jax.nn.softmax(hg_lb_logits.astype(jnp.float32), axis=0)
    lower_bounds = jnp.cumsum(p, axis=0) - p[0:1]
    for l in range(DEPTH):
        h = _rmsnorm(x, norm_w[l])
        parts = _split_columns(h @ w_in[l] + b_in[l])
        y_hg = _gated_head_norm(_hgrn2_branch(parts, lower_bounds[l]), parts["hg_z"], hg_norm_w[l])
        y_gla = _gated_head_norm(_gla_branch(parts, gla_w_a2[l], gla_b_a2[l]), parts["gla_z"], gla_norm_w[l])
        y_ml = _gated_head_norm(_mlstm_branch(parts, ml_conv_w[l], ml_conv_b[l]), parts["ml_z"], ml_norm_w[l])
        y = jnp.concatenate([y_hg, y_gla, y_ml], axis=-1).astype(x.dtype)
        x = x + y @ w_out[l]
    return _rmsnorm(x, final_norm_w)


_first_inputs = first_inputs


def first_inputs(seed=0):
    import zlib

    import numpy as np

    out = dict(_first_inputs(seed))
    spreads = {}
    factors = {'norm_w': 4.852,
     'hg_norm_w': 38.697,
     'gla_w_a2': 3.289,
     'gla_b_a2': 64.0,
     'gla_norm_w': 41.516,
     'ml_conv_b': 64.0,
     'ml_norm_w': 38.52,
     'final_norm_w': 7.508}
    for name, (base, spread) in spreads.items():
        noise = np.random.default_rng([zlib.crc32(name.encode()), seed]).standard_normal(out[name].shape)
        drawn = base * np.exp(spread * noise) if base else spread * noise
        out[name] = jnp.asarray(drawn.astype(out[name].dtype))
    for name, factor in factors.items():
        out[name] = (out[name] * factor).astype(out[name].dtype)
    return out


_narrow_inputs = first_inputs


def first_inputs(seed=0):

    out = dict(_narrow_inputs(seed))
    wider = {'hg_norm_w': 5.55, 'gla_norm_w': 5.56, 'ml_norm_w': 5.55, 'final_norm_w': 3.08}
    for name, times in wider.items():
        mean = out[name].mean()
        out[name] = (mean + times * (out[name] - mean)).astype(out[name].dtype)
    return out


CONV_CH = D_MODEL
CONV_WIDTH = 31
RET_HEADS = 4
RET_QK_DIM = 256
RET_V_DIM = 512
RET_QK = RET_HEADS * RET_QK_DIM
RET_V = RET_HEADS * RET_V_DIM
RET_CHUNK = 128
ROPE_BASE = 10000.0
LN_EPS = 1e-5

SPLIT_SIZES = (
    CONV_CH,
    CONV_CH,
    CONV_CH,
    RET_QK,
    RET_QK,
    RET_V,
    RET_V,
    D_MODEL,
    D_MODEL,
)
IN_COLS = int(sum(SPLIT_SIZES))
SPLIT_POINTS = tuple(int(s) for s in np.cumsum(SPLIT_SIZES)[:-1])


def _rmsnorm_2(x, g):
    xf = x.astype(jnp.float32)
    y = xf * lax.rsqrt(jnp.mean(xf * xf, axis=-1, keepdims=True) + NORM_EPS)
    return (y * g.astype(jnp.float32)).astype(x.dtype)

def _layernorm(x, g, b):
    xf = x.astype(jnp.float32)
    mu = jnp.mean(xf, axis=-1, keepdims=True)
    var = jnp.mean(jnp.square(xf - mu), axis=-1, keepdims=True)
    y = (xf - mu) * lax.rsqrt(var + LN_EPS)
    return (y * g.astype(jnp.float32) + b.astype(jnp.float32)).astype(x.dtype)

def _rotate_half(t):
    t1, t2 = jnp.split(t, 2, axis=-1)
    return jnp.concatenate([-t2, t1], axis=-1)

def _rotary(t, cos, sin):
    return t * cos[None, :, None, :] + _rotate_half(t) * sin[None, :, None, :]

def _retention_chunkwise(q, k, v, log_gamma):
    B, S, H, dk = q.shape
    dv = v.shape[-1]
    C = RET_CHUNK
    N = S // C
    qc = q.reshape(B, N, C, H, dk)
    kc = k.reshape(B, N, C, H, dk)
    vc = v.reshape(B, N, C, H, dv)

    idx = jnp.arange(C, dtype=jnp.float32)
    diff = idx[:, None] - idx[None, :]
    decay = jnp.where((diff >= 0)[None],
                      jnp.exp(log_gamma[:, None, None] * jnp.maximum(diff, 0.0)[None]),
                      0.0)

    scores = jnp.einsum('bnihd,bnjhd->bnhij', qc, kc) * decay[None, None]
    inner = jnp.einsum('bnhij,bnjhe->bnihe', scores, vc)

    xi = jnp.exp(log_gamma[None, :] * (idx[:, None] + 1.0))
    zeta = jnp.exp(log_gamma[None, :] * (C - 1.0 - idx[:, None]))
    gamma_c = jnp.exp(log_gamma * C)

    def step(R, inp):
        qi, ki, vi = inp
        cross = jnp.einsum('bihd,bhde->bihe', qi, R) * xi[None, :, :, None]
        R = R * gamma_c[None, :, None, None] + jnp.einsum(
            'bjhd,bjhe->bhde', ki * zeta[None, :, :, None], vi)
        return R, cross

    R0 = jnp.zeros((B, H, dk, dv), jnp.float32)
    _, cross = lax.scan(step, R0, (qc.transpose(1, 0, 2, 3, 4),
                                   kc.transpose(1, 0, 2, 3, 4),
                                   vc.transpose(1, 0, 2, 3, 4)))
    cross = cross.transpose(1, 0, 2, 3, 4)
    return (inner + cross).reshape(B, S, H, dv)

def second_inputs(seed: int = 0) -> dict:
    key = jax.random.key(seed)
    ks = jax.random.split(key, 16)
    f32 = jnp.float32
    x = jax.random.normal(ks[0], (BATCH, SEQ, D_MODEL), f32)
    norm_gain = 1.0 + 0.02 * jax.random.normal(ks[1], (DEPTH, D_MODEL), f32)
    w_in = jax.random.normal(ks[2], (DEPTH, D_MODEL, IN_COLS), f32) * D_MODEL ** -0.5
    conv_dw_w = jax.random.normal(ks[3], (DEPTH, CONV_WIDTH, CONV_CH), f32) * CONV_WIDTH ** -0.5
    conv_dw_b = 0.02 * jax.random.normal(ks[4], (DEPTH, CONV_CH), f32)
    conv_ln_g = 1.0 + 0.02 * jax.random.normal(ks[5], (DEPTH, CONV_CH), f32)
    conv_ln_b = 0.02 * jax.random.normal(ks[6], (DEPTH, CONV_CH), f32)
    w_conv_proj = jax.random.normal(ks[7], (DEPTH, CONV_CH, D_MODEL), f32) * CONV_CH ** -0.5
    ret_gn_g = 1.0 + 0.02 * jax.random.normal(ks[8], (DEPTH, RET_V), f32)
    w_ret_proj = jax.random.normal(ks[9], (DEPTH, RET_V, D_MODEL), f32) * RET_V ** -0.5
    w_out = jax.random.normal(ks[10], (DEPTH, D_MODEL, D_MODEL), f32) * D_MODEL ** -0.5
    final_gain = 1.0 + 0.02 * jax.random.normal(ks[11], (D_MODEL,), f32)
    return {"x": x, "norm_gain": norm_gain, "w_in": w_in, "conv_dw_w": conv_dw_w,
            "conv_dw_b": conv_dw_b, "conv_ln_g": conv_ln_g, "conv_ln_b": conv_ln_b,
            "w_conv_proj": w_conv_proj, "ret_gn_g": ret_gn_g, "w_ret_proj": w_ret_proj,
            "w_out": w_out, "final_gain": final_gain}

def second_block(x, norm_gain, w_in, conv_dw_w, conv_dw_b, conv_ln_g, conv_ln_b,
              w_conv_proj, ret_gn_g, w_ret_proj, w_out, final_gain):
    B, S, _ = x.shape
    dt = x.dtype
    pos = jnp.arange(S, dtype=jnp.float32)
    inv_freq = ROPE_BASE ** (-jnp.arange(0, RET_QK_DIM, 2, dtype=jnp.float32) / RET_QK_DIM)
    ang = pos[:, None] * inv_freq[None, :]
    cos = jnp.cos(jnp.concatenate([ang, ang], axis=-1))
    sin = jnp.sin(jnp.concatenate([ang, ang], axis=-1))
    log_gamma = jnp.log1p(-jnp.exp2(-5.0 - jnp.arange(RET_HEADS, dtype=jnp.float32)))

    for l in range(DEPTH):
        h = _rmsnorm_2(x, norm_gain[l])
        proj = jnp.einsum('bsd,de->bse', h, w_in[l])
        a_val, a_glu, a_gate, q, k, v, r_gate, g_a, g_b = jnp.split(proj, SPLIT_POINTS, axis=-1)

        u = a_val * jax.nn.sigmoid(a_glu)
        u = lax.conv_general_dilated(
            u, conv_dw_w[l][:, None, :].astype(u.dtype), window_strides=(1,),
            padding=[(CONV_WIDTH - 1, 0)],
            dimension_numbers=('NWC', 'WIO', 'NWC'),
            feature_group_count=CONV_CH) + conv_dw_b[l]
        u = jax.nn.silu(_layernorm(u, conv_ln_g[l], conv_ln_b[l]))
        u = u * jax.nn.silu(a_gate)
        y_a = jnp.einsum('bsc,cd->bsd', u, w_conv_proj[l])

        qh = _rotary(q.astype(jnp.float32).reshape(B, S, RET_HEADS, RET_QK_DIM), cos, sin)
        kh = _rotary(k.astype(jnp.float32).reshape(B, S, RET_HEADS, RET_QK_DIM), cos, sin)
        kh = kh * (RET_QK_DIM ** -0.5)
        vh = v.astype(jnp.float32).reshape(B, S, RET_HEADS, RET_V_DIM)
        o = _retention_chunkwise(qh, kh, vh, log_gamma)
        mu = jnp.mean(o, axis=-1, keepdims=True)
        var = jnp.mean(jnp.square(o - mu), axis=-1, keepdims=True)
        o = ((o - mu) * lax.rsqrt(var + LN_EPS)).reshape(B, S, RET_V)
        o = (o * ret_gn_g[l].astype(jnp.float32)).astype(dt)
        o = o * jax.nn.silu(r_gate)
        y_b = jnp.einsum('bsc,cd->bsd', o, w_ret_proj[l])

        m = jax.nn.sigmoid(g_a) * y_a + jax.nn.sigmoid(g_b) * y_b
        x = x + jnp.einsum('bsd,de->bse', m, w_out[l])

    return _rmsnorm_2(x, final_gain)


_first_inputs_2 = second_inputs


def second_inputs(seed=0):
    import zlib

    import numpy as np

    out = dict(_first_inputs_2(seed))
    spreads = {}
    factors = {'norm_gain': 3.791,
     'conv_dw_b': 8.0,
     'conv_ln_g': 8.0,
     'conv_ln_b': 8.0,
     'ret_gn_g': 8.0,
     'final_gain': 2.828}
    for name, (base, spread) in spreads.items():
        noise = np.random.default_rng([zlib.crc32(name.encode()), seed]).standard_normal(out[name].shape)
        drawn = base * np.exp(spread * noise) if base else spread * noise
        out[name] = __import__('jax').numpy.asarray(drawn.astype(out[name].dtype))
    for name, factor in factors.items():
        out[name] = (out[name] * factor).astype(out[name].dtype)
    return out


_narrow_inputs_2 = second_inputs


def second_inputs(seed=0):

    out = dict(_narrow_inputs_2(seed))
    wider = {'conv_ln_g': 5.31, 'conv_ln_b': 5.27, 'ret_gn_g': 3.95, 'final_gain': 3.18}
    for name, times in wider.items():
        mean = out[name].mean()
        out[name] = (mean + times * (out[name] - mean)).astype(out[name].dtype)
    return out


SB_HEADS = 8
SB_HEAD_DIM = 64
SB_WIDTH = SB_HEADS * SB_HEAD_DIM
SB_BLOCK = 128
SSD_WIDTH = D_MODEL
SSD_HEAD_DIM = 64
SSD_HEADS = SSD_WIDTH // SSD_HEAD_DIM
SSD_GROUPS = 2
SSD_STATE = 64
SSD_CONV = 4
SSD_CHUNK = 128
SSD_CONV_CH = SSD_WIDTH + 2 * SSD_GROUPS * SSD_STATE
RW_HEAD_DIM = 64
RW_WIDTH = D_MODEL // 2
RW_HEADS = RW_WIDTH // RW_HEAD_DIM
RW_DECAY_RANK = 64
RW_ICLR_RANK = 64
N_BRANCH = 3
SB_COLS = 4 * SB_WIDTH
SSD_COLS = SSD_WIDTH + SSD_CONV_CH + SSD_HEADS
RW_COLS = 4 * RW_WIDTH + RW_DECAY_RANK + RW_ICLR_RANK
GATE_COLS = N_BRANCH * D_MODEL
N_IN_3 = SB_COLS + SSD_COLS + RW_COLS + GATE_COLS
RMS_EPS = 1e-6
GN_EPS = 64e-5


def _split(x, sizes):
    idx = np.cumsum(sizes)[:-1].tolist()
    return jnp.split(x, idx, axis=-1)

def rms_norm(x, g):
    xf = x.astype(jnp.float32)
    y = xf * lax.rsqrt(jnp.mean(xf * xf, axis=-1, keepdims=True) + RMS_EPS)
    return (y * g.astype(jnp.float32)).astype(x.dtype)

def stick_breaking_attention(q, k, v):
    b, s, h, dh = q.shape
    scale = dh ** -0.5
    outs = []
    for i in range(s // SB_BLOCK):
        q0 = i * SB_BLOCK
        end = q0 + SB_BLOCK
        qb, kb, vb = q[:, q0:end], k[:, :end], v[:, :end]
        z = jnp.einsum('bqhd,bkhd->bhqk', qb, kb).astype(jnp.float32) * scale
        t_idx = q0 + jnp.arange(SB_BLOCK)
        s_idx = jnp.arange(end)
        mask = s_idx[None, :] < t_idx[:, None]
        log_beta = jax.nn.log_sigmoid(z)
        log_keep = jnp.where(mask, jax.nn.log_sigmoid(-z), 0.0)
        after = lax.cumsum(log_keep, axis=3, reverse=True) - log_keep
        att = jnp.where(mask, jnp.exp(log_beta + after), 0.0)
        outs.append(jnp.einsum('bhqk,bkhd->bqhd', att.astype(v.dtype), vb))
    return jnp.concatenate(outs, axis=1).reshape(b, s, h * dh)

def causal_depthwise_conv(x, w, bias):
    kw, ch = w.shape
    y = lax.conv_general_dilated(x, w[:, None, :], window_strides=(1,), padding=[(kw - 1, 0)],
                                 dimension_numbers=('NWC', 'WIO', 'NWC'), feature_group_count=ch)
    return y + bias

def segsum(a):
    t = a.shape[-1]
    rep = jnp.broadcast_to(a[..., None], a.shape + (t,))
    strict = jnp.tril(jnp.ones((t, t), dtype=bool), -1)
    cs = jnp.cumsum(jnp.where(strict, rep, 0), axis=-2)
    return jnp.where(jnp.tril(jnp.ones((t, t), dtype=bool)), cs, -jnp.inf)

def ssd_mixer(xbc_raw, dt_raw, conv_w, conv_b, dt_bias, a_log, d_skip):
    b, s, _ = xbc_raw.shape
    c, l, g = s // SSD_CHUNK, SSD_CHUNK, SSD_GROUPS
    j, p, n = SSD_HEADS // SSD_GROUPS, SSD_HEAD_DIM, SSD_STATE
    xbc = jax.nn.silu(causal_depthwise_conv(xbc_raw, conv_w, conv_b))
    xs, bm, cm = _split(xbc, [SSD_WIDTH, g * n, g * n])
    xs = xs.reshape(b, c, l, g, j, p)
    bm = bm.reshape(b, c, l, g, n)
    cm = cm.reshape(b, c, l, g, n)
    dt = jax.nn.softplus(dt_raw + dt_bias).reshape(b, c, l, g, j)
    a_head = -jnp.exp(a_log).reshape(g, j)
    da = jnp.moveaxis(dt * a_head, 2, -1)
    x_dt = xs * dt[..., None]
    a_cs = jnp.cumsum(da, axis=-1)
    decay_in = jnp.exp(segsum(da))
    cb = jnp.einsum('bclgn,bcsgn->bcgls', cm, bm)
    y_diag = jnp.einsum('bcgls,bcgjls,bcsgjp->bclgjp', cb, decay_in, x_dt)
    decay_states = jnp.exp(a_cs[..., -1:] - a_cs)
    states = jnp.einsum('bclgn,bcgjl,bclgjp->bcgjpn', bm, decay_states, x_dt)
    last = jnp.pad(jnp.moveaxis(a_cs[..., -1], 1, -1), [(0, 0), (0, 0), (0, 0), (1, 0)])
    decay_chunk = jnp.exp(segsum(last))
    states_p = jnp.concatenate([jnp.zeros_like(states[:, :1]), states], axis=1)
    new_states = jnp.einsum('bgjzc,bcgjpn->bzgjpn', decay_chunk, states_p)
    prev_states = new_states[:, :-1]
    y_off = jnp.einsum('bclgn,bcgjpn,bcgjl->bclgjp', cm, prev_states, jnp.exp(a_cs))
    y = y_diag + y_off + xs * d_skip.reshape(g, j)[:, :, None]
    return y.reshape(b, s, SSD_WIDTH)

def _rwkv7_step(state, inp):
    r_t, w_t, k_t, v_t, kk_t, a_t = inp
    sa = jnp.einsum('bhij,bhj->bhi', state, -kk_t)
    state = (state * w_t[:, :, None, :] + sa[..., None] * (kk_t * a_t)[:, :, None, :]
             + v_t[..., None] * k_t[:, :, None, :])
    y_t = jnp.einsum('bhij,bhj->bhi', state, r_t)
    return state, y_t

def rwkv7_mixer(slab, mu, w0, w_up, a0, a_up, k_k, k_a, r_k, ln_g, ln_b):
    b, s, _ = slab.shape
    hh, nn = RW_HEADS, RW_HEAD_DIM
    prev = jnp.pad(slab[:, :-1], [(0, 0), (1, 0), (0, 0)])
    mixed = slab + (prev - slab) * mu
    r, k, v, gate, w_lo, a_lo = _split(mixed, [RW_WIDTH] * 4 + [RW_DECAY_RANK, RW_ICLR_RANK])
    w = -jax.nn.softplus(-(w0 + jnp.tanh(w_lo) @ w_up)) - 0.5
    decay = jnp.exp(-jnp.exp(w.astype(jnp.float32)))
    a = jax.nn.sigmoid(a0 + a_lo @ a_up)
    kk = (k * k_k).reshape(b, s, hh, nn).astype(jnp.float32)
    kk = kk / jnp.maximum(jnp.sqrt(jnp.sum(kk * kk, axis=-1, keepdims=True)), 1e-12)
    k = k * (1 + (a - 1) * k_a)
    heads = lambda t: t.reshape(b, s, hh, nn).astype(jnp.float32)
    r4, k4, v4, a4, w4 = heads(r), heads(k), heads(v), heads(a), heads(decay)
    seq_first = lambda t: jnp.moveaxis(t, 1, 0)
    state0 = jnp.zeros((b, hh, nn, nn), jnp.float32)
    _, ys = lax.scan(_rwkv7_step, state0,
                     (seq_first(r4), seq_first(w4), seq_first(k4), seq_first(v4), seq_first(kk), seq_first(a4)))
    y = jnp.moveaxis(ys, 0, 1)
    mean = jnp.mean(y, axis=-1, keepdims=True)
    var = jnp.mean(jnp.square(y - mean), axis=-1, keepdims=True)
    y = ((y - mean) * lax.rsqrt(var + GN_EPS)).reshape(b, s, RW_WIDTH) * ln_g + ln_b
    bonus = jnp.sum(r4 * k4 * r_k, axis=-1, keepdims=True) * v4
    y = y + bonus.reshape(b, s, RW_WIDTH)
    return y.astype(slab.dtype), gate

def hybrid_layer(x, norm_g, w_in, conv_w, conv_b, dt_bias, a_log, d_skip, ssd_norm_g,
                 rw_mu, rw_w0, rw_w_up, rw_a0, rw_a_up, rw_k_k, rw_k_a, rw_r_k, rw_ln_g, rw_ln_b,
                 w_out_sb, w_out_ssd, w_out_rw, w_o):
    b, s, _ = x.shape
    h = rms_norm(x, norm_g)
    proj = h @ w_in
    sb_cols, ssd_cols, rw_cols, gate_cols = _split(proj, [SB_COLS, SSD_COLS, RW_COLS, GATE_COLS])
    q, k, v, sb_gate = _split(sb_cols, [SB_WIDTH] * 4)
    shp = (b, s, SB_HEADS, SB_HEAD_DIM)
    y_sb = stick_breaking_attention(q.reshape(shp), k.reshape(shp), v.reshape(shp)) * jax.nn.silu(sb_gate)
    z, xbc, dt_raw = _split(ssd_cols, [SSD_WIDTH, SSD_CONV_CH, SSD_HEADS])
    y_ssd = ssd_mixer(xbc, dt_raw, conv_w, conv_b, dt_bias, a_log, d_skip)
    y_ssd = rms_norm(y_ssd * jax.nn.silu(z), ssd_norm_g)
    y_rw, rw_gate = rwkv7_mixer(rw_cols, rw_mu, rw_w0, rw_w_up, rw_a0, rw_a_up, rw_k_k, rw_k_a,
                                rw_r_k, rw_ln_g, rw_ln_b)
    y_rw = y_rw * jax.nn.silu(rw_gate)
    g_sb, g_ssd, g_rw = _split(jax.nn.sigmoid(gate_cols), [D_MODEL] * N_BRANCH)
    merged = g_sb * (y_sb @ w_out_sb) + g_ssd * (y_ssd @ w_out_ssd) + g_rw * (y_rw @ w_out_rw)
    return x + merged @ w_o

def third_inputs(seed: int = 0) -> dict:
    key = jax.random.key(seed)
    ks = jax.random.split(key, 24)
    f32 = jnp.float32
    nrm = lambda k, shp, sc: jax.random.normal(k, shp, f32) * sc
    dt0 = jnp.exp(jax.random.uniform(ks[5], (DEPTH, SSD_HEADS), f32, np.log(1e-3), np.log(1e-1)))
    return {
        "x": nrm(ks[0], (BATCH, SEQ, D_MODEL), 1.0),
        "norm_g": 1.0 + nrm(ks[1], (DEPTH, D_MODEL), 0.02),
        "w_in": nrm(ks[2], (DEPTH, D_MODEL, N_IN_3), D_MODEL ** -0.5),
        "conv_w": nrm(ks[3], (DEPTH, SSD_CONV, SSD_CONV_CH), SSD_CONV ** -0.5),
        "conv_b": nrm(ks[4], (DEPTH, SSD_CONV_CH), 0.02),
        "dt_bias": dt0 + jnp.log(-jnp.expm1(-dt0)),
        "a_log": jnp.log(jax.random.uniform(ks[6], (DEPTH, SSD_HEADS), f32, 1.0, 16.0)),
        "d_skip": 1.0 + nrm(ks[7], (DEPTH, SSD_HEADS), 0.02),
        "ssd_norm_g": 1.0 + nrm(ks[8], (DEPTH, SSD_WIDTH), 0.02),
        "rw_mu": jax.random.uniform(ks[9], (DEPTH, RW_COLS), f32, 0.0, 1.0),
        "rw_w0": jax.random.uniform(ks[10], (DEPTH, RW_WIDTH), f32, -6.0, -1.0),
        "rw_w_up": nrm(ks[11], (DEPTH, RW_DECAY_RANK, RW_WIDTH), 0.1),
        "rw_a0": nrm(ks[12], (DEPTH, RW_WIDTH), 0.1),
        "rw_a_up": nrm(ks[13], (DEPTH, RW_ICLR_RANK, RW_WIDTH), 0.1),
        "rw_k_k": 0.85 + nrm(ks[14], (DEPTH, RW_WIDTH), 0.02),
        "rw_k_a": 1.0 + nrm(ks[15], (DEPTH, RW_WIDTH), 0.02),
        "rw_r_k": nrm(ks[16], (DEPTH, RW_HEADS, RW_HEAD_DIM), 0.1),
        "rw_ln_g": 1.0 + nrm(ks[17], (DEPTH, RW_WIDTH), 0.02),
        "rw_ln_b": nrm(ks[18], (DEPTH, RW_WIDTH), 0.02),
        "w_out_sb": nrm(ks[19], (DEPTH, SB_WIDTH, D_MODEL), SB_WIDTH ** -0.5),
        "w_out_ssd": nrm(ks[20], (DEPTH, SSD_WIDTH, D_MODEL), SSD_WIDTH ** -0.5),
        "w_out_rw": nrm(ks[21], (DEPTH, RW_WIDTH, D_MODEL), RW_WIDTH ** -0.5),
        "w_o": nrm(ks[22], (DEPTH, D_MODEL, D_MODEL), D_MODEL ** -0.5),
        "final_g": 1.0 + nrm(ks[23], (D_MODEL,), 0.02),
    }

def third_block(x, norm_g, w_in, conv_w, conv_b, dt_bias, a_log, d_skip, ssd_norm_g,
              rw_mu, rw_w0, rw_w_up, rw_a0, rw_a_up, rw_k_k, rw_k_a, rw_r_k, rw_ln_g, rw_ln_b,
              w_out_sb, w_out_ssd, w_out_rw, w_o, final_g):
    for i in range(DEPTH):
        x = hybrid_layer(x, norm_g[i], w_in[i], conv_w[i], conv_b[i], dt_bias[i], a_log[i], d_skip[i],
                         ssd_norm_g[i], rw_mu[i], rw_w0[i], rw_w_up[i], rw_a0[i], rw_a_up[i], rw_k_k[i],
                         rw_k_a[i], rw_r_k[i], rw_ln_g[i], rw_ln_b[i], w_out_sb[i], w_out_ssd[i],
                         w_out_rw[i], w_o[i])
    return rms_norm(x, final_g)


_first_inputs_3 = third_inputs


def third_inputs(seed=0):
    import zlib

    import numpy as np

    out = dict(_first_inputs_3(seed))
    spreads = {}
    factors = {'norm_g': 2.904,
     'conv_b': 40.76,
     'd_skip': 64.0,
     'ssd_norm_g': 53.968,
     'rw_w_up': 6.82,
     'rw_a0': 6.952,
     'rw_k_k': 64.0,
     'rw_k_a': 8.0,
     'rw_ln_g': 64.0,
     'rw_ln_b': 64.0,
     'final_g': 8.442}
    for name, (base, spread) in spreads.items():
        noise = np.random.default_rng([zlib.crc32(name.encode()), seed]).standard_normal(out[name].shape)
        drawn = base * np.exp(spread * noise) if base else spread * noise
        out[name] = __import__('jax').numpy.asarray(drawn.astype(out[name].dtype))
    for name, factor in factors.items():
        out[name] = (out[name] * factor).astype(out[name].dtype)
    return out


_narrow_inputs_3 = third_inputs


def third_inputs(seed=0):

    out = dict(_narrow_inputs_3(seed))
    wider = {'d_skip': 12.0,
     'ssd_norm_g': 8.26,
     'rw_k_k': 11.72,
     'rw_ln_g': 4.29,
     'rw_ln_b': 4.36,
     'final_g': 3.27}
    for name, times in wider.items():
        mean = out[name].mean()
        out[name] = (mean + times * (out[name] - mean)).astype(out[name].dtype)
    return out


def setup_inputs(seed=0):
    out = dict(first_inputs(seed))
    for name, value in second_inputs(seed + 1).items():
        if name != "x":
            out[name + "_2"] = value
    for name, value in third_inputs(seed + 2).items():
        if name != "x":
            out[name + "_3"] = value
    return out


def reference(
    x, norm_w, w_in, b_in, hg_lb_logits, hg_norm_w, gla_w_a2, gla_b_a2, gla_norm_w, ml_conv_w,
    ml_conv_b, ml_norm_w, w_out, final_norm_w, norm_gain_2, w_in_2, conv_dw_w_2, conv_dw_b_2,
    conv_ln_g_2, conv_ln_b_2, w_conv_proj_2, ret_gn_g_2, w_ret_proj_2, w_out_2, final_gain_2,
    norm_g_3, w_in_3, conv_w_3, conv_b_3, dt_bias_3, a_log_3, d_skip_3, ssd_norm_g_3, rw_mu_3,
    rw_w0_3, rw_w_up_3, rw_a0_3, rw_a_up_3, rw_k_k_3, rw_k_a_3, rw_r_k_3, rw_ln_g_3, rw_ln_b_3,
    w_out_sb_3, w_out_ssd_3, w_out_rw_3, w_o_3, final_g_3,
):
    x = first_block(
        x, norm_w, w_in, b_in, hg_lb_logits, hg_norm_w, gla_w_a2, gla_b_a2, gla_norm_w,
        ml_conv_w, ml_conv_b, ml_norm_w, w_out, final_norm_w,
    )
    x = second_block(
        x, norm_gain_2, w_in_2, conv_dw_w_2, conv_dw_b_2, conv_ln_g_2, conv_ln_b_2,
        w_conv_proj_2, ret_gn_g_2, w_ret_proj_2, w_out_2, final_gain_2,
    )
    return third_block(
        x, norm_g_3, w_in_3, conv_w_3, conv_b_3, dt_bias_3, a_log_3, d_skip_3, ssd_norm_g_3,
        rw_mu_3, rw_w0_3, rw_w_up_3, rw_a0_3, rw_a_up_3, rw_k_k_3, rw_k_a_3, rw_r_k_3,
        rw_ln_g_3, rw_ln_b_3, w_out_sb_3, w_out_ssd_3, w_out_rw_3, w_o_3, final_g_3,
    )


_drawn_inputs = setup_inputs


def setup_inputs(seed=0):
    import zlib

    import numpy as np

    out = dict(_drawn_inputs(seed))
    spreads = {}
    factors = {}
    for name, (base, spread) in spreads.items():
        noise = np.random.default_rng([zlib.crc32(name.encode()), seed]).standard_normal(out[name].shape)
        drawn = base * np.exp(spread * noise) if base else spread * noise
        out[name] = jnp.asarray(drawn.astype(out[name].dtype))
    for name, factor in factors.items():
        out[name] = (out[name] * factor).astype(out[name].dtype)
    return out
```

```python
from contextlib import ExitStack

import numpy as np

import concourse.bass as bass
from concourse import mybir
from concourse.alu_op_type import AluOpType as ALU

ACT = mybir.ActivationFunctionType
F32 = mybir.dt.float32
U32 = mybir.dt.uint32

P = 128
T = 1024
D = 1024
KD = D // P
C = 128
NCH = T // C
NORM_EPS = 1e-6
LN_EPS = 1e-5
GN_EPS = 64e-5


def segments(sizes):
    at, out = 0, {}
    for name, n in sizes:
        out[name] = (at, at + n)
        at += n
    return out


class Chain:

    def __init__(self, eng, sem, base=0):
        self.eng, self.sem, self.base, self.k = eng, sem, base, 0

    def __call__(self, ins):
        self.k += 1
        ins.then_inc(self.sem, 1)
        self.eng.wait_ge(self.sem, self.base + self.k)

    def ends(self, per):
        assert self.k == per, (self.k, per)


def wait_alone(eng, sem, value, passed):
    eng.wait_ge(sem, value)
    eng.sem_inc(passed, 1)


def per_chunk(mat):
    return mat.unsqueeze(1).to_broadcast([P, NCH, C])


def bits(mask):
    return per_chunk(mask.bitcast(U32))


def chunks(ap, n=NCH):
    return ap.rearrange("p (c t) -> p c t", c=n)


class Stage:

    ended = []

    def __init__(self, nc, name):
        self.nc, self.name, self.ctx, self.sems = nc, name, ExitStack(), []

    def __enter__(self):
        self.ctx.__enter__()
        return self

    def __exit__(self, *a):
        self.ctx.__exit__(*a)
        if self.sems:
            for s in Stage.ended:
                self.nc.release_semaphore(s)
            Stage.ended = self.sems

    def sb(self, name, shape, dt=F32):
        return self.ctx.enter_context(self.nc.sbuf_tensor(f"{self.name}_{name}", shape, dt))

    def sem(self, name):
        self.sems.append(self.nc.alloc_semaphore(f"{self.name}_{name}"))
        return self.sems[-1]

    def block(self):
        block = self.ctx.enter_context(self.nc.Block())

        @block.gpsimd
        def _(pool):
            for s in Stage.ended:
                pool.sem_clear(s)

        return block


class Core:
    pass


def pair(core, n):
    return core.ps[:, n * T:(n + 1) * T]


def project_half(pe, out, w, h, half, m=P, c0=0, nk=KD):
    t = slice(half * 512, half * 512 + 512)
    for k in range(nk):
        ins = pe.matmul(out[0:m, t], w[:, k * P + c0:k * P + c0 + m], h[:, k, t], start=(k == 0), stop=(k == nk - 1))
    return ins


def project_features(pe, out, w, h, m=P, c0=0, nk=KD):
    for half in range(2):
        ins = project_half(pe, out, w, h, half, m, c0, nk)
    return ins


def project_chunk(pe, out, w, h, c, ones=None, bias=None, nk=KD):
    o = out[:, c * C:c * C + P]
    for k in range(nk):
        ins = pe.matmul(o, h[:, k, c * C:c * C + C], w[:, k * P:k * P + P],
                        start=(k == 0), stop=(k == nk - 1 and bias is None))
    if bias is not None:
        ins = pe.matmul(o, ones[0:1, :], bias, start=False, stop=True)
    return ins


def project_tokens(pe, out, w, h, ones=None, bias=None, nk=KD):
    for c in range(NCH):
        ins = project_chunk(pe, out, w, h, c, ones, bias, nk)
    return ins


def load_tiles(sp, core, st, wt, slots, loaded, proj_done, first, ntile, units):
    for t in range(ntile):
        sp.dma_start(slots[:, t, :], wt[(first + t) * P:(first + t + 1) * P, :]).then_inc(loaded[t], 16)
    if units > 1:
        with sp.Fori(1, units) as u:
            for t in range(ntile):
                at = sp.snap(u * (ntile * P) + (first + t) * P)
                sp.wait_ge(proj_done, u * ntile + (t + 1 - ntile))
                sp.dma_start(slots[:, t, :], wt[bass.ds(at, P), :]).then_inc(loaded[t], 16)


class Filler:

    def __init__(self, core, st, name, pair_n, wt, first, park, park_first, kinds, ring=2):
        self.core, self.wt, self.first, self.park, self.park_first = core, wt, first, park, park_first
        self.kinds, self.n, self.ring, self.out = kinds, len(kinds), ring, pair(core, pair_n)
        assert self.n % ring == 0
        self.w, self.kept_sb = st.sb(name + "_w", [P, ring, D]), st.sb(name + "_out", [P, ring, T])
        self.loaded = [st.sem(f"{name}_loaded{s}") for s in range(ring)]
        self.stored = [st.sem(f"{name}_stored{s}") for s in range(ring)]
        self.done, self.kept = st.sem(name + "_done"), st.sem(name + "_kept")

    def load(self, sp, u, head=False):
        for i in range(self.n):
            at = (self.first + i) * P if head else sp.snap(u * (self.n * P) + (self.first + i) * P)
            if not head or i >= self.ring:
                sp.wait_ge(self.done, u * self.n + (i + 1 - self.ring))
            src = self.wt[at:at + P, :] if head else self.wt[bass.ds(at, P), :]
            sp.dma_start(self.w[:, i % self.ring, :], src).then_inc(self.loaded[i % self.ring], 16)

    def multiply(self, pe, u, i, halves=(0, 1)):
        s, (layout, _, bias) = i % self.ring, self.kinds[i]
        w, h = self.w[:, s, :], self.core.hT
        if 0 in halves:
            pe.wait_ge(self.loaded[s], u * (16 * self.n // self.ring) + 16 * (i // self.ring + 1))
            pe.wait_ge(self.kept, u * self.n + (i + 1))
        for half in halves:
            if layout == "features":
                ins = project_half(pe, self.out, w, h, half)
            else:
                row = self.core.brow[0:1, bass.ds(u * P + bias, P)]
                for c in range(half * NCH // 2, (half + 1) * NCH // 2):
                    ins = project_chunk(pe, self.out, w, h, c, self.core.ones, row)
        if 1 in halves:
            ins.then_inc(self.done, 1)

    def keep(self, act, u, i):
        s, (layout, func, bias) = i % self.ring, self.kinds[i]
        act.wait_ge(self.done, u * self.n + (i + 1))
        if i >= self.ring:
            act.wait_ge(self.stored[s], u * (16 * self.n // self.ring) + 16 * (i // self.ring))
        kw = {"bias": self.core.col_at(bias, u)} if layout == "features" and bias else {}
        act.activation(self.kept_sb[:, s, :], self.out, func, **kw).then_inc(self.kept, 1)
        at = act.snap(u * (self.n * P) + (self.park_first + i) * P)
        act.wait_ge(self.kept, u * self.n + (i + 2))
        act.dma_start(self.park[bass.ds(at, P), :], self.kept_sb[:, s, :]).then_inc(self.stored[s], 16)

    def begin(self, act):
        act.sem_inc(self.kept, 1)

    def end(self, act, u):
        for s in range(self.ring):
            act.wait_ge(self.stored[s], u * (16 * self.n // self.ring) + 16 * (self.n // self.ring))


def load_input(core, x_dram):
    nc = core.nc
    with Stage(nc, "ldx") as st:
        xin = st.sb("xin", [P, 2, D])
        loaded = [st.sem("x_loaded0"), st.sem("x_loaded1")]
        turned, kept = st.sem("turned"), st.sem("kept")
        block = st.block()

        @block.sync
        def _(sp):
            for c in range(NCH):
                if c >= 2:
                    sp.wait_ge(turned, c - 1)
                sp.dma_start(xin[:, c % 2, :], x_dram[c * P:(c + 1) * P, :]).then_inc(loaded[c % 2], 16)

        @block.tensor
        def _(pe):
            for c in range(NCH):
                pe.wait_ge(loaded[c % 2], 16 * (c // 2 + 1))
                if c >= 2:
                    pe.wait_ge(kept, c - 1)
                for k in range(KD):
                    ins = pe.transpose(pair(core, c % 2)[:, k * P:(k + 1) * P],
                                       xin[:, c % 2, k * P:(k + 1) * P], core.ident[:, :])
                ins.then_inc(turned, 1)

        @block.vector
        def _(dve):
            for c in range(NCH):
                dve.wait_ge(turned, c + 1)
                dve.tensor_copy(core.xT[:, :, c * C:(c + 1) * C], chunks(pair(core, c % 2))).then_inc(kept, 1)


def rms_norm(core, name, src, gain, dst, eps=NORM_EPS):
    with Stage(core.nc, name) as st:
        sq = st.sb("sq", [P, 2, T])
        rstd = st.sb("rstd", [P, T])
        squared, summed, rooted, normed = (st.sem(n) for n in ("squared", "summed", "rooted", "normed"))
        block = st.block()

        @block.scalar
        def _(act):
            for k in range(KD):
                if k >= 2:
                    act.wait_ge(summed, k - 1)
                act.activation(sq[:, k % 2, :], src[:, k, :], ACT.Square).then_inc(squared, 1)
            act.wait_ge(summed, KD)
            act.activation(rstd[:, :], pair(core, 0), ACT.Sqrt, bias=core.const(eps)).then_inc(rooted, 1)

        @block.tensor
        def _(pe):
            for k in range(KD):
                pe.wait_ge(squared, k + 1)
                for half in range(2):
                    ins = pe.matmul(pair(core, 0)[:, half * 512:half * 512 + 512], core.mean_d[:, :],
                                    sq[:, k % 2, half * 512:half * 512 + 512],
                                    start=(k == 0), stop=(k == KD - 1))
                ins.then_inc(summed, 1)

        @block.vector
        def _(dve):
            dve.wait_ge(rooted, 1)
            step = Chain(dve, normed)
            step(dve.reciprocal(rstd[:, :], rstd[:, :]))
            for k in range(KD):
                dve.scalar_tensor_tensor(dst[:, k, :], src[:, k, :], core.col(gain, k), rstd[:, :],
                                         ALU.mult, ALU.mult)


def out_projection(core, name, y, nk, wt, dst, gate=None):
    with Stage(core.nc, name) as st:
        w = st.sb("w", [P, 2, nk * P])
        loaded = [st.sem("w_loaded0"), st.sem("w_loaded1")]
        done, added = st.sem("projected"), st.sem("added")
        block = st.block()

        @block.sync
        def _(sp):
            for s in range(2):
                sp.dma_start(w[:, s, :], wt[s * P:(s + 1) * P, :]).then_inc(loaded[s], 16)
            with sp.Fori(1, KD // 2) as i:
                for s in range(2):
                    sp.wait_ge(done, 2 * i + (s - 1))
                    sp.dma_start(w[:, s, :], wt[bass.ds(i * (2 * P) + s * P, P), :]).then_inc(loaded[s], 16)

        @block.tensor
        def _(pe):
            with pe.Fori(0, KD // 2) as i:
                for s in range(2):
                    pe.wait_ge(loaded[s], 16 * i + 16)
                    pe.wait_ge(added, 2 * i + (s + 1))
                    project_features(pe, pair(core, s), w[:, s, :], y, nk=nk).then_inc(done, 1)

        @block.vector
        def _(dve):
            dve.sem_inc(added, 2)
            with dve.Fori(0, KD // 2) as i:
                for s in range(2):
                    dve.wait_ge(done, 2 * i + (s + 1))
                    o = dst[:, bass.ds(2 * i + s, 1), :].rearrange("p a t -> p (a t)")
                    dve.tensor_tensor(o, pair(core, s), o, ALU.add).then_inc(added, 1)


def store_output(core, src, out_dram):
    with Stage(core.nc, "out") as st:
        rows = st.sb("rows", [P, 2, D])
        stored = [st.sem("stored0"), st.sem("stored1")]
        turned, copied = st.sem("turned"), st.sem("copied")
        block = st.block()

        @block.tensor
        def _(pe):
            for c in range(NCH):
                if c >= 2:
                    pe.wait_ge(copied, c - 1)
                for k in range(KD):
                    ins = pe.transpose(pair(core, c % 2)[:, k * P:(k + 1) * P],
                                       src[:, k, c * C:(c + 1) * C], core.ident[:, :])
                ins.then_inc(turned, 1)

        @block.vector
        def _(dve):
            for c in range(NCH):
                dve.wait_ge(turned, c + 1)
                if c >= 2:
                    dve.wait_ge(stored[c % 2], 16 * (c // 2))
                dve.tensor_copy(rows[:, c % 2, :], pair(core, c % 2)).then_inc(copied, 1)

        @block.sync
        def _(sp):
            for c in range(NCH):
                sp.wait_ge(copied, c + 1)
                sp.dma_start(out_dram[c * P:(c + 1) * P, :], rows[:, c % 2, :]).then_inc(stored[c % 2], 16)
            for s in range(2):
                sp.wait_ge(stored[s], 16 * (NCH // 2))


LEVELS = 7


def level_views(ap, lvl):
    v = ap.rearrange("p (n two m) -> p n two m", two=2, m=1 << lvl)
    return v[:, :, 0, :], v[:, :, 1, :]


def flat(ap):
    return ap.rearrange("p a t -> p (a t)")


def gla_gates(core, wt, tile, w_a2, gl):
    with Stage(core.nc, "glagate") as st:
        w = st.sb("w", [P, D])
        wa2 = st.sb("wa2", [16, 2 * P])
        aT = st.sb("aT", [16, T])
        mag = st.sb("mag", [P, 2, T])
        w_loaded, a2_loaded, a_done, a_kept, logit_done, mag_ready, softened, dve_step, act_step = (
            st.sem(n) for n in ("w_loaded", "a2_loaded", "a_done", "a_kept", "logit_done", "mag_ready",
                                "softened", "dve_step", "act_step"))
        block = st.block()

        @block.sync
        def _(sp):
            sp.dma_start(w[:, :], wt[tile * P:(tile + 1) * P, :]).then_inc(w_loaded, 16)
            sp.dma_start(wa2[:, :], w_a2).then_inc(a2_loaded, 16)

        @block.tensor
        def _(pe):
            pe.wait_ge(w_loaded, 16)
            project_features(pe, pair(core, 0), w, core.hT, m=16).then_inc(a_done, 1)
            pe.wait_ge(a2_loaded, 16)
            pe.wait_ge(a_kept, 1)
            for n in range(2):
                for half in range(2):
                    ins = pe.matmul(pair(core, 1 + n)[:, half * 512:half * 512 + 512],
                                    wa2[:, n * P:n * P + P], aT[:, half * 512:half * 512 + 512],
                                    start=True, stop=True)
                ins.then_inc(logit_done, 1)

        @block.scalar
        def _(act):
            act.wait_ge(a_done, 1)
            act.activation(aT[:, :], pair(core, 0)[0:16, :], ACT.Identity, bias=core.col("gla_a_b", 0)[0:16, :]) \
                .then_inc(a_kept, 1)
            step = Chain(act, act_step)
            for n in range(2):
                act.wait_ge(mag_ready, n + 1)
                step(act.activation(mag[:, n, :], mag[:, n, :], ACT.Exp, scale=-1.0))
                act.activation(mag[:, n, :], mag[:, n, :], ACT.Ln, bias=1.0).then_inc(softened, 1)

        @block.vector
        def _(dve):
            step = Chain(dve, dve_step)
            for n in range(2):
                dve.wait_ge(logit_done, n + 1)
                b = core.col("gla_b_a2", n)
                dve.tensor_scalar(gl[:, n, :], pair(core, 1 + n), b, 0.0, ALU.add, ALU.min)
                step(dve.tensor_scalar(mag[:, n, :], pair(core, 1 + n), b, None, ALU.add))
                dve.scalar_tensor_tensor(mag[:, n, :], mag[:, n, :], -1.0, mag[:, n, :], ALU.mult, ALU.max).then_inc(mag_ready, 1)
            for n in range(2):
                dve.wait_ge(softened, n + 1)
                step(dve.tensor_tensor(gl[:, n, :], gl[:, n, :], mag[:, n, :], ALU.subtract))
                step(dve.tensor_scalar(gl[:, n, :], gl[:, n, :], 1.0 / 16.0, None, ALU.mult))


def hg_lower_bound(core):
    with Stage(core.nc, "lb") as st:
        e, one = st.sb("e", [P, 4]), st.sb("one", [P, 4])
        dve_step, exped, shifted = st.sem("dve_step"), st.sem("exped"), st.sem("shifted")
        block = st.block()
        logits = core.cols[:, core.index["hg_lb"]:core.index["hg_lb"] + 4]
        lb = core.cols[:, core.index["lb"]:core.index["lb"] + 4]
        om = core.cols[:, core.index["one_minus_lb"]:core.index["one_minus_lb"] + 4]

        @block.vector
        def _(dve):
            step = Chain(dve, dve_step)
            dve.tensor_tensor(e[:, :], logits, logits, ALU.subtract).then_inc(shifted, 1)
            dve.wait_ge(exped, 1)
            step(dve.reciprocal(one[:, :], e[:, :]))
            step(dve.tensor_tensor(e[:, :], e[:, :], one[:, :], ALU.mult))
            step(dve.tensor_tensor(lb, e[:, :], e[:, :], ALU.subtract))
            step(dve.tensor_scalar(om, lb, -1.0, 1.0, ALU.mult, ALU.add))

        @block.scalar
        def _(act):
            act.wait_ge(shifted, 1)
            act.activation(e[:, :], e[:, :], ACT.Exp).then_inc(exped, 1)


def vector_decay_branch(core, name, nsub, units, wt, first, col_q, col_k, col_z, brow, wcol, y, gl=None):
    hg = nsub == 1
    order = ["f", "q", "v0", "z0"] if hg else ["q", "k", "v0", "v1", "z0", "z1"]
    nt = len(order)
    NE = LEVELS + 1
    with Stage(core.nc, name) as st:
        w = st.sb("w", [P, nt, D])
        loaded = [st.sem(f"w_loaded{t}") for t in range(nt)]
        q, k, b = st.sb("q", [P, T]), st.sb("k", [P, T]), st.sb("b", [P, T])
        v = st.sb("v", [P, NCH, nsub, P])
        ex = st.sb("ex", [P, 2, T])
        qs, ks = st.sb("qs", [P, 2, T]), st.sb("ks", [P, 2, T])
        att = st.sb("att", [P, nsub, T])
        state = st.sb("state", [P, NCH, nsub * P])
        ktok, sq = qs[:, 0, :], qs[:, 1, :]
        S = {n: st.sem(n) for n in (
            "proj_done", "evacuated", "unit_free", "qk_ready", "gate_ready", "log_ready", "expo_ready", "expd",
            "factors", "level_done", "att_kept", "keys_turned", "keys_kept", "update_done", "state_ready",
            "out_done", "squared", "mean_done", "rooted", "dve_step", "passed")}
        A, B = [pair(core, 0), pair(core, 1)], [pair(core, 2), pair(core, 3)]
        Bflat = core.ps[:, 4 * 512:8 * 512]

        def rows(sub):
            return slice(sub * 64, sub * 64 + 64) if nsub == 2 else slice(0, P)

        block = st.block()

        @block.sync
        def _(sp):
            load_tiles(sp, core, st, wt, w, loaded, S["proj_done"], first, nt, units)

        @block.tensor
        def _(pe):
            with pe.Fori(0, units) as u:
                pe.wait_ge(S["unit_free"], u + 1)
                for t, what in enumerate(order):
                    pe.wait_ge(loaded[t], 16 * u + 16)
                    if t >= 2:
                        pe.wait_ge(S["evacuated"], u * nt + (t - 1))
                    if what[0] == "v":
                        bias = core.brow[0:1, bass.ds(u * (nsub * P) + (brow + int(what[1]) * P), P)]
                        ins = project_tokens(pe, B[t % 2], w[:, t, :], core.hT, core.ones, bias)
                    else:
                        ins = project_features(pe, B[t % 2], w[:, t, :], core.hT)
                    ins.then_inc(S["proj_done"], 1)
                pe.wait_ge(S["qk_ready"], u + 1)
                for l in range(-1, LEVELS):
                    if l >= 0:
                        pe.wait_ge(S["factors"], u * NE + (l + 1))
                        if not hg:
                            pe.wait_ge(S["att_kept"], u * (LEVELS + 1) + (l + 1))
                        elif l >= 1:
                            pe.wait_ge(S["att_kept"], u * (LEVELS + 1) + l)
                    lhs, rhs = (k[:, :], q[:, :]) if l < 0 else (ks[:, l % 2, :], qs[:, l % 2, :])
                    for sub in range(nsub):
                        o = A[(l + 1) % 2] if hg else A[sub]
                        for c in range(NCH):
                            cs = slice(c * C, c * C + C)
                            ins = pe.matmul(o[:, cs], lhs[rows(sub), cs], rhs[rows(sub), cs], start=True, stop=True)
                    ins.then_inc(S["level_done"], 1)
                pe.wait_ge(S["factors"], u * NE + NE)
                pe.wait_ge(S["evacuated"], u * nt + nt)
                for c in range(NCH):
                    ins = pe.transpose(B[0][:, c * C:c * C + C], k[:, c * C:c * C + C], core.ident[:, :])
                ins.then_inc(S["keys_turned"], 1)
                pe.wait_ge(S["keys_kept"], u + 1)
                for c in range(NCH - 1):
                    ins = pe.matmul(Bflat[:, c * nsub * P:(c + 1) * nsub * P], ktok[:, c * C:c * C + C],
                                    v[:, c, :, :].rearrange("p n d -> p (n d)"), start=True, stop=True)
                ins.then_inc(S["update_done"], 1)
                pe.wait_ge(S["state_ready"], u + 1)
                pe.wait_ge(S["att_kept"], u * (LEVELS + 1) + (LEVELS + 1))
                for sub in range(nsub):
                    for c in range(NCH):
                        cs = slice(c * C, c * C + C)
                        ins = pe.matmul(A[sub][:, cs], v[:, c, sub, :], att[:, sub, cs], start=True, stop=(c == 0))
                        if c:
                            ins = pe.matmul(A[sub][:, cs], state[rows(sub), c, sub * P:sub * P + P],
                                            q[rows(sub), cs], start=False, stop=True)
                    ins.then_inc(S["out_done"], 1)
                for sub in range(nsub):
                    pe.wait_ge(S["squared"], u * nsub + (sub + 1))
                    for half in range(2):
                        ins = pe.matmul(B[sub][:, half * 512:half * 512 + 512], core.mean_p[:, :],
                                        sq[:, half * 512:half * 512 + 512], start=True, stop=True)
                    ins.then_inc(S["mean_done"], 1)

        @block.scalar
        def _(act):
            with act.Fori(0, units) as u:
                for t, what in enumerate(order):
                    act.wait_ge(S["proj_done"], u * nt + (t + 1))
                    src = B[t % 2]
                    if what == "f":
                        ins = act.activation(b[:, :], src, ACT.Sigmoid, bias=core.col_at(col_k, u))
                    elif what == "q":
                        ins = act.activation(q[:, :], src, ACT.Silu if hg else ACT.Identity, bias=core.col_at(col_q, u))
                    elif what == "k":
                        ins = act.activation(k[:, :], src, ACT.Identity, bias=core.col_at(col_k, u))
                    elif what[0] == "v":
                        ins = act.activation(v[:, :, int(what[1]), :], chunks(src), ACT.Copy)
                    else:
                        n = int(what[1])
                        ins = act.activation(flat(y[:, bass.ds(u * nsub + n, 1), :]), src, ACT.Silu,
                                             bias=core.col_at(col_z, u * nsub + n))
                    ins.then_inc(S["evacuated"], 1)
                if hg:
                    act.wait_ge(S["gate_ready"], u + 1)
                    act.activation(b[:, :], b[:, :], ACT.Ln).then_inc(S["log_ready"], 1)
                for e in range(LEVELS):
                    act.wait_ge(S["expo_ready"], u * NE + (e + 1))
                    act.activation(ex[:, e % 2, :], ex[:, e % 2, :], ACT.Exp).then_inc(S["expd"], 1)
                act.wait_ge(S["expo_ready"], u * NE + NE)
                act.activation(ex[:, 1, :], b[:, :], ACT.Exp)
                act.activation(ex[:, 0, :], ex[:, 0, :], ACT.Exp).then_inc(S["expd"], 1)
                act.wait_ge(S["keys_turned"], u + 1)
                act.activation(ktok, B[0], ACT.Copy).then_inc(S["keys_kept"], 1)
                for sub in range(nsub):
                    act.wait_ge(S["out_done"], u * nsub + (sub + 1))
                    if sub:
                        act.wait_ge(S["mean_done"], u * nsub + sub)
                    act.activation(sq, A[sub], ACT.Square).then_inc(S["squared"], 1)
                for sub in range(nsub):
                    act.wait_ge(S["mean_done"], u * nsub + (sub + 1))
                    act.activation(ks[:, sub, :], B[sub], ACT.Sqrt, bias=core.const(NORM_EPS)).then_inc(S["rooted"], 1)

        @block.vector
        def _(dve):
            per = (2 if hg else 1) + (NCH - 3) + 1 + 3 * nsub - 1
            dve.memset(qs[:, :, :], 0.0)
            dve.memset(ks[:, :, :], 0.0).then_inc(S["unit_free"], 1)

            def exponents(l):
                be, bo = level_views(b[:, :], l)
                ee, eo = level_views(ex[:, l % 2, :], l)
                m = 1 << l
                ref = be[:, :, m - 1:m].to_broadcast([P, T // (2 * m), m])
                dve.tensor_tensor(ee, ref, be, ALU.subtract)
                dve.tensor_tensor(eo, bo, ref, ALU.subtract).then_inc(S["expo_ready"], 1)

            def keep(n, u):
                wait_alone(dve, S["level_done"], u * (LEVELS + 1) + (n + 1), S["passed"])
                for sub in range(nsub):
                    src = chunks(A[n % 2] if hg else A[sub])
                    dst = chunks(att[:, sub, :])
                    if n == 0:
                        ins = dve.tensor_tensor(dst, src, per_chunk(core.ident[:, :]), ALU.mult)
                    else:
                        ins = dve.copy_predicated(dst, bits(core.level_mask[:, n - 1, :]), src)
                ins.then_inc(S["att_kept"], 1)
                dve.wait_ge(S["att_kept"], u * (LEVELS + 1) + (n + 1))

            with dve.Fori(0, units) as u:
                step = Chain(dve, S["dve_step"], u * per)
                if hg:
                    dve.wait_ge(S["evacuated"], u * nt + 2)
                    step(dve.tensor_scalar(b[:, :], b[:, :], core.col_at("one_minus_lb", u), core.col_at("lb", u),
                                           ALU.mult, ALU.add))
                    dve.tensor_scalar(k[:, :], b[:, :], -1.0, 1.0, ALU.mult, ALU.add).then_inc(S["gate_ready"], 1)
                    dve.wait_ge(S["gate_ready"], u + 1)
                    dve.sem_inc(S["qk_ready"], 1)
                    dve.wait_ge(S["log_ready"], u + 1)
                    decay = b[:, :]
                else:
                    dve.wait_ge(S["evacuated"], u * nt + 2)
                    dve.tensor_scalar(q[:, :], q[:, :], 64 ** -0.5, None, ALU.mult).then_inc(S["qk_ready"], 1)
                    dve.wait_ge(S["qk_ready"], u + 1)
                    decay = flat(gl[:, bass.ds(u, 1), :])
                for c in range(NCH):
                    cs = slice(c * C, c * C + C)
                    ins = dve.tensor_tensor_scan(b[:, cs], decay[:, cs], decay[:, cs], 0.0, ALU.add, ALU.bypass)
                step(ins)
                exponents(0)
                for l in range(LEVELS):
                    if l + 1 < LEVELS:
                        exponents(l + 1)
                    dve.wait_ge(S["expd"], u * NE + (l + 1))
                    ee, eo = level_views(ex[:, l % 2, :], l)
                    dve.tensor_tensor(level_views(qs[:, l % 2, :], l)[1], level_views(q[:, :], l)[1], eo, ALU.mult)
                    dve.tensor_tensor(level_views(ks[:, l % 2, :], l)[0], level_views(k[:, :], l)[0], ee, ALU.mult) \
                        .then_inc(S["factors"], 1)
                    keep(l, u)
                keep(LEVELS, u)
                last = chunks(b[:, :])[:, :, C - 1:C].to_broadcast([P, NCH, C])
                dve.tensor_tensor(chunks(ex[:, 0, :]), last, chunks(b[:, :]), ALU.subtract).then_inc(S["expo_ready"], 1)
                dve.wait_ge(S["expd"], u * NE + NE)
                dve.tensor_tensor(q[:, :], q[:, :], ex[:, 1, :], ALU.mult)
                dve.tensor_tensor(k[:, :], k[:, :], ex[:, 0, :], ALU.mult).then_inc(S["factors"], 1)
                dve.wait_ge(S["update_done"], u + 1)
                step(dve.tensor_copy(state[:, 1, :], Bflat[:, 0:nsub * P]))
                for c in range(1, NCH - 1):
                    ins = dve.scalar_tensor_tensor(state[:, c + 1, :], state[:, c, :],
                                                   ex[:, 1, c * C + C - 1:c * C + C],
                                                   Bflat[:, c * nsub * P:(c + 1) * nsub * P], ALU.mult, ALU.add)
                    if c + 1 < NCH - 1:
                        step(ins)
                ins.then_inc(S["state_ready"], 1)
                for sub in range(nsub):
                    dve.wait_ge(S["rooted"], u * nsub + (sub + 1))
                    yo = flat(y[:, bass.ds(u * nsub + sub, 1), :])
                    step(dve.reciprocal(ks[:, sub, :], ks[:, sub, :]))
                    step(dve.scalar_tensor_tensor(ks[:, sub, :], A[sub], core.col_at(wcol, u * nsub + sub),
                                                  ks[:, sub, :], ALU.mult, ALU.mult))
                    ins = dve.tensor_tensor(yo, yo, ks[:, sub, :], ALU.mult)
                    if sub + 1 < nsub:
                        step(ins)
                ins.then_inc(S["unit_free"], 1)
                step.ends(per)


def ml_gates(core, wt, tile, rows_dram, cols):
    H = 4
    with Stage(core.nc, "mlgate") as st:
        w = st.sb("w", [P, D])
        ip, lf, mag, m, lam, b, ke, eb, em = (st.sb(n, [H, T]) for n in (
            "ip", "lf", "mag", "m", "lam", "b", "ke", "eb", "em"))
        w_loaded, proj_done, mag_ready, softened, b_ready, exped, turned, dve_step, act_step, stored, copied = (
            st.sem(n) for n in ("w_loaded", "proj_done", "mag_ready", "softened", "b_ready", "exped", "turned",
                                "dve_step", "act_step", "stored", "copied"))
        block = st.block()

        @block.sync
        def _(sp):
            sp.dma_start(w[:, :], wt[tile * P:(tile + 1) * P, :]).then_inc(w_loaded, 16)
            sp.wait_ge(exped, 1)
            for n, r in enumerate((b, eb, em)):
                sp.dma_start(rows_dram[n * H:(n + 1) * H, :], r[:, :]).then_inc(stored, 16)
            sp.wait_ge(stored, 48)

        @block.tensor
        def _(pe):
            pe.wait_ge(w_loaded, 16)
            project_features(pe, pair(core, 0), w, core.hT, m=H, c0=0)
            project_features(pe, pair(core, 1), w, core.hT, m=H, c0=H).then_inc(proj_done, 1)
            pe.wait_ge(exped, 1)
            for n, r in enumerate((b, ip, ke)):
                for c in range(NCH):
                    ins = pe.matmul(pair(core, 2)[:, (n * NCH + c) * H:(n * NCH + c + 1) * H],
                                    r[:, c * C:c * C + C], core.ident[0:H, 0:H], start=True, stop=True)
            ins.then_inc(turned, 1)

        @block.vector
        def _(dve):
            step = Chain(dve, dve_step)
            dve.wait_ge(proj_done, 1)
            dve.tensor_scalar(ip[:, :], pair(core, 0)[0:H, :], core.col("ml_i_b", 0)[0:H, :], None, ALU.add)
            bf = core.col("ml_f_b", 0)[0:H, :]
            dve.tensor_scalar(lf[:, :], pair(core, 1)[0:H, :], bf, 0.0, ALU.add, ALU.min)
            step(dve.tensor_scalar(mag[:, :], pair(core, 1)[0:H, :], bf, None, ALU.add))
            dve.scalar_tensor_tensor(mag[:, :], mag[:, :], -1.0, mag[:, :], ALU.mult, ALU.max).then_inc(mag_ready, 1)
            dve.wait_ge(softened, 1)
            step(dve.tensor_tensor(lf[:, :], lf[:, :], mag[:, :], ALU.subtract))
            step(dve.tensor_tensor_scan(m[:, :], lf[:, :], ip[:, :], 0.0, ALU.add, ALU.max))
            step(dve.tensor_tensor(lam[:, :], lf[:, :], m[:, :], ALU.subtract))
            dve.tensor_tensor(lam[:, 1:T], lam[:, 1:T], m[:, 0:T - 1], ALU.add)
            step(dve.tensor_tensor(ip[:, :], ip[:, :], m[:, :], ALU.subtract))
            for c in range(NCH):
                cs = slice(c * C, c * C + C)
                ins = dve.tensor_tensor_scan(b[:, cs], lam[:, cs], lam[:, cs], 0.0, ALU.add, ALU.bypass)
            step(ins)
            last = chunks(b[:, :])[:, :, C - 1:C].to_broadcast([H, NCH, C])
            step(dve.tensor_tensor(chunks(ke[:, :]), last, chunks(b[:, :]), ALU.subtract))
            dve.tensor_tensor(ke[:, :], ke[:, :], ip[:, :], ALU.add).then_inc(b_ready, 1)
            dve.wait_ge(turned, 1)
            step(dve.tensor_copy(cols[:, :], pair(core, 2)[:, 0:3 * NCH * H]))

        @block.scalar
        def _(act):
            step = Chain(act, act_step)
            act.wait_ge(mag_ready, 1)
            step(act.activation(mag[:, :], mag[:, :], ACT.Exp, scale=-1.0))
            act.activation(mag[:, :], mag[:, :], ACT.Ln, bias=1.0).then_inc(softened, 1)
            act.wait_ge(b_ready, 1)
            act.activation(eb[:, :], b[:, :], ACT.Exp)
            act.activation(em[:, :], m[:, :], ACT.Exp, scale=-1.0)
            act.activation(ke[:, :], ke[:, :], ACT.Exp).then_inc(exped, 1)


def mlstm_branch(core, wt, first, rows_dram, cols, y):
    order = ["q", "k", "v0", "v1", "o0", "o1", "z0", "z1"]
    nt, ring, units, nsub, H = len(order), 4, 2, 2, 4
    colv = cols[:, :].rearrange("p (n c h) -> p n c h", n=3, c=NCH)
    with Stage(core.nc, "ml") as st:
        w = st.sb("w", [P, ring, D])
        loaded = [st.sem(f"w_loaded{t}") for t in range(ring)]
        rows_loaded = st.sem("rows_loaded")
        pre = st.sb("pre", [P, 2, 3 + T])
        q, k = st.sb("q", [P, T]), st.sb("k", [P, T])
        v = st.sb("v", [P, NCH, nsub, P])
        og = st.sb("og", [P, nsub, T])
        brep, em = st.sb("brep", [P, nsub, T]), st.sb("em", [P, nsub, T])
        qdec = st.sb("qdec", [P, T])
        att = st.sb("att", [P, nsub, T])
        state = st.sb("state", [P, NCH, nsub * P])
        nstate, nrep = st.sb("nstate", [P, NCH]), st.sb("nrep", [P, NCH, P])
        ktok = pre[:, 0, 0:T]
        S = {n: st.sem(n) for n in (
            "proj_done", "evacuated", "unit_free", "conv_done", "silu_done", "qk_ready", "expo_ready", "expd",
            "prod_done", "att_ready", "keys_turned", "keys_kept", "update_done", "state_ready", "out_done",
            "h_ready", "squared", "mean_done", "rooted", "dve_step")}
        A, B = [pair(core, 0), pair(core, 1)], [pair(core, 2), pair(core, 3)]
        Bflat = core.ps[:, 4 * 512:8 * 512]
        N0 = (NCH - 1) * nsub * P

        def rows(sub):
            return slice(sub * 64, sub * 64 + 64)

        block = st.block()

        @block.sync
        def _(sp):
            def unit(u, head):
                if not head:
                    sp.wait_ge(S["unit_free"], u + 1)
                for t in range(nt):
                    at = (u * (nt * P) + (first + t) * P) if not head else (first + t) * P
                    src = wt[bass.ds(at, P), :] if not head else wt[at:at + P, :]
                    if not head or t >= ring:
                        sp.wait_ge(S["proj_done"], u * nt + (t + 1 - ring))
                    sp.dma_start(w[:, t % ring, :], src).then_inc(loaded[t % ring], 16)
                for sub in range(nsub):
                    def row(n):
                        h = n * H + sub
                        r = rows_dram[bass.ds(u * nsub + h, 1), :] if not head else rows_dram[h:h + 1, :]
                        return r
                    sp.dma_start(brep[:, sub, :], row(0).to_broadcast([P, T])).then_inc(rows_loaded, 16)
                    sp.dma_start(qdec[rows(sub), :], row(1).to_broadcast([64, T])).then_inc(rows_loaded, 16)
                    sp.dma_start(em[:, sub, :], row(2).to_broadcast([P, T])).then_inc(rows_loaded, 16)
            unit(0, True)
            with sp.Fori(1, units) as u:
                unit(u, False)

        @block.tensor
        def _(pe):
            with pe.Fori(0, units) as u:
                pe.wait_ge(S["unit_free"], u + 1)
                for t, what in enumerate(order):
                    pe.wait_ge(loaded[t % ring], u * (16 * nt // ring) + 16 * (t // ring + 1))
                    if t >= 2:
                        pe.wait_ge(S["evacuated"], u * nt + (t - 1))
                    if what[0] == "v":
                        bias = core.brow[0:1, bass.ds(u * (nsub * P) + (1024 + int(what[1]) * P), P)]
                        ins = project_tokens(pe, B[t % 2], w[:, t % ring, :], core.hT, core.ones, bias)
                    else:
                        ins = project_features(pe, B[t % 2], w[:, t % ring, :], core.hT)
                    ins.then_inc(S["proj_done"], 1)
                pe.wait_ge(S["qk_ready"], u + 1)
                for sub in range(nsub):
                    for c in range(NCH):
                        cs = slice(c * C, c * C + C)
                        ins = pe.matmul(A[sub][:, cs], k[rows(sub), cs], q[rows(sub), cs], start=True, stop=True)
                    ins.then_inc(S["prod_done"], 1)
                pe.wait_ge(S["evacuated"], u * nt + nt)
                for c in range(NCH):
                    ins = pe.transpose(B[0][:, c * C:c * C + C], k[:, c * C:c * C + C], core.ident[:, :])
                ins.then_inc(S["keys_turned"], 1)
                pe.wait_ge(S["keys_kept"], u + 1)
                for c in range(NCH - 1):
                    pe.matmul(Bflat[:, c * nsub * P:(c + 1) * nsub * P], ktok[:, c * C:c * C + C],
                              v[:, c, :, :].rearrange("p n d -> p (n d)"), start=True, stop=True)
                    ins = pe.matmul(Bflat[:, N0 + c:N0 + c + 1], ktok[:, c * C:c * C + C], core.ones[:, 0:1],
                                    start=True, stop=True)
                ins.then_inc(S["update_done"], 1)
                pe.wait_ge(S["state_ready"], u + 1)
                pe.wait_ge(S["att_ready"], u * nsub + nsub)
                for sub in range(nsub):
                    for c in range(NCH):
                        cs = slice(c * C, c * C + C)
                        for o, lv, ls in ((A[sub], v[:, c, sub, :], state[rows(sub), c, sub * P:sub * P + P]),
                                          (B[sub], core.ones[:, :], nrep[rows(sub), c, :])):
                            ins = pe.matmul(o[:, cs], lv, att[:, sub, cs], start=True, stop=(c == 0))
                            if c:
                                ins = pe.matmul(o[:, cs], ls, q[rows(sub), cs], start=False, stop=True)
                    ins.then_inc(S["out_done"], 1)
                for sub in range(nsub):
                    pe.wait_ge(S["squared"], u * nsub + (sub + 1))
                    for half in range(2):
                        ins = pe.matmul(B[sub][:, half * 512:half * 512 + 512], core.mean_p[:, :],
                                        pre[:, sub, half * 512:half * 512 + 512], start=True, stop=True)
                    ins.then_inc(S["mean_done"], 1)

        @block.scalar
        def _(act):
            with act.Fori(0, units) as u:
                for t, what in enumerate(order):
                    act.wait_ge(S["proj_done"], u * nt + (t + 1))
                    src = B[t % 2]
                    if what in "qk":
                        n = "qk".index(what)
                        ins = act.activation(pre[:, n, 3:3 + T], src, ACT.Identity, bias=core.col_at("ml_" + what, u))
                    elif what[0] == "v":
                        ins = act.activation(v[:, :, int(what[1]), :], chunks(src), ACT.Copy)
                    else:
                        n = int(what[1])
                        dst = og[:, n, :] if what[0] == "o" else flat(y[:, bass.ds(u * nsub + n, 1), :])
                        ins = act.activation(dst, src, ACT.Sigmoid if what[0] == "o" else ACT.Silu,
                                             bias=core.col_at("ml_" + what[0], u * nsub + n))
                    ins.then_inc(S["evacuated"], 1)
                for n, dst in enumerate((q, k)):
                    act.wait_ge(S["conv_done"], u * 2 + (n + 1))
                    act.activation(dst[:, :], dst[:, :], ACT.Silu, bias=core.col_at("ml_cb", u + 2 * n)) \
                        .then_inc(S["silu_done"], 1)
                for sub in range(nsub):
                    act.wait_ge(S["expo_ready"], u * nsub + (sub + 1))
                    act.activation(att[:, sub, :], att[:, sub, :], ACT.Exp).then_inc(S["expd"], 1)
                for sub in range(nsub):
                    act.wait_ge(S["h_ready"], u * nsub + (sub + 1))
                    act.activation(pre[:, sub, 0:T], og[:, sub, :], ACT.Square).then_inc(S["squared"], 1)
                for sub in range(nsub):
                    act.wait_ge(S["mean_done"], u * nsub + (sub + 1))
                    act.activation(em[:, sub, :], B[sub], ACT.Sqrt, bias=core.const(NORM_EPS)).then_inc(S["rooted"], 1)

        @block.vector
        def _(dve):
            per = 1 + 2 * 3 + 3 * nsub + 1 + (NCH - 1) + 5 * nsub + (3 * nsub - 1)
            dve.sem_inc(S["unit_free"], 1)
            with dve.Fori(0, units) as u:
                step = Chain(dve, S["dve_step"], u * per)
                dve.wait_ge(S["evacuated"], u * nt + 2)
                dve.memset(pre[:, 0, 0:3], 0.0)
                step(dve.memset(pre[:, 1, 0:3], 0.0))
                for n, dst in enumerate((q, k)):
                    step(dve.tensor_scalar(dst[:, :], pre[:, n, 0:T], core.col_at("ml_cw0", u + 2 * n), None, ALU.mult))
                    for j in range(1, 4):
                        ins = dve.scalar_tensor_tensor(dst[:, :], pre[:, n, j:j + T],
                                                       core.col_at(f"ml_cw{j}", u + 2 * n), dst[:, :],
                                                       ALU.mult, ALU.add)
                        if j < 3:
                            step(ins)
                    ins.then_inc(S["conv_done"], 1)
                dve.wait_ge(rows_loaded, u * (96) + 96)
                for sub in range(nsub):
                    def spread(n):
                        return colv[:, n, :, bass.ds(u * nsub + sub, 1)].to_broadcast([P, NCH, C])
                    a = chunks(att[:, sub, :])
                    step(dve.tensor_tensor(a, chunks(brep[:, sub, :]), spread(0), ALU.subtract))
                    step(dve.tensor_scalar(a, a, 0.0, None, ALU.min))
                    dve.tensor_tensor(a, a, spread(1), ALU.add).then_inc(S["expo_ready"], 1)
                dve.wait_ge(S["silu_done"], u * 2 + 2)
                dve.tensor_scalar(q[:, :], q[:, :], 64 ** -0.5, None, ALU.mult).then_inc(S["qk_ready"], 1)
                for sub in range(nsub):
                    a = chunks(att[:, sub, :])
                    dve.wait_ge(S["expd"], u * nsub + (sub + 1))
                    step(dve.tensor_tensor(a, a, per_chunk(core.tri[:, :]), ALU.mult))
                    dve.wait_ge(S["prod_done"], u * nsub + (sub + 1))
                    dve.tensor_tensor(a, a, chunks(A[sub]), ALU.mult).then_inc(S["att_ready"], 1)
                step(dve.tensor_tensor(q[:, :], q[:, :], qdec[:, :], ALU.mult))
                dve.wait_ge(S["keys_turned"], u + 1)
                for sub in range(nsub):
                    kd = colv[:, 2, :, bass.ds(u * nsub + sub, 1)].to_broadcast([P, NCH, 64])
                    ins = dve.tensor_tensor(chunks(ktok)[:, :, sub * 64:sub * 64 + 64],
                                            chunks(B[0])[:, :, sub * 64:sub * 64 + 64], kd, ALU.mult)
                ins.then_inc(S["keys_kept"], 1)
                dve.wait_ge(S["update_done"], u + 1)
                dve.tensor_copy(nstate[:, 1:2], Bflat[:, N0:N0 + 1])
                step(dve.tensor_copy(state[:, 1, :], Bflat[:, 0:nsub * P]))
                for c in range(1, NCH - 1):
                    g = qdec[:, c * C + C - 1:c * C + C]
                    dve.scalar_tensor_tensor(nstate[:, c + 1:c + 2], nstate[:, c:c + 1], g, Bflat[:, N0 + c:N0 + c + 1],
                                             ALU.mult, ALU.add)
                    step(dve.scalar_tensor_tensor(state[:, c + 1, :], state[:, c, :], g,
                                                  Bflat[:, c * nsub * P:(c + 1) * nsub * P], ALU.mult, ALU.add))
                dve.tensor_copy(nrep[:, 1:NCH, :], nstate[:, 1:NCH].unsqueeze(2).to_broadcast([P, NCH - 1, P])) \
                    .then_inc(S["state_ready"], 1)
                for sub in range(nsub):
                    dve.wait_ge(S["out_done"], u * nsub + (sub + 1))
                    step(dve.tensor_scalar(att[:, sub, :], B[sub], -1.0, None, ALU.mult))
                    step(dve.tensor_tensor(att[:, sub, :], B[sub], att[:, sub, :], ALU.max))
                    step(dve.tensor_tensor(att[:, sub, :], att[:, sub, :], em[:, sub, :], ALU.max))
                    step(dve.reciprocal(att[:, sub, :], att[:, sub, :]))
                    step(dve.tensor_tensor(att[:, sub, :], A[sub], att[:, sub, :], ALU.mult))
                    dve.tensor_tensor(og[:, sub, :], og[:, sub, :], att[:, sub, :], ALU.mult).then_inc(S["h_ready"], 1)
                for sub in range(nsub):
                    dve.wait_ge(S["rooted"], u * nsub + (sub + 1))
                    yo = flat(y[:, bass.ds(u * nsub + sub, 1), :])
                    step(dve.reciprocal(em[:, sub, :], em[:, sub, :]))
                    step(dve.scalar_tensor_tensor(em[:, sub, :], og[:, sub, :], core.col_at("ml_nw", u * nsub + sub),
                                                  em[:, sub, :], ALU.mult, ALU.mult))
                    ins = dve.tensor_tensor(yo, yo, em[:, sub, :], ALU.mult)
                    if sub + 1 < nsub:
                        step(ins)
                ins.then_inc(S["unit_free"], 1)
                step.ends(per)


def block_1(core, d):
    with Stage(core.nc, "b1") as st:
        core.hT = st.sb("hT", [P, KD, T])
        core.brow = st.sb("brow", [1, 3 * 512])
        y = st.sb("y", [P, 4, T])
        with Stage(core.nc, "b1row") as s2:
            got = s2.sem("brow_loaded")
            block = s2.block()

            @block.sync
            def _(sp):
                sp.dma_start(core.brow[:, :], d["b1_vrow"]).then_inc(got, 16)
                sp.wait_ge(got, 16)
        rms_norm(core, "rms1", core.xT, "norm_w", core.hT)
        hg_lower_bound(core)
        vector_decay_branch(core, "hg", 1, 4, d["w1"], 0, "hg_q", "hg_f", "hg_z", 0, "hg_nw", y)
        out_projection(core, "o1a", y, 4, d["wo1a"], core.xT)
        with Stage(core.nc, "glas") as s2:
            gl = s2.sb("gl", [P, 2, T])
            gla_gates(core, d["w1"], 16, d["gla_w_a2"], gl)
            vector_decay_branch(core, "gla", 2, 2, d["w1"], 17, "gla_q", "gla_k", "gla_z", 512, "gla_nw", y, gl)
        out_projection(core, "o1b", y, 4, d["wo1b"], core.xT)
        with Stage(core.nc, "mls") as s2:
            cols = s2.sb("cols", [P, 3 * NCH * 4])
            ml_gates(core, d["w1"], 29, d["ml_rows"], cols)
            mlstm_branch(core, d["w1"], 30, d["ml_rows"], cols, y)
        out_projection(core, "o1c", y, 4, d["wo1c"], core.xT)
    rms_norm(core, "fin1", core.xT, "final_norm_w", core.xT)


RH, RDK, RDV = 4, 256, 512
CW = 31
SEG2 = segments([("val", D), ("glu", D), ("gate", D), ("q", RH * RDK), ("k", RH * RDK), ("v", RH * RDV),
                 ("rg", RH * RDV), ("ga", D), ("gb", D)])
RET_TILES = 12
GB_TILE, CONV_TILE, GA_TILE = RH * RET_TILES, RH * RET_TILES + KD, RH * RET_TILES + KD + 3 * KD


def tile_order_2():
    def tile(name, n):
        s = SEG2[name][0] + n * P
        return s, s + P
    out = []
    for h in range(RH):
        out += [tile("q", 2 * h), tile("q", 2 * h + 1), tile("k", 2 * h), tile("k", 2 * h + 1)]
        out += [tile(n, 4 * h + j) for n in ("v", "rg") for j in range(4)]
    out += [tile("gb", e) for e in range(KD)]
    for e in range(KD):
        out += [tile("glu", e), tile("val", e), tile("gate", e)]
    return out + [tile("ga", e) for e in range(KD)]


def columns_2(i):
    f = np.float32
    lg = np.log1p(-np.exp2(f(-5.0) - np.arange(RH, dtype=f))).astype(f)
    idx = np.arange(C, dtype=f)
    zeta = np.exp(lg[:, None] * (f(C - 1.0) - idx)).astype(f) * f(RDK ** -0.5)
    out = [("norm_gain_2", i["norm_gain_2"][0]), ("conv_b_2", i["conv_dw_b_2"][0]),
           ("ln_g_2", i["conv_ln_g_2"][0]), ("ln_b_2", i["conv_ln_b_2"][0]), ("ret_gn", i["ret_gn_g_2"][0]),
           ("final_gain_2", i["final_gain_2"]), ("zeta", zeta),
           ("gamma_chunk", np.repeat(np.exp(lg * f(C)).astype(f), P))]
    return out + [(f"cw{j}", i["conv_dw_w_2"][0, j]) for j in range(CW)]


def lay_out_2(i, d):
    f = np.float32
    d["w2"] = in_tiles(i["w_in_2"][0], tile_order_2())
    d["wret"] = out_tiles(i["w_ret_proj_2"][0])
    d["wconv"] = out_tiles(i["w_conv_proj_2"][0])
    d["wo2"] = out_tiles(i["w_out_2"][0])
    pos = np.arange(T, dtype=f)
    inv = np.power(f(10000.0), -np.arange(0, RDK, 2, dtype=f) / f(RDK)).astype(f)
    ang = (inv[:, None] * pos[None, :]).astype(f)
    d["c_rope"] = np.concatenate([np.cos(ang), np.sin(ang)], 1).astype(f)
    lg = np.log1p(-np.exp2(f(-5.0) - np.arange(RH, dtype=f))).astype(f)
    idx = np.arange(C, dtype=f)
    diff = idx[None, :] - idx[:, None]
    dec = np.where(diff >= 0, np.exp(lg[:, None, None] * np.maximum(diff, 0)), 0).astype(f) * f(RDK ** -0.5)
    xi = np.exp(lg[:, None] * (idx + 1)).astype(f)
    d["c_ret"] = np.concatenate([dec.transpose(1, 0, 2).reshape(P, RH * C),
                                 np.broadcast_to(xi.reshape(1, RH * C), (P, RH * C))], 1)


def gated_projection(core, name, y, nk, wt, wg, first_g, h, dst, accumulate):
    with Stage(core.nc, name) as st:
        w, g = st.sb("w", [P, 2, nk * P]), st.sb("g", [P, 2, D])
        sg = st.sb("sg", [P, 2, T])
        w_loaded = [st.sem("w_loaded0"), st.sem("w_loaded1")]
        g_loaded = [st.sem("g_loaded0"), st.sem("g_loaded1")]
        done, gate_ready, added, dve_step = (st.sem(n) for n in ("projected", "gate_ready", "added", "dve_step"))
        block = st.block()

        @block.sync
        def _(sp):
            for s in range(2):
                sp.dma_start(g[:, s, :], wg[(first_g + s) * P:(first_g + s + 1) * P, :]).then_inc(g_loaded[s], 16)
                sp.dma_start(w[:, s, :], wt[s * P:(s + 1) * P, :]).then_inc(w_loaded[s], 16)
            with sp.Fori(1, KD // 2) as i:
                for s in range(2):
                    sp.wait_ge(done, 2 * i + (s - 1))
                    sp.dma_start(g[:, s, :], wg[bass.ds(i * (2 * P) + (first_g + s) * P, P), :]).then_inc(g_loaded[s], 16)
                    sp.dma_start(w[:, s, :], wt[bass.ds(i * (2 * P) + s * P, P), :]).then_inc(w_loaded[s], 16)

        @block.tensor
        def _(pe):
            with pe.Fori(0, KD // 2) as i:
                for s in range(2):
                    pe.wait_ge(g_loaded[s], 16 * i + 16)
                    pe.wait_ge(w_loaded[s], 16 * i + 16)
                    pe.wait_ge(added, 2 * i + (s + 1))
                    project_features(pe, pair(core, 2 + s), g[:, s, :], h)
                    project_features(pe, pair(core, s), w[:, s, :], y, nk=nk).then_inc(done, 1)

        @block.scalar
        def _(act):
            with act.Fori(0, KD // 2) as i:
                for s in range(2):
                    act.wait_ge(done, 2 * i + (s + 1))
                    act.activation(sg[:, s, :], pair(core, 2 + s), ACT.Sigmoid).then_inc(gate_ready, 1)

        @block.vector
        def _(dve):
            dve.sem_inc(added, 2)
            with dve.Fori(0, KD // 2) as i:
                step = Chain(dve, dve_step, i * 2)
                for s in range(2):
                    dve.wait_ge(gate_ready, 2 * i + (s + 1))
                    o = flat(dst[:, bass.ds(2 * i + s, 1), :])
                    if accumulate:
                        step(dve.tensor_tensor(sg[:, s, :], pair(core, s), sg[:, s, :], ALU.mult))
                        dve.tensor_tensor(o, o, sg[:, s, :], ALU.add).then_inc(added, 1)
                    else:
                        dve.tensor_tensor(o, pair(core, s), sg[:, s, :], ALU.mult).then_inc(added, 1)
                step.ends(2 if accumulate else 0)


def weighted_projection(core, name, y, nk, wt, gates, first, dst, accumulate):
    with Stage(core.nc, name) as st:
        w, sg = st.sb("w", [P, 2, nk * P]), st.sb("sg", [P, 2, T])
        w_loaded = [st.sem("w_loaded0"), st.sem("w_loaded1")]
        g_loaded = [st.sem("g_loaded0"), st.sem("g_loaded1")]
        done, added, dve_step = (st.sem(n) for n in ("projected", "added", "dve_step"))
        block = st.block()

        @block.sync
        def _(sp):
            for s in range(2):
                sp.dma_start(w[:, s, :], wt[s * P:(s + 1) * P, :]).then_inc(w_loaded[s], 16)
                sp.dma_start(sg[:, s, :], gates[(first + s) * P:(first + s + 1) * P, :]).then_inc(g_loaded[s], 16)
            with sp.Fori(1, KD // 2) as i:
                for s in range(2):
                    sp.wait_ge(done, 2 * i + (s - 1))
                    sp.dma_start(w[:, s, :], wt[bass.ds(i * (2 * P) + s * P, P), :]).then_inc(w_loaded[s], 16)
                    sp.wait_ge(added, 2 * i + (s + 1))
                    sp.dma_start(sg[:, s, :], gates[bass.ds(i * (2 * P) + (first + s) * P, P), :]).then_inc(g_loaded[s], 16)

        @block.tensor
        def _(pe):
            with pe.Fori(0, KD // 2) as i:
                for s in range(2):
                    pe.wait_ge(w_loaded[s], 16 * i + 16)
                    pe.wait_ge(added, 2 * i + (s + 1))
                    project_features(pe, pair(core, s), w[:, s, :], y, nk=nk).then_inc(done, 1)

        @block.vector
        def _(dve):
            dve.sem_inc(added, 2)
            with dve.Fori(0, KD // 2) as i:
                step = Chain(dve, dve_step, i * 2)
                for s in range(2):
                    dve.wait_ge(g_loaded[s], 16 * i + 16)
                    dve.wait_ge(done, 2 * i + (s + 1))
                    o = flat(dst[:, bass.ds(2 * i + s, 1), :])
                    if accumulate:
                        step(dve.tensor_tensor(sg[:, s, :], pair(core, s), sg[:, s, :], ALU.mult))
                        dve.tensor_tensor(o, o, sg[:, s, :], ALU.add).then_inc(added, 1)
                    else:
                        dve.tensor_tensor(o, pair(core, s), sg[:, s, :], ALU.mult).then_inc(added, 1)
                step.ends(2 if accumulate else 0)


def retention_branch(core, wt, d):
    order = ["q0", "q1", "k0", "k1", "v0", "v1", "v2", "v3", "g0", "g1", "g2", "g3"]
    nt, ring, units, NV = len(order), 4, RH, RDV // P
    with Stage(core.nc, "ret") as st:
        w = st.sb("w", [P, ring, D])
        loaded = [st.sem(f"w_loaded{t}") for t in range(ring)]
        rope = st.sb("rope", [P, 2, T])
        tab = st.sb("tab", [P, 2, RH, C])
        q, k = st.sb("q", [P, 2, T]), st.sb("k", [P, 2, T])
        v = st.sb("v", [P, NCH, NV, P])
        g, o = st.sb("g", [P, NV, T]), st.sb("o", [P, NV, T])
        att = st.sb("att", [P, T])
        ktok = st.sb("ktok", [P, NCH, RDK])
        R = st.sb("R", [P, 2, 2 * RDV])
        turn = ktok[:, :, :].rearrange("p c d -> p (c d)").rearrange("p (a t) -> p a t", a=2)
        sq = v[:, :, :, :].rearrange("p c n d -> p (c n d)").rearrange("p (n t) -> p n t", n=NV)
        S = {n: st.sem(n) for n in (
            "tables", "proj_done", "evacuated", "unit_free", "roped", "prod_done", "att_ready", "q_decayed",
            "keys_turned", "keys_kept", "update_done", "r_ready", "out_done", "o_kept", "mean_done", "centred",
            "squared", "var_done", "rooted", "o_ready", "stored", "o_free", "dve_step", "passed")}
        A, B = [pair(core, 0), pair(core, 1)], [pair(core, 2), pair(core, 3)]
        block = st.block()

        @block.sync
        def _(sp):
            sp.dma_start(rope[:, :, :].rearrange("p a t -> p (a t)"), d["c_rope"]).then_inc(S["tables"], 16)
            sp.dma_start(tab[:, :, :, :].rearrange("p a h t -> p (a h t)"), d["c_ret"]).then_inc(S["tables"], 16)
            sp.sem_inc(S["o_free"], 1)
            for t in range(nt):
                if t >= ring:
                    sp.wait_ge(S["proj_done"], t + 1 - ring)
                sp.dma_start(w[:, t % ring, :], wt[t * P:(t + 1) * P, :]).then_inc(loaded[t % ring], 16)

            def store(u):
                for j in range(NV):
                    sp.dma_start(d["o_park"][bass.ds(u * (NV * P) + j * P, P), :], o[:, j, :]).then_inc(S["stored"], 16)
            with sp.Fori(1, units) as u:
                for t in range(nt):
                    sp.wait_ge(S["proj_done"], u * nt + (t + 1 - ring))
                    if t == ring:
                        sp.wait_ge(S["o_ready"], u)
                        store(u - 1)
                    sp.dma_start(w[:, t % ring, :], wt[bass.ds(u * (nt * P) + t * P, P), :]).then_inc(loaded[t % ring], 16)
                stored = sp.snap(u * (16 * NV))
                sp.wait_ge(S["stored"], stored)
                sp.sem_inc(S["o_free"], 1)
            sp.wait_ge(S["o_ready"], units)
            for j in range(NV):
                at = ((units - 1) * NV + j) * P
                sp.dma_start(d["o_park"][at:at + P, :], o[:, j, :]).then_inc(S["stored"], 16)
            sp.wait_ge(S["stored"], 16 * NV * units)

        @block.tensor
        def _(pe):
            with pe.Fori(0, units) as u:
                pe.wait_ge(S["unit_free"], u + 1)
                for t, what in enumerate(order):
                    pe.wait_ge(loaded[t % ring], u * (16 * nt // ring) + 16 * (t // ring + 1))
                    if t >= 2:
                        pe.wait_ge(S["evacuated"], u * nt + (t - 1))
                    project = project_tokens if what[0] == "v" else project_features
                    project(pe, B[t % 2], w[:, t % ring, :], core.hT).then_inc(S["proj_done"], 1)
                pe.wait_ge(S["roped"], u * 2 + 2)
                for c in range(NCH):
                    cs = slice(c * C, c * C + C)
                    for i in range(2):
                        ins = pe.matmul(A[0][:, cs], k[:, i, cs], q[:, i, cs], start=(i == 0), stop=(i == 1))
                ins.then_inc(S["prod_done"], 1)
                pe.wait_ge(S["evacuated"], u * nt + nt)
                for i in range(2):
                    for c in range(NCH):
                        cs = slice(c * C, c * C + C)
                        ins = pe.transpose(B[i][:, cs], k[:, i, cs], core.ident[:, :])
                    ins.then_inc(S["keys_turned"], 1)
                pe.wait_ge(S["keys_kept"], u * 2 + 2)
                pe.wait_ge(S["att_ready"], u + 1)
                pe.wait_ge(S["q_decayed"], u + 1)
                for c in range(NCH):
                    cs = slice(c * C, c * C + C)
                    if c < NCH - 1:
                        if c >= 2:
                            pe.wait_ge(S["r_ready"], u * (NCH - 1) + (c - 1))
                        for i in range(2):
                            ins = pe.matmul(B[c % 2][:, i * RDV:(i + 1) * RDV], ktok[:, c, i * P:(i + 1) * P],
                                            v[:, c, :, :].rearrange("p n d -> p (n d)"), start=True, stop=True)
                        ins.then_inc(S["update_done"], 1)
                    if c >= 2:
                        pe.wait_ge(S["o_kept"], u * NCH + (c - 1))
                    if c >= 1:
                        pe.wait_ge(S["r_ready"], u * (NCH - 1) + c)
                    for j in range(NV):
                        dst = A[0][:, (c % 2) * 512 + j * P:(c % 2) * 512 + (j + 1) * P]
                        ins = pe.matmul(dst, v[:, c, j, :], att[:, cs], start=True, stop=(c == 0))
                        if c >= 1:
                            for i in range(2):
                                ins = pe.matmul(dst, R[:, c % 2, i * RDV + j * P:i * RDV + (j + 1) * P],
                                                q[:, i, cs], start=False, stop=(i == 1))
                    ins.then_inc(S["out_done"], 1)
                for src, ready, n, done in ((o, "o_kept", NCH, "mean_done"), (sq, "squared", 1, "var_done")):
                    pe.wait_ge(S[ready], u * n + n)
                    for half in range(2):
                        for j in range(NV):
                            ins = pe.matmul(A[1][:, half * 512:half * 512 + 512], core.mean_v[:, :],
                                            src[:, j, half * 512:half * 512 + 512],
                                            start=(j == 0), stop=(j == NV - 1))
                    ins.then_inc(S[done], 1)

        @block.scalar
        def _(act):
            with act.Fori(0, units) as u:
                for t, what in enumerate(order):
                    act.wait_ge(S["proj_done"], u * nt + (t + 1))
                    src, n = B[t % 2], int(what[1])
                    if what[0] == "v":
                        ins = act.activation(v[:, :, n, :], chunks(src), ACT.Copy)
                    elif what[0] == "g":
                        ins = act.activation(g[:, n, :], src, ACT.Silu)
                    else:
                        ins = act.activation((q if what[0] == "q" else k)[:, n, :], src, ACT.Copy)
                    ins.then_inc(S["evacuated"], 1)
                for i in range(2):
                    wait_alone(act, S["keys_turned"], u * 2 + (i + 1), S["passed"])
                    act.activation(ktok[:, :, i * P:(i + 1) * P], chunks(B[i]), ACT.Copy,
                                   scale=core.col_at("zeta", u)).then_inc(S["keys_kept"], 1)
                act.wait_ge(S["o_free"], u + 1)
                for c in range(NCH):
                    act.wait_ge(S["out_done"], u * NCH + (c + 1))
                    src = A[0][:, (c % 2) * 512:(c % 2) * 512 + 512].rearrange("p (n t) -> p n t", n=NV)
                    act.activation(o[:, :, c * C:c * C + C], src, ACT.Copy).then_inc(S["o_kept"], 1)
                act.wait_ge(S["centred"], u + 1)
                act.activation(sq, o[:, :, :], ACT.Square).then_inc(S["squared"], 1)
                act.wait_ge(S["var_done"], u + 1)
                act.activation(att[:, :], A[1], ACT.Sqrt, bias=core.const(LN_EPS)).then_inc(S["rooted"], 1)

        @block.vector
        def _(dve):
            per = 2 * 2 + 2
            dve.sem_inc(S["unit_free"], 1)
            dve.wait_ge(S["tables"], 32)
            with dve.Fori(0, units) as u:
                step = Chain(dve, S["dve_step"], u * per)
                for n, x in enumerate((q, k)):
                    dve.wait_ge(S["evacuated"], u * nt + (2 * n + 2))
                    dve.tensor_tensor(turn[:, 0, :], x[:, 1, :], rope[:, 1, :], ALU.mult)
                    step(dve.tensor_tensor(turn[:, 1, :], x[:, 0, :], rope[:, 1, :], ALU.mult))
                    dve.tensor_tensor(x[:, 0, :], x[:, 0, :], rope[:, 0, :], ALU.mult)
                    step(dve.tensor_tensor(x[:, 1, :], x[:, 1, :], rope[:, 0, :], ALU.mult))
                    dve.tensor_tensor(x[:, 0, :], x[:, 0, :], turn[:, 0, :], ALU.subtract)
                    dve.tensor_tensor(x[:, 1, :], x[:, 1, :], turn[:, 1, :], ALU.add).then_inc(S["roped"], 1)
                    dve.wait_ge(S["roped"], u * 2 + (n + 1))
                dve.wait_ge(S["prod_done"], u + 1)
                dve.tensor_tensor(chunks(att[:, :]), chunks(A[0]),
                                  tab[:, 0, bass.ds(u, 1), :].to_broadcast([P, NCH, C]), ALU.mult) \
                    .then_inc(S["att_ready"], 1)
                qc = q[:, :, :].rearrange("p a (c t) -> p (a c) t", t=C)
                dve.tensor_tensor(qc, qc, tab[:, 1, bass.ds(u, 1), :].to_broadcast([P, 2 * NCH, C]), ALU.mult) \
                    .then_inc(S["q_decayed"], 1)
                for c in range(NCH - 1):
                    dve.wait_ge(S["update_done"], u * (NCH - 1) + (c + 1))
                    if c == 0:
                        ins = dve.tensor_copy(R[:, 1, :], B[0])
                    else:
                        dve.wait_ge(S["out_done"], u * NCH + c)
                        ins = dve.scalar_tensor_tensor(R[:, (c + 1) % 2, :], R[:, c % 2, :],
                                                       core.col_at("gamma_chunk", u), B[c % 2], ALU.mult, ALU.add)
                    ins.then_inc(S["r_ready"], 1)
                    dve.wait_ge(S["r_ready"], u * (NCH - 1) + (c + 1))
                dve.wait_ge(S["mean_done"], u + 1)
                dve.tensor_tensor(o[:, :, :], o[:, :, :], A[1].unsqueeze(1).to_broadcast([P, NV, T]), ALU.subtract) \
                    .then_inc(S["centred"], 1)
                dve.wait_ge(S["rooted"], u + 1)
                step(dve.reciprocal(att[:, :], att[:, :]))
                for j in range(NV):
                    ins = dve.scalar_tensor_tensor(o[:, j, :], o[:, j, :], core.col_at("ret_gn", u * NV + j),
                                                   att[:, :], ALU.mult, ALU.mult)
                step(ins)
                dve.tensor_tensor(o[:, :, :], o[:, :, :], g[:, :, :], ALU.mult).then_inc(S["o_ready"], 1)
                dve.wait_ge(S["o_ready"], u + 1)
                dve.sem_inc(S["unit_free"], 1)
                step.ends(per)


def conv_branch(core, wt, first, uT, gate):
    nt = 3
    with Stage(core.nc, "conv") as st:
        w = st.sb("w", [P, nt, D])
        loaded = [st.sem(f"w_loaded{t}") for t in range(nt)]
        sg, val = st.sb("sg", [P, T]), st.sb("val", [P, T])
        pad = st.sb("pad", [P, CW - 1 + T])
        proj_done, evacuated, consumed, dve_step = (st.sem(n) for n in ("proj_done", "evacuated", "consumed", "dve_step"))
        block = st.block()

        @block.sync
        def _(sp):
            load_tiles(sp, core, st, wt, w, loaded, proj_done, first, nt, KD)

        @block.tensor
        def _(pe):
            with pe.Fori(0, KD) as u:
                for t in range(nt):
                    pe.wait_ge(loaded[t], 16 * u + 16)
                    pe.wait_ge(evacuated, u * nt + (t + 1))
                    project_features(pe, pair(core, t), w[:, t, :], core.hT).then_inc(proj_done, 1)

        @block.scalar
        def _(act):
            act.sem_inc(evacuated, nt)
            with act.Fori(0, KD) as u:
                act.wait_ge(consumed, u + 1)
                for t, (dst, fn) in enumerate(((sg[:, :], ACT.Sigmoid), (val[:, :], ACT.Copy),
                                               (flat(gate[:, bass.ds(u, 1), :]), ACT.Silu))):
                    act.wait_ge(proj_done, u * nt + (t + 1))
                    act.activation(dst, pair(core, t), fn).then_inc(evacuated, 1)

        @block.vector
        def _(dve):
            dve.memset(pad[:, 0:CW - 1], 0.0).then_inc(consumed, 1)
            with dve.Fori(0, KD) as u:
                step = Chain(dve, dve_step, u * CW)
                dve.wait_ge(evacuated, u * nt + (nt + 2))
                dve.tensor_tensor(pad[:, CW - 1:], val[:, :], sg[:, :], ALU.mult).then_inc(consumed, 1)
                dve.wait_ge(consumed, u + 2)
                acc = flat(uT[:, bass.ds(u, 1), :])
                step(dve.tensor_scalar(acc, pad[:, 0:T], core.col_at("cw0", u), core.col_at("conv_b_2", u),
                                       ALU.mult, ALU.add))
                for j in range(1, CW):
                    step(dve.scalar_tensor_tensor(acc, pad[:, j:j + T], core.col_at(f"cw{j}", u), acc,
                                                  ALU.mult, ALU.add))
                step.ends(CW)


def conv_norm(core, uT, gate):
    with Stage(core.nc, "cnorm") as st:
        sq, rstd = st.sb("sq", [P, 2, T]), st.sb("rstd", [P, T])
        mean_done, centred, squared, summed, rooted, scaled, activated, dve_step = (
            st.sem(n) for n in ("mean_done", "centred", "squared", "summed", "rooted", "scaled", "activated", "dve_step"))
        block = st.block()

        @block.tensor
        def _(pe):
            for half in range(2):
                for k in range(KD):
                    ins = pe.matmul(pair(core, 0)[:, half * 512:half * 512 + 512], core.mean_d[:, :],
                                    uT[:, k, half * 512:half * 512 + 512], start=(k == 0), stop=(k == KD - 1))
            ins.then_inc(mean_done, 1)
            for k in range(KD):
                pe.wait_ge(squared, k + 1)
                for half in range(2):
                    ins = pe.matmul(pair(core, 1)[:, half * 512:half * 512 + 512], core.mean_d[:, :],
                                    sq[:, k % 2, half * 512:half * 512 + 512], start=(k == 0), stop=(k == KD - 1))
                ins.then_inc(summed, 1)

        @block.scalar
        def _(act):
            for k in range(KD):
                act.wait_ge(centred, k + 1)
                if k >= 2:
                    act.wait_ge(summed, k - 1)
                act.activation(sq[:, k % 2, :], uT[:, k, :], ACT.Square).then_inc(squared, 1)
            act.wait_ge(summed, KD)
            act.activation(rstd[:, :], pair(core, 1), ACT.Sqrt, bias=core.const(LN_EPS)).then_inc(rooted, 1)
            for k in range(KD):
                act.wait_ge(scaled, k + 1)
                act.activation(uT[:, k, :], uT[:, k, :], ACT.Silu, bias=core.col("ln_b_2", k)).then_inc(activated, 1)

        @block.vector
        def _(dve):
            step = Chain(dve, dve_step)
            dve.wait_ge(mean_done, 1)
            for k in range(KD):
                dve.tensor_tensor(uT[:, k, :], uT[:, k, :], pair(core, 0), ALU.subtract).then_inc(centred, 1)
            dve.wait_ge(rooted, 1)
            step(dve.reciprocal(rstd[:, :], rstd[:, :]))
            for k in range(KD):
                dve.scalar_tensor_tensor(uT[:, k, :], uT[:, k, :], core.col("ln_g_2", k), rstd[:, :],
                                         ALU.mult, ALU.mult).then_inc(scaled, 1)
            for k in range(KD):
                dve.wait_ge(activated, k + 1)
                dve.tensor_tensor(uT[:, k, :], uT[:, k, :], gate[:, k, :], ALU.mult)


def block_2(core, d):
    with Stage(core.nc, "b2") as st:
        core.hT = st.sb("hT", [P, KD, T])
        rms_norm(core, "rms2", core.xT, "norm_gain_2", core.hT)
        retention_branch(core, d["w2"], d)
        mixed = st.sb("mixed", [P, KD, T])
        with Stage(core.nc, "retout") as s2:
            o = s2.sb("o", [P, RH * RDV // P, T])
            with Stage(core.nc, "oload") as s3:
                got = s3.sem("o_loaded")
                block = s3.block()

                @block.sync
                def _(sp):
                    for n in range(RH * RDV // P):
                        sp.dma_start(o[:, n, :], d["o_park"][n * P:(n + 1) * P, :]).then_inc(got, 16)
                    sp.wait_ge(got, 16 * (RH * RDV // P))
            gated_projection(core, "yb", o, RH * RDV // P, d["wret"], d["w2"], GB_TILE, core.hT, mixed, False)
        with Stage(core.nc, "convs") as s2:
            uT, gate = s2.sb("uT", [P, KD, T]), s2.sb("gate", [P, KD, T])
            conv_branch(core, d["w2"], CONV_TILE, uT, gate)
            conv_norm(core, uT, gate)
            gated_projection(core, "ya", uT, KD, d["wconv"], d["w2"], GA_TILE, core.hT, mixed, True)
        out_projection(core, "o2", mixed, KD, d["wo2"], core.xT)
    rms_norm(core, "fin2", core.xT, "final_gain_2", core.xT)


SBW, SSH, RWW = 512, 16, 512
SEG3 = segments([("sb_q", SBW), ("sb_k", SBW), ("sb_v", SBW), ("sb_g", SBW), ("z", D), ("xs", D), ("bm", P), ("cm", P),
                 ("dt", SSH), ("r", RWW), ("k", RWW), ("v", RWW), ("rw_g", RWW), ("lo", P),
                 ("g_sb", D), ("g_ssd", D), ("g_rw", D)])
SB_TILE, SSD_TILE, SSD_UNIT, RW_LO, RW_TILE, GATE3 = 0, 16, 19, 35, 36, 52


def tile_order_3():
    def tile(name, n):
        s = SEG3[name][0] + n * P
        return s, min(s + P, SEG3[name][1])
    out = []
    for u in range(4):
        out += [tile(n, u) for n in ("sb_q", "sb_k", "sb_v", "sb_g")]
    out += [tile("bm", 0), tile("cm", 0), tile("dt", 0)]
    for u in range(8):
        out += [tile("xs", u), tile("z", u)]
    out.append(tile("lo", 0))
    for u in range(4):
        out += [tile(n, u) for n in ("r", "k", "v", "rw_g")]
    return out + [tile(n, e) for n in ("g_sb", "g_ssd", "g_rw") for e in range(KD)]


def columns_3(i):
    cw, cb, mu = i["conv_w_3"][0], i["conv_b_3"][0], i["rw_mu_3"][0]
    out = [("norm_g_3", i["norm_g_3"][0]), ("final_g_3", i["final_g_3"]), ("ssd_ng", i["ssd_norm_g_3"][0]),
           ("ssd_cb", cb), ("dt_bias", i["dt_bias_3"][0]), ("a_log", i["a_log_3"][0]),
           ("a_head", np.zeros(SSH, np.float32)),
           ("d_skip", np.repeat(i["d_skip_3"][0], D // SSH)),
           ("w0", i["rw_w0_3"][0]), ("a0", i["rw_a0_3"][0]), ("k_k", i["rw_k_k_3"][0]), ("k_a", i["rw_k_a_3"][0]),
           ("r_k", i["rw_r_k_3"][0]), ("rw_ln_g", i["rw_ln_g_3"][0]), ("rw_ln_b", i["rw_ln_b_3"][0])]
    for n, name in enumerate(("r", "k", "v", "g")):
        out.append(("mu_" + name, mu[n * RWW:(n + 1) * RWW]))
    out.append(("mu_lo", mu[4 * RWW:]))
    return out + [(f"ssd_cw{j}", cw[j]) for j in range(4)]


def lay_out_3(i, d):
    d["w3"] = in_tiles(i["w_in_3"][0], tile_order_3())
    for n, name in (("wsb", "w_out_sb_3"), ("wssd", "w_out_ssd_3"), ("wrw", "w_out_rw_3"), ("wo3", "w_o_3")):
        d[n] = out_tiles(i[name][0])
    up = np.concatenate([i["rw_w_up_3"][0], i["rw_a_up_3"][0]], 0)
    d["w_up"] = up.reshape(P, 4, P).transpose(1, 0, 2).reshape(4 * P, P)
    s, t = np.arange(P)[:, None], np.arange(P)[None, :]
    same = s // 64 == t // 64
    d["c_mat3"] = np.concatenate([same, same / 64.0, s >= t], 1).astype(np.float32)
    level0 = level_masks()[:, 0, :]
    d["c_mask3"] = np.concatenate([s < t, s <= t, level0.T], 1).astype(np.float32)


def park(core, src, dram, back=False):
    with Stage(core.nc, "unpark" if back else "park") as st:
        moved = st.sem("moved")
        block = st.block()

        @block.sync
        def _(sp):
            for k in range(KD):
                a, b = dram[k * P:(k + 1) * P, :], src[:, k, :]
                sp.dma_start(*((b, a) if back else (a, b))).then_inc(moved, 16)
            sp.wait_ge(moved, 16 * KD)


def spans(lo):
    return [(max(lo, h * 512), h * 512 + 512) for h in range(2) if lo < h * 512 + 512]


def stick_breaking_branch(core, wt, y):
    order = ["q", "k", "v", "g"]
    nt, units = 4, 4
    steps = [(b, sub) for b in reversed(range(NCH)) for sub in range(2)]
    NS = len(steps)
    with Stage(core.nc, "sb") as st:
        w = st.sb("w", [P, nt, D])
        loaded = [st.sem(f"w_loaded{t}") for t in range(nt)]
        q, k = st.sb("q", [P, T]), st.sb("k", [P, T])
        v = st.sb("v", [P, NCH, P])
        neg, soft, keep, later, att = (st.sb(n, [P, 2, T]) for n in ("neg", "soft", "keep", "later", "att"))
        diag = st.sb("diag", [P, 2, C])
        zeros = st.sb("zeros", [P, 512])
        S = {n: st.sem(n) for n in (
            "proj_done", "evacuated", "unit_free", "q_scaled", "z_done", "mag_ready", "softened", "keep_ready",
            "sum_done", "att_expd", "att_ready", "out_done", "dve_step", "act_step")}
        Z, O = [pair(core, 0), pair(core, 1)], pair(core, 2)

        def rows(sub):
            return slice(sub * 64, sub * 64 + 64)

        block = st.block()

        @block.sync
        def _(sp):
            load_tiles(sp, core, st, wt, w, loaded, S["proj_done"], SB_TILE, nt, units)

        @block.tensor
        def _(pe):
            with pe.Fori(0, units) as u:
                pe.wait_ge(S["unit_free"], u + 1)
                for t, what in enumerate(order):
                    pe.wait_ge(loaded[t], 16 * u + 16)
                    if t >= 2:
                        pe.wait_ge(S["evacuated"], u * nt + (t - 1))
                    project = project_tokens if what == "v" else project_features
                    project(pe, Z[t % 2], w[:, t, :], core.hT).then_inc(S["proj_done"], 1)
                pe.wait_ge(S["evacuated"], u * nt + nt)
                pe.wait_ge(S["q_scaled"], u + 1)
                for n in range(NS + 2):
                    if n < NS:
                        b, sub = steps[n]
                        if n >= 2:
                            pe.wait_ge(S["att_expd"], u * NS + (n - 1))
                        for lo, hi in spans(b * C):
                            ins = pe.matmul(Z[sub][:, lo:hi], k[rows(sub), b * C:b * C + C], q[rows(sub), lo:hi],
                                            start=True, stop=True)
                        ins.then_inc(S["z_done"], 1)
                    if 1 <= n <= NS:
                        b, sub = steps[n - 1]
                        pe.wait_ge(S["keep_ready"], u * NS + n)
                        for lo, hi in spans(b * C):
                            ins = pe.matmul(Z[sub][:, lo:hi], core.triangle[:, :], keep[:, sub, lo:hi],
                                            start=False, stop=True, skip_group_check=True)
                        for lo, hi in spans((b + 1) * C):
                            ins = pe.matmul(Z[sub][:, lo:hi], core.ones[:, :], later[:, sub, lo:hi],
                                            start=False, stop=True, skip_group_check=True)
                        ins.then_inc(S["sum_done"], 1)
                    if n >= 2:
                        b, sub = steps[n - 2]
                        pe.wait_ge(S["att_ready"], u * NS + (n - 1))
                        vb = v[:, b, sub * 64:sub * 64 + 64]
                        if b == NCH - 1:
                            for lo, hi in spans(0):
                                pe.matmul(O[rows(sub), lo:hi], vb, zeros[:, :], start=True, stop=True)
                        ins = pe.matmul(O[rows(sub), b * C:b * C + C], vb, diag[:, sub, :], start=False, stop=True,
                                        skip_group_check=True)
                        for lo, hi in spans((b + 1) * C):
                            ins = pe.matmul(O[rows(sub), lo:hi], vb, att[:, sub, lo:hi], start=False, stop=True,
                                            skip_group_check=True)
                        ins.then_inc(S["out_done"], 1)

        @block.scalar
        def _(act):
            with act.Fori(0, units) as u:
                for t, what in enumerate(order):
                    act.wait_ge(S["proj_done"], u * nt + (t + 1))
                    src = Z[t % 2]
                    if what == "v":
                        ins = act.activation(v[:, :, :], chunks(src), ACT.Copy)
                    elif what == "g":
                        ins = act.activation(flat(y[:, bass.ds(u, 1), :]), src, ACT.Silu)
                    else:
                        ins = act.activation((q if what == "q" else k)[:, :], src, ACT.Copy)
                    ins.then_inc(S["evacuated"], 1)
                step = Chain(act, S["act_step"], u * NS)
                for n in range(NS + 1):
                    if n < NS:
                        b, sub = steps[n]
                        act.wait_ge(S["mag_ready"], u * NS + (n + 1))
                        a = soft[:, sub, b * C:T]
                        step(act.activation(a, a, ACT.Exp))
                        act.activation(a, a, ACT.Ln, bias=1.0).then_inc(S["softened"], 1)
                    if n >= 1:
                        b, sub = steps[n - 1]
                        act.wait_ge(S["sum_done"], u * NS + n)
                        if n >= 3:
                            act.wait_ge(S["out_done"], u * NS + (n - 2))
                        act.activation(att[:, sub, b * C:T], Z[sub][:, b * C:T], ACT.Exp).then_inc(S["att_expd"], 1)
                step.ends(NS)

        @block.vector
        def _(dve):
            dve.memset(zeros[:, :], 0.0)
            dve.memset(diag[:, :, :], 0.0).then_inc(S["unit_free"], 1)
            per = 2 * NS
            with dve.Fori(0, units) as u:
                step = Chain(dve, S["dve_step"], u * per)
                dve.wait_ge(S["evacuated"], u * nt + 1)
                dve.tensor_scalar(q[:, :], q[:, :], 64 ** -0.5, None, ALU.mult).then_inc(S["q_scaled"], 1)
                for n in range(NS + 1):
                    if n < NS:
                        b, sub = steps[n]
                        lo = b * C
                        dve.wait_ge(S["z_done"], u * NS + (n + 1))
                        step(dve.tensor_scalar(neg[:, sub, lo:T], Z[sub][:, lo:T], -1.0, None, ALU.mult))
                        dve.tensor_tensor(soft[:, sub, lo:T], Z[sub][:, lo:T], neg[:, sub, lo:T], ALU.min) \
                            .then_inc(S["mag_ready"], 1)
                        dve.wait_ge(S["softened"], u * NS + (n + 1))
                        step(dve.scalar_tensor_tensor(keep[:, sub, lo:T], neg[:, sub, lo:T], 0.0, soft[:, sub, lo:T],
                                                      ALU.min, ALU.subtract))
                        dve.tensor_tensor(keep[:, sub, lo:lo + C], keep[:, sub, lo:lo + C], core.strict[:, :], ALU.mult) \
                            .then_inc(S["keep_ready"], 1)
                    if n >= 1:
                        b, sub = steps[n - 1]
                        lo = b * C
                        dve.wait_ge(S["att_expd"], u * NS + n)
                        if b < NCH - 1:
                            dve.wait_ge(S["out_done"], u * NS + (n - 2))
                            dve.tensor_tensor(later[:, sub, lo + C:T], later[:, sub, lo + C:T], keep[:, sub, lo + C:T],
                                              ALU.add)
                        dve.tensor_copy(later[:, sub, lo:lo + C], keep[:, sub, lo:lo + C])
                        dve.copy_predicated(diag[:, sub, :], core.strict[:, :].bitcast(U32), att[:, sub, lo:lo + C]) \
                            .then_inc(S["att_ready"], 1)
                        dve.wait_ge(S["att_ready"], u * NS + n)
                dve.wait_ge(S["out_done"], u * NS + NS)
                yo = flat(y[:, bass.ds(u, 1), :])
                dve.tensor_tensor(yo, yo, O, ALU.mult).then_inc(S["unit_free"], 1)
                step.ends(per)


def ssd_gates(core, wt, rows_dram, cols, bt, ct, btok, cb):
    H = SSH
    with Stage(core.nc, "ssdgate") as st:
        w = st.sb("w", [P, 3, D])
        pre = st.sb("pre", [P, 2, 3 + T])
        raw, mag, dt, cs, ec, de = (st.sb(n, [H, T]) for n in ("raw", "mag", "dt", "cs", "ec", "de"))
        (w_loaded, proj_done, evacuated, conv_done, activated, mag_ready, softened, a_ready, cs_ready, exped, turned,
         prod_done, b_turned, b_kept, dve_step, act_step, stored) = (st.sem(n) for n in (
             "w_loaded", "proj_done", "evacuated", "conv_done", "activated", "mag_ready", "softened", "a_ready", "cs_ready",
             "exped", "turned", "prod_done", "b_turned", "b_kept", "dve_step", "act_step", "stored"))
        a_head = core.col("a_head", 0)[0:H, :]
        block = st.block()

        @block.sync
        def _(sp):
            for n in range(3):
                sp.dma_start(w[:, n, :], wt[(SSD_TILE + n) * P:(SSD_TILE + n + 1) * P, :]).then_inc(w_loaded, 16)
            sp.wait_ge(exped, 1)
            sp.dma_start(rows_dram[0:H, :], cs[:, :]).then_inc(stored, 16)
            sp.dma_start(rows_dram[H:2 * H, :], ec[:, :]).then_inc(stored, 16)
            sp.wait_ge(stored, 32)

        @block.tensor
        def _(pe):
            pe.wait_ge(w_loaded, 48)
            project_features(pe, pair(core, 2), w[:, 2, :], core.hT, m=H).then_inc(proj_done, 1)
            for n in range(2):
                project_features(pe, pair(core, n), w[:, n, :], core.hT).then_inc(proj_done, 1)
            pe.wait_ge(exped, 1)
            for n, r in enumerate((cs, dt, de)):
                for c in range(NCH):
                    ins = pe.matmul(pair(core, 3)[:, (n * NCH + c) * H:(n * NCH + c + 1) * H],
                                    r[:, c * C:c * C + C], core.ident[0:H, 0:H], start=True, stop=True)
            ins.then_inc(turned, 1)
            pe.wait_ge(activated, 2)
            for g in range(2):
                for c in range(NCH):
                    s = slice(c * C, c * C + C)
                    ins = pe.matmul(pair(core, g)[:, s], bt[g * 64:g * 64 + 64, s], ct[g * 64:g * 64 + 64, s],
                                    start=True, stop=True)
                ins.then_inc(prod_done, 1)
            for c in range(NCH):
                s = slice(c * C, c * C + C)
                ins = pe.transpose(pair(core, 2)[:, s], bt[:, s], core.ident[:, :])
            ins.then_inc(b_turned, 1)

        @block.scalar
        def _(act):
            step = Chain(act, act_step)
            act.activation(a_head, core.col("a_log", 0)[0:H, :], ACT.Exp).then_inc(a_ready, 1)
            act.wait_ge(mag_ready, 1)
            step(act.activation(mag[:, :], mag[:, :], ACT.Exp, scale=-1.0))
            act.activation(mag[:, :], mag[:, :], ACT.Ln, bias=1.0).then_inc(softened, 1)
            for n in range(2):
                act.wait_ge(proj_done, n + 2)
                act.activation(pre[:, n, 3:3 + T], pair(core, n), ACT.Copy).then_inc(evacuated, 1)
            act.wait_ge(cs_ready, 1)
            act.activation(ec[:, :], cs[:, :], ACT.Exp)
            act.activation(de[:, :], de[:, :], ACT.Exp).then_inc(exped, 1)
            for n, dst in enumerate((bt, ct)):
                act.wait_ge(conv_done, n + 1)
                act.activation(dst[:, :], dst[:, :], ACT.Silu, bias=core.col("ssd_cb", KD + n)).then_inc(activated, 1)
            act.wait_ge(b_turned, 1)
            act.activation(btok[:, :, :], chunks(pair(core, 2)), ACT.Copy).then_inc(b_kept, 1)

        @block.vector
        def _(dve):
            step = Chain(dve, dve_step)
            dve.wait_ge(proj_done, 1)
            step(dve.tensor_scalar(raw[:, :], pair(core, 2)[0:H, :], core.col("dt_bias", 0)[0:H, :], None, ALU.add))
            dve.scalar_tensor_tensor(mag[:, :], raw[:, :], -1.0, raw[:, :], ALU.mult, ALU.max).then_inc(mag_ready, 1)
            dve.wait_ge(softened, 1)
            step(dve.scalar_tensor_tensor(dt[:, :], raw[:, :], 0.0, mag[:, :], ALU.max, ALU.add))
            dve.wait_ge(a_ready, 1)
            step(dve.tensor_scalar(raw[:, :], dt[:, :], a_head, -1.0, ALU.mult, ALU.mult))
            for c in range(NCH):
                s = slice(c * C, c * C + C)
                ins = dve.tensor_tensor_scan(cs[:, s], raw[:, s], raw[:, s], 0.0, ALU.add, ALU.bypass)
            step(ins)
            last = chunks(cs[:, :])[:, :, C - 1:C].to_broadcast([H, NCH, C])
            dve.tensor_tensor(chunks(de[:, :]), last, chunks(cs[:, :]), ALU.subtract).then_inc(cs_ready, 1)
            dve.wait_ge(evacuated, 2)
            step(dve.memset(pre[:, :, 0:3], 0.0))
            for n, dst in enumerate((bt, ct)):
                step(dve.tensor_scalar(dst[:, :], pre[:, n, 0:T], core.col("ssd_cw0", KD + n), None, ALU.mult))
                for j in range(1, 4):
                    ins = dve.scalar_tensor_tensor(dst[:, :], pre[:, n, j:j + T], core.col(f"ssd_cw{j}", KD + n),
                                                   dst[:, :], ALU.mult, ALU.add)
                    if j < 3:
                        step(ins)
                ins.then_inc(conv_done, 1)
            dve.wait_ge(turned, 1)
            dve.tensor_copy(cols[:, :], pair(core, 3)[:, 0:3 * NCH * H])
            for g in range(2):
                dve.wait_ge(prod_done, g + 1)
                dve.tensor_tensor(chunks(cb[:, g, :]), chunks(pair(core, g)),
                                  per_chunk(core.tri[:, :]), ALU.mult)


def ssd_branch(core, wt, rows_dram, cols, ct, btok, cb, y):
    units, per_group, H, nt = 8, 4, SSH, 2
    colv = cols[:, :].rearrange("p (n c h) -> p n c h", n=3, c=NCH)
    with Stage(core.nc, "ssd") as st:
        w = st.sb("w", [P, nt, D])
        loaded = [st.sem(f"w_loaded{t}") for t in range(nt)]
        pre = st.sb("pre", [P, 3 + T])
        xs = st.sb("xs", [P, T])
        xdt, xend = st.sb("xdt", [P, NCH, P]), st.sb("xend", [P, NCH, P])
        crep, erep, att, cdec = (st.sb(n, [P, 2, T]) for n in ("crep", "erep", "att", "cdec"))
        state = st.sb("state", [P, NCH, P])
        S = {n: st.sem(n) for n in (
            "rows_loaded", "proj_done", "evacuated", "unit_free", "conv_done", "activated", "expo_ready", "expd", "att_ready",
            "x_turned", "x_ready", "update_done", "state_ready", "out_done", "dve_step")}
        A, B, X, U = (pair(core, n) for n in range(4))

        def g_rows(g):
            return slice(g * 64, g * 64 + 64)

        block = st.block()

        @block.sync
        def _(sp):
            with sp.Fori(0, units) as u:
                sp.wait_ge(S["unit_free"], u + 1)
                for t in range(nt):
                    sp.dma_start(w[:, t, :], wt[bass.ds(u * (nt * P) + (SSD_UNIT + t) * P, P), :]).then_inc(loaded[t], 16)
                for sub in range(2):
                    for n, dst in enumerate((crep, erep)):
                        sp.dma_start(dst[:, sub, :], rows_dram[bass.ds(u * 2 + (n * H + sub), 1), :].to_broadcast([P, T])) \
                            .then_inc(S["rows_loaded"], 16)

        @block.tensor
        def _(pe):
            for g in range(2):
                with pe.Fori(g * per_group, (g + 1) * per_group) as u:
                    pe.wait_ge(S["unit_free"], u + 1)
                    for t, dst in enumerate((A, B)):
                        pe.wait_ge(loaded[t], 16 * u + 16)
                        project_features(pe, dst, w[:, t, :], core.hT).then_inc(S["proj_done"], 1)
                    pe.wait_ge(S["activated"], u + 1)
                    for c in range(NCH):
                        s = slice(c * C, c * C + C)
                        ins = pe.transpose(X[:, s], xs[:, s], core.ident[:, :])
                    ins.then_inc(S["x_turned"], 1)
                    pe.wait_ge(S["x_ready"], u + 1)
                    for c in range(NCH - 1):
                        ins = pe.matmul(U[g_rows(g), c * P:c * P + P], btok[:, c, g * 64:g * 64 + 64], xend[:, c, :],
                                        start=True, stop=True)
                    ins.then_inc(S["update_done"], 1)
                    pe.wait_ge(S["state_ready"], u + 1)
                    pe.wait_ge(S["att_ready"], u * 2 + 2)
                    pe.wait_ge(S["evacuated"], u * 2 + 2)
                    for sub in range(2):
                        h = slice(sub * 64, sub * 64 + 64)
                        for c in range(NCH):
                            s = slice(c * C, c * C + C)
                            ins = pe.matmul(A[h, s], xdt[:, c, h], att[:, sub, s], start=True, stop=(c == 0))
                            if c:
                                ins = pe.matmul(A[h, s], state[g_rows(g), c, h], cdec[g_rows(g), sub, s],
                                                start=False, stop=True)
                    ins.then_inc(S["out_done"], 1)

        @block.scalar
        def _(act):
            with act.Fori(0, units) as u:
                act.wait_ge(S["proj_done"], u * 2 + 1)
                act.activation(pre[:, 3:3 + T], A, ACT.Copy).then_inc(S["evacuated"], 1)
                act.wait_ge(S["proj_done"], u * 2 + 2)
                act.activation(flat(y[:, bass.ds(u, 1), :]), B, ACT.Silu).then_inc(S["evacuated"], 1)
                act.wait_ge(S["conv_done"], u + 1)
                act.activation(xs[:, :], xs[:, :], ACT.Silu, bias=core.col_at("ssd_cb", u)).then_inc(S["activated"], 1)
                for sub in range(2):
                    act.wait_ge(S["expo_ready"], u * 2 + (sub + 1))
                    act.activation(att[:, sub, :], att[:, sub, :], ACT.Exp).then_inc(S["expd"], 1)

        @block.vector
        def _(dve):
            per = 3 + 2 + 1 + 2 * (NCH - 2) + 1
            dve.memset(pre[:, 0:3], 0.0).then_inc(S["unit_free"], 1)
            for g in range(2):
                with dve.Fori(g * per_group, (g + 1) * per_group) as u:
                    step = Chain(dve, S["dve_step"], u * per)

                    def spread(n, h, width):
                        return colv[:, n, :, bass.ds(u * 2 + h, 1)].to_broadcast([P, NCH, width])
                    dve.wait_ge(S["rows_loaded"], u * 64 + 64)
                    dve.wait_ge(S["evacuated"], u * 2 + 1)
                    step(dve.tensor_scalar(xs[:, :], pre[:, 0:T], core.col_at("ssd_cw0", u), None, ALU.mult))
                    for j in range(1, 4):
                        ins = dve.scalar_tensor_tensor(xs[:, :], pre[:, j:j + T], core.col_at(f"ssd_cw{j}", u), xs[:, :],
                                                       ALU.mult, ALU.add)
                        if j < 3:
                            step(ins)
                    ins.then_inc(S["conv_done"], 1)
                    for sub in range(2):
                        a = chunks(att[:, sub, :])
                        step(dve.tensor_tensor(a, chunks(crep[:, sub, :]), spread(0, sub, C), ALU.subtract))
                        dve.tensor_scalar(a, a, 0.0, None, ALU.min).then_inc(S["expo_ready"], 1)
                        dve.tensor_tensor(cdec[g_rows(g), sub, :], ct[g_rows(g), :], erep[g_rows(g), sub, :], ALU.mult)
                    dve.wait_ge(S["x_turned"], u + 1)
                    for sub in range(2):
                        h = slice(sub * 64, sub * 64 + 64)
                        ins = dve.tensor_tensor(xdt[:, :, h], chunks(X)[:, :, h], spread(1, sub, 64), ALU.mult)
                    step(ins)
                    for sub in range(2):
                        h = slice(sub * 64, sub * 64 + 64)
                        ins = dve.tensor_tensor(xend[:, :, h], xdt[:, :, h], spread(2, sub, 64), ALU.mult)
                    ins.then_inc(S["x_ready"], 1)
                    for sub in range(2):
                        dve.wait_ge(S["expd"], u * 2 + (sub + 1))
                        dve.tensor_tensor(att[:, sub, :], att[:, sub, :], cb[:, g, :], ALU.mult).then_inc(S["att_ready"], 1)
                    dve.wait_ge(S["update_done"], u + 1)
                    r = g_rows(g)
                    step(dve.tensor_copy(state[r, 1, :], U[r, 0:P]))
                    for c in range(1, NCH - 1):
                        for sub in range(2):
                            h = slice(sub * 64, sub * 64 + 64)
                            ins = dve.scalar_tensor_tensor(state[r, c + 1, h], state[r, c, h],
                                                           erep[r, sub, c * C + C - 1:c * C + C],
                                                           U[r, c * P + sub * 64:c * P + sub * 64 + 64], ALU.mult, ALU.add)
                            if (c, sub) != (NCH - 2, 1):
                                step(ins)
                    ins.then_inc(S["state_ready"], 1)
                    dve.wait_ge(S["out_done"], u + 1)
                    step(dve.scalar_tensor_tensor(xs[:, :], xs[:, :], core.col_at("d_skip", u), A, ALU.mult, ALU.add))
                    yo = flat(y[:, bass.ds(u, 1), :])
                    dve.tensor_tensor(yo, yo, xs[:, :], ALU.mult).then_inc(S["unit_free"], 1)
                    step.ends(per)


def rwkv_low_rank(core, wt, lo):
    with Stage(core.nc, "rwlo") as st:
        w = st.sb("w", [P, D])
        raw, delta = st.sb("raw", [P, 1 + T]), st.sb("delta", [P, T])
        w_loaded, done, kept, mixed, step_sem, out = (st.sem(n) for n in ("w_loaded", "done", "kept", "mixed", "dve_step", "out"))
        block = st.block()

        @block.sync
        def _(sp):
            sp.dma_start(w[:, :], wt[RW_LO * P:(RW_LO + 1) * P, :]).then_inc(w_loaded, 16)

        @block.tensor
        def _(pe):
            pe.wait_ge(w_loaded, 16)
            project_features(pe, pair(core, 0), w, core.hT).then_inc(done, 1)

        @block.scalar
        def _(act):
            act.wait_ge(done, 1)
            act.activation(raw[:, 1:], pair(core, 0), ACT.Copy).then_inc(kept, 1)
            act.wait_ge(mixed, 1)
            act.activation(lo[0:64, :], lo[0:64, :], ACT.Tanh).then_inc(out, 1)

        @block.vector
        def _(dve):
            step = Chain(dve, step_sem)
            step(dve.memset(raw[:, 0:1], 0.0))
            dve.wait_ge(kept, 1)
            step(dve.tensor_tensor(delta[:, :], raw[:, 0:T], raw[:, 1:], ALU.subtract))
            dve.scalar_tensor_tensor(lo[:, :], delta[:, :], core.col("mu_lo", 0), raw[:, 1:], ALU.mult, ALU.add) \
                .then_inc(mixed, 1)


def rwkv_branch(core, wt, w_up, lo, F, y, gate_park):
    order = ["r", "k", "v", "g"]
    nt, units = 4, 4
    r, k, v, kk, b, lw, cum, bonus = (F[:, n, :] for n in range(8))
    NL = LEVELS - 1
    with Stage(core.nc, "rw") as st:
        w = st.sb("w", [P, nt, D])
        up = st.sb("up", [P, P])
        loaded = [st.sem(f"w_loaded{t}") for t in range(nt)]
        raw = st.sb("raw", [P, 1 + T])
        tmp = st.sb("tmp", [P, T])
        tok = st.sb("tok", [P, 4, NCH, P])
        at, ak = (st.sb(n, [P, T]) for n in ("at", "ak"))
        ab, ar = (st.sb(n, [P, 2, T]) for n in ("ab", "ar"))
        X, XT, al1 = (st.sb(n, [P, T]) for n in ("X", "XT", "al1"))
        Y, al = v, (cum, al1)
        WT = st.sb("WT", [P, T])
        G = st.sb("G", [P, NCH, 64])
        U0, sa = (st.sb(n, [P, NCH, 2, 64]) for n in ("U0", "sa"))
        M = st.sb("M", [P, NCH, 64])
        gc = st.sb("gc", [P, NCH])
        S = {n: st.sem(n) for n in (
            "up_loaded", "proj_done", "evacuated", "unit_free", "raw_free", "mixed", "silu_done", "low_done", "low_kept",
            "kk_raw", "squared", "normed", "rooted", "bonus_in", "bonus_done", "cum_ready", "expd", "factors", "turned", "tok_ready",
            "prods", "prods2", "kept", "level_a", "y_done", "y_kept", "xyx", "x_ready", "w_done", "w_kept",
            "u_done", "u_kept", "sa_done", "sa_ready", "m_done", "m_ready", "out_done", "out_kept",
            "mean_done", "centred", "sq2", "var_done", "rooted2", "dve_step", "passed")}
        PA, PB, PC = (pair(core, n) for n in range(3))
        fill = Filler(core, st, "gates", 3, wt, GATE3, gate_park, 0, [("features", ACT.Sigmoid, None)] * (3 * KD // units))

        def rows(sub):
            return slice(sub * 64, sub * 64 + 64)

        def cs(c):
            return slice(c * C, c * C + C)

        block = st.block()

        @block.sync
        def _(sp):
            def unit(u, head):
                for t in range(nt):
                    at = (RW_TILE + t) * P if head else sp.snap(u * (nt * P) + (RW_TILE + t) * P)
                    if not head:
                        sp.wait_ge(S["proj_done"], u * nt + (t + 1 - nt))
                    src = wt[at:at + P, :] if head else wt[bass.ds(at, P), :]
                    sp.dma_start(w[:, t, :], src).then_inc(loaded[t], 16)
                at = 0 if head else sp.snap(u * P)
                if not head:
                    sp.wait_ge(S["low_done"], u)
                sp.dma_start(up[:, :], w_up[0:P, :] if head else w_up[bass.ds(at, P), :]).then_inc(S["up_loaded"], 16)
                fill.load(sp, u, head)
            unit(0, True)
            with sp.Fori(1, units) as u:
                unit(u, False)

        @block.tensor
        def _(pe):
            def block_sum(mat, src, dst):
                for half in range(2):
                    h = slice(half * 512, half * 512 + 512)
                    ins = pe.matmul(dst[:, h], mat, src[:, h], start=True, stop=True)
                return ins

            def products(dst, lhs, rhs, sub):
                for c in range(NCH):
                    ins = pe.matmul(dst[:, cs(c)], lhs[rows(sub), cs(c)], rhs[rows(sub), cs(c)], start=True, stop=True)
                return ins

            def by_chunk(dst, lhs, rhs):
                for c in range(NCH):
                    ins = pe.matmul(dst[:, cs(c)], lhs[:, cs(c)], rhs[:, cs(c)], start=True, stop=True)
                return ins

            with pe.Fori(0, units) as u:
                pe.wait_ge(S["unit_free"], u + 1)
                for t in range(nt):
                    pe.wait_ge(loaded[t], 16 * u + 16)
                    if t >= 2:
                        pe.wait_ge(S["evacuated"], u * nt + (t - 1))
                    project_features(pe, (PA, PB)[t % 2], w[:, t, :], core.hT).then_inc(S["proj_done"], 1)
                pe.wait_ge(S["up_loaded"], 16 * u + 16)
                pe.wait_ge(S["evacuated"], u * nt + (nt - 1))
                for half in range(2):
                    h = slice(half * 512, half * 512 + 512)
                    pe.matmul(PC[:, h], up[0:64, :], lo[0:64, h], start=True, stop=True)
                    ins = pe.matmul(PA[:, h], up[64:128, :], lo[64:128, h], start=True, stop=True)
                ins.then_inc(S["low_done"], 1)
                fill.multiply(pe, u, 0)
                pe.wait_ge(S["evacuated"], u * nt + nt)
                pe.wait_ge(S["squared"], u + 1)
                block_sum(core.same_head[:, :], tmp, PB).then_inc(S["normed"], 1)
                fill.multiply(pe, u, 1)
                pe.wait_ge(S["low_kept"], u + 1)
                pe.wait_ge(S["bonus_in"], u + 1)
                block_sum(core.same_head[:, :], bonus, PC).then_inc(S["bonus_done"], 1)
                fill.multiply(pe, u, 2)
                fill.multiply(pe, u, 3)
                pe.wait_ge(S["factors"], u + 1)
                for n, src in enumerate((v, b, k, kk)):
                    dst = (PA, PC, PB, PA)[n]
                    if n == 3:
                        pe.wait_ge(S["tok_ready"], u * 4 + 1)
                    for c in range(NCH):
                        ins = pe.transpose(dst[:, cs(c)], src[:, cs(c)], core.ident[:, :])
                    ins.then_inc(S["turned"], 1)
                pe.wait_ge(S["tok_ready"], u * 4 + 4)
                for sub in range(2):
                    e = u * 2 + sub
                    if sub:
                        pe.wait_ge(S["u_kept"], u * 2 + 1)
                    products(PA, b, kk, sub)
                    products(PB, kk, b, sub)
                    products(PC, k, kk, sub).then_inc(S["prods"], 1)
                    fill.multiply(pe, u, 4 + sub)
                    pe.wait_ge(S["kept"], e * 2 + 1)
                    products(PC, b, r, sub)
                    products(PA, k, r, sub).then_inc(S["prods2"], 1)
                    for l in range(1, LEVELS):
                        n = e * NL + (l - 1)
                        pe.wait_ge(S["level_a"], n + 1)
                        for hf in range(2):
                            if l > 1:
                                pe.wait_ge(S["x_ready"], n * 2 + (hf - 1))
                            elif hf == 0:
                                pe.wait_ge(S["kept"], e * 2 + 2)
                            for c in range(hf * NCH // 2, (hf + 1) * NCH // 2):
                                ins = pe.matmul(PC[:, cs(c)], al[l % 2][:, cs(c)], X[:, cs(c)], start=True, stop=True)
                            ins.then_inc(S["y_done"], 1)
                        for hf in range(2):
                            pe.wait_ge(S["y_kept"], n * 2 + (hf + 1))
                            for c in range(hf * NCH // 2, (hf + 1) * NCH // 2):
                                if l < NL:
                                    pe.matmul(level_views(PA[:, cs(c)], l)[0], XT[:, cs(c)],
                                              level_views(Y[:, cs(c)], l)[0], start=True, stop=True)
                                ins = pe.matmul(level_views(PB[:, cs(c)], l)[1], Y[:, cs(c)],
                                                level_views(XT[:, cs(c)], l)[1], start=True, stop=True)
                            ins.then_inc(S["xyx"], 1)
                    pe.wait_ge(S["x_ready"], (e * NL + NL) * 2)
                    for c in range(NCH):
                        pe.matmul(PC[rows(sub), cs(c)], tok[:, 3, c, rows(sub)], XT[:, cs(c)], start=True, stop=True)
                        ins = pe.matmul(PB[:, c * 64:c * 64 + 64], ak[:, cs(c)], tok[:, 0, c, rows(sub)], start=True, stop=True)
                    ins.then_inc(S["w_done"], 1)
                    pe.wait_ge(S["w_kept"], e + 1)
                    for c in range(NCH):
                        ins = pe.matmul(PA[:, c * 64:c * 64 + 64], XT[:, cs(c)], G[:, c, :], start=True, stop=True)
                    ins.then_inc(S["u_done"], 1)
                pe.wait_ge(S["u_kept"], u * 2 + 2)
                for c in range(NCH):
                    if c:
                        pe.wait_ge(S["m_ready"], u * (NCH - 1) + c)
                        for sub in range(2):
                            ins = pe.matmul(PB[:, sub * 512 + c * 64:sub * 512 + c * 64 + 64], WT[rows(sub), cs(c)],
                                            M[rows(sub), c, :], start=True, stop=True)
                        ins.then_inc(S["sa_done"], 1)
                    if c < NCH - 1:
                        mc = slice(c * 64, c * 64 + 64)
                        for sub in range(2):
                            pe.matmul(PC[rows(sub), mc], tok[:, 2, c, rows(sub)], tok[:, 0, c, rows(sub)],
                                      start=True, stop=False)
                            if c:
                                pe.matmul(PC[rows(sub), mc], core.ident[rows(sub), rows(sub)], M[rows(sub), c, :],
                                          start=False, stop=False)
                    pe.wait_ge(S["sa_ready"], u * NCH + (c + 1))
                    if c < NCH - 1:
                        for sub in range(2):
                            ins = pe.matmul(PC[rows(sub), mc], tok[:, 1, c, rows(sub)], sa[:, c, sub, :],
                                            start=False, stop=True)
                        ins.then_inc(S["m_done"], 1)
                for sub in range(2):
                    for c in range(NCH):
                        o = PA[rows(sub), cs(c)]
                        pe.matmul(o, tok[:, 0, c, rows(sub)], ar[:, sub, cs(c)], start=True, stop=False)
                        ins = pe.matmul(o, sa[:, c, sub, :], ab[:, sub, cs(c)], start=False, stop=(c == 0))
                        if c:
                            ins = pe.matmul(o, M[rows(sub), c, :], r[rows(sub), cs(c)], start=False, stop=True)
                ins.then_inc(S["out_done"], 1)
                pe.wait_ge(S["out_kept"], u + 1)
                block_sum(core.mean_head[:, :], lw, PB).then_inc(S["mean_done"], 1)
                pe.wait_ge(S["sq2"], u + 1)
                block_sum(core.mean_head[:, :], cum, PC).then_inc(S["var_done"], 1)

        @block.scalar
        def _(act):
            fill.begin(act)
            with act.Fori(0, units) as u:
                for t in range(nt):
                    act.wait_ge(S["proj_done"], u * nt + (t + 1))
                    act.wait_ge(S["raw_free"], u * nt + (t + 1))
                    act.activation(raw[:, 1:], (PA, PB)[t % 2], ACT.Copy).then_inc(S["evacuated"], 1)
                act.wait_ge(S["low_done"], u + 1)
                act.activation(lw, PC, ACT.Sigmoid, bias=core.col_at("w0", u))
                act.activation(b, PA, ACT.Sigmoid, bias=core.col_at("a0", u)).then_inc(S["low_kept"], 1)
                act.wait_ge(S["mixed"], u * nt + nt)
                yo = flat(y[:, bass.ds(u, 1), :])
                act.activation(yo, yo, ACT.Silu).then_inc(S["silu_done"], 1)
                act.wait_ge(S["kk_raw"], u + 1)
                act.activation(tmp[:, :], kk, ACT.Square).then_inc(S["squared"], 1)
                fill.keep(act, u, 0)
                act.wait_ge(S["normed"], u + 1)
                act.activation(tmp[:, :], PB, ACT.Sqrt).then_inc(S["rooted"], 1)
                fill.keep(act, u, 1)
                act.wait_ge(S["cum_ready"], u + 1)
                act.activation(gc[:, 0:NCH - 1], gc[:, 0:NCH - 1], ACT.Exp)
                act.activation(lw, lw, ACT.Exp)
                act.activation(tmp[:, :], cum, ACT.Exp, scale=-1.0).then_inc(S["expd"], 1)
                act.wait_ge(S["expd"], u * 2 + 1)
                act.activation(cum, cum, ACT.Exp).then_inc(S["expd"], 1)
                fill.keep(act, u, 2)
                fill.keep(act, u, 3)
                for n in range(4):
                    act.wait_ge(S["turned"], u * 4 + (n + 1))
                    act.activation(tok[:, n, :, :], chunks((PA, PC, PB, PA)[n]), ACT.Copy).then_inc(S["tok_ready"], 1)
                for sub in range(2):
                    e = u * 2 + sub
                    fill.keep(act, u, 4 + sub)
                    for l in range(1, LEVELS):
                        for hf in range(2):
                            h = slice(hf * 512, hf * 512 + 512)
                            act.wait_ge(S["y_done"], (e * NL + (l - 1)) * 2 + (hf + 1))
                            act.activation(Y[:, h], PC[:, h], ACT.Copy).then_inc(S["y_kept"], 1)
                    act.wait_ge(S["w_done"], e + 1)
                    act.activation(WT[rows(sub), :], PC[rows(sub), :], ACT.Copy)
                    act.activation(G[:, :, :], PB[:, 0:NCH * 64].rearrange("p (c i) -> p c i", c=NCH), ACT.Copy) \
                        .then_inc(S["w_kept"], 1)
                act.wait_ge(S["out_done"], u + 1)
                act.activation(lw, PA, ACT.Copy).then_inc(S["out_kept"], 1)
                act.wait_ge(S["centred"], u + 1)
                act.activation(cum, lw, ACT.Square).then_inc(S["sq2"], 1)
                act.wait_ge(S["var_done"], u + 1)
                act.activation(tmp[:, :], PC, ACT.Sqrt, bias=core.const(GN_EPS)).then_inc(S["rooted2"], 1)
                fill.end(act, u)

        @block.gpsimd
        def _(pool):
            with pool.Fori(0, 2 * units) as e:
                pool.wait_ge(S["kept"], e * 2 + 1)
                for l in range(1, LEVELS):
                    if l >= 3:
                        pool.wait_ge(S["y_done"], (e * NL + (l - 2)) * 2)
                    pool.tensor_tensor(chunks(al[l % 2][:, :]), chunks(at[:, :]), per_chunk(core.level_mask[:, l, :]),
                                       ALU.mult).then_inc(S["level_a"], 1)

        @block.vector
        def _(dve):
            for a in (at[:, :], ak[:, :], ab[:, :, :], ar[:, :, :]):
                dve.memset(a, 0.0)
            dve.memset(raw[:, 0:1], 0.0).then_inc(S["unit_free"], 1)
            dve.sem_inc(S["raw_free"], 1)
            per = 4 + 3 + 2 + 7 + 2 + 3
            with dve.Fori(0, units) as u:
                step = Chain(dve, S["dve_step"], u * per)
                yo = flat(y[:, bass.ds(u, 1), :])
                for t, (dst, what) in enumerate(((r, "r"), (k, "k"), (v, "v"), (yo, "g"))):
                    dve.wait_ge(S["evacuated"], u * nt + (t + 1))
                    step(dve.tensor_tensor(bonus, raw[:, 0:T], raw[:, 1:], ALU.subtract))
                    dve.scalar_tensor_tensor(dst, bonus, core.col_at("mu_" + what, u), raw[:, 1:], ALU.mult, ALU.add) \
                        .then_inc(S["mixed"], 1)
                    dve.wait_ge(S["mixed"], u * nt + (t + 1))
                    dve.sem_inc(S["raw_free"], 1)
                dve.tensor_scalar(kk, k, core.col_at("k_k", u), None, ALU.mult).then_inc(S["kk_raw"], 1)
                dve.wait_ge(S["rooted"], u + 1)
                step(dve.tensor_scalar(tmp[:, :], tmp[:, :], 1e-12, None, ALU.max))
                step(dve.reciprocal(tmp[:, :], tmp[:, :]))
                step(dve.tensor_tensor(kk, kk, tmp[:, :], ALU.mult))
                dve.wait_ge(S["low_kept"], u + 1)
                step(dve.tensor_scalar(tmp[:, :], b, -1.0, core.col_at("k_a", u), ALU.add, ALU.mult))
                step(dve.scalar_tensor_tensor(k, tmp[:, :], 1.0, k, ALU.add, ALU.mult))
                dve.scalar_tensor_tensor(bonus, r, core.col_at("r_k", u), k, ALU.mult, ALU.mult).then_inc(S["bonus_in"], 1)
                dve.tensor_tensor(b, kk, b, ALU.mult)
                step(dve.tensor_scalar(lw, lw, -float(np.exp(-0.5)), None, ALU.mult))
                for c in range(NCH):
                    ins = dve.tensor_tensor_scan(cum[:, cs(c)], lw[:, cs(c)], lw[:, cs(c)], 0.0, ALU.add, ALU.bypass)
                step(ins)
                cc = chunks(cum)
                last, mid = cc[:, :, C - 1:C], cc[:, :, C // 2 - 1:C // 2]
                gv = gc[:, :].unsqueeze(2)
                step(dve.tensor_tensor(gv[:, 0:NCH - 1, :], last[:, 0:NCH - 1, :], mid[:, 0:NCH - 1, :], ALU.subtract))
                step(dve.tensor_tensor(gv[:, 0:NCH - 1, :], gv[:, 0:NCH - 1, :], mid[:, 1:NCH, :], ALU.add))
                step(dve.tensor_tensor(chunks(WT[:, :]), cc, mid.to_broadcast([P, NCH, C]), ALU.subtract))
                step(dve.tensor_tensor(lw, WT[:, :], lw, ALU.subtract))
                dve.tensor_copy(cum, WT[:, :]).then_inc(S["cum_ready"], 1)
                dve.wait_ge(S["bonus_done"], u + 1)
                step(dve.tensor_tensor(bonus, PC, v, ALU.mult))
                dve.wait_ge(S["expd"], u * 2 + 2)
                dve.tensor_tensor(r, r, cum, ALU.mult)
                dve.tensor_tensor(kk, kk, lw, ALU.mult)
                dve.scalar_tensor_tensor(b, b, -1.0, tmp[:, :], ALU.mult, ALU.mult)
                dve.tensor_tensor(k, k, tmp[:, :], ALU.mult).then_inc(S["factors"], 1)
                for sub in range(2):
                    e = u * 2 + sub
                    eye = per_chunk(core.ident[:, :])
                    dve.tensor_copy(chunks(X[:, :]), eye)
                    step(dve.tensor_copy(chunks(XT[:, :]), eye))
                    wait_alone(dve, S["prods"], e + 1, S["passed"])
                    dve.copy_predicated(chunks(at[:, :]), bits(core.strict[:, :]), chunks(PA))
                    dve.copy_predicated(chunks(XT[:, :]), bits(core.level_mask[:, 0, :]), chunks(PA))
                    dve.copy_predicated(chunks(X[:, :]), bits(core.level0_T[:, :]), chunks(PB))
                    dve.copy_predicated(chunks(ak[:, :]), bits(core.strict[:, :]), chunks(PC)).then_inc(S["kept"], 1)
                    wait_alone(dve, S["prods2"], e + 1, S["passed"])
                    dve.copy_predicated(chunks(ab[:, sub, :]), bits(core.upto[:, :]), chunks(PC))
                    dve.copy_predicated(chunks(ar[:, sub, :]), bits(core.upto[:, :]), chunks(PA)).then_inc(S["kept"], 1)
                    for l in range(1, LEVELS):
                        for hf in range(2):
                            n = (e * NL + (l - 1)) * 2 + (hf + 1)
                            h = slice(hf * 512, hf * 512 + 512)
                            dve.wait_ge(S["xyx"], n)
                            if l < NL:
                                xe = level_views(X[:, h], l)[0]
                                dve.tensor_tensor(xe, xe, level_views(PA[:, h], l)[0], ALU.add)
                            xo = level_views(XT[:, h], l)[1]
                            dve.tensor_tensor(xo, xo, level_views(PB[:, h], l)[1], ALU.add).then_inc(S["x_ready"], 1)
                    dve.wait_ge(S["u_done"], e + 1)
                    uc = PA[:, 0:NCH * 64].rearrange("p (c i) -> p c i", c=NCH)
                    dve.tensor_copy(sa[:, 0, sub, :], uc[:, 0, :])
                    dve.tensor_copy(U0[:, 1:, sub, :], uc[:, 1:, :]).then_inc(S["u_kept"], 1)
                dve.wait_ge(S["u_kept"], u * 2 + 2)
                dve.sem_inc(S["sa_ready"], 1)
                for c in range(NCH):
                    if c:
                        dve.wait_ge(S["sa_done"], u * (NCH - 1) + c)
                        dve.tensor_tensor(sa[:, c, :, :], PB.rearrange("p (a n) -> p a n", a=2)[:, :, c * 64:c * 64 + 64],
                                          U0[:, c, :, :], ALU.add).then_inc(S["sa_ready"], 1)
                    if c < NCH - 1:
                        dve.wait_ge(S["m_done"], u * (NCH - 1) + (c + 1))
                        dve.tensor_scalar(M[:, c + 1, :], PC[:, c * 64:c * 64 + 64], gc[:, c:c + 1], None, ALU.mult) \
                            .then_inc(S["m_ready"], 1)
                dve.wait_ge(S["mean_done"], u + 1)
                dve.tensor_tensor(lw, lw, PB, ALU.subtract).then_inc(S["centred"], 1)
                dve.wait_ge(S["rooted2"], u + 1)
                step(dve.reciprocal(tmp[:, :], tmp[:, :]))
                step(dve.scalar_tensor_tensor(lw, lw, core.col_at("rw_ln_g", u), tmp[:, :], ALU.mult, ALU.mult))
                step(dve.scalar_tensor_tensor(lw, lw, core.col_at("rw_ln_b", u), bonus, ALU.add, ALU.add))
                dve.wait_ge(S["silu_done"], u + 1)
                dve.tensor_tensor(yo, yo, lw, ALU.mult).then_inc(S["unit_free"], 1)
                step.ends(per)


def block_3(core, d):
    nc = core.nc
    with Stage(nc, "b3") as st:
        core.hT = st.sb("hT", [P, KD, T])
        mats, masks = st.sb("mats", [P, 3, P]), st.sb("masks", [P, 3, P])
        core.same_head, core.mean_head, core.triangle = (mats[:, n, :] for n in range(3))
        core.strict, core.upto, core.level0_T = (masks[:, n, :] for n in range(3))
        with Stage(nc, "consts3") as s2:
            got = s2.sem("consts_loaded")
            block = s2.block()

            @block.sync
            def _(sp):
                sp.dma_start(mats[:, :, :].rearrange("p a b -> p (a b)"), d["c_mat3"]).then_inc(got, 16)
                sp.dma_start(masks[:, :, :].rearrange("p a b -> p (a b)"), d["c_mask3"]).then_inc(got, 16)
                sp.wait_ge(got, 32)
        rms_norm(core, "rms3", core.xT, "norm_g_3", core.hT)
        park(core, core.xT, d["x_park"])
        with Stage(nc, "rws") as s2:
            y, lo = s2.sb("y", [P, 4, T]), s2.sb("lo", [P, T])
            rwkv_low_rank(core, d["w3"], lo)
            rwkv_branch(core, d["w3"], d["w_up"], lo, core.xT, y, d["gate_park"])
            weighted_projection(core, "yrw", y, 4, d["wrw"], d["gate_park"], 2 * KD, core.xT, False)
        with Stage(nc, "sbs") as s2:
            y = s2.sb("y", [P, 4, T])
            stick_breaking_branch(core, d["w3"], y)
            weighted_projection(core, "ysb", y, 4, d["wsb"], d["gate_park"], 0, core.xT, True)
        with Stage(nc, "ssds") as s2:
            y = s2.sb("y", [P, KD, T])
            with Stage(nc, "ssdp") as s3:
                cols = s3.sb("cols", [P, 3 * NCH * SSH])
                bt, ct, btok, cb = (s3.sb("bt", [P, T]), s3.sb("ct", [P, T]), s3.sb("btok", [P, NCH, P]),
                                    s3.sb("cb", [P, 2, T]))
                ssd_gates(core, d["w3"], d["ssd_rows"], cols, bt, ct, btok, cb)
                ssd_branch(core, d["w3"], d["ssd_rows"], cols, ct, btok, cb, y)
            rms_norm(core, "rms_ssd", y, "ssd_ng", y)
            weighted_projection(core, "yssd", y, KD, d["wssd"], d["gate_park"], KD, core.xT, True)
        park(core, core.hT, d["x_park"], back=True)
        out_projection(core, "o3", core.xT, KD, d["wo3"], core.hT)
        rms_norm(core, "fin3", core.hT, "final_g_3", core.xT)


SEG1 = segments([("hg_q", 512), ("hg_f", 512), ("hg_i", 512), ("hg_z", 512), ("gla_q", 256), ("gla_k", 256),
                 ("gla_v", 512), ("gla_a", 16), ("gla_z", 512), ("ml_q", 256), ("ml_k", 256), ("ml_v", 512),
                 ("ml_i", 4), ("ml_f", 4), ("ml_o", 512), ("ml_z", 512)])


def tile_order_1():
    def tile(name, n):
        s = SEG1[name][0] + n * P
        return s, min(s + P, SEG1[name][1])
    out = []
    for h in range(4):
        out += [tile("hg_f", h), tile("hg_q", h), tile("hg_i", h), tile("hg_z", h)]
    out.append(tile("gla_a", 0))
    for u in range(2):
        out += [tile("gla_q", u), tile("gla_k", u), tile("gla_v", 2 * u), tile("gla_v", 2 * u + 1),
                tile("gla_z", 2 * u), tile("gla_z", 2 * u + 1)]
    out.append((SEG1["ml_i"][0], SEG1["ml_f"][1]))
    for u in range(2):
        out += [tile("ml_q", u), tile("ml_k", u)]
        out += [tile(n, 2 * u + s) for n in ("ml_v", "ml_o", "ml_z") for s in range(2)]
    return out


def in_tiles(w, ranges):
    k = w.shape[0] // P
    out = np.zeros((len(ranges), P, k, P), np.float32)
    v = w.reshape(k, P, -1)
    for n, (a, b) in enumerate(ranges):
        out[n, :, :, :b - a] = v[:, :, a:b].transpose(1, 0, 2)
    return out.reshape(len(ranges) * P, k * P)


def out_tiles(w):
    return in_tiles(w, [(e * P, e * P + P) for e in range(w.shape[1] // P)])


def columns(i):
    b = i["b_in"][0]
    out = [("norm_w", i["norm_w"][0])]
    for n in ("hg_q", "hg_f", "hg_z", "gla_q", "gla_k", "gla_z", "ml_q", "ml_k", "ml_o", "ml_z"):
        out.append((n, b[slice(*SEG1[n])]))
    out += [("gla_a_b", b[slice(*SEG1["gla_a"])]), ("ml_i_b", b[slice(*SEG1["ml_i"])]),
            ("ml_f_b", b[slice(*SEG1["ml_f"])]), ("hg_lb", i["hg_lb_logits"][0]),
            ("lb", np.zeros(512, np.float32)), ("one_minus_lb", np.zeros(512, np.float32)),
            ("hg_nw", i["hg_norm_w"][0]), ("gla_b_a2", i["gla_b_a2"][0]), ("gla_nw", i["gla_norm_w"][0]),
            ("ml_cb", i["ml_conv_b"][0]), ("ml_nw", i["ml_norm_w"][0]), ("final_norm_w", i["final_norm_w"])]
    out += [(f"ml_cw{j}", i["ml_conv_w"][0, j]) for j in range(4)]
    return out + columns_2(i) + columns_3(i)


CONSTS = (NORM_EPS, LN_EPS, GN_EPS, -0.5)


def pack_columns(i):
    index, parts, at = {}, [], 0
    for name, vec in columns(i):
        n = -(-vec.size // P)
        col = np.zeros(n * P, np.float32)
        col[:vec.size] = vec.reshape(-1)
        parts.append(col.reshape(n, P).T)
        index[name] = at
        at += n
    for v in CONSTS:
        parts.append(np.full((P, 1), v, np.float32))
        index[v] = at
        at += 1
    return np.ascontiguousarray(np.concatenate(parts, 1)), index


def level_masks():
    s, t = np.arange(P)[:, None], np.arange(P)[None, :]
    top = np.floor(np.log2(np.maximum(s ^ t, 1))).astype(int)
    return np.stack([((s < t) & (top == l)) for l in range(LEVELS)], 1).astype(np.float32)


def shape_constants():
    s, t = np.arange(P)[:, None], np.arange(P)[None, :]
    mats = {"ident": np.eye(P), "ones": np.ones((P, P)), "mean_d": np.full((P, P), 1.0 / D),
            "mean_p": np.full((P, P), 1.0 / P),
            "mean_v": np.full((P, P), 1.0 / RDV), "tri": (t >= s)}
    return {n: m.astype(np.float32) for n, m in mats.items()}


def lay_out(i):
    i = {n: np.asarray(a) for n, a in i.items()}
    d = {"x": i["x"][0]}
    w1 = i["w_in"][0]
    d["w1"] = in_tiles(w1, tile_order_1())
    b = i["b_in"][0]
    d["b1_vrow"] = np.concatenate([b[slice(*SEG1[n])] for n in ("hg_i", "gla_v", "ml_v")])[None, :]
    d["gla_w_a2"] = i["gla_w_a2"][0]
    for n, name in enumerate(("wo1a", "wo1b", "wo1c")):
        d[name] = out_tiles(i["w_out"][0, n * 512:(n + 1) * 512])
    d["cols"], index = pack_columns(i)
    for n, m in shape_constants().items():
        d["c_" + n] = m
    d["c_level_mask"] = level_masks().reshape(P, LEVELS * P)
    lay_out_2(i, d)
    lay_out_3(i, d)
    return {n: np.ascontiguousarray(a) for n, a in d.items()}, index


def build(nc, d, out, index, blocks=(1, 2, 3)):
    core = Core()
    core.nc, core.index = nc, index
    Stage.ended = []
    with ExitStack() as ctx:
        core.ps = ctx.enter_context(nc.psum_tensor("ps", [P, 8 * 512], F32))
        core.xT = ctx.enter_context(nc.sbuf_tensor("xT", [P, KD, T], F32))
        core.cols = ctx.enter_context(nc.sbuf_tensor("cols_sb", list(d["cols"].shape), F32))
        core.col = lambda name, n: core.cols[:, index[name] + n:index[name] + n + 1]
        core.col_at = lambda name, n: core.cols[:, bass.ds(n + index[name], 1)]
        core.const = lambda v: core.col(v, 0)
        names = ["ident", "ones", "mean_d", "mean_p", "mean_v", "tri"]
        tiles = {n: ctx.enter_context(nc.sbuf_tensor("c_" + n + "_sb", [P, P], F32)) for n in names}
        core.ident, core.ones, core.mean_d, core.mean_p, core.mean_v, core.tri = (tiles[n] for n in names)
        core.level_mask = ctx.enter_context(nc.sbuf_tensor("level_mask", [P, LEVELS, P], F32))
        with Stage(nc, "consts") as st:
            got = st.sem("consts_loaded")
            block = st.block()

            @block.sync
            def _(sp):
                for n in names:
                    sp.dma_start(tiles[n][:, :], d["c_" + n]).then_inc(got, 16)
                sp.dma_start(core.level_mask[:, :, :].rearrange("p l t -> p (l t)"), d["c_level_mask"]).then_inc(got, 16)
                sp.dma_start(core.cols[:, :], d["cols"]).then_inc(got, 16)
                sp.wait_ge(got, 16 * (len(names) + 2))
        load_input(core, d["x"])
        if 1 in blocks:
            block_1(core, d)
        if 2 in blocks:
            block_2(core, d)
        if 3 in blocks:
            block_3(core, d)
        store_output(core, core.xT, out)


SCRATCH = {"ml_rows": (12, T), "o_park": (RH * RDV, T), "x_park": (D, T), "gate_park": (3 * D, T), "ssd_rows": (2 * SSH, T)}


def kernel(**inputs):
    from concourse import bacc
    from concourse.bass_utils import run_bass_kernel_spmd

    arrays, index = lay_out(inputs)
    nc = bacc.Bacc("TRN2", target_bir_lowering=False, num_devices=1)
    d = {n: nc.dram_tensor("in_" + n, a.shape, mybir.dt.from_np(a.dtype), kind="ExternalInput").ap()
         for n, a in arrays.items()}
    for n, shape in SCRATCH.items():
        d[n] = nc.dram_tensor("scratch_" + n, shape, F32, kind="Internal").ap()
    out = nc.dram_tensor("out_0", (T, D), F32, kind="ExternalOutput").ap()
    build(nc, d, out, index)
    r = run_bass_kernel_spmd(nc, [{"in_" + n: a for n, a in arrays.items()}], core_ids=[0])
    return r.results[0]["out_0"].reshape(1, T, D)
```

```python
from contextlib import ExitStack

import numpy as np

import concourse.bass as bass
from concourse import mybir
from concourse.alu_op_type import AluOpType as ALU

ACT = mybir.ActivationFunctionType
F32 = mybir.dt.float32
F32R = mybir.dt.float32r
U32 = mybir.dt.uint32

P = 128
T = 1024
D = 1024
KD = D // P
C = 128
NCH = T // C
NORM_EPS = 1e-6
LN_EPS = 1e-5
GN_EPS = 64e-5


def segments(sizes):
    at, out = 0, {}
    for name, n in sizes:
        out[name] = (at, at + n)
        at += n
    return out


class Chain:

    def __init__(self, eng, sem, base=0):
        self.eng, self.sem, self.base, self.k = eng, sem, base, 0

    def __call__(self, ins):
        self.k += 1
        ins.then_inc(self.sem, 1)
        self.eng.wait_ge(self.sem, self.base + self.k)

    def ends(self, per):
        assert self.k == per, (self.k, per)


def wait_alone(eng, sem, value, passed):
    eng.wait_ge(sem, value)
    eng.sem_inc(passed, 1)


def per_chunk(mat):
    return mat.unsqueeze(1).to_broadcast([P, NCH, C])


def bits(mask):
    return per_chunk(mask.bitcast(U32))


def chunks(ap, n=NCH):
    return ap.rearrange("p (c t) -> p c t", c=n)


class Stage:

    ended = []

    def __init__(self, nc, name):
        self.nc, self.name, self.ctx, self.sems = nc, name, ExitStack(), []

    def __enter__(self):
        self.ctx.__enter__()
        return self

    def __exit__(self, *a):
        self.ctx.__exit__(*a)
        if self.sems:
            for s in Stage.ended:
                self.nc.release_semaphore(s)
            Stage.ended = self.sems

    def sb(self, name, shape, dt=F32):
        return self.ctx.enter_context(self.nc.sbuf_tensor(f"{self.name}_{name}", shape, dt))

    def sem(self, name):
        self.sems.append(self.nc.alloc_semaphore(f"{self.name}_{name}"))
        return self.sems[-1]

    def block(self):
        block = self.ctx.enter_context(self.nc.Block())

        @block.gpsimd
        def _(pool):
            for s in Stage.ended:
                pool.sem_clear(s)

        return block


class Core:
    pass


def pair(core, n):
    return core.ps[:, n * T:(n + 1) * T]


def project_half(pe, out, w, h, half, m=P, c0=0, nk=KD):
    t = slice(half * 512, half * 512 + 512)
    for k in range(nk):
        ins = pe.matmul(out[0:m, t], w[:, k * P + c0:k * P + c0 + m], h[:, k, t], start=(k == 0), stop=(k == nk - 1))
    return ins


def project_features(pe, out, w, h, m=P, c0=0, nk=KD):
    for half in range(2):
        ins = project_half(pe, out, w, h, half, m, c0, nk)
    return ins


def project_chunk(pe, out, w, h, c, ones=None, bias=None, nk=KD):
    o = out[:, c * C:c * C + P]
    for k in range(nk):
        ins = pe.matmul(o, h[:, k, c * C:c * C + C], w[:, k * P:k * P + P],
                        start=(k == 0), stop=(k == nk - 1 and bias is None))
    if bias is not None:
        ins = pe.matmul(o, ones[0:1, :], bias, start=False, stop=True)
    return ins


def project_tokens(pe, out, w, h, ones=None, bias=None, nk=KD):
    for c in range(NCH):
        ins = project_chunk(pe, out, w, h, c, ones, bias, nk)
    return ins


def load_tiles(sp, core, st, wt, slots, loaded, proj_done, first, ntile, units):
    for t in range(ntile):
        sp.dma_start(slots[:, t, :], wt[(first + t) * P:(first + t + 1) * P, :]).then_inc(loaded[t], 16)
    if units > 1:
        with sp.Fori(1, units) as u:
            for t in range(ntile):
                at = sp.snap(u * (ntile * P) + (first + t) * P)
                sp.wait_ge(proj_done, u * ntile + (t + 1 - ntile))
                sp.dma_start(slots[:, t, :], wt[bass.ds(at, P), :]).then_inc(loaded[t], 16)


class Filler:

    def __init__(self, core, st, name, pair_n, wt, first, places, kinds, ring=2):
        self.core, self.wt, self.first, self.places = core, wt, first, places
        self.kinds, self.n, self.ring, self.out = kinds, len(kinds), ring, pair(core, pair_n)
        assert self.n % ring == 0
        self.w, self.kept_sb = st.sb(name + "_w", [P, ring, D]), st.sb(name + "_out", [P, ring, T])
        self.loaded = [st.sem(f"{name}_loaded{s}") for s in range(ring)]
        self.stored = [st.sem(f"{name}_stored{s}") for s in range(ring)]
        self.done, self.kept = st.sem(name + "_done"), st.sem(name + "_kept")

    def load(self, sp, u, head=False):
        for i in range(self.n):
            at = (self.first + i) * P if head else sp.snap(u * (self.n * P) + (self.first + i) * P)
            if not head or i >= self.ring:
                sp.wait_ge(self.done, u * self.n + (i + 1 - self.ring))
            src = self.wt[at:at + P, :] if head else self.wt[bass.ds(at, P), :]
            sp.dma_start(self.w[:, i % self.ring, :], src).then_inc(self.loaded[i % self.ring], 16)

    def multiply(self, pe, u, i, part=0, parts=1):
        s, (layout, _, bias) = i % self.ring, self.kinds[i]
        w, h = self.w[:, s, :], self.core.hT
        if part == 0:
            pe.wait_ge(self.loaded[s], u * (16 * self.n // self.ring) + 16 * (i // self.ring + 1))
            pe.wait_ge(self.kept, u * self.n + (i + 1))
        if layout == "features":
            todo = [(half * 512, k) for half in range(2) for k in range(KD)]
            for lo, k in todo[part * len(todo) // parts:(part + 1) * len(todo) // parts]:
                ins = pe.matmul(self.out[:, lo:lo + 512], w[:, k * P:k * P + P], h[:, k, lo:lo + 512],
                                start=(k == 0), stop=(k == KD - 1))
        else:
            row = None if bias is None else self.core.brow[0:1, bass.ds(u * (bias[1] * P) + bias[0], P)]
            for c in range(part * NCH // parts, (part + 1) * NCH // parts):
                ins = project_chunk(pe, self.out, w, h, c, self.core.ones, row)
        if part == parts - 1:
            ins.then_inc(self.done, 1)

    def advance(self, pe, u, begin, end):
        for n in range(begin, end):
            self.multiply(pe, u, n // 16, n % 16, 16)

    def keep(self, act, u, i):
        s, (layout, func, bias) = i % self.ring, self.kinds[i]
        act.wait_ge(self.done, u * self.n + (i + 1))
        if i >= self.ring:
            act.wait_ge(self.stored[s], u * (16 * self.n // self.ring) + 16 * (i // self.ring))
        kw = {"bias": self.core.col_at(bias[0], u * bias[2] + bias[1])} if layout == "features" and bias is not None else {}
        act.activation(self.kept_sb[:, s, :], self.out, func, **kw).then_inc(self.kept, 1)
        park, first, stride = self.places[i]
        at = act.snap(u * (stride * P) + first * P)
        act.wait_ge(self.kept, u * self.n + (i + 2))
        act.dma_start(park[bass.ds(at, P), :], self.kept_sb[:, s, :]).then_inc(self.stored[s], 16)

    def begin(self, act):
        act.sem_inc(self.kept, 1)

    def end(self, act, u):
        for s in range(self.ring):
            act.wait_ge(self.stored[s], u * (16 * self.n // self.ring) + 16 * (self.n // self.ring))


def places(dram, n, first=0):
    return [(dram, first + i, n) for i in range(n)]


def load_input(core, x_dram):
    nc = core.nc
    with Stage(nc, "ldx") as st:
        xin = st.sb("xin", [P, 2, D])
        loaded = [st.sem("x_loaded0"), st.sem("x_loaded1")]
        turned, kept = st.sem("turned"), st.sem("kept")
        block = st.block()

        @block.sync
        def _(sp):
            for c in range(NCH):
                if c >= 2:
                    sp.wait_ge(turned, c - 1)
                sp.dma_start(xin[:, c % 2, :], x_dram[c * P:(c + 1) * P, :]).then_inc(loaded[c % 2], 16)

        @block.tensor
        def _(pe):
            for c in range(NCH):
                pe.wait_ge(loaded[c % 2], 16 * (c // 2 + 1))
                if c >= 2:
                    pe.wait_ge(kept, c - 1)
                for k in range(KD):
                    ins = pe.transpose(pair(core, c % 2)[:, k * P:(k + 1) * P],
                                       xin[:, c % 2, k * P:(k + 1) * P], core.ident[:, :])
                ins.then_inc(turned, 1)

        @block.vector
        def _(dve):
            for c in range(NCH):
                dve.wait_ge(turned, c + 1)
                dve.tensor_copy(core.xT[:, :, c * C:(c + 1) * C], chunks(pair(core, c % 2))).then_inc(kept, 1)


def rms_norm(core, name, src, gain, dst, eps=NORM_EPS, park=None):
    with Stage(core.nc, name) as st:
        sq = st.sb("sq", [P, 2, T])
        rstd = st.sb("rstd", [P, T])
        squared, summed, rooted, normed, parked = (st.sem(n) for n in ("squared", "summed", "rooted", "normed", "parked"))
        block = st.block()

        @block.sync
        def _(sp):
            if park is not None:
                for k in range(KD):
                    sp.dma_start(park[k * P:(k + 1) * P, :], src[:, k, :]).then_inc(parked, 16)
                sp.wait_ge(parked, 16 * KD)

        @block.scalar
        def _(act):
            for k in range(KD):
                if k >= 2:
                    act.wait_ge(summed, k - 1)
                act.activation(sq[:, k % 2, :], src[:, k, :], ACT.Square).then_inc(squared, 1)
            act.wait_ge(summed, KD)
            act.activation(rstd[:, :], pair(core, 0), ACT.Sqrt, bias=core.const(eps)).then_inc(rooted, 1)

        @block.tensor
        def _(pe):
            for k in range(KD):
                pe.wait_ge(squared, k + 1)
                for half in range(2):
                    ins = pe.matmul(pair(core, 0)[:, half * 512:half * 512 + 512], core.mean_d[:, :],
                                    sq[:, k % 2, half * 512:half * 512 + 512],
                                    start=(k == 0), stop=(k == KD - 1))
                ins.then_inc(summed, 1)

        @block.vector
        def _(dve):
            dve.wait_ge(rooted, 1)
            step = Chain(dve, normed)
            step(dve.reciprocal(rstd[:, :], rstd[:, :]))
            for k in range(KD):
                dve.scalar_tensor_tensor(dst[:, k, :], src[:, k, :], core.col(gain, k), rstd[:, :],
                                         ALU.mult, ALU.mult)


class SplitProjection:

    def __init__(self, st, y, nk, ring):
        self.y, self.nk, self.ring = y, nk, ring
        self.y_hi, self.y_lo = (st.sb(n, [P, nk, T], F32R) for n in ("y_hi", "y_lo"))
        self.w = st.sb("w", [P, ring, nk * P])
        self.w_hi, self.w_lo = (st.sb(n, [P, ring, nk * P], F32R) for n in ("w_hi", "w_lo"))
        self.loaded = [st.sem(f"w_loaded{s}") for s in range(ring)]
        self.w_rounded, self.w_cut, self.y_rounded, self.y_cut, self.done, self.passed = (
            st.sem(n) for n in ("w_rounded", "w_cut", "y_rounded", "y_cut", "projected", "passed"))

    def load(self, sp, wt, first, count):
        for s in range(self.ring):
            sp.dma_start(self.w[:, s, :], wt[(first + s) * P:(first + s + 1) * P, :]).then_inc(self.loaded[s], 16)
        with sp.Fori(1, count // self.ring) as i:
            for s in range(self.ring):
                self.load_next(sp, wt, first, i, s)

    def load_next(self, sp, wt, first, i, s):
        at = sp.snap(i * (self.ring * P) + (first + s) * P)
        sp.wait_ge(self.w_cut, i * self.ring + (s + 1 - self.ring))
        sp.dma_start(self.w[:, s, :], wt[bass.ds(at, P), :]).then_inc(self.loaded[s], 16)

    def cut_weights(self, pool, count):
        def cut(i, s):
            w, hi, lo = self.w[:, s, :], self.w_hi[:, s, :], self.w_lo[:, s, :]
            wait_alone(pool, self.loaded[s], 16 * i + 16, self.passed)
            pool.tensor_copy(hi, w).then_inc(self.w_rounded, 1)
            pool.wait_ge(self.w_rounded, i * self.ring + (s + 1))
            pool.tensor_tensor(lo, w, hi, ALU.subtract).then_inc(self.w_cut, 1)
        for s in range(self.ring):
            cut(0, s)
        with pool.Fori(1, count // self.ring) as i:
            for s in range(self.ring):
                pool.wait_ge(self.done, i * self.ring + (s + 1 - self.ring))
                cut(i, s)

    def round_y(self, act):
        for k in range(self.nk):
            act.activation(self.y_hi[:, k, :], self.y[:, k, :], ACT.Copy).then_inc(self.y_rounded, 1)

    def cut_y(self, dve):
        for k in range(self.nk):
            dve.wait_ge(self.y_rounded, k + 1)
            dve.tensor_tensor(self.y_lo[:, k, :], self.y[:, k, :], self.y_hi[:, k, :], ALU.subtract).then_inc(self.y_cut, 1)

    def multiply(self, pe, out, i, s):
        pe.wait_ge(self.w_cut, i * self.ring + (s + 1))
        for k in range(self.nk):
            pe.wait_ge(self.y_cut, k + 1)
            for w, parts in ((self.w_hi, (self.y_hi, self.y_lo)), (self.w_lo, (self.y_hi,))):
                for half in range(2):
                    t = slice(half * 512, half * 512 + 512)
                    for y in parts:
                        ins = pe.matmul(out[:, t], w[:, s, k * P:k * P + P], y[:, k, t],
                                        start=(k == 0 and w is self.w_hi and y is self.y_hi),
                                        stop=(k == self.nk - 1 and w is self.w_lo))
        ins.then_inc(self.done, 1)


def out_projection(core, name, y, nk, wt, dst):
    with Stage(core.nc, name) as st:
        proj = SplitProjection(st, y, nk, 2)
        added = st.sem("added")
        block = st.block()

        @block.sync
        def _(sp):
            proj.load(sp, wt, 0, KD)

        @block.gpsimd
        def _(pool):
            proj.cut_weights(pool, KD)

        @block.tensor
        def _(pe):
            with pe.Fori(0, KD // 2) as i:
                for s in range(2):
                    pe.wait_ge(added, 2 * i + (s + 1))
                    proj.multiply(pe, pair(core, s), i, s)

        @block.scalar
        def _(act):
            proj.round_y(act)

        @block.vector
        def _(dve):
            dve.sem_inc(added, 2)
            proj.cut_y(dve)
            with dve.Fori(0, KD // 2) as i:
                for s in range(2):
                    dve.wait_ge(proj.done, 2 * i + (s + 1))
                    o = dst[:, bass.ds(2 * i + s, 1), :].rearrange("p a t -> p (a t)")
                    dve.tensor_tensor(o, pair(core, s), o, ALU.add).then_inc(added, 1)


def store_output(core, src, out_dram):
    with Stage(core.nc, "out") as st:
        rows = st.sb("rows", [P, 2, D])
        stored = [st.sem("stored0"), st.sem("stored1")]
        turned, copied = st.sem("turned"), st.sem("copied")
        block = st.block()

        @block.tensor
        def _(pe):
            for c in range(NCH):
                if c >= 2:
                    pe.wait_ge(copied, c - 1)
                for k in range(KD):
                    ins = pe.transpose(pair(core, c % 2)[:, k * P:(k + 1) * P],
                                       src[:, k, c * C:(c + 1) * C], core.ident[:, :])
                ins.then_inc(turned, 1)

        @block.vector
        def _(dve):
            for c in range(NCH):
                dve.wait_ge(turned, c + 1)
                if c >= 2:
                    dve.wait_ge(stored[c % 2], 16 * (c // 2))
                dve.tensor_copy(rows[:, c % 2, :], pair(core, c % 2)).then_inc(copied, 1)

        @block.sync
        def _(sp):
            for c in range(NCH):
                sp.wait_ge(copied, c + 1)
                sp.dma_start(out_dram[c * P:(c + 1) * P, :], rows[:, c % 2, :]).then_inc(stored[c % 2], 16)
            for s in range(2):
                sp.wait_ge(stored[s], 16 * (NCH // 2))


GLA_A, ML_IF, GLA_FILL, ML_FILL = 16, 17, 18, 30
LEVELS = 7


def level_views(ap, lvl):
    v = ap.rearrange("p (n two m) -> p n two m", two=2, m=1 << lvl)
    return v[:, :, 0, :], v[:, :, 1, :]


def flat(ap):
    return ap.rearrange("p a t -> p (a t)")


def gla_gates(core, wt, tile, w_a2, gl):
    with Stage(core.nc, "glagate") as st:
        w = st.sb("w", [P, D])
        wa2 = st.sb("wa2", [16, 2 * P])
        aT = st.sb("aT", [16, T])
        mag = st.sb("mag", [P, 2, T])
        w_loaded, a2_loaded, a_done, a_kept, logit_done, mag_ready, softened, dve_step, act_step = (
            st.sem(n) for n in ("w_loaded", "a2_loaded", "a_done", "a_kept", "logit_done", "mag_ready",
                                "softened", "dve_step", "act_step"))
        block = st.block()

        @block.sync
        def _(sp):
            sp.dma_start(w[:, :], wt[tile * P:(tile + 1) * P, :]).then_inc(w_loaded, 16)
            sp.dma_start(wa2[:, :], w_a2).then_inc(a2_loaded, 16)

        @block.tensor
        def _(pe):
            pe.wait_ge(w_loaded, 16)
            project_features(pe, pair(core, 0), w, core.hT, m=16).then_inc(a_done, 1)
            pe.wait_ge(a2_loaded, 16)
            pe.wait_ge(a_kept, 1)
            for n in range(2):
                for half in range(2):
                    ins = pe.matmul(pair(core, 1 + n)[:, half * 512:half * 512 + 512],
                                    wa2[:, n * P:n * P + P], aT[:, half * 512:half * 512 + 512],
                                    start=True, stop=True)
                ins.then_inc(logit_done, 1)

        @block.scalar
        def _(act):
            act.wait_ge(a_done, 1)
            act.activation(aT[:, :], pair(core, 0)[0:16, :], ACT.Identity, bias=core.col("gla_a_b", 0)[0:16, :]) \
                .then_inc(a_kept, 1)
            step = Chain(act, act_step)
            for n in range(2):
                act.wait_ge(mag_ready, n + 1)
                step(act.activation(mag[:, n, :], mag[:, n, :], ACT.Exp, scale=-1.0))
                act.activation(mag[:, n, :], mag[:, n, :], ACT.Ln, bias=1.0).then_inc(softened, 1)

        @block.vector
        def _(dve):
            step = Chain(dve, dve_step)
            for n in range(2):
                dve.wait_ge(logit_done, n + 1)
                b = core.col("gla_b_a2", n)
                dve.tensor_scalar(gl[:, n, :], pair(core, 1 + n), b, 0.0, ALU.add, ALU.min)
                step(dve.tensor_scalar(mag[:, n, :], pair(core, 1 + n), b, None, ALU.add))
                dve.scalar_tensor_tensor(mag[:, n, :], mag[:, n, :], -1.0, mag[:, n, :], ALU.mult, ALU.max).then_inc(mag_ready, 1)
            for n in range(2):
                dve.wait_ge(softened, n + 1)
                step(dve.tensor_tensor(gl[:, n, :], gl[:, n, :], mag[:, n, :], ALU.subtract))
                step(dve.tensor_scalar(gl[:, n, :], gl[:, n, :], 1.0 / 16.0, None, ALU.mult))


def hg_lower_bound(core):
    with Stage(core.nc, "lb") as st:
        e, one = st.sb("e", [P, 4]), st.sb("one", [P, 4])
        dve_step, exped, shifted = st.sem("dve_step"), st.sem("exped"), st.sem("shifted")
        block = st.block()
        logits = core.cols[:, core.index["hg_lb"]:core.index["hg_lb"] + 4]
        lb = core.cols[:, core.index["lb"]:core.index["lb"] + 4]
        om = core.cols[:, core.index["one_minus_lb"]:core.index["one_minus_lb"] + 4]

        @block.vector
        def _(dve):
            step = Chain(dve, dve_step)
            dve.tensor_tensor(e[:, :], logits, logits, ALU.subtract).then_inc(shifted, 1)
            dve.wait_ge(exped, 1)
            step(dve.reciprocal(one[:, :], e[:, :]))
            step(dve.tensor_tensor(e[:, :], e[:, :], one[:, :], ALU.mult))
            step(dve.tensor_tensor(lb, e[:, :], e[:, :], ALU.subtract))
            step(dve.tensor_scalar(om, lb, -1.0, 1.0, ALU.mult, ALU.add))

        @block.scalar
        def _(act):
            act.wait_ge(shifted, 1)
            act.activation(e[:, :], e[:, :], ACT.Exp).then_inc(exped, 1)


def vector_decay_branch(core, name, nsub, units, wt, fill_first, fill_places, fill_kinds, parts, wcol, y, source=None, gl=None):
    hg = nsub == 1
    order = ["f", "q", "v0", "z0"] if hg else []
    nt = len(order)
    NE = LEVELS + 1
    places_of_parts = ["start"] + list(range(-1, LEVELS)) + ["keys", "update", "out"] + [f"mean{n}" for n in range(nsub)]
    ends = np.cumsum(parts).tolist()
    span = dict(zip(places_of_parts, zip([0] + ends, ends)))
    with Stage(core.nc, name) as st:
        if hg:
            w = st.sb("w", [P, nt, D])
            loaded = [st.sem(f"w_loaded{t}") for t in range(nt)]
        else:
            q_loaded, k_loaded, v_loaded, z_loaded = (st.sem(n + "_loaded") for n in "qkvz")
        fill = Filler(core, st, "fill", 3, wt, fill_first, fill_places, fill_kinds, ring=3 if hg else 2)
        assert ends[-1] == 16 * fill.n
        q, k, b = st.sb("q", [P, T]), st.sb("k", [P, T]), st.sb("b", [P, T])
        v = st.sb("v", [P, NCH, nsub, P])
        ex = st.sb("ex", [P, 2, T])
        qs, ks = st.sb("qs", [P, 2, T]), st.sb("ks", [P, 2, T])
        att = st.sb("att", [P, nsub, T])
        state = st.sb("state", [P, NCH, P])
        ktok, sq = qs[:, 0, :], qs[:, 1, :]
        S = {n: st.sem(n) for n in (
            "proj_done", "evacuated", "unit_free", "qk_ready", "gate_ready", "log_ready", "expo_ready", "expd",
            "factors", "level_done", "att_kept", "keys_turned", "keys_kept", "update_done", "state_ready",
            "out_done", "squared", "mean_done", "rooted", "dve_step", "passed")}
        A, B = [pair(core, 0), pair(core, 1)], pair(core, 2)
        into = (A[1], B)

        def rows(sub):
            return slice(sub * 64, sub * 64 + 64) if nsub == 2 else slice(0, P)

        block = st.block()

        @block.sync
        def _(sp):
            if hg:
                for n in range(nt):
                    sp.dma_start(w[:, n, :], wt[n * P:(n + 1) * P, :]).then_inc(loaded[n], 16)
                fill.load(sp, 0, True)
                with sp.Fori(1, units) as u:
                    for n in range(nt):
                        at = sp.snap(u * (nt * P) + n * P)
                        sp.wait_ge(S["proj_done"], u * nt + (n + 1 - nt))
                        sp.dma_start(w[:, n, :], wt[bass.ds(at, P), :]).then_inc(loaded[n], 16)
                    fill.load(sp, u)
            else:
                def inputs(q_at, k_at, v_at):
                    sp.dma_start(q[:, :], q_at).then_inc(q_loaded, 16)
                    sp.dma_start(k[:, :], k_at).then_inc(k_loaded, 16)
                    for sub in range(2):
                        sp.dma_start(v[:, :, sub, :], v_at[sub]).then_inc(v_loaded, 16)
                tiles = source.rearrange("(n p) t -> n p t", p=P)
                inputs(tiles[0], tiles[1], [chunks(tiles[4 + sub]) for sub in range(2)])
                fill.load(sp, 0, True)
                for n in range(2 * units):
                    sp.dma_start(y[:, n, :], tiles[8 + n]).then_inc(z_loaded, 16)
                with sp.Fori(1, units) as u:
                    at = [sp.snap(u * (2 * P) + n * P) for n in (0, 1, 4, 5)]
                    sp.wait_ge(S["unit_free"], u + 1)
                    q_at, k_at, *v_at = [source[bass.ds(a, P), :] for a in at]
                    inputs(q_at, k_at, [chunks(a) for a in v_at])
                    fill.load(sp, u)

        @block.tensor
        def _(pe):
            with pe.Fori(0, units) as u:
                pe.wait_ge(S["unit_free"], u + 1)
                for t, what in enumerate(order):
                    pe.wait_ge(loaded[t], 16 * u + 16)
                    if t >= 2:
                        pe.wait_ge(S["evacuated"], u * nt + (t - 1))
                    if what[0] == "v":
                        bias = core.brow[0:1, bass.ds(u * P, P)]
                        ins = project_tokens(pe, into[t % 2], w[:, t, :], core.hT, core.ones, bias)
                    else:
                        ins = project_features(pe, into[t % 2], w[:, t, :], core.hT)
                    ins.then_inc(S["proj_done"], 1)
                fill.advance(pe, u, *span["start"])
                pe.wait_ge(S["qk_ready"], u + 1)
                for l in range(-1, LEVELS):
                    if l >= 0:
                        pe.wait_ge(S["factors"], u * NE + (l + 1))
                        if not hg:
                            pe.wait_ge(S["att_kept"], u * (LEVELS + 1) + (l + 1))
                        elif l >= 1:
                            pe.wait_ge(S["att_kept"], u * (LEVELS + 1) + l)
                        else:
                            pe.wait_ge(S["evacuated"], u * nt + nt)
                    lhs, rhs = (k[:, :], q[:, :]) if l < 0 else (ks[:, l % 2, :], qs[:, l % 2, :])
                    for sub in range(nsub):
                        o = A[(l + 1) % 2] if hg else A[sub]
                        for c in range(NCH):
                            cs = slice(c * C, c * C + C)
                            ins = pe.matmul(o[:, cs], lhs[rows(sub), cs], rhs[rows(sub), cs], start=True, stop=True)
                    ins.then_inc(S["level_done"], 1)
                    fill.advance(pe, u, *span[l])
                pe.wait_ge(S["factors"], u * NE + NE)
                for c in range(NCH):
                    ins = pe.transpose(B[:, c * C:c * C + C], k[:, c * C:c * C + C], core.ident[:, :])
                ins.then_inc(S["keys_turned"], 1)
                fill.advance(pe, u, *span["keys"])
                pe.wait_ge(S["keys_kept"], u + 1)
                if not hg:
                    pe.wait_ge(v_loaded, u * 32 + 32)
                for c in range(NCH - 1):
                    for sub in range(nsub):
                        r = rows(sub)
                        ins = pe.matmul(B[r, c * P:c * P + P], ktok[:, c * C + r.start:c * C + r.stop], v[:, c, sub, :],
                                        start=True, stop=True)
                ins.then_inc(S["update_done"], 1)
                fill.advance(pe, u, *span["update"])
                pe.wait_ge(S["state_ready"], u + 1)
                pe.wait_ge(S["att_kept"], u * (LEVELS + 1) + (LEVELS + 1))
                for sub in range(nsub):
                    for c in range(NCH):
                        cs = slice(c * C, c * C + C)
                        ins = pe.matmul(A[sub][:, cs], v[:, c, sub, :], att[:, sub, cs], start=True, stop=(c == 0))
                        if c:
                            ins = pe.matmul(A[sub][:, cs], state[rows(sub), c, :],
                                            q[rows(sub), cs], start=False, stop=True)
                    ins.then_inc(S["out_done"], 1)
                fill.advance(pe, u, *span["out"])
                for sub in range(nsub):
                    pe.wait_ge(S["squared"], u * nsub + (sub + 1))
                    if sub:
                        pe.wait_ge(S["rooted"], u * nsub + sub)
                    for half in range(2):
                        ins = pe.matmul(B[:, half * 512:half * 512 + 512], core.mean_p[:, :],
                                        sq[:, half * 512:half * 512 + 512], start=True, stop=True)
                    ins.then_inc(S["mean_done"], 1)
                    fill.advance(pe, u, *span[f"mean{sub}"])

        @block.scalar
        def _(act):
            def keep_tiles(place):
                for n in range(span[place][0] // 16, span[place][1] // 16):
                    fill.keep(act, u, n)

            fill.begin(act)
            with act.Fori(0, units) as u:
                for t, what in enumerate(order):
                    act.wait_ge(S["proj_done"], u * nt + (t + 1))
                    src = into[t % 2]
                    if what == "f":
                        ins = act.activation(b[:, :], src, ACT.Sigmoid, bias=core.col_at("hg_f", u))
                    elif what == "q":
                        ins = act.activation(q[:, :], src, ACT.Silu, bias=core.col_at("hg_q", u))
                    elif what[0] == "v":
                        ins = act.activation(v[:, :, 0, :], chunks(src), ACT.Copy)
                    else:
                        ins = act.activation(flat(y[:, bass.ds(u, 1), :]), src, ACT.Silu, bias=core.col_at("hg_z", u))
                    ins.then_inc(S["evacuated"], 1)
                if hg:
                    act.wait_ge(S["gate_ready"], u + 1)
                    act.activation(b[:, :], b[:, :], ACT.Ln).then_inc(S["log_ready"], 1)
                for e in range(LEVELS):
                    act.wait_ge(S["expo_ready"], u * NE + (e + 1))
                    act.activation(ex[:, e % 2, :], ex[:, e % 2, :], ACT.Exp).then_inc(S["expd"], 1)
                    keep_tiles(e - 1)
                act.wait_ge(S["expo_ready"], u * NE + NE)
                act.activation(ex[:, 1, :], b[:, :], ACT.Exp)
                act.activation(ex[:, 0, :], ex[:, 0, :], ACT.Exp).then_inc(S["expd"], 1)
                keep_tiles(LEVELS - 1)
                act.wait_ge(S["keys_turned"], u + 1)
                act.activation(ktok, B, ACT.Copy).then_inc(S["keys_kept"], 1)
                keep_tiles("keys")
                for sub in range(nsub):
                    act.wait_ge(S["out_done"], u * nsub + (sub + 1))
                    if sub:
                        act.wait_ge(S["mean_done"], u * nsub + sub)
                    act.activation(sq, A[sub], ACT.Square).then_inc(S["squared"], 1)
                    if sub:
                        act.activation(ks[:, 0, :], B, ACT.Sqrt, bias=core.const(NORM_EPS)).then_inc(S["rooted"], 1)
                    else:
                        keep_tiles("out")
                act.wait_ge(S["mean_done"], u * nsub + nsub)
                act.activation(ks[:, nsub - 1, :], B, ACT.Sqrt, bias=core.const(NORM_EPS)).then_inc(S["rooted"], 1)
                for sub in range(nsub):
                    keep_tiles(f"mean{sub}")
                fill.end(act, u)

        @block.vector
        def _(dve):
            per = (2 if hg else 1) + (NCH - 3) + 1 + 3 * nsub - 1
            dve.memset(qs[:, :, :], 0.0)
            dve.memset(ks[:, :, :], 0.0).then_inc(S["unit_free"], 1)

            def exponents(l):
                be, bo = level_views(b[:, :], l)
                ee, eo = level_views(ex[:, l % 2, :], l)
                m = 1 << l
                ref = be[:, :, m - 1:m].to_broadcast([P, T // (2 * m), m])
                dve.tensor_tensor(ee, ref, be, ALU.subtract)
                dve.tensor_tensor(eo, bo, ref, ALU.subtract).then_inc(S["expo_ready"], 1)

            def keep(n, u):
                wait_alone(dve, S["level_done"], u * (LEVELS + 1) + (n + 1), S["passed"])
                for sub in range(nsub):
                    src = chunks(A[n % 2] if hg else A[sub])
                    dst = chunks(att[:, sub, :])
                    if n == 0:
                        ins = dve.tensor_tensor(dst, src, per_chunk(core.ident[:, :]), ALU.mult)
                    else:
                        ins = dve.copy_predicated(dst, bits(core.level_mask[:, n - 1, :]), src)
                ins.then_inc(S["att_kept"], 1)
                dve.wait_ge(S["att_kept"], u * (LEVELS + 1) + (n + 1))

            with dve.Fori(0, units) as u:
                step = Chain(dve, S["dve_step"], u * per)
                if hg:
                    dve.wait_ge(S["evacuated"], u * nt + 2)
                    step(dve.tensor_scalar(b[:, :], b[:, :], core.col_at("one_minus_lb", u), core.col_at("lb", u),
                                           ALU.mult, ALU.add))
                    dve.tensor_scalar(k[:, :], b[:, :], -1.0, 1.0, ALU.mult, ALU.add).then_inc(S["gate_ready"], 1)
                    dve.wait_ge(S["gate_ready"], u + 1)
                    dve.sem_inc(S["qk_ready"], 1)
                    dve.wait_ge(S["log_ready"], u + 1)
                    decay = b[:, :]
                else:
                    dve.wait_ge(k_loaded, u * 16 + 16)
                    dve.wait_ge(q_loaded, u * 16 + 16)
                    dve.tensor_scalar(q[:, :], q[:, :], 64 ** -0.5, None, ALU.mult).then_inc(S["qk_ready"], 1)
                    dve.wait_ge(S["qk_ready"], u + 1)
                    decay = flat(gl[:, bass.ds(u, 1), :])
                for c in range(NCH):
                    cs = slice(c * C, c * C + C)
                    ins = dve.tensor_tensor_scan(b[:, cs], decay[:, cs], decay[:, cs], 0.0, ALU.add, ALU.bypass)
                step(ins)
                exponents(0)
                for l in range(LEVELS):
                    if l + 1 < LEVELS:
                        exponents(l + 1)
                    dve.wait_ge(S["expd"], u * NE + (l + 1))
                    ee, eo = level_views(ex[:, l % 2, :], l)
                    dve.tensor_tensor(level_views(qs[:, l % 2, :], l)[1], level_views(q[:, :], l)[1], eo, ALU.mult)
                    dve.tensor_tensor(level_views(ks[:, l % 2, :], l)[0], level_views(k[:, :], l)[0], ee, ALU.mult) \
                        .then_inc(S["factors"], 1)
                    keep(l, u)
                keep(LEVELS, u)
                last = chunks(b[:, :])[:, :, C - 1:C].to_broadcast([P, NCH, C])
                dve.tensor_tensor(chunks(ex[:, 0, :]), last, chunks(b[:, :]), ALU.subtract).then_inc(S["expo_ready"], 1)
                dve.wait_ge(S["expd"], u * NE + NE)
                dve.tensor_tensor(q[:, :], q[:, :], ex[:, 1, :], ALU.mult)
                dve.tensor_tensor(k[:, :], k[:, :], ex[:, 0, :], ALU.mult).then_inc(S["factors"], 1)
                dve.wait_ge(S["update_done"], u + 1)
                step(dve.tensor_copy(state[:, 1, :], B[:, 0:P]))
                for c in range(1, NCH - 1):
                    ins = dve.scalar_tensor_tensor(state[:, c + 1, :], state[:, c, :],
                                                   ex[:, 1, c * C + C - 1:c * C + C],
                                                   B[:, c * P:(c + 1) * P], ALU.mult, ALU.add)
                    if c + 1 < NCH - 1:
                        step(ins)
                ins.then_inc(S["state_ready"], 1)
                if not hg:
                    dve.wait_ge(z_loaded, 16 * 2 * units)
                for sub in range(nsub):
                    dve.wait_ge(S["rooted"], u * nsub + (sub + 1))
                    yo = flat(y[:, bass.ds(u * nsub + sub, 1), :])
                    step(dve.reciprocal(ks[:, sub, :], ks[:, sub, :]))
                    step(dve.scalar_tensor_tensor(ks[:, sub, :], A[sub], core.col_at(wcol, u * nsub + sub),
                                                  ks[:, sub, :], ALU.mult, ALU.mult))
                    ins = dve.tensor_tensor(yo, yo, ks[:, sub, :], ALU.mult)
                    if sub + 1 < nsub:
                        step(ins)
                ins.then_inc(S["unit_free"], 1)
                step.ends(per)


def ml_gates(core, wt, tile, rows_dram, cols):
    H = 4
    with Stage(core.nc, "mlgate") as st:
        w = st.sb("w", [P, D])
        ip, lf, mag, m, lam, b, ke, eb, em = (st.sb(n, [H, T]) for n in (
            "ip", "lf", "mag", "m", "lam", "b", "ke", "eb", "em"))
        w_loaded, proj_done, mag_ready, softened, b_ready, exped, turned, dve_step, act_step, stored, copied = (
            st.sem(n) for n in ("w_loaded", "proj_done", "mag_ready", "softened", "b_ready", "exped", "turned",
                                "dve_step", "act_step", "stored", "copied"))
        block = st.block()

        @block.sync
        def _(sp):
            sp.dma_start(w[:, :], wt[tile * P:(tile + 1) * P, :]).then_inc(w_loaded, 16)
            sp.wait_ge(exped, 1)
            for n, r in enumerate((b, eb, em)):
                sp.dma_start(rows_dram[n * H:(n + 1) * H, :], r[:, :]).then_inc(stored, 16)
            sp.wait_ge(stored, 48)

        @block.tensor
        def _(pe):
            pe.wait_ge(w_loaded, 16)
            project_features(pe, pair(core, 0), w, core.hT, m=H, c0=0)
            project_features(pe, pair(core, 1), w, core.hT, m=H, c0=H).then_inc(proj_done, 1)
            pe.wait_ge(exped, 1)
            for n, r in enumerate((b, ip, ke)):
                for c in range(NCH):
                    ins = pe.matmul(pair(core, 2)[:, (n * NCH + c) * H:(n * NCH + c + 1) * H],
                                    r[:, c * C:c * C + C], core.ident[0:H, 0:H], start=True, stop=True)
            ins.then_inc(turned, 1)

        @block.vector
        def _(dve):
            step = Chain(dve, dve_step)
            dve.wait_ge(proj_done, 1)
            dve.tensor_scalar(ip[:, :], pair(core, 0)[0:H, :], core.col("ml_i_b", 0)[0:H, :], None, ALU.add)
            bf = core.col("ml_f_b", 0)[0:H, :]
            dve.tensor_scalar(lf[:, :], pair(core, 1)[0:H, :], bf, 0.0, ALU.add, ALU.min)
            step(dve.tensor_scalar(mag[:, :], pair(core, 1)[0:H, :], bf, None, ALU.add))
            dve.scalar_tensor_tensor(mag[:, :], mag[:, :], -1.0, mag[:, :], ALU.mult, ALU.max).then_inc(mag_ready, 1)
            dve.wait_ge(softened, 1)
            step(dve.tensor_tensor(lf[:, :], lf[:, :], mag[:, :], ALU.subtract))
            step(dve.tensor_tensor_scan(m[:, :], lf[:, :], ip[:, :], 0.0, ALU.add, ALU.max))
            step(dve.tensor_tensor(lam[:, :], lf[:, :], m[:, :], ALU.subtract))
            dve.tensor_tensor(lam[:, 1:T], lam[:, 1:T], m[:, 0:T - 1], ALU.add)
            step(dve.tensor_tensor(ip[:, :], ip[:, :], m[:, :], ALU.subtract))
            for c in range(NCH):
                cs = slice(c * C, c * C + C)
                ins = dve.tensor_tensor_scan(b[:, cs], lam[:, cs], lam[:, cs], 0.0, ALU.add, ALU.bypass)
            step(ins)
            last = chunks(b[:, :])[:, :, C - 1:C].to_broadcast([H, NCH, C])
            step(dve.tensor_tensor(chunks(ke[:, :]), last, chunks(b[:, :]), ALU.subtract))
            dve.tensor_tensor(ke[:, :], ke[:, :], ip[:, :], ALU.add).then_inc(b_ready, 1)
            dve.wait_ge(turned, 1)
            step(dve.tensor_copy(cols[:, :], pair(core, 2)[:, 0:3 * NCH * H]))

        @block.scalar
        def _(act):
            step = Chain(act, act_step)
            act.wait_ge(mag_ready, 1)
            step(act.activation(mag[:, :], mag[:, :], ACT.Exp, scale=-1.0))
            act.activation(mag[:, :], mag[:, :], ACT.Ln, bias=1.0).then_inc(softened, 1)
            act.wait_ge(b_ready, 1)
            act.activation(eb[:, :], b[:, :], ACT.Exp)
            act.activation(em[:, :], m[:, :], ACT.Exp, scale=-1.0)
            act.activation(ke[:, :], ke[:, :], ACT.Exp).then_inc(exped, 1)


def mlstm_branch(core, source, rows_dram, cols, y):
    order = ["q", "k", "v0", "v1", "o0", "o1", "z0", "z1"]
    nt, units, nsub, H = len(order), 2, 2, 4
    colv = cols[:, :].rearrange("p (n c h) -> p n c h", n=3, c=NCH)
    with Stage(core.nc, "ml") as st:
        qk_loaded, v_loaded, oz_loaded = (st.sem(n + "_loaded") for n in ("qk", "v", "oz"))
        rows_loaded = st.sem("rows_loaded")
        pre = st.sb("pre", [P, 2, 3 + T])
        q, k = st.sb("q", [P, T]), st.sb("k", [P, T])
        v = st.sb("v", [P, NCH, nsub, P])
        og, ktok, sq = core.hT[:, 0:4, :], core.hT[:, 4, :], core.hT[:, 5:7, :]
        brep, em = st.sb("brep", [P, nsub, T]), st.sb("em", [P, nsub, T])
        qdec = st.sb("qdec", [P, T])
        att = st.sb("att", [P, nsub, T])
        state = st.sb("state", [P, NCH, nsub * P])
        nstate, nrep = st.sb("nstate", [P, NCH]), st.sb("nrep", [P, NCH, P])
        S = {n: st.sem(n) for n in (
            "unit_free", "conv_done", "silu_done", "qk_ready", "expo_ready", "expd",
            "prod_done", "att_ready", "keys_turned", "keys_kept", "update_done", "state_ready", "out_done",
            "h_ready", "squared", "mean_done", "rooted", "dve_step")}
        A, B = [pair(core, 0), pair(core, 1)], [pair(core, 2), pair(core, 3)]
        Bflat = core.ps[:, 4 * 512:8 * 512]
        N0 = (NCH - 1) * nsub * P

        def rows(sub):
            return slice(sub * 64, sub * 64 + 64)

        block = st.block()

        @block.sync
        def _(sp):
            def tile(u, n, head):
                at = n * P if head else sp.snap(u * (nt * P) + n * P)
                return source[at:at + P, :] if head else source[bass.ds(at, P), :]

            def unit(u, head):
                qk, vs = [tile(u, n, head) for n in range(2)], [chunks(tile(u, 2 + n, head)) for n in range(nsub)]
                if not head:
                    sp.wait_ge(S["conv_done"], u * 2)
                for n in range(2):
                    sp.dma_start(pre[:, n, 3:], qk[n]).then_inc(qk_loaded, 16)
                if not head:
                    sp.wait_ge(S["unit_free"], u + 1)
                for sub in range(nsub):
                    sp.dma_start(v[:, :, sub, :], vs[sub]).then_inc(v_loaded, 16)
                for sub in range(nsub):
                    def row(n):
                        h = n * H + sub
                        r = rows_dram[bass.ds(u * nsub + h, 1), :] if not head else rows_dram[h:h + 1, :]
                        return r
                    sp.dma_start(brep[:, sub, :], row(0).to_broadcast([P, T])).then_inc(rows_loaded, 16)
                    sp.dma_start(qdec[rows(sub), :], row(1).to_broadcast([64, T])).then_inc(rows_loaded, 16)
                    sp.dma_start(em[:, sub, :], row(2).to_broadcast([P, T])).then_inc(rows_loaded, 16)
            unit(0, True)
            for u in range(units):
                for n in range(nsub):
                    for dst, first in ((og, 4), (y, 6)):
                        at = (u * nt + first + n) * P
                        sp.dma_start(dst[:, u * nsub + n, :], source[at:at + P, :]).then_inc(oz_loaded, 16)
            with sp.Fori(1, units) as u:
                unit(u, False)

        @block.tensor
        def _(pe):
            with pe.Fori(0, units) as u:
                pe.wait_ge(S["unit_free"], u + 1)
                pe.wait_ge(S["qk_ready"], u + 1)
                for sub in range(nsub):
                    for c in range(NCH):
                        cs = slice(c * C, c * C + C)
                        ins = pe.matmul(A[sub][:, cs], k[rows(sub), cs], q[rows(sub), cs], start=True, stop=True)
                    ins.then_inc(S["prod_done"], 1)
                for c in range(NCH):
                    ins = pe.transpose(B[0][:, c * C:c * C + C], k[:, c * C:c * C + C], core.ident[:, :])
                ins.then_inc(S["keys_turned"], 1)
                pe.wait_ge(S["keys_kept"], u + 1)
                pe.wait_ge(v_loaded, u * 32 + 32)
                for c in range(NCH - 1):
                    pe.matmul(Bflat[:, c * nsub * P:(c + 1) * nsub * P], ktok[:, c * C:c * C + C],
                              v[:, c, :, :].rearrange("p n d -> p (n d)"), start=True, stop=True)
                    ins = pe.matmul(Bflat[:, N0 + c:N0 + c + 1], ktok[:, c * C:c * C + C], core.ones[:, 0:1],
                                    start=True, stop=True)
                ins.then_inc(S["update_done"], 1)
                pe.wait_ge(S["state_ready"], u + 1)
                pe.wait_ge(S["att_ready"], u * nsub + nsub)
                for sub in range(nsub):
                    for c in range(NCH):
                        cs = slice(c * C, c * C + C)
                        for o, lv, ls in ((A[sub], v[:, c, sub, :], state[rows(sub), c, sub * P:sub * P + P]),
                                          (B[sub], core.ones[:, :], nrep[rows(sub), c, :])):
                            ins = pe.matmul(o[:, cs], lv, att[:, sub, cs], start=True, stop=(c == 0))
                            if c:
                                ins = pe.matmul(o[:, cs], ls, q[rows(sub), cs], start=False, stop=True)
                    ins.then_inc(S["out_done"], 1)
                for sub in range(nsub):
                    pe.wait_ge(S["squared"], u * nsub + (sub + 1))
                    for half in range(2):
                        ins = pe.matmul(B[sub][:, half * 512:half * 512 + 512], core.mean_p[:, :],
                                        sq[:, sub, half * 512:half * 512 + 512], start=True, stop=True)
                    ins.then_inc(S["mean_done"], 1)

        @block.scalar
        def _(act):
            with act.Fori(0, units) as u:
                for n, dst in enumerate((q, k)):
                    act.wait_ge(S["conv_done"], u * 2 + (n + 1))
                    act.activation(dst[:, :], dst[:, :], ACT.Silu, bias=core.col_at("ml_cb", u + 2 * n)) \
                        .then_inc(S["silu_done"], 1)
                for sub in range(nsub):
                    act.wait_ge(S["expo_ready"], u * nsub + (sub + 1))
                    act.activation(att[:, sub, :], att[:, sub, :], ACT.Exp).then_inc(S["expd"], 1)
                for sub in range(nsub):
                    act.wait_ge(S["h_ready"], u * nsub + (sub + 1))
                    act.activation(sq[:, sub, :], flat(og[:, bass.ds(u * nsub + sub, 1), :]), ACT.Square).then_inc(S["squared"], 1)
                for sub in range(nsub):
                    act.wait_ge(S["mean_done"], u * nsub + (sub + 1))
                    act.activation(em[:, sub, :], B[sub], ACT.Sqrt, bias=core.const(NORM_EPS)).then_inc(S["rooted"], 1)

        @block.vector
        def _(dve):
            per = 2 * 3 + 3 * nsub + 1 + (NCH - 1) + 5 * nsub + (3 * nsub - 1)
            dve.memset(pre[:, :, 0:3], 0.0).then_inc(S["unit_free"], 1)
            dve.wait_ge(S["unit_free"], 1)
            with dve.Fori(0, units) as u:
                step = Chain(dve, S["dve_step"], u * per)
                dve.wait_ge(qk_loaded, u * 32 + 32)
                for n, dst in enumerate((q, k)):
                    step(dve.tensor_scalar(dst[:, :], pre[:, n, 0:T], core.col_at("ml_cw0", u + 2 * n), None, ALU.mult))
                    for j in range(1, 4):
                        ins = dve.scalar_tensor_tensor(dst[:, :], pre[:, n, j:j + T],
                                                       core.col_at(f"ml_cw{j}", u + 2 * n), dst[:, :],
                                                       ALU.mult, ALU.add)
                        if j < 3:
                            step(ins)
                    ins.then_inc(S["conv_done"], 1)
                dve.wait_ge(rows_loaded, u * (96) + 96)
                for sub in range(nsub):
                    def spread(n):
                        return colv[:, n, :, bass.ds(u * nsub + sub, 1)].to_broadcast([P, NCH, C])
                    a = chunks(att[:, sub, :])
                    step(dve.tensor_tensor(a, chunks(brep[:, sub, :]), spread(0), ALU.subtract))
                    step(dve.tensor_scalar(a, a, 0.0, None, ALU.min))
                    dve.tensor_tensor(a, a, spread(1), ALU.add).then_inc(S["expo_ready"], 1)
                dve.wait_ge(S["silu_done"], u * 2 + 2)
                dve.tensor_scalar(q[:, :], q[:, :], 64 ** -0.5, None, ALU.mult).then_inc(S["qk_ready"], 1)
                for sub in range(nsub):
                    a = chunks(att[:, sub, :])
                    dve.wait_ge(S["expd"], u * nsub + (sub + 1))
                    step(dve.tensor_tensor(a, a, per_chunk(core.tri[:, :]), ALU.mult))
                    dve.wait_ge(S["prod_done"], u * nsub + (sub + 1))
                    dve.tensor_tensor(a, a, chunks(A[sub]), ALU.mult).then_inc(S["att_ready"], 1)
                step(dve.tensor_tensor(q[:, :], q[:, :], qdec[:, :], ALU.mult))
                dve.wait_ge(S["keys_turned"], u + 1)
                for sub in range(nsub):
                    kd = colv[:, 2, :, bass.ds(u * nsub + sub, 1)].to_broadcast([P, NCH, 64])
                    ins = dve.tensor_tensor(chunks(ktok)[:, :, sub * 64:sub * 64 + 64],
                                            chunks(B[0])[:, :, sub * 64:sub * 64 + 64], kd, ALU.mult)
                ins.then_inc(S["keys_kept"], 1)
                dve.wait_ge(S["update_done"], u + 1)
                dve.tensor_copy(nstate[:, 1:2], Bflat[:, N0:N0 + 1])
                step(dve.tensor_copy(state[:, 1, :], Bflat[:, 0:nsub * P]))
                for c in range(1, NCH - 1):
                    g = qdec[:, c * C + C - 1:c * C + C]
                    dve.scalar_tensor_tensor(nstate[:, c + 1:c + 2], nstate[:, c:c + 1], g, Bflat[:, N0 + c:N0 + c + 1],
                                             ALU.mult, ALU.add)
                    step(dve.scalar_tensor_tensor(state[:, c + 1, :], state[:, c, :], g,
                                                  Bflat[:, c * nsub * P:(c + 1) * nsub * P], ALU.mult, ALU.add))
                dve.tensor_copy(nrep[:, 1:NCH, :], nstate[:, 1:NCH].unsqueeze(2).to_broadcast([P, NCH - 1, P])) \
                    .then_inc(S["state_ready"], 1)
                dve.wait_ge(oz_loaded, 16 * 2 * nsub * units)
                for sub in range(nsub):
                    gate = flat(og[:, bass.ds(u * nsub + sub, 1), :])
                    dve.wait_ge(S["out_done"], u * nsub + (sub + 1))
                    step(dve.tensor_scalar(att[:, sub, :], B[sub], -1.0, None, ALU.mult))
                    step(dve.tensor_tensor(att[:, sub, :], B[sub], att[:, sub, :], ALU.max))
                    step(dve.tensor_tensor(att[:, sub, :], att[:, sub, :], em[:, sub, :], ALU.max))
                    step(dve.reciprocal(att[:, sub, :], att[:, sub, :]))
                    step(dve.tensor_tensor(att[:, sub, :], A[sub], att[:, sub, :], ALU.mult))
                    dve.tensor_tensor(gate, gate, att[:, sub, :], ALU.mult).then_inc(S["h_ready"], 1)
                for sub in range(nsub):
                    dve.wait_ge(S["rooted"], u * nsub + (sub + 1))
                    yo = flat(y[:, bass.ds(u * nsub + sub, 1), :])
                    step(dve.reciprocal(em[:, sub, :], em[:, sub, :]))
                    gate = flat(og[:, bass.ds(u * nsub + sub, 1), :])
                    step(dve.scalar_tensor_tensor(em[:, sub, :], gate, core.col_at("ml_nw", u * nsub + sub),
                                                  em[:, sub, :], ALU.mult, ALU.mult))
                    ins = dve.tensor_tensor(yo, yo, em[:, sub, :], ALU.mult)
                    if sub + 1 < nsub:
                        step(ins)
                ins.then_inc(S["unit_free"], 1)
                step.ends(per)


def block_1(core, d):
    with Stage(core.nc, "b1") as st:
        core.hT = st.sb("hT", [P, KD, T])
        core.brow = st.sb("brow", [1, 3 * 512])
        y = st.sb("y", [P, 4, T])
        with Stage(core.nc, "b1row") as s2:
            got = s2.sem("brow_loaded")
            block = s2.block()

            @block.sync
            def _(sp):
                sp.dma_start(core.brow[:, :], d["b1_vrow"]).then_inc(got, 16)
                sp.wait_ge(got, 16)
        rms_norm(core, "rms1", core.xT, "norm_w", core.hT)
        hg_lower_bound(core)
        vector_decay_branch(core, "hg", 1, 4, d["w1"], GLA_FILL, [(d["gla_park"], 4 * n, 1) for n in range(3)],
                            [("features", ACT.Identity, ("gla_qk", 0, 1)), ("tokens", ACT.Copy, (512, 1)),
                             ("features", ACT.Silu, ("gla_z", 0, 1))],
                            [8] + [2] + [3] * 6 + [4] + [4, 4, 4] + [4], "hg_nw", y)
        out_projection(core, "o1a", y, 4, d["wo1a"], core.xT)
        with Stage(core.nc, "glas") as s2:
            gl = s2.sb("gl", [P, 2, T])
            gla_gates(core, d["w1"], GLA_A, d["gla_w_a2"], gl)
            kinds = [("features", ACT.Identity, ("ml_q", 0, 1)), ("features", ACT.Identity, ("ml_k", 0, 1))]
            kinds += [("tokens", ACT.Copy, (1024 + n * P, 2)) for n in range(2)]
            kinds += [("features", f, (c, n, 2)) for c, f in (("ml_o", ACT.Sigmoid), ("ml_z", ACT.Silu)) for n in range(2)]
            vector_decay_branch(core, "gla", 2, 2, d["w1"], ML_FILL, places(d["ml_park"], 8), kinds,
                                [8] + [8] * 8 + [8, 8, 8] + [8, 24], "gla_nw", y, d["gla_park"], gl)
        out_projection(core, "o1b", y, 4, d["wo1b"], core.xT)
        with Stage(core.nc, "mls") as s2:
            cols = s2.sb("cols", [P, 3 * NCH * 4])
            ml_gates(core, d["w1"], ML_IF, d["ml_rows"], cols)
            mlstm_branch(core, d["ml_park"], d["ml_rows"], cols, y)
        out_projection(core, "o1c", y, 4, d["wo1c"], core.xT)
    rms_norm(core, "fin1", core.xT, "final_norm_w", core.xT)


RH, RDK, RDV = 4, 256, 512
CW = 31
SEG2 = segments([("val", D), ("glu", D), ("gate", D), ("q", RH * RDK), ("k", RH * RDK), ("v", RH * RDV),
                 ("rg", RH * RDV), ("ga", D), ("gb", D)])
RET_TILES = 12
GATE_TILE, CONV_TILE = RH * RET_TILES, RH * RET_TILES + 2 * KD


def tile_order_2():
    def tile(name, n):
        s = SEG2[name][0] + n * P
        return s, s + P
    out = []
    for h in range(RH):
        out += [tile("q", 2 * h), tile("q", 2 * h + 1), tile("k", 2 * h), tile("k", 2 * h + 1)]
        out += [tile(n, 4 * h + j) for n in ("v", "rg") for j in range(4)]
    out += [tile(n, e) for n in ("gb", "ga") for e in range(KD)]
    for e in range(KD):
        out += [tile("glu", e), tile("val", e), tile("gate", e)]
    return out


def columns_2(i):
    f = np.float32
    lg = np.log1p(-np.exp2(f(-5.0) - np.arange(RH, dtype=f))).astype(f)
    idx = np.arange(C, dtype=f)
    zeta = np.exp(lg[:, None] * (f(C - 1.0) - idx)).astype(f) * f(RDK ** -0.5)
    out = [("norm_gain_2", i["norm_gain_2"][0]), ("conv_b_2", i["conv_dw_b_2"][0]),
           ("ln_g_2", i["conv_ln_g_2"][0]), ("ln_b_2", i["conv_ln_b_2"][0]), ("ret_gn", i["ret_gn_g_2"][0]),
           ("final_gain_2", i["final_gain_2"]), ("zeta", zeta),
           ("gamma_chunk", np.repeat(np.exp(lg * f(C)).astype(f), P))]
    return out + [(f"cw{j}", i["conv_dw_w_2"][0, j]) for j in range(CW)]


def lay_out_2(i, d):
    f = np.float32
    d["w2"] = in_tiles(i["w_in_2"][0], tile_order_2())
    d["wret"] = out_tiles(i["w_ret_proj_2"][0])
    d["wconv"] = out_tiles(i["w_conv_proj_2"][0])
    d["wo2"] = out_tiles(i["w_out_2"][0])
    pos = np.arange(T, dtype=f)
    inv = np.power(f(10000.0), -np.arange(0, RDK, 2, dtype=f) / f(RDK)).astype(f)
    ang = (inv[:, None] * pos[None, :]).astype(f)
    d["c_rope"] = np.concatenate([np.cos(ang), np.sin(ang)], 1).astype(f)
    lg = np.log1p(-np.exp2(f(-5.0) - np.arange(RH, dtype=f))).astype(f)
    idx = np.arange(C, dtype=f)
    diff = idx[None, :] - idx[:, None]
    dec = np.where(diff >= 0, np.exp(lg[:, None, None] * np.maximum(diff, 0)), 0).astype(f) * f(RDK ** -0.5)
    xi = np.exp(lg[:, None] * (idx + 1)).astype(f)
    d["c_ret"] = np.concatenate([dec.transpose(1, 0, 2).reshape(P, RH * C),
                                 np.broadcast_to(xi.reshape(1, RH * C), (P, RH * C))], 1)


def weighted_projection(core, name, y, nk, wt, gates, first, dst, accumulate, back=None):
    with Stage(core.nc, name) as st:
        proj = SplitProjection(st, y, nk, 2)
        sg = st.sb("sg", [P, 2, T])
        g_loaded = [st.sem("g_loaded0"), st.sem("g_loaded1")]
        added, dve_step, back_loaded = (st.sem(n) for n in ("added", "dve_step", "back_loaded"))
        block = st.block()

        @block.sync
        def _(sp):
            for s in range(2):
                sp.dma_start(proj.w[:, s, :], wt[s * P:(s + 1) * P, :]).then_inc(proj.loaded[s], 16)
                sp.dma_start(sg[:, s, :], gates[(first + s) * P:(first + s + 1) * P, :]).then_inc(g_loaded[s], 16)
            if back is not None:
                for k in range(KD):
                    sp.wait_ge(proj.y_cut, k + 1)
                    sp.dma_start(y[:, k, :], back[k * P:(k + 1) * P, :]).then_inc(back_loaded, 16)
            with sp.Fori(1, KD // 2) as i:
                for s in range(2):
                    proj.load_next(sp, wt, 0, i, s)
                    sp.wait_ge(added, 2 * i + (s + 1))
                    sp.dma_start(sg[:, s, :], gates[bass.ds(i * (2 * P) + (first + s) * P, P), :]).then_inc(g_loaded[s], 16)
            if back is not None:
                sp.wait_ge(back_loaded, 16 * KD)

        @block.gpsimd
        def _(pool):
            proj.cut_weights(pool, KD)

        @block.tensor
        def _(pe):
            with pe.Fori(0, KD // 2) as i:
                for s in range(2):
                    pe.wait_ge(added, 2 * i + (s + 1))
                    proj.multiply(pe, pair(core, s), i, s)

        @block.scalar
        def _(act):
            proj.round_y(act)

        @block.vector
        def _(dve):
            dve.sem_inc(added, 2)
            proj.cut_y(dve)
            with dve.Fori(0, KD // 2) as i:
                step = Chain(dve, dve_step, i * 2)
                for s in range(2):
                    dve.wait_ge(g_loaded[s], 16 * i + 16)
                    dve.wait_ge(proj.done, 2 * i + (s + 1))
                    o = flat(dst[:, bass.ds(2 * i + s, 1), :])
                    if accumulate:
                        step(dve.tensor_tensor(sg[:, s, :], pair(core, s), sg[:, s, :], ALU.mult))
                        dve.tensor_tensor(o, o, sg[:, s, :], ALU.add).then_inc(added, 1)
                    else:
                        dve.tensor_tensor(o, pair(core, s), sg[:, s, :], ALU.mult).then_inc(added, 1)
                step.ends(2 if accumulate else 0)


def retention_branch(core, wt, d):
    order = ["q0", "q1", "k0", "k1", "v0", "v1", "v2", "v3", "g0", "g1", "g2", "g3"]
    nt, ring, units, NV = len(order), 4, RH, RDV // P
    with Stage(core.nc, "ret") as st:
        w = st.sb("w", [P, ring, D])
        loaded = [st.sem(f"w_loaded{t}") for t in range(ring)]
        rope = st.sb("rope", [P, 2, T])
        tab = st.sb("tab", [P, 2, RH, C])
        q, k = core.xT[:, 0:2, :], core.xT[:, 2:4, :]
        v = core.xT[:, 4:8, :].rearrange("p a t -> p (a t)").rearrange("p (c n d) -> p c n d", c=NCH, n=NV)
        g, o = st.sb("g", [P, NV, T]), st.sb("o", [P, NV, T])
        att = st.sb("att", [P, T])
        ktok = st.sb("ktok", [P, NCH, RDK])
        R = st.sb("R", [P, 2, 2 * RDV])
        turn = ktok[:, :, :].rearrange("p c d -> p (c d)").rearrange("p (a t) -> p a t", a=2)
        sq = v[:, :, :, :].rearrange("p c n d -> p (c n d)").rearrange("p (n t) -> p n t", n=NV)
        S = {n: st.sem(n) for n in (
            "tables", "proj_done", "evacuated", "unit_free", "roped", "prod_done", "att_ready", "q_decayed",
            "keys_turned", "keys_kept", "update_done", "r_ready", "out_done", "o_kept", "mean_done", "centred",
            "squared", "var_done", "rooted", "o_ready", "stored", "o_free", "dve_step", "passed")}
        A, B = pair(core, 0), [pair(core, 2), pair(core, 3)]
        fill = Filler(core, st, "gates", 1, wt, GATE_TILE, places(d["gate_park"], 2 * KD // units),
                      [("features", ACT.Sigmoid, None)] * (2 * KD // units))
        cut = [8, 24]
        per_chunk_parts = (cut[1] - cut[0]) // NCH
        block = st.block()

        @block.sync
        def _(sp):
            sp.dma_start(rope[:, :, :].rearrange("p a t -> p (a t)"), d["c_rope"]).then_inc(S["tables"], 16)
            sp.dma_start(tab[:, :, :, :].rearrange("p a h t -> p (a h t)"), d["c_ret"]).then_inc(S["tables"], 16)
            sp.sem_inc(S["o_free"], 1)
            for t in range(nt):
                if t >= ring:
                    sp.wait_ge(S["proj_done"], t + 1 - ring)
                sp.dma_start(w[:, t % ring, :], wt[t * P:(t + 1) * P, :]).then_inc(loaded[t % ring], 16)
            fill.load(sp, 0, True)

            def store(u):
                for j in range(NV):
                    sp.dma_start(d["o_park"][bass.ds(u * (NV * P) + j * P, P), :], o[:, j, :]).then_inc(S["stored"], 16)
            with sp.Fori(1, units) as u:
                for t in range(nt):
                    sp.wait_ge(S["proj_done"], u * nt + (t + 1 - ring))
                    if t == ring:
                        sp.wait_ge(S["o_ready"], u)
                        store(u - 1)
                    sp.dma_start(w[:, t % ring, :], wt[bass.ds(u * (nt * P) + t * P, P), :]).then_inc(loaded[t % ring], 16)
                stored = sp.snap(u * (16 * NV))
                sp.wait_ge(S["stored"], stored)
                sp.sem_inc(S["o_free"], 1)
                fill.load(sp, u)
            sp.wait_ge(S["o_ready"], units)
            for j in range(NV):
                at = ((units - 1) * NV + j) * P
                sp.dma_start(d["o_park"][at:at + P, :], o[:, j, :]).then_inc(S["stored"], 16)
            sp.wait_ge(S["stored"], 16 * NV * units)

        @block.tensor
        def _(pe):
            with pe.Fori(0, units) as u:
                pe.wait_ge(S["unit_free"], u + 1)
                for t, what in enumerate(order):
                    pe.wait_ge(loaded[t % ring], u * (16 * nt // ring) + 16 * (t // ring + 1))
                    if t >= 2:
                        pe.wait_ge(S["evacuated"], u * nt + (t - 1))
                    project = project_tokens if what[0] == "v" else project_features
                    project(pe, B[t % 2], w[:, t % ring, :], core.hT).then_inc(S["proj_done"], 1)
                pe.wait_ge(S["roped"], u * 2 + 2)
                for c in range(NCH):
                    cs = slice(c * C, c * C + C)
                    for i in range(2):
                        ins = pe.matmul(A[:, cs], k[:, i, cs], q[:, i, cs], start=(i == 0), stop=(i == 1))
                ins.then_inc(S["prod_done"], 1)
                pe.wait_ge(S["evacuated"], u * nt + nt)
                for i in range(2):
                    for c in range(NCH):
                        cs = slice(c * C, c * C + C)
                        ins = pe.transpose(B[i][:, cs], k[:, i, cs], core.ident[:, :])
                    ins.then_inc(S["keys_turned"], 1)
                fill.advance(pe, u, 0, cut[0])
                pe.wait_ge(S["keys_kept"], u * 2 + 2)
                pe.wait_ge(S["att_ready"], u + 1)
                pe.wait_ge(S["q_decayed"], u + 1)
                for c in range(NCH):
                    cs = slice(c * C, c * C + C)
                    if c < NCH - 1:
                        if c >= 2:
                            pe.wait_ge(S["r_ready"], u * (NCH - 1) + (c - 1))
                        for i in range(2):
                            ins = pe.matmul(B[c % 2][:, i * RDV:(i + 1) * RDV], ktok[:, c, i * P:(i + 1) * P],
                                            v[:, c, :, :].rearrange("p n d -> p (n d)"), start=True, stop=True)
                        ins.then_inc(S["update_done"], 1)
                    fill.advance(pe, u, cut[0] + c * per_chunk_parts, cut[0] + (c + 1) * per_chunk_parts)
                    if c >= 2:
                        pe.wait_ge(S["o_kept"], u * NCH + (c - 1))
                    if c >= 1:
                        pe.wait_ge(S["r_ready"], u * (NCH - 1) + c)
                    for j in range(NV):
                        dst = A[:, (c % 2) * 512 + j * P:(c % 2) * 512 + (j + 1) * P]
                        ins = pe.matmul(dst, v[:, c, j, :], att[:, cs], start=True, stop=(c == 0))
                        if c >= 1:
                            for i in range(2):
                                ins = pe.matmul(dst, R[:, c % 2, i * RDV + j * P:i * RDV + (j + 1) * P],
                                                q[:, i, cs], start=False, stop=(i == 1))
                    ins.then_inc(S["out_done"], 1)
                for src, ready, n, done, end in ((o, "o_kept", NCH, "mean_done", 3 * 16), (sq, "squared", 1, "var_done", 4 * 16)):
                    pe.wait_ge(S[ready], u * n + n)
                    for half in range(2):
                        for j in range(NV):
                            ins = pe.matmul(A[:, half * 512:half * 512 + 512], core.mean_v[:, :],
                                            src[:, j, half * 512:half * 512 + 512],
                                            start=(j == 0), stop=(j == NV - 1))
                    ins.then_inc(S[done], 1)
                    fill.advance(pe, u, cut[1] if n > 1 else 3 * 16, end)

        @block.scalar
        def _(act):
            fill.begin(act)
            with act.Fori(0, units) as u:
                for t, what in enumerate(order):
                    act.wait_ge(S["proj_done"], u * nt + (t + 1))
                    src, n = B[t % 2], int(what[1])
                    if what[0] == "v":
                        ins = act.activation(v[:, :, n, :], chunks(src), ACT.Copy)
                    elif what[0] == "g":
                        ins = act.activation(g[:, n, :], src, ACT.Silu)
                    else:
                        ins = act.activation((q if what[0] == "q" else k)[:, n, :], src, ACT.Copy)
                    ins.then_inc(S["evacuated"], 1)
                for i in range(2):
                    wait_alone(act, S["keys_turned"], u * 2 + (i + 1), S["passed"])
                    act.activation(ktok[:, :, i * P:(i + 1) * P], chunks(B[i]), ACT.Copy,
                                   scale=core.col_at("zeta", u)).then_inc(S["keys_kept"], 1)
                act.wait_ge(S["o_free"], u + 1)
                for c in range(NCH):
                    if c == (16 - cut[0]) // per_chunk_parts - 1:
                        fill.keep(act, u, 0)
                    act.wait_ge(S["out_done"], u * NCH + (c + 1))
                    src = A[:, (c % 2) * 512:(c % 2) * 512 + 512].rearrange("p (n t) -> p n t", n=NV)
                    act.activation(o[:, :, c * C:c * C + C], src, ACT.Copy).then_inc(S["o_kept"], 1)
                fill.keep(act, u, 1)
                act.wait_ge(S["centred"], u + 1)
                act.activation(sq, o[:, :, :], ACT.Square).then_inc(S["squared"], 1)
                fill.keep(act, u, 2)
                act.wait_ge(S["var_done"], u + 1)
                act.activation(att[:, :], A, ACT.Sqrt, bias=core.const(LN_EPS)).then_inc(S["rooted"], 1)
                fill.keep(act, u, 3)
                fill.end(act, u)

        @block.vector
        def _(dve):
            per = 2 * 2 + 2
            dve.sem_inc(S["unit_free"], 1)
            dve.wait_ge(S["tables"], 32)
            with dve.Fori(0, units) as u:
                step = Chain(dve, S["dve_step"], u * per)
                for n, x in enumerate((q, k)):
                    dve.wait_ge(S["evacuated"], u * nt + (2 * n + 2))
                    dve.tensor_tensor(turn[:, 0, :], x[:, 1, :], rope[:, 1, :], ALU.mult)
                    step(dve.tensor_tensor(turn[:, 1, :], x[:, 0, :], rope[:, 1, :], ALU.mult))
                    dve.tensor_tensor(x[:, 0, :], x[:, 0, :], rope[:, 0, :], ALU.mult)
                    step(dve.tensor_tensor(x[:, 1, :], x[:, 1, :], rope[:, 0, :], ALU.mult))
                    dve.tensor_tensor(x[:, 0, :], x[:, 0, :], turn[:, 0, :], ALU.subtract)
                    dve.tensor_tensor(x[:, 1, :], x[:, 1, :], turn[:, 1, :], ALU.add).then_inc(S["roped"], 1)
                    dve.wait_ge(S["roped"], u * 2 + (n + 1))
                dve.wait_ge(S["prod_done"], u + 1)
                dve.tensor_tensor(chunks(att[:, :]), chunks(A),
                                  tab[:, 0, bass.ds(u, 1), :].to_broadcast([P, NCH, C]), ALU.mult) \
                    .then_inc(S["att_ready"], 1)
                qc = q[:, :, :].rearrange("p a (c t) -> p (a c) t", t=C)
                dve.tensor_tensor(qc, qc, tab[:, 1, bass.ds(u, 1), :].to_broadcast([P, 2 * NCH, C]), ALU.mult) \
                    .then_inc(S["q_decayed"], 1)
                for c in range(NCH - 1):
                    dve.wait_ge(S["update_done"], u * (NCH - 1) + (c + 1))
                    if c == 0:
                        ins = dve.tensor_copy(R[:, 1, :], B[0])
                    else:
                        dve.wait_ge(S["out_done"], u * NCH + c)
                        ins = dve.scalar_tensor_tensor(R[:, (c + 1) % 2, :], R[:, c % 2, :],
                                                       core.col_at("gamma_chunk", u), B[c % 2], ALU.mult, ALU.add)
                    ins.then_inc(S["r_ready"], 1)
                    dve.wait_ge(S["r_ready"], u * (NCH - 1) + (c + 1))
                dve.wait_ge(S["mean_done"], u + 1)
                dve.tensor_tensor(o[:, :, :], o[:, :, :], A.unsqueeze(1).to_broadcast([P, NV, T]), ALU.subtract) \
                    .then_inc(S["centred"], 1)
                dve.wait_ge(S["rooted"], u + 1)
                step(dve.reciprocal(att[:, :], att[:, :]))
                for j in range(NV):
                    ins = dve.scalar_tensor_tensor(o[:, j, :], o[:, j, :], core.col_at("ret_gn", u * NV + j),
                                                   att[:, :], ALU.mult, ALU.mult)
                step(ins)
                dve.tensor_tensor(o[:, :, :], o[:, :, :], g[:, :, :], ALU.mult).then_inc(S["o_ready"], 1)
                dve.wait_ge(S["o_ready"], u + 1)
                dve.sem_inc(S["unit_free"], 1)
                step.ends(per)


def conv_branch(core, wt, first, h, uT, gate):
    nt = 3
    with Stage(core.nc, "conv") as st:
        proj = SplitProjection(st, h, KD, nt)
        sg, val = st.sb("sg", [P, T]), st.sb("val", [P, T])
        pad = st.sb("pad", [P, CW - 1 + T])
        evacuated, consumed, dve_step = (st.sem(n) for n in ("evacuated", "consumed", "dve_step"))
        block = st.block()

        @block.sync
        def _(sp):
            proj.load(sp, wt, first, nt * KD)

        @block.gpsimd
        def _(pool):
            proj.cut_weights(pool, nt * KD)

        @block.tensor
        def _(pe):
            with pe.Fori(0, KD) as u:
                for t in range(nt):
                    pe.wait_ge(evacuated, u * nt + (t + 1))
                    proj.multiply(pe, pair(core, t), u, t)

        @block.scalar
        def _(act):
            act.sem_inc(evacuated, nt)
            proj.round_y(act)
            with act.Fori(0, KD) as u:
                act.wait_ge(consumed, u + 1)
                for t, (dst, fn) in enumerate(((sg[:, :], ACT.Sigmoid), (val[:, :], ACT.Copy),
                                               (flat(gate[:, bass.ds(u, 1), :]), ACT.Silu))):
                    act.wait_ge(proj.done, u * nt + (t + 1))
                    act.activation(dst, pair(core, t), fn).then_inc(evacuated, 1)

        @block.vector
        def _(dve):
            proj.cut_y(dve)
            dve.memset(pad[:, 0:CW - 1], 0.0).then_inc(consumed, 1)
            with dve.Fori(0, KD) as u:
                step = Chain(dve, dve_step, u * CW)
                dve.wait_ge(evacuated, u * nt + (nt + 2))
                dve.tensor_tensor(pad[:, CW - 1:], val[:, :], sg[:, :], ALU.mult).then_inc(consumed, 1)
                dve.wait_ge(consumed, u + 2)
                acc = flat(uT[:, bass.ds(u, 1), :])
                step(dve.tensor_scalar(acc, pad[:, 0:T], core.col_at("cw0", u), core.col_at("conv_b_2", u),
                                       ALU.mult, ALU.add))
                for j in range(1, CW):
                    step(dve.scalar_tensor_tensor(acc, pad[:, j:j + T], core.col_at(f"cw{j}", u), acc,
                                                  ALU.mult, ALU.add))
                step.ends(CW)


def conv_norm(core, uT, gate):
    with Stage(core.nc, "cnorm") as st:
        sq, rstd = st.sb("sq", [P, 2, T]), st.sb("rstd", [P, T])
        mean_done, centred, squared, summed, rooted, scaled, activated, dve_step = (
            st.sem(n) for n in ("mean_done", "centred", "squared", "summed", "rooted", "scaled", "activated", "dve_step"))
        block = st.block()

        @block.tensor
        def _(pe):
            for half in range(2):
                for k in range(KD):
                    ins = pe.matmul(pair(core, 0)[:, half * 512:half * 512 + 512], core.mean_d[:, :],
                                    uT[:, k, half * 512:half * 512 + 512], start=(k == 0), stop=(k == KD - 1))
            ins.then_inc(mean_done, 1)
            for k in range(KD):
                pe.wait_ge(squared, k + 1)
                for half in range(2):
                    ins = pe.matmul(pair(core, 1)[:, half * 512:half * 512 + 512], core.mean_d[:, :],
                                    sq[:, k % 2, half * 512:half * 512 + 512], start=(k == 0), stop=(k == KD - 1))
                ins.then_inc(summed, 1)

        @block.scalar
        def _(act):
            for k in range(KD):
                act.wait_ge(centred, k + 1)
                if k >= 2:
                    act.wait_ge(summed, k - 1)
                act.activation(sq[:, k % 2, :], uT[:, k, :], ACT.Square).then_inc(squared, 1)
            act.wait_ge(summed, KD)
            act.activation(rstd[:, :], pair(core, 1), ACT.Sqrt, bias=core.const(LN_EPS)).then_inc(rooted, 1)
            for k in range(KD):
                act.wait_ge(scaled, k + 1)
                act.activation(uT[:, k, :], uT[:, k, :], ACT.Silu, bias=core.col("ln_b_2", k)).then_inc(activated, 1)

        @block.vector
        def _(dve):
            step = Chain(dve, dve_step)
            dve.wait_ge(mean_done, 1)
            for k in range(KD):
                dve.tensor_tensor(uT[:, k, :], uT[:, k, :], pair(core, 0), ALU.subtract).then_inc(centred, 1)
            dve.wait_ge(rooted, 1)
            step(dve.reciprocal(rstd[:, :], rstd[:, :]))
            for k in range(KD):
                dve.scalar_tensor_tensor(uT[:, k, :], uT[:, k, :], core.col("ln_g_2", k), rstd[:, :],
                                         ALU.mult, ALU.mult).then_inc(scaled, 1)
            for k in range(KD):
                dve.wait_ge(activated, k + 1)
                dve.tensor_tensor(uT[:, k, :], uT[:, k, :], gate[:, k, :], ALU.mult)


def block_2(core, d):
    with Stage(core.nc, "b2") as st:
        core.hT = st.sb("hT", [P, KD, T])
        rms_norm(core, "rms2", core.xT, "norm_gain_2", core.hT, park=d["x_park"])
        retention_branch(core, d["w2"], d)
        uT, gate, mixed = core.xT, core.hT, core.hT
        conv_branch(core, d["w2"], CONV_TILE, core.hT, uT, gate)
        conv_norm(core, uT, gate)
        weighted_projection(core, "ya", uT, KD, d["wconv"], d["gate_park"], KD, mixed, False, back=d["o_park"][0:D, :])
        weighted_projection(core, "yb1", core.xT, KD, d["wret"][:, 0:D], d["gate_park"], 0, mixed, True,
                            back=d["o_park"][D:2 * D, :])
        weighted_projection(core, "yb2", core.xT, KD, d["wret"][:, D:2 * D], d["gate_park"], 0, mixed, True,
                            back=d["x_park"])
        out_projection(core, "o2", mixed, KD, d["wo2"], core.xT)
    rms_norm(core, "fin2", core.xT, "final_gain_2", core.xT)


SBW, SSH, RWW = 512, 16, 512
SEG3 = segments([("sb_q", SBW), ("sb_k", SBW), ("sb_v", SBW), ("sb_g", SBW), ("z", D), ("xs", D), ("bm", P), ("cm", P),
                 ("dt", SSH), ("r", RWW), ("k", RWW), ("v", RWW), ("rw_g", RWW), ("lo", P),
                 ("g_sb", D), ("g_ssd", D), ("g_rw", D)])
RW_LO, RW_TILE, RW_FILL, SSD_TILE, SSD_UNIT = 0, 1, 17, 57, 60


def tile_order_3():
    def tile(name, n):
        s = SEG3[name][0] + n * P
        return s, min(s + P, SEG3[name][1])
    gates = [tile(n, e) for n in ("g_sb", "g_ssd", "g_rw") for e in range(KD)]
    out = [tile("lo", 0)]
    for u in range(4):
        out += [tile(n, u) for n in ("r", "k", "v", "rw_g")]
    for u in range(4):
        out += gates[6 * u:6 * u + 6] + [tile(n, u) for n in ("sb_q", "sb_k", "sb_v", "sb_g")]
    out += [tile("bm", 0), tile("cm", 0), tile("dt", 0)]
    for u in range(8):
        out += [tile("xs", u), tile("z", u)]
    return out


def columns_3(i):
    cw, cb, mu = i["conv_w_3"][0], i["conv_b_3"][0], i["rw_mu_3"][0]
    out = [("norm_g_3", i["norm_g_3"][0]), ("final_g_3", i["final_g_3"]), ("ssd_ng", i["ssd_norm_g_3"][0]),
           ("ssd_cb", cb), ("dt_bias", i["dt_bias_3"][0]), ("a_log", i["a_log_3"][0]),
           ("a_head", np.zeros(SSH, np.float32)),
           ("d_skip", np.repeat(i["d_skip_3"][0], D // SSH)),
           ("w0", i["rw_w0_3"][0]), ("a0", i["rw_a0_3"][0]), ("k_k", i["rw_k_k_3"][0]), ("k_a", i["rw_k_a_3"][0]),
           ("r_k", i["rw_r_k_3"][0]), ("rw_ln_g", i["rw_ln_g_3"][0]), ("rw_ln_b", i["rw_ln_b_3"][0])]
    for n, name in enumerate(("r", "k", "v", "g")):
        out.append(("mu_" + name, mu[n * RWW:(n + 1) * RWW]))
    out.append(("mu_lo", mu[4 * RWW:]))
    return out + [(f"ssd_cw{j}", cw[j]) for j in range(4)]


def lay_out_3(i, d):
    d["w3"] = in_tiles(i["w_in_3"][0], tile_order_3())
    for n, name in (("wsb", "w_out_sb_3"), ("wssd", "w_out_ssd_3"), ("wrw", "w_out_rw_3"), ("wo3", "w_o_3")):
        d[n] = out_tiles(i[name][0])
    up = np.concatenate([i["rw_w_up_3"][0], i["rw_a_up_3"][0]], 0)
    d["w_up"] = up.reshape(P, 4, P).transpose(1, 0, 2).reshape(4 * P, P)
    s, t = np.arange(P)[:, None], np.arange(P)[None, :]
    same = s // 64 == t // 64
    d["c_mat3"] = np.concatenate([same, same / 64.0, s >= t], 1).astype(np.float32)
    level0 = level_masks()[:, 0, :]
    d["c_mask3"] = np.concatenate([s < t, s <= t, level0.T], 1).astype(np.float32)


def spans(lo):
    return [(max(lo, h * 512), h * 512 + 512) for h in range(2) if lo < h * 512 + 512]


def stick_breaking_branch(core, wt, y, sb_park, xz_park):
    units, nt = 4, 4
    steps = [(b, sub) for b in reversed(range(NCH)) for sub in range(2)]
    NS = len(steps)
    with Stage(core.nc, "sb") as st:
        q_loaded, k_loaded, v_loaded, y_loaded = (st.sem(n + "_loaded") for n in "qkvy")
        q, k = st.sb("q", [P, T]), st.sb("k", [P, T])
        v = st.sb("v", [P, NCH, P])
        neg, soft, keep, later, att = (st.sb(n, [P, 2, T]) for n in ("neg", "soft", "keep", "later", "att"))
        diag = st.sb("diag", [P, 2, C])
        zeros = st.sb("zeros", [P, 512])
        S = {n: st.sem(n) for n in (
            "unit_free", "q_scaled", "z_done", "mag_ready", "softened", "keep_ready",
            "sum_done", "att_expd", "att_ready", "out_done", "dve_step", "act_step")}
        Z, O = [pair(core, 0), pair(core, 1)], pair(core, 2)
        fill = Filler(core, st, "xz", 3, wt, SSD_UNIT, places(xz_park, 4),
                      [("features", ACT.Copy, None), ("features", ACT.Silu, None)] * 2)
        parts = NS // fill.n

        def rows(sub):
            return slice(sub * 64, sub * 64 + 64)

        block = st.block()

        @block.sync
        def _(sp):
            def load(dst, sem, at):
                src = sb_park[at:at + P, :] if isinstance(at, int) else sb_park[bass.ds(at, P), :]
                sp.dma_start(dst, src).then_inc(sem, 16)
            vf = v[:, :, :].rearrange("p c d -> p (c d)")
            for n, (dst, sem) in enumerate(((q[:, :], q_loaded), (k[:, :], k_loaded), (vf, v_loaded))):
                load(dst, sem, n * P)
            fill.load(sp, 0, True)
            for u in range(units):
                load(y[:, u, :], y_loaded, (u * nt + 3) * P)
            with sp.Fori(1, units) as u:
                at = [sp.snap(u * (nt * P) + n * P) for n in range(nt)]
                sp.wait_ge(S["z_done"], u * NS)
                load(q[:, :], q_loaded, at[0])
                load(k[:, :], k_loaded, at[1])
                sp.wait_ge(S["out_done"], u * NS)
                load(vf, v_loaded, at[2])
                fill.load(sp, u)

        @block.tensor
        def _(pe):
            with pe.Fori(0, units) as u:
                pe.wait_ge(S["unit_free"], u + 1)
                pe.wait_ge(k_loaded, u * 16 + 16)
                pe.wait_ge(S["q_scaled"], u + 1)
                for n in range(NS + 2):
                    if n < NS:
                        b, sub = steps[n]
                        if n >= 2:
                            pe.wait_ge(S["att_expd"], u * NS + (n - 1))
                        for lo, hi in spans(b * C):
                            ins = pe.matmul(Z[sub][:, lo:hi], k[rows(sub), b * C:b * C + C], q[rows(sub), lo:hi],
                                            start=True, stop=True)
                        ins.then_inc(S["z_done"], 1)
                        fill.multiply(pe, u, n // parts, n % parts, parts)
                    if 1 <= n <= NS:
                        b, sub = steps[n - 1]
                        pe.wait_ge(S["keep_ready"], u * NS + n)
                        for lo, hi in spans(b * C):
                            ins = pe.matmul(Z[sub][:, lo:hi], core.triangle[:, :], keep[:, sub, lo:hi],
                                            start=False, stop=True, skip_group_check=True)
                        for lo, hi in spans((b + 1) * C):
                            ins = pe.matmul(Z[sub][:, lo:hi], core.ones[:, :], later[:, sub, lo:hi],
                                            start=False, stop=True, skip_group_check=True)
                        ins.then_inc(S["sum_done"], 1)
                    if n >= 2:
                        b, sub = steps[n - 2]
                        pe.wait_ge(S["att_ready"], u * NS + (n - 1))
                        if n == 2:
                            pe.wait_ge(v_loaded, u * 16 + 16)
                        vb = v[:, b, sub * 64:sub * 64 + 64]
                        if b == NCH - 1:
                            for lo, hi in spans(0):
                                pe.matmul(O[rows(sub), lo:hi], vb, zeros[:, :], start=True, stop=True)
                        ins = pe.matmul(O[rows(sub), b * C:b * C + C], vb, diag[:, sub, :], start=False, stop=True,
                                        skip_group_check=True)
                        for lo, hi in spans((b + 1) * C):
                            ins = pe.matmul(O[rows(sub), lo:hi], vb, att[:, sub, lo:hi], start=False, stop=True,
                                            skip_group_check=True)
                        ins.then_inc(S["out_done"], 1)

        @block.scalar
        def _(act):
            fill.begin(act)
            with act.Fori(0, units) as u:
                step = Chain(act, S["act_step"], u * NS)
                for n in range(NS + 1):
                    if n < NS:
                        b, sub = steps[n]
                        act.wait_ge(S["mag_ready"], u * NS + (n + 1))
                        a = soft[:, sub, b * C:T]
                        step(act.activation(a, a, ACT.Exp))
                        act.activation(a, a, ACT.Ln, bias=1.0).then_inc(S["softened"], 1)
                    if n >= 1:
                        b, sub = steps[n - 1]
                        act.wait_ge(S["sum_done"], u * NS + n)
                        if n >= 3:
                            act.wait_ge(S["out_done"], u * NS + (n - 2))
                        act.activation(att[:, sub, b * C:T], Z[sub][:, b * C:T], ACT.Exp).then_inc(S["att_expd"], 1)
                    if n % parts == parts - 1:
                        fill.keep(act, u, n // parts)
                step.ends(NS)
                fill.end(act, u)

        @block.vector
        def _(dve):
            dve.memset(zeros[:, :], 0.0)
            dve.memset(diag[:, :, :], 0.0).then_inc(S["unit_free"], 1)
            per = 2 * NS
            with dve.Fori(0, units) as u:
                step = Chain(dve, S["dve_step"], u * per)
                dve.wait_ge(q_loaded, u * 16 + 16)
                dve.tensor_scalar(q[:, :], q[:, :], 64 ** -0.5, None, ALU.mult).then_inc(S["q_scaled"], 1)
                for n in range(NS + 1):
                    if n < NS:
                        b, sub = steps[n]
                        lo = b * C
                        dve.wait_ge(S["z_done"], u * NS + (n + 1))
                        step(dve.tensor_scalar(neg[:, sub, lo:T], Z[sub][:, lo:T], -1.0, None, ALU.mult))
                        dve.tensor_tensor(soft[:, sub, lo:T], Z[sub][:, lo:T], neg[:, sub, lo:T], ALU.min) \
                            .then_inc(S["mag_ready"], 1)
                        dve.wait_ge(S["softened"], u * NS + (n + 1))
                        step(dve.scalar_tensor_tensor(keep[:, sub, lo:T], neg[:, sub, lo:T], 0.0, soft[:, sub, lo:T],
                                                      ALU.min, ALU.subtract))
                        dve.tensor_tensor(keep[:, sub, lo:lo + C], keep[:, sub, lo:lo + C], core.strict[:, :], ALU.mult) \
                            .then_inc(S["keep_ready"], 1)
                    if n >= 1:
                        b, sub = steps[n - 1]
                        lo = b * C
                        dve.wait_ge(S["att_expd"], u * NS + n)
                        if b < NCH - 1:
                            dve.wait_ge(S["out_done"], u * NS + (n - 2))
                            dve.tensor_tensor(later[:, sub, lo + C:T], later[:, sub, lo + C:T], keep[:, sub, lo + C:T],
                                              ALU.add)
                        dve.tensor_copy(later[:, sub, lo:lo + C], keep[:, sub, lo:lo + C])
                        dve.copy_predicated(diag[:, sub, :], core.strict[:, :].bitcast(U32), att[:, sub, lo:lo + C]) \
                            .then_inc(S["att_ready"], 1)
                        dve.wait_ge(S["att_ready"], u * NS + n)
                dve.wait_ge(S["out_done"], u * NS + NS)
                dve.wait_ge(y_loaded, 16 * units)
                yo = flat(y[:, bass.ds(u, 1), :])
                dve.tensor_tensor(yo, yo, O, ALU.mult).then_inc(S["unit_free"], 1)
                step.ends(per)


def ssd_gates(core, wt, rows_dram, cols, bt, ct, btok, cb):
    H = SSH
    with Stage(core.nc, "ssdgate") as st:
        w = st.sb("w", [P, 3, D])
        pre = st.sb("pre", [P, 2, 3 + T])
        raw, mag, dt, cs, ec, de = (st.sb(n, [H, T]) for n in ("raw", "mag", "dt", "cs", "ec", "de"))
        (w_loaded, proj_done, evacuated, conv_done, activated, mag_ready, softened, a_ready, cs_ready, exped, turned,
         prod_done, b_turned, b_kept, dve_step, act_step, stored) = (st.sem(n) for n in (
             "w_loaded", "proj_done", "evacuated", "conv_done", "activated", "mag_ready", "softened", "a_ready", "cs_ready",
             "exped", "turned", "prod_done", "b_turned", "b_kept", "dve_step", "act_step", "stored"))
        a_head = core.col("a_head", 0)[0:H, :]
        block = st.block()

        @block.sync
        def _(sp):
            for n in range(3):
                sp.dma_start(w[:, n, :], wt[(SSD_TILE + n) * P:(SSD_TILE + n + 1) * P, :]).then_inc(w_loaded, 16)
            sp.wait_ge(exped, 1)
            sp.dma_start(rows_dram[0:H, :], cs[:, :]).then_inc(stored, 16)
            sp.dma_start(rows_dram[H:2 * H, :], ec[:, :]).then_inc(stored, 16)
            sp.wait_ge(stored, 32)

        @block.tensor
        def _(pe):
            pe.wait_ge(w_loaded, 48)
            project_features(pe, pair(core, 2), w[:, 2, :], core.hT, m=H).then_inc(proj_done, 1)
            for n in range(2):
                project_features(pe, pair(core, n), w[:, n, :], core.hT).then_inc(proj_done, 1)
            pe.wait_ge(exped, 1)
            for n, r in enumerate((cs, dt, de)):
                for c in range(NCH):
                    ins = pe.matmul(pair(core, 3)[:, (n * NCH + c) * H:(n * NCH + c + 1) * H],
                                    r[:, c * C:c * C + C], core.ident[0:H, 0:H], start=True, stop=True)
            ins.then_inc(turned, 1)
            pe.wait_ge(activated, 2)
            for g in range(2):
                for c in range(NCH):
                    s = slice(c * C, c * C + C)
                    ins = pe.matmul(pair(core, g)[:, s], bt[g * 64:g * 64 + 64, s], ct[g * 64:g * 64 + 64, s],
                                    start=True, stop=True)
                ins.then_inc(prod_done, 1)
            for c in range(NCH):
                s = slice(c * C, c * C + C)
                ins = pe.transpose(pair(core, 2)[:, s], bt[:, s], core.ident[:, :])
            ins.then_inc(b_turned, 1)

        @block.scalar
        def _(act):
            step = Chain(act, act_step)
            act.activation(a_head, core.col("a_log", 0)[0:H, :], ACT.Exp).then_inc(a_ready, 1)
            act.wait_ge(mag_ready, 1)
            step(act.activation(mag[:, :], mag[:, :], ACT.Exp, scale=-1.0))
            act.activation(mag[:, :], mag[:, :], ACT.Ln, bias=1.0).then_inc(softened, 1)
            for n in range(2):
                act.wait_ge(proj_done, n + 2)
                act.activation(pre[:, n, 3:3 + T], pair(core, n), ACT.Copy).then_inc(evacuated, 1)
            act.wait_ge(cs_ready, 1)
            act.activation(ec[:, :], cs[:, :], ACT.Exp)
            act.activation(de[:, :], de[:, :], ACT.Exp).then_inc(exped, 1)
            for n, dst in enumerate((bt, ct)):
                act.wait_ge(conv_done, n + 1)
                act.activation(dst[:, :], dst[:, :], ACT.Silu, bias=core.col("ssd_cb", KD + n)).then_inc(activated, 1)
            act.wait_ge(b_turned, 1)
            act.activation(btok[:, :, :], chunks(pair(core, 2)), ACT.Copy).then_inc(b_kept, 1)

        @block.vector
        def _(dve):
            step = Chain(dve, dve_step)
            dve.wait_ge(proj_done, 1)
            step(dve.tensor_scalar(raw[:, :], pair(core, 2)[0:H, :], core.col("dt_bias", 0)[0:H, :], None, ALU.add))
            dve.scalar_tensor_tensor(mag[:, :], raw[:, :], -1.0, raw[:, :], ALU.mult, ALU.max).then_inc(mag_ready, 1)
            dve.wait_ge(softened, 1)
            step(dve.scalar_tensor_tensor(dt[:, :], raw[:, :], 0.0, mag[:, :], ALU.max, ALU.add))
            dve.wait_ge(a_ready, 1)
            step(dve.tensor_scalar(raw[:, :], dt[:, :], a_head, -1.0, ALU.mult, ALU.mult))
            for c in range(NCH):
                s = slice(c * C, c * C + C)
                ins = dve.tensor_tensor_scan(cs[:, s], raw[:, s], raw[:, s], 0.0, ALU.add, ALU.bypass)
            step(ins)
            last = chunks(cs[:, :])[:, :, C - 1:C].to_broadcast([H, NCH, C])
            dve.tensor_tensor(chunks(de[:, :]), last, chunks(cs[:, :]), ALU.subtract).then_inc(cs_ready, 1)
            dve.wait_ge(evacuated, 2)
            step(dve.memset(pre[:, :, 0:3], 0.0))
            for n, dst in enumerate((bt, ct)):
                step(dve.tensor_scalar(dst[:, :], pre[:, n, 0:T], core.col("ssd_cw0", KD + n), None, ALU.mult))
                for j in range(1, 4):
                    ins = dve.scalar_tensor_tensor(dst[:, :], pre[:, n, j:j + T], core.col(f"ssd_cw{j}", KD + n),
                                                   dst[:, :], ALU.mult, ALU.add)
                    if j < 3:
                        step(ins)
                ins.then_inc(conv_done, 1)
            dve.wait_ge(turned, 1)
            dve.tensor_copy(cols[:, :], pair(core, 3)[:, 0:3 * NCH * H])
            for g in range(2):
                dve.wait_ge(prod_done, g + 1)
                dve.tensor_tensor(chunks(cb[:, g, :]), chunks(pair(core, g)),
                                  per_chunk(core.tri[:, :]), ALU.mult)


def ssd_branch(core, xz_park, rows_dram, cols, ct, btok, cb, y):
    units, per_group, H = 8, 4, SSH
    colv = cols[:, :].rearrange("p (n c h) -> p n c h", n=3, c=NCH)
    with Stage(core.nc, "ssd") as st:
        pre = st.sb("pre", [P, 2, 3 + T])
        xs = st.sb("xs", [P, T])
        xdt, xend = st.sb("xdt", [P, NCH, P]), st.sb("xend", [P, NCH, P])
        crep, erep = (st.sb(n, [P, 2, 2, T]) for n in ("crep", "erep"))
        att, cdec = (st.sb(n, [P, 2, T]) for n in ("att", "cdec"))
        state = st.sb("state", [P, NCH, P])
        S = {n: st.sem(n) for n in (
            "unit_done", "out_free", "conv_done", "activated", "expo_ready", "expd", "att_ready",
            "x_turned", "x_ready", "update_done", "state_ready", "out_done", "dve_step")}
        loaded, z_loaded = [st.sem("loaded0"), st.sem("loaded1")], [st.sem("z_loaded0"), st.sem("z_loaded1")]
        A, _, X, U = (pair(core, n) for n in range(4))

        def g_rows(g):
            return slice(g * 64, g * 64 + 64)

        block = st.block()

        @block.sync
        def _(sp):
            def load(u, par, head):
                def row(n, count=1):
                    return slice(n, n + count) if head else bass.ds(n, count)
                x_at, z_at = (u * (2 * P) + n * P if head else sp.snap(u * (2 * P) + n * P) for n in range(2))
                rows_at = [[u * 2 + (n * H + sub) if head else sp.snap(u * 2 + (n * H + sub)) for sub in range(2)]
                           for n in range(2)]
                y_at = y[:, u, :] if head else flat(y[:, bass.ds(u, 1), :])
                if not head:
                    sp.wait_ge(S["unit_done"], u - 1)
                sp.dma_start(pre[:, par, 3:], xz_park[row(x_at, P), :]).then_inc(loaded[par], 16)
                for n, dst in enumerate((crep, erep)):
                    for sub in range(2):
                        sp.dma_start(dst[:, par, sub, :], rows_dram[row(rows_at[n][sub]), :].to_broadcast([P, T])) \
                            .then_inc(loaded[par], 16)
                sp.dma_start(y_at, xz_park[row(z_at, P), :]).then_inc(z_loaded[par], 16)
            for par in range(2):
                load(par, par, True)
            with sp.Fori(1, units // 2) as two:
                for par in range(2):
                    load(two * 2 + par, par, False)

        @block.tensor
        def _(pe):
            for g in range(2):
                with pe.Fori(g * per_group, (g + 1) * per_group) as u:
                    pe.wait_ge(S["activated"], u + 1)
                    for c in range(NCH):
                        s = slice(c * C, c * C + C)
                        ins = pe.transpose(X[:, s], xs[:, s], core.ident[:, :])
                    ins.then_inc(S["x_turned"], 1)
                    pe.wait_ge(S["x_ready"], u + 1)
                    for c in range(NCH - 1):
                        ins = pe.matmul(U[g_rows(g), c * P:c * P + P], btok[:, c, g * 64:g * 64 + 64], xend[:, c, :],
                                        start=True, stop=True)
                    ins.then_inc(S["update_done"], 1)
                    pe.wait_ge(S["state_ready"], u + 1)
                    pe.wait_ge(S["att_ready"], u * 2 + 2)
                    pe.wait_ge(S["out_free"], u + 1)
                    for sub in range(2):
                        h = slice(sub * 64, sub * 64 + 64)
                        for c in range(NCH):
                            s = slice(c * C, c * C + C)
                            ins = pe.matmul(A[h, s], xdt[:, c, h], att[:, sub, s], start=True, stop=(c == 0))
                            if c:
                                ins = pe.matmul(A[h, s], state[g_rows(g), c, h], cdec[g_rows(g), sub, s],
                                                start=False, stop=True)
                    ins.then_inc(S["out_done"], 1)

        @block.scalar
        def _(act):
            with act.Fori(0, units) as u:
                act.wait_ge(S["conv_done"], u + 1)
                act.activation(xs[:, :], xs[:, :], ACT.Silu, bias=core.col_at("ssd_cb", u)).then_inc(S["activated"], 1)
                for sub in range(2):
                    act.wait_ge(S["expo_ready"], u * 2 + (sub + 1))
                    act.activation(att[:, sub, :], att[:, sub, :], ACT.Exp).then_inc(S["expd"], 1)

        @block.vector
        def _(dve):
            per = 3 + 2 + 1 + 2 * (NCH - 2) + 1

            def unit(g, u, par, two):
                step = Chain(dve, S["dve_step"], u * per)

                def spread(n, h, width):
                    return colv[:, n, :, bass.ds(u * 2 + h, 1)].to_broadcast([P, NCH, width])
                dve.wait_ge(loaded[par], two * (16 * 5) + 16 * 5)
                step(dve.tensor_scalar(xs[:, :], pre[:, par, 0:T], core.col_at("ssd_cw0", u), None, ALU.mult))
                for j in range(1, 4):
                    ins = dve.scalar_tensor_tensor(xs[:, :], pre[:, par, j:j + T], core.col_at(f"ssd_cw{j}", u), xs[:, :],
                                                   ALU.mult, ALU.add)
                    if j < 3:
                        step(ins)
                ins.then_inc(S["conv_done"], 1)
                for sub in range(2):
                    a = chunks(att[:, sub, :])
                    step(dve.tensor_tensor(a, chunks(crep[:, par, sub, :]), spread(0, sub, C), ALU.subtract))
                    dve.tensor_scalar(a, a, 0.0, None, ALU.min).then_inc(S["expo_ready"], 1)
                    dve.tensor_tensor(cdec[g_rows(g), sub, :], ct[g_rows(g), :], erep[g_rows(g), par, sub, :], ALU.mult)
                dve.wait_ge(S["x_turned"], u + 1)
                for sub in range(2):
                    h = slice(sub * 64, sub * 64 + 64)
                    ins = dve.tensor_tensor(xdt[:, :, h], chunks(X)[:, :, h], spread(1, sub, 64), ALU.mult)
                step(ins)
                for sub in range(2):
                    h = slice(sub * 64, sub * 64 + 64)
                    ins = dve.tensor_tensor(xend[:, :, h], xdt[:, :, h], spread(2, sub, 64), ALU.mult)
                ins.then_inc(S["x_ready"], 1)
                for sub in range(2):
                    dve.wait_ge(S["expd"], u * 2 + (sub + 1))
                    dve.tensor_tensor(att[:, sub, :], att[:, sub, :], cb[:, g, :], ALU.mult).then_inc(S["att_ready"], 1)
                dve.wait_ge(S["update_done"], u + 1)
                r = g_rows(g)
                step(dve.tensor_copy(state[r, 1, :], U[r, 0:P]))
                for c in range(1, NCH - 1):
                    for sub in range(2):
                        h = slice(sub * 64, sub * 64 + 64)
                        ins = dve.scalar_tensor_tensor(state[r, c + 1, h], state[r, c, h],
                                                       erep[r, par, sub, c * C + C - 1:c * C + C],
                                                       U[r, c * P + sub * 64:c * P + sub * 64 + 64], ALU.mult, ALU.add)
                        if (c, sub) != (NCH - 2, 1):
                            step(ins)
                ins.then_inc(S["state_ready"], 1)
                dve.wait_ge(S["out_done"], u + 1)
                step(dve.scalar_tensor_tensor(xs[:, :], xs[:, :], core.col_at("d_skip", u), A, ALU.mult, ALU.add))
                dve.sem_inc(S["out_free"], 1)
                dve.wait_ge(z_loaded[par], two * 16 + 16)
                yo = flat(y[:, bass.ds(u, 1), :])
                dve.tensor_tensor(yo, yo, xs[:, :], ALU.mult).then_inc(S["unit_done"], 1)
                dve.wait_ge(S["unit_done"], u + 1)
                step.ends(per)

            dve.memset(pre[:, :, 0:3], 0.0).then_inc(S["out_free"], 1)
            dve.wait_ge(S["out_free"], 1)
            for g in range(2):
                with dve.Fori(g * per_group // 2, (g + 1) * per_group // 2) as two:
                    for par in range(2):
                        unit(g, two * 2 + par, par, two)


def rwkv_low_rank(core, wt, lo):
    with Stage(core.nc, "rwlo") as st:
        w = st.sb("w", [P, D])
        raw, delta = st.sb("raw", [P, 1 + T]), st.sb("delta", [P, T])
        w_loaded, done, kept, mixed, step_sem, out = (st.sem(n) for n in ("w_loaded", "done", "kept", "mixed", "dve_step", "out"))
        block = st.block()

        @block.sync
        def _(sp):
            sp.dma_start(w[:, :], wt[RW_LO * P:(RW_LO + 1) * P, :]).then_inc(w_loaded, 16)

        @block.tensor
        def _(pe):
            pe.wait_ge(w_loaded, 16)
            project_features(pe, pair(core, 0), w, core.hT).then_inc(done, 1)

        @block.scalar
        def _(act):
            act.wait_ge(done, 1)
            act.activation(raw[:, 1:], pair(core, 0), ACT.Copy).then_inc(kept, 1)
            act.wait_ge(mixed, 1)
            act.activation(lo[0:64, :], lo[0:64, :], ACT.Tanh).then_inc(out, 1)

        @block.vector
        def _(dve):
            step = Chain(dve, step_sem)
            step(dve.memset(raw[:, 0:1], 0.0))
            dve.wait_ge(kept, 1)
            step(dve.tensor_tensor(delta[:, :], raw[:, 0:T], raw[:, 1:], ALU.subtract))
            dve.scalar_tensor_tensor(lo[:, :], delta[:, :], core.col("mu_lo", 0), raw[:, 1:], ALU.mult, ALU.add) \
                .then_inc(mixed, 1)


def rwkv_branch(core, wt, w_up, lo, F, y, gate_park, sb_park):
    order = ["r", "k", "v", "g"]
    nt, units = 4, 4
    r, k, v, kk, b, lw, cum, bonus = (F[:, n, :] for n in range(8))
    NL = LEVELS - 1
    with Stage(core.nc, "rw") as st:
        w = st.sb("w", [P, nt, D])
        up = st.sb("up", [P, P])
        loaded = [st.sem(f"w_loaded{t}") for t in range(nt)]
        raw = st.sb("raw", [P, 1 + T])
        tmp = st.sb("tmp", [P, T])
        tok = st.sb("tok", [P, 4, NCH, P])
        at, ak = (st.sb(n, [P, T]) for n in ("at", "ak"))
        ab, ar = (st.sb(n, [P, 2, T]) for n in ("ab", "ar"))
        X, XT, al1 = (st.sb(n, [P, T]) for n in ("X", "XT", "al1"))
        Y, al = v, (cum, al1)
        WT = st.sb("WT", [P, T])
        G = st.sb("G", [P, NCH, 64])
        U0, sa = (st.sb(n, [P, NCH, 2, 64]) for n in ("U0", "sa"))
        M = st.sb("M", [P, NCH, 64])
        gc = st.sb("gc", [P, NCH])
        S = {n: st.sem(n) for n in (
            "up_loaded", "proj_done", "evacuated", "unit_free", "raw_free", "mixed", "silu_done", "low_done", "low_kept",
            "kk_raw", "squared", "normed", "rooted", "bonus_in", "bonus_done", "cum_ready", "expd", "factors", "turned", "tok_ready",
            "prods", "prods2", "kept", "level_a", "y_done", "y_kept", "xyx", "x_ready", "w_done", "w_kept",
            "u_done", "u_kept", "sa_done", "sa_ready", "m_done", "m_ready", "out_done", "out_kept",
            "mean_done", "centred", "sq2", "var_done", "rooted2", "dve_step", "passed")}
        PA, PB, PC = (pair(core, n) for n in range(3))
        ng = 3 * KD // units
        fill = Filler(core, st, "fill", 3, wt, RW_FILL, places(gate_park, ng) + places(sb_park, 4),
                      [("features", ACT.Sigmoid, None)] * ng +
                      [(layout, func, None) for layout, func in (("features", ACT.Copy), ("features", ACT.Copy),
                                                                 ("tokens", ACT.Copy), ("features", ACT.Silu))])
        EARLY, HEAD, LEVEL, CHUNK = 4 * 16, 8, 2, 2
        PER_HEAD = HEAD + LEVEL * 2 * NL
        TAIL = EARLY + 2 * PER_HEAD + NCH * CHUNK
        assert TAIL == 16 * (fill.n - 1)

        def rows(sub):
            return slice(sub * 64, sub * 64 + 64)

        def cs(c):
            return slice(c * C, c * C + C)

        block = st.block()

        @block.sync
        def _(sp):
            def unit(u, head):
                for t in range(nt):
                    at = (RW_TILE + t) * P if head else sp.snap(u * (nt * P) + (RW_TILE + t) * P)
                    if not head:
                        sp.wait_ge(S["proj_done"], u * nt + (t + 1 - nt))
                    src = wt[at:at + P, :] if head else wt[bass.ds(at, P), :]
                    sp.dma_start(w[:, t, :], src).then_inc(loaded[t], 16)
                at = 0 if head else sp.snap(u * P)
                if not head:
                    sp.wait_ge(S["low_done"], u)
                sp.dma_start(up[:, :], w_up[0:P, :] if head else w_up[bass.ds(at, P), :]).then_inc(S["up_loaded"], 16)
                fill.load(sp, u, head)
            unit(0, True)
            with sp.Fori(1, units) as u:
                unit(u, False)

        @block.tensor
        def _(pe):
            def block_sum(mat, src, dst):
                for half in range(2):
                    h = slice(half * 512, half * 512 + 512)
                    ins = pe.matmul(dst[:, h], mat, src[:, h], start=True, stop=True)
                return ins

            def products(dst, lhs, rhs, sub):
                for c in range(NCH):
                    ins = pe.matmul(dst[:, cs(c)], lhs[rows(sub), cs(c)], rhs[rows(sub), cs(c)], start=True, stop=True)
                return ins

            def by_chunk(dst, lhs, rhs):
                for c in range(NCH):
                    ins = pe.matmul(dst[:, cs(c)], lhs[:, cs(c)], rhs[:, cs(c)], start=True, stop=True)
                return ins

            with pe.Fori(0, units) as u:
                pe.wait_ge(S["unit_free"], u + 1)
                for t in range(nt):
                    pe.wait_ge(loaded[t], 16 * u + 16)
                    if t >= 2:
                        pe.wait_ge(S["evacuated"], u * nt + (t - 1))
                    project_features(pe, (PA, PB)[t % 2], w[:, t, :], core.hT).then_inc(S["proj_done"], 1)
                pe.wait_ge(S["up_loaded"], 16 * u + 16)
                pe.wait_ge(S["evacuated"], u * nt + (nt - 1))
                for half in range(2):
                    h = slice(half * 512, half * 512 + 512)
                    pe.matmul(PC[:, h], up[0:64, :], lo[0:64, h], start=True, stop=True)
                    ins = pe.matmul(PA[:, h], up[64:128, :], lo[64:128, h], start=True, stop=True)
                ins.then_inc(S["low_done"], 1)
                fill.advance(pe, u, 0, 16)
                pe.wait_ge(S["evacuated"], u * nt + nt)
                pe.wait_ge(S["squared"], u + 1)
                block_sum(core.same_head[:, :], tmp, PB).then_inc(S["normed"], 1)
                fill.advance(pe, u, 16, 32)
                pe.wait_ge(S["low_kept"], u + 1)
                pe.wait_ge(S["bonus_in"], u + 1)
                block_sum(core.same_head[:, :], bonus, PC).then_inc(S["bonus_done"], 1)
                fill.advance(pe, u, 32, EARLY)
                pe.wait_ge(S["factors"], u + 1)
                for n, src in enumerate((v, b, k, kk)):
                    dst = (PA, PC, PB, PA)[n]
                    if n == 3:
                        pe.wait_ge(S["tok_ready"], u * 4 + 1)
                    for c in range(NCH):
                        ins = pe.transpose(dst[:, cs(c)], src[:, cs(c)], core.ident[:, :])
                    ins.then_inc(S["turned"], 1)
                pe.wait_ge(S["tok_ready"], u * 4 + 4)
                for sub in range(2):
                    e = u * 2 + sub
                    if sub:
                        pe.wait_ge(S["u_kept"], u * 2 + 1)
                    products(PA, b, kk, sub)
                    products(PB, kk, b, sub)
                    products(PC, k, kk, sub).then_inc(S["prods"], 1)
                    at = EARLY + sub * PER_HEAD
                    fill.advance(pe, u, at, at + HEAD)
                    at += HEAD
                    pe.wait_ge(S["kept"], e * 2 + 1)
                    products(PC, b, r, sub)
                    products(PA, k, r, sub).then_inc(S["prods2"], 1)
                    for l in range(1, LEVELS):
                        n = e * NL + (l - 1)
                        pe.wait_ge(S["level_a"], n + 1)
                        for hf in range(2):
                            if l > 1:
                                pe.wait_ge(S["x_ready"], n * 2 + (hf - 1))
                            elif hf == 0:
                                pe.wait_ge(S["kept"], e * 2 + 2)
                            for c in range(hf * NCH // 2, (hf + 1) * NCH // 2):
                                ins = pe.matmul(PC[:, cs(c)], al[l % 2][:, cs(c)], X[:, cs(c)], start=True, stop=True)
                            ins.then_inc(S["y_done"], 1)
                            fill.advance(pe, u, at, at + LEVEL)
                            at += LEVEL
                        for hf in range(2):
                            pe.wait_ge(S["y_kept"], n * 2 + (hf + 1))
                            for c in range(hf * NCH // 2, (hf + 1) * NCH // 2):
                                if l < NL:
                                    pe.matmul(level_views(PA[:, cs(c)], l)[0], XT[:, cs(c)],
                                              level_views(Y[:, cs(c)], l)[0], start=True, stop=True)
                                ins = pe.matmul(level_views(PB[:, cs(c)], l)[1], Y[:, cs(c)],
                                                level_views(XT[:, cs(c)], l)[1], start=True, stop=True)
                            ins.then_inc(S["xyx"], 1)
                    pe.wait_ge(S["x_ready"], (e * NL + NL) * 2)
                    for c in range(NCH):
                        pe.matmul(PC[rows(sub), cs(c)], tok[:, 3, c, rows(sub)], XT[:, cs(c)], start=True, stop=True)
                        ins = pe.matmul(PB[:, c * 64:c * 64 + 64], ak[:, cs(c)], tok[:, 0, c, rows(sub)], start=True, stop=True)
                    ins.then_inc(S["w_done"], 1)
                    pe.wait_ge(S["w_kept"], e + 1)
                    for c in range(NCH):
                        ins = pe.matmul(PA[:, c * 64:c * 64 + 64], XT[:, cs(c)], G[:, c, :], start=True, stop=True)
                    ins.then_inc(S["u_done"], 1)
                pe.wait_ge(S["u_kept"], u * 2 + 2)
                for c in range(NCH):
                    if c:
                        pe.wait_ge(S["m_ready"], u * (NCH - 1) + c)
                        for sub in range(2):
                            ins = pe.matmul(PB[:, sub * 512 + c * 64:sub * 512 + c * 64 + 64], WT[rows(sub), cs(c)],
                                            M[rows(sub), c, :], start=True, stop=True)
                        ins.then_inc(S["sa_done"], 1)
                    if c < NCH - 1:
                        mc = slice(c * 64, c * 64 + 64)
                        for sub in range(2):
                            pe.matmul(PC[rows(sub), mc], tok[:, 2, c, rows(sub)], tok[:, 0, c, rows(sub)],
                                      start=True, stop=False)
                            if c:
                                pe.matmul(PC[rows(sub), mc], core.ident[rows(sub), rows(sub)], M[rows(sub), c, :],
                                          start=False, stop=False)
                    at = EARLY + 2 * PER_HEAD + c * CHUNK
                    fill.advance(pe, u, at, at + CHUNK)
                    pe.wait_ge(S["sa_ready"], u * NCH + (c + 1))
                    if c < NCH - 1:
                        for sub in range(2):
                            ins = pe.matmul(PC[rows(sub), mc], tok[:, 1, c, rows(sub)], sa[:, c, sub, :],
                                            start=False, stop=True)
                        ins.then_inc(S["m_done"], 1)
                for sub in range(2):
                    for c in range(NCH):
                        o = PA[rows(sub), cs(c)]
                        pe.matmul(o, tok[:, 0, c, rows(sub)], ar[:, sub, cs(c)], start=True, stop=False)
                        ins = pe.matmul(o, sa[:, c, sub, :], ab[:, sub, cs(c)], start=False, stop=(c == 0))
                        if c:
                            ins = pe.matmul(o, M[rows(sub), c, :], r[rows(sub), cs(c)], start=False, stop=True)
                ins.then_inc(S["out_done"], 1)
                pe.wait_ge(S["out_kept"], u + 1)
                block_sum(core.mean_head[:, :], lw, PB).then_inc(S["mean_done"], 1)
                fill.advance(pe, u, TAIL, TAIL + 8)
                pe.wait_ge(S["sq2"], u + 1)
                block_sum(core.mean_head[:, :], cum, PC).then_inc(S["var_done"], 1)
                fill.advance(pe, u, TAIL + 8, 16 * fill.n)

        @block.scalar
        def _(act):
            fill.begin(act)
            with act.Fori(0, units) as u:
                for t in range(nt):
                    act.wait_ge(S["proj_done"], u * nt + (t + 1))
                    act.wait_ge(S["raw_free"], u * nt + (t + 1))
                    act.activation(raw[:, 1:], (PA, PB)[t % 2], ACT.Copy).then_inc(S["evacuated"], 1)
                act.wait_ge(S["low_done"], u + 1)
                act.activation(lw, PC, ACT.Sigmoid, bias=core.col_at("w0", u))
                act.activation(b, PA, ACT.Sigmoid, bias=core.col_at("a0", u)).then_inc(S["low_kept"], 1)
                act.wait_ge(S["mixed"], u * nt + nt)
                yo = flat(y[:, bass.ds(u, 1), :])
                act.activation(yo, yo, ACT.Silu).then_inc(S["silu_done"], 1)
                act.wait_ge(S["kk_raw"], u + 1)
                act.activation(tmp[:, :], kk, ACT.Square).then_inc(S["squared"], 1)
                fill.keep(act, u, 0)
                act.wait_ge(S["normed"], u + 1)
                act.activation(tmp[:, :], PB, ACT.Sqrt).then_inc(S["rooted"], 1)
                fill.keep(act, u, 1)
                act.wait_ge(S["cum_ready"], u + 1)
                act.activation(gc[:, 0:NCH - 1], gc[:, 0:NCH - 1], ACT.Exp)
                act.activation(lw, lw, ACT.Exp)
                act.activation(tmp[:, :], cum, ACT.Exp, scale=-1.0).then_inc(S["expd"], 1)
                act.wait_ge(S["expd"], u * 2 + 1)
                act.activation(cum, cum, ACT.Exp).then_inc(S["expd"], 1)
                fill.keep(act, u, 2)
                fill.keep(act, u, 3)
                for n in range(4):
                    act.wait_ge(S["turned"], u * 4 + (n + 1))
                    act.activation(tok[:, n, :, :], chunks((PA, PC, PB, PA)[n]), ACT.Copy).then_inc(S["tok_ready"], 1)
                for sub in range(2):
                    e = u * 2 + sub
                    at = EARLY + sub * PER_HEAD + HEAD
                    for l in range(1, LEVELS):
                        for hf in range(2):
                            h = slice(hf * 512, hf * 512 + 512)
                            act.wait_ge(S["y_done"], (e * NL + (l - 1)) * 2 + (hf + 1))
                            act.activation(Y[:, h], PC[:, h], ACT.Copy).then_inc(S["y_kept"], 1)
                            at += LEVEL
                            if at % 16 == 0:
                                fill.keep(act, u, at // 16 - 1)
                    act.wait_ge(S["w_done"], e + 1)
                    act.activation(WT[rows(sub), :], PC[rows(sub), :], ACT.Copy)
                    act.activation(G[:, :, :], PB[:, 0:NCH * 64].rearrange("p (c i) -> p c i", c=NCH), ACT.Copy) \
                        .then_inc(S["w_kept"], 1)
                fill.keep(act, u, fill.n - 2)
                act.wait_ge(S["out_done"], u + 1)
                act.activation(lw, PA, ACT.Copy).then_inc(S["out_kept"], 1)
                act.wait_ge(S["centred"], u + 1)
                act.activation(cum, lw, ACT.Square).then_inc(S["sq2"], 1)
                act.wait_ge(S["var_done"], u + 1)
                act.activation(tmp[:, :], PC, ACT.Sqrt, bias=core.const(GN_EPS)).then_inc(S["rooted2"], 1)
                fill.keep(act, u, fill.n - 1)
                fill.end(act, u)

        @block.gpsimd
        def _(pool):
            with pool.Fori(0, 2 * units) as e:
                pool.wait_ge(S["kept"], e * 2 + 1)
                for l in range(1, LEVELS):
                    if l >= 3:
                        pool.wait_ge(S["y_done"], (e * NL + (l - 2)) * 2)
                    pool.tensor_tensor(chunks(al[l % 2][:, :]), chunks(at[:, :]), per_chunk(core.level_mask[:, l, :]),
                                       ALU.mult).then_inc(S["level_a"], 1)

        @block.vector
        def _(dve):
            for a in (at[:, :], ak[:, :], ab[:, :, :], ar[:, :, :]):
                dve.memset(a, 0.0)
            dve.memset(raw[:, 0:1], 0.0).then_inc(S["unit_free"], 1)
            dve.sem_inc(S["raw_free"], 1)
            per = 4 + 3 + 2 + 7 + 2 + 3
            with dve.Fori(0, units) as u:
                step = Chain(dve, S["dve_step"], u * per)
                yo = flat(y[:, bass.ds(u, 1), :])
                for t, (dst, what) in enumerate(((r, "r"), (k, "k"), (v, "v"), (yo, "g"))):
                    dve.wait_ge(S["evacuated"], u * nt + (t + 1))
                    step(dve.tensor_tensor(bonus, raw[:, 0:T], raw[:, 1:], ALU.subtract))
                    dve.scalar_tensor_tensor(dst, bonus, core.col_at("mu_" + what, u), raw[:, 1:], ALU.mult, ALU.add) \
                        .then_inc(S["mixed"], 1)
                    dve.wait_ge(S["mixed"], u * nt + (t + 1))
                    dve.sem_inc(S["raw_free"], 1)
                dve.tensor_scalar(kk, k, core.col_at("k_k", u), None, ALU.mult).then_inc(S["kk_raw"], 1)
                dve.wait_ge(S["rooted"], u + 1)
                step(dve.tensor_scalar(tmp[:, :], tmp[:, :], 1e-12, None, ALU.max))
                step(dve.reciprocal(tmp[:, :], tmp[:, :]))
                step(dve.tensor_tensor(kk, kk, tmp[:, :], ALU.mult))
                dve.wait_ge(S["low_kept"], u + 1)
                step(dve.tensor_scalar(tmp[:, :], b, -1.0, core.col_at("k_a", u), ALU.add, ALU.mult))
                step(dve.scalar_tensor_tensor(k, tmp[:, :], 1.0, k, ALU.add, ALU.mult))
                dve.scalar_tensor_tensor(bonus, r, core.col_at("r_k", u), k, ALU.mult, ALU.mult).then_inc(S["bonus_in"], 1)
                dve.tensor_tensor(b, kk, b, ALU.mult)
                step(dve.tensor_scalar(lw, lw, -float(np.exp(-0.5)), None, ALU.mult))
                for c in range(NCH):
                    ins = dve.tensor_tensor_scan(cum[:, cs(c)], lw[:, cs(c)], lw[:, cs(c)], 0.0, ALU.add, ALU.bypass)
                step(ins)
                cc = chunks(cum)
                last, mid = cc[:, :, C - 1:C], cc[:, :, C // 2 - 1:C // 2]
                gv = gc[:, :].unsqueeze(2)
                step(dve.tensor_tensor(gv[:, 0:NCH - 1, :], last[:, 0:NCH - 1, :], mid[:, 0:NCH - 1, :], ALU.subtract))
                step(dve.tensor_tensor(gv[:, 0:NCH - 1, :], gv[:, 0:NCH - 1, :], mid[:, 1:NCH, :], ALU.add))
                step(dve.tensor_tensor(chunks(WT[:, :]), cc, mid.to_broadcast([P, NCH, C]), ALU.subtract))
                step(dve.tensor_tensor(lw, WT[:, :], lw, ALU.subtract))
                dve.tensor_copy(cum, WT[:, :]).then_inc(S["cum_ready"], 1)
                dve.wait_ge(S["bonus_done"], u + 1)
                step(dve.tensor_tensor(bonus, PC, v, ALU.mult))
                dve.wait_ge(S["expd"], u * 2 + 2)
                dve.tensor_tensor(r, r, cum, ALU.mult)
                dve.tensor_tensor(kk, kk, lw, ALU.mult)
                dve.scalar_tensor_tensor(b, b, -1.0, tmp[:, :], ALU.mult, ALU.mult)
                dve.tensor_tensor(k, k, tmp[:, :], ALU.mult).then_inc(S["factors"], 1)
                for sub in range(2):
                    e = u * 2 + sub
                    eye = per_chunk(core.ident[:, :])
                    dve.tensor_copy(chunks(X[:, :]), eye)
                    step(dve.tensor_copy(chunks(XT[:, :]), eye))
                    wait_alone(dve, S["prods"], e + 1, S["passed"])
                    dve.copy_predicated(chunks(at[:, :]), bits(core.strict[:, :]), chunks(PA))
                    dve.copy_predicated(chunks(XT[:, :]), bits(core.level_mask[:, 0, :]), chunks(PA))
                    dve.copy_predicated(chunks(X[:, :]), bits(core.level0_T[:, :]), chunks(PB))
                    dve.copy_predicated(chunks(ak[:, :]), bits(core.strict[:, :]), chunks(PC)).then_inc(S["kept"], 1)
                    wait_alone(dve, S["prods2"], e + 1, S["passed"])
                    dve.copy_predicated(chunks(ab[:, sub, :]), bits(core.upto[:, :]), chunks(PC))
                    dve.copy_predicated(chunks(ar[:, sub, :]), bits(core.upto[:, :]), chunks(PA)).then_inc(S["kept"], 1)
                    for l in range(1, LEVELS):
                        for hf in range(2):
                            n = (e * NL + (l - 1)) * 2 + (hf + 1)
                            h = slice(hf * 512, hf * 512 + 512)
                            dve.wait_ge(S["xyx"], n)
                            if l < NL:
                                xe = level_views(X[:, h], l)[0]
                                dve.tensor_tensor(xe, xe, level_views(PA[:, h], l)[0], ALU.add)
                            xo = level_views(XT[:, h], l)[1]
                            dve.tensor_tensor(xo, xo, level_views(PB[:, h], l)[1], ALU.add).then_inc(S["x_ready"], 1)
                    dve.wait_ge(S["u_done"], e + 1)
                    uc = PA[:, 0:NCH * 64].rearrange("p (c i) -> p c i", c=NCH)
                    dve.tensor_copy(sa[:, 0, sub, :], uc[:, 0, :])
                    dve.tensor_copy(U0[:, 1:, sub, :], uc[:, 1:, :]).then_inc(S["u_kept"], 1)
                dve.wait_ge(S["u_kept"], u * 2 + 2)
                dve.sem_inc(S["sa_ready"], 1)
                for c in range(NCH):
                    if c:
                        dve.wait_ge(S["sa_done"], u * (NCH - 1) + c)
                        dve.tensor_tensor(sa[:, c, :, :], PB.rearrange("p (a n) -> p a n", a=2)[:, :, c * 64:c * 64 + 64],
                                          U0[:, c, :, :], ALU.add).then_inc(S["sa_ready"], 1)
                    if c < NCH - 1:
                        dve.wait_ge(S["m_done"], u * (NCH - 1) + (c + 1))
                        dve.tensor_scalar(M[:, c + 1, :], PC[:, c * 64:c * 64 + 64], gc[:, c:c + 1], None, ALU.mult) \
                            .then_inc(S["m_ready"], 1)
                dve.wait_ge(S["mean_done"], u + 1)
                dve.tensor_tensor(lw, lw, PB, ALU.subtract).then_inc(S["centred"], 1)
                dve.wait_ge(S["rooted2"], u + 1)
                step(dve.reciprocal(tmp[:, :], tmp[:, :]))
                step(dve.scalar_tensor_tensor(lw, lw, core.col_at("rw_ln_g", u), tmp[:, :], ALU.mult, ALU.mult))
                step(dve.scalar_tensor_tensor(lw, lw, core.col_at("rw_ln_b", u), bonus, ALU.add, ALU.add))
                dve.wait_ge(S["silu_done"], u + 1)
                dve.tensor_tensor(yo, yo, lw, ALU.mult).then_inc(S["unit_free"], 1)
                step.ends(per)


def block_3(core, d):
    nc = core.nc
    with Stage(nc, "b3") as st:
        core.hT = st.sb("hT", [P, KD, T])
        mats, masks = st.sb("mats", [P, 3, P]), st.sb("masks", [P, 3, P])
        core.same_head, core.mean_head, core.triangle = (mats[:, n, :] for n in range(3))
        core.strict, core.upto, core.level0_T = (masks[:, n, :] for n in range(3))
        with Stage(nc, "consts3") as s2:
            got = s2.sem("consts_loaded")
            block = s2.block()

            @block.sync
            def _(sp):
                sp.dma_start(mats[:, :, :].rearrange("p a b -> p (a b)"), d["c_mat3"]).then_inc(got, 16)
                sp.dma_start(masks[:, :, :].rearrange("p a b -> p (a b)"), d["c_mask3"]).then_inc(got, 16)
                sp.wait_ge(got, 32)
        rms_norm(core, "rms3", core.xT, "norm_g_3", core.hT, park=d["x_park"])
        with Stage(nc, "rws") as s2:
            y, lo = s2.sb("y", [P, 4, T]), s2.sb("lo", [P, T])
            rwkv_low_rank(core, d["w3"], lo)
            rwkv_branch(core, d["w3"], d["w_up"], lo, core.xT, y, d["gate_park"], d["sb_park"])
            weighted_projection(core, "yrw", y, 4, d["wrw"], d["gate_park"], 2 * KD, core.xT, False)
        with Stage(nc, "sbs") as s2:
            y = s2.sb("y", [P, 4, T])
            stick_breaking_branch(core, d["w3"], y, d["sb_park"], d["xz_park"])
            weighted_projection(core, "ysb", y, 4, d["wsb"], d["gate_park"], 0, core.xT, True)
        with Stage(nc, "ssds") as s2:
            y = core.hT
            with Stage(nc, "ssdp") as s3:
                cols = s3.sb("cols", [P, 3 * NCH * SSH])
                bt, ct, btok, cb = (s3.sb("bt", [P, T]), s3.sb("ct", [P, T]), s3.sb("btok", [P, NCH, P]),
                                    s3.sb("cb", [P, 2, T]))
                ssd_gates(core, d["w3"], d["ssd_rows"], cols, bt, ct, btok, cb)
                ssd_branch(core, d["xz_park"], d["ssd_rows"], cols, ct, btok, cb, y)
            rms_norm(core, "rms_ssd", y, "ssd_ng", y)
            weighted_projection(core, "yssd", y, KD, d["wssd"], d["gate_park"], KD, core.xT, True,
                                back=d["x_park"])
        out_projection(core, "o3", core.xT, KD, d["wo3"], core.hT)
        rms_norm(core, "fin3", core.hT, "final_g_3", core.xT)


SEG1 = segments([("hg_q", 512), ("hg_f", 512), ("hg_i", 512), ("hg_z", 512), ("gla_q", 256), ("gla_k", 256),
                 ("gla_v", 512), ("gla_a", 16), ("gla_z", 512), ("ml_q", 256), ("ml_k", 256), ("ml_v", 512),
                 ("ml_i", 4), ("ml_f", 4), ("ml_o", 512), ("ml_z", 512)])


def tile_order_1():
    def tile(name, n):
        s = SEG1[name][0] + n * P
        return s, min(s + P, SEG1[name][1])
    out = []
    for h in range(4):
        out += [tile("hg_f", h), tile("hg_q", h), tile("hg_i", h), tile("hg_z", h)]
    out += [tile("gla_a", 0), (SEG1["ml_i"][0], SEG1["ml_f"][1])]
    for u in range(4):
        out += [tile("gla_" + "qk"[u % 2], u // 2), tile("gla_v", u), tile("gla_z", u)]
    for u in range(2):
        out += [tile("ml_q", u), tile("ml_k", u)]
        out += [tile(n, 2 * u + s) for n in ("ml_v", "ml_o", "ml_z") for s in range(2)]
    return out


def in_tiles(w, ranges):
    k = w.shape[0] // P
    out = np.zeros((len(ranges), P, k, P), np.float32)
    v = w.reshape(k, P, -1)
    for n, (a, b) in enumerate(ranges):
        out[n, :, :, :b - a] = v[:, :, a:b].transpose(1, 0, 2)
    return out.reshape(len(ranges) * P, k * P)


def out_tiles(w):
    return in_tiles(w, [(e * P, e * P + P) for e in range(w.shape[1] // P)])


def columns(i):
    b = i["b_in"][0]
    out = [("norm_w", i["norm_w"][0])]
    g = b[SEG1["gla_q"][0]:SEG1["gla_k"][1]].reshape(2, 2, P)
    out.append(("gla_qk", g.transpose(1, 0, 2).reshape(-1)))
    for n in ("hg_q", "hg_f", "hg_z", "gla_z", "ml_q", "ml_k", "ml_o", "ml_z"):
        out.append((n, b[slice(*SEG1[n])]))
    out += [("gla_a_b", b[slice(*SEG1["gla_a"])]), ("ml_i_b", b[slice(*SEG1["ml_i"])]),
            ("ml_f_b", b[slice(*SEG1["ml_f"])]), ("hg_lb", i["hg_lb_logits"][0]),
            ("lb", np.zeros(512, np.float32)), ("one_minus_lb", np.zeros(512, np.float32)),
            ("hg_nw", i["hg_norm_w"][0]), ("gla_b_a2", i["gla_b_a2"][0]), ("gla_nw", i["gla_norm_w"][0]),
            ("ml_cb", i["ml_conv_b"][0]), ("ml_nw", i["ml_norm_w"][0]), ("final_norm_w", i["final_norm_w"])]
    out += [(f"ml_cw{j}", i["ml_conv_w"][0, j]) for j in range(4)]
    return out + columns_2(i) + columns_3(i)


CONSTS = (NORM_EPS, LN_EPS, GN_EPS, -0.5)


def pack_columns(i):
    index, parts, at = {}, [], 0
    for name, vec in columns(i):
        n = -(-vec.size // P)
        col = np.zeros(n * P, np.float32)
        col[:vec.size] = vec.reshape(-1)
        parts.append(col.reshape(n, P).T)
        index[name] = at
        at += n
    for v in CONSTS:
        parts.append(np.full((P, 1), v, np.float32))
        index[v] = at
        at += 1
    return np.ascontiguousarray(np.concatenate(parts, 1)), index


def level_masks():
    s, t = np.arange(P)[:, None], np.arange(P)[None, :]
    top = np.floor(np.log2(np.maximum(s ^ t, 1))).astype(int)
    return np.stack([((s < t) & (top == l)) for l in range(LEVELS)], 1).astype(np.float32)


def shape_constants():
    s, t = np.arange(P)[:, None], np.arange(P)[None, :]
    mats = {"ident": np.eye(P), "ones": np.ones((P, P)), "mean_d": np.full((P, P), 1.0 / D),
            "mean_p": np.full((P, P), 1.0 / P),
            "mean_v": np.full((P, P), 1.0 / RDV), "tri": (t >= s)}
    return {n: m.astype(np.float32) for n, m in mats.items()}


def lay_out(i):
    i = {n: np.asarray(a) for n, a in i.items()}
    d = {"x": i["x"][0]}
    w1 = i["w_in"][0]
    d["w1"] = in_tiles(w1, tile_order_1())
    b = i["b_in"][0]
    d["b1_vrow"] = np.concatenate([b[slice(*SEG1[n])] for n in ("hg_i", "gla_v", "ml_v")])[None, :]
    d["gla_w_a2"] = i["gla_w_a2"][0]
    for n, name in enumerate(("wo1a", "wo1b", "wo1c")):
        d[name] = out_tiles(i["w_out"][0, n * 512:(n + 1) * 512])
    d["cols"], index = pack_columns(i)
    for n, m in shape_constants().items():
        d["c_" + n] = m
    d["c_level_mask"] = level_masks().reshape(P, LEVELS * P)
    lay_out_2(i, d)
    lay_out_3(i, d)
    return {n: np.ascontiguousarray(a) for n, a in d.items()}, index


def build(nc, d, out, index, blocks=(1, 2, 3)):
    core = Core()
    core.nc, core.index = nc, index
    Stage.ended = []
    with ExitStack() as ctx:
        core.ps = ctx.enter_context(nc.psum_tensor("ps", [P, 8 * 512], F32))
        core.xT = ctx.enter_context(nc.sbuf_tensor("xT", [P, KD, T], F32))
        core.cols = ctx.enter_context(nc.sbuf_tensor("cols_sb", list(d["cols"].shape), F32))
        core.col = lambda name, n: core.cols[:, index[name] + n:index[name] + n + 1]
        core.col_at = lambda name, n: core.cols[:, bass.ds(n + index[name], 1)]
        core.const = lambda v: core.col(v, 0)
        names = ["ident", "ones", "mean_d", "mean_p", "mean_v", "tri"]
        tiles = {n: ctx.enter_context(nc.sbuf_tensor("c_" + n + "_sb", [P, P], F32)) for n in names}
        core.ident, core.ones, core.mean_d, core.mean_p, core.mean_v, core.tri = (tiles[n] for n in names)
        core.level_mask = ctx.enter_context(nc.sbuf_tensor("level_mask", [P, LEVELS, P], F32))
        with Stage(nc, "consts") as st:
            got = st.sem("consts_loaded")
            block = st.block()

            @block.sync
            def _(sp):
                for n in names:
                    sp.dma_start(tiles[n][:, :], d["c_" + n]).then_inc(got, 16)
                sp.dma_start(core.level_mask[:, :, :].rearrange("p l t -> p (l t)"), d["c_level_mask"]).then_inc(got, 16)
                sp.dma_start(core.cols[:, :], d["cols"]).then_inc(got, 16)
                sp.wait_ge(got, 16 * (len(names) + 2))
        load_input(core, d["x"])
        if 1 in blocks:
            block_1(core, d)
        if 2 in blocks:
            block_2(core, d)
        if 3 in blocks:
            block_3(core, d)
        store_output(core, core.xT, out)


SCRATCH = {"gla_park": (12 * P, T), "ml_park": (16 * P, T), "ml_rows": (12, T), "o_park": (RH * RDV, T), "x_park": (D, T), "gate_park": (3 * D, T), "xz_park": (2 * D, T), "sb_park": (4 * SBW, T), "ssd_rows": (2 * SSH, T)}


def kernel(**inputs):
    from concourse import bacc
    from concourse.bass_utils import run_bass_kernel_spmd

    arrays, index = lay_out(inputs)
    nc = bacc.Bacc("TRN2", target_bir_lowering=False, num_devices=1)
    d = {n: nc.dram_tensor("in_" + n, a.shape, mybir.dt.from_np(a.dtype), kind="ExternalInput").ap()
         for n, a in arrays.items()}
    for n, shape in SCRATCH.items():
        d[n] = nc.dram_tensor("scratch_" + n, shape, F32, kind="Internal").ap()
    out = nc.dram_tensor("out_0", (T, D), F32, kind="ExternalOutput").ap()
    build(nc, d, out, index)
    r = run_bass_kernel_spmd(nc, [{"in_" + n: a for n, a in arrays.items()}], core_ids=[0])
    return r.results[0]["out_0"].reshape(1, T, D)
```

```python
from contextlib import ExitStack

import numpy as np

import concourse.bass as bass
from concourse import mybir
from concourse.alu_op_type import AluOpType as ALU

ACT = mybir.ActivationFunctionType
F32 = mybir.dt.float32
F32R = mybir.dt.float32r
U32 = mybir.dt.uint32

P = 128
T = 1024
D = 1024
KD = D // P
C = 128
NCH = T // C
NORM_EPS = 1e-6
LN_EPS = 1e-5
GN_EPS = 64e-5


def segments(sizes):
    at, out = 0, {}
    for name, n in sizes:
        out[name] = (at, at + n)
        at += n
    return out


class Chain:

    def __init__(self, eng, sem, base=0):
        self.eng, self.sem, self.base, self.k = eng, sem, base, 0

    def __call__(self, ins):
        self.k += 1
        ins.then_inc(self.sem, 1)
        self.eng.wait_ge(self.sem, self.base + self.k)

    def ends(self, per):
        assert self.k == per, (self.k, per)


def wait_alone(eng, sem, value, passed):
    eng.wait_ge(sem, value)
    eng.sem_inc(passed, 1)


def per_chunk(mat):
    return mat.unsqueeze(1).to_broadcast([P, NCH, C])


def bits(mask):
    return per_chunk(mask.bitcast(U32))


def flat(ap):
    return ap.rearrange("p a t -> p (a t)")


def chunks(ap, n=NCH):
    return ap.rearrange("p (c t) -> p c t", c=n)


class Stage:

    ended = []

    def __init__(self, nc, name):
        self.nc, self.name, self.ctx, self.sems = nc, name, ExitStack(), []

    def __enter__(self):
        self.ctx.__enter__()
        return self

    def __exit__(self, *a):
        self.ctx.__exit__(*a)
        if self.sems:
            for s in Stage.ended:
                self.nc.release_semaphore(s)
            Stage.ended = self.sems

    def sb(self, name, shape, dt=F32):
        return self.ctx.enter_context(self.nc.sbuf_tensor(f"{self.name}_{name}", shape, dt))

    def sem(self, name):
        self.sems.append(self.nc.alloc_semaphore(f"{self.name}_{name}"))
        return self.sems[-1]

    def block(self):
        block = self.ctx.enter_context(self.nc.Block())

        @block.gpsimd
        def _(pool):
            for s in Stage.ended:
                pool.sem_clear(s)

        return block


class Core:
    pass


def pair(core, n):
    return core.ps[:, n * T:(n + 1) * T]


def project_half(pe, out, w, h, half, m=P, c0=0, nk=KD):
    t = slice(half * 512, half * 512 + 512)
    for k in range(nk):
        ins = pe.matmul(out[0:m, t], w[:, k * P + c0:k * P + c0 + m], h[:, k, t], start=(k == 0), stop=(k == nk - 1))
    return ins


def project_features(pe, out, w, h, m=P, c0=0, nk=KD):
    for half in range(2):
        ins = project_half(pe, out, w, h, half, m, c0, nk)
    return ins


def project_chunk(pe, out, w, h, c, ones=None, bias=None, nk=KD):
    o = out[:, c * C:c * C + P]
    for k in range(nk):
        ins = pe.matmul(o, h[:, k, c * C:c * C + C], w[:, k * P:k * P + P],
                        start=(k == 0), stop=(k == nk - 1 and bias is None))
    if bias is not None:
        ins = pe.matmul(o, ones[0:1, :], bias, start=False, stop=True)
    return ins


def project_tokens(pe, out, w, h, ones=None, bias=None, nk=KD):
    for c in range(NCH):
        ins = project_chunk(pe, out, w, h, c, ones, bias, nk)
    return ins


def load_tiles(sp, core, st, wt, slots, loaded, proj_done, first, ntile, units):
    for t in range(ntile):
        sp.dma_start(slots[:, t, :], wt[(first + t) * P:(first + t + 1) * P, :]).then_inc(loaded[t], 16)
    if units > 1:
        with sp.Fori(1, units) as u:
            for t in range(ntile):
                at = sp.snap(u * (ntile * P) + (first + t) * P)
                sp.wait_ge(proj_done, u * ntile + (t + 1 - ntile))
                sp.dma_start(slots[:, t, :], wt[bass.ds(at, P), :]).then_inc(loaded[t], 16)


class Filler:

    def __init__(self, core, st, name, pair_n, wt, first, places, kinds, ring=2, proj=None, before=0):
        self.proj, self.before = proj, before
        self.core, self.wt, self.first, self.places = core, wt, first, places
        self.kinds, self.n, self.ring, self.out = kinds, len(kinds), ring, pair(core, pair_n)
        assert self.n % ring == 0
        self.kept_sb = st.sb(name + "_out", [P, ring, T])
        self.stored = [st.sem(f"{name}_stored{s}") for s in range(ring)]
        self.kept = st.sem(name + "_kept")
        if proj is None:
            self.w, self.done = st.sb(name + "_w", [P, ring, D]), st.sem(name + "_done")
            self.loaded = [st.sem(f"{name}_loaded{s}") for s in range(ring)]
        else:
            self.done = proj.done

    def count(self, u, i):
        return u * (self.n + self.before) + (self.before + i + 1)

    def load(self, sp, u):
        fixed = isinstance(u, int)
        for i in range(self.n):
            at = (u * self.n + self.first + i) * P if fixed else sp.snap(u * (self.n * P) + (self.first + i) * P)
            if not fixed or u * self.n + i >= self.ring:
                sp.wait_ge(self.done, u * self.n + (i + 1 - self.ring))
            src = self.wt[at:at + P, :] if fixed else self.wt[bass.ds(at, P), :]
            sp.dma_start(self.w[:, i % self.ring, :], src).then_inc(self.loaded[i % self.ring], 16)

    def multiply(self, pe, u, i, part=0, parts=1):
        s, (layout, _, bias) = i % self.ring, self.kinds[i]
        if part == 0:
            pe.wait_ge(self.kept, u * self.n + (i + 1))
            if self.proj is None:
                pe.wait_ge(self.loaded[s], u * (16 * self.n // self.ring) + 16 * (i // self.ring + 1))
            else:
                pe.wait_ge(self.proj.w_cut, self.count(u, i))
        if self.proj is not None:
            todo = list(self.proj.passes((self.before + i) % self.proj.ring))
            for _, w, y, t, start, stop in todo[part * len(todo) // parts:(part + 1) * len(todo) // parts]:
                ins = pe.matmul(self.out[:, t], w, y, start=start, stop=stop)
            if part == parts - 1:
                ins.then_inc(self.done, 1)
            return
        w, h = self.w[:, s, :], self.core.hT
        if layout == "features":
            todo = [(half * 512, k) for half in range(2) for k in range(KD)]
            for lo, k in todo[part * len(todo) // parts:(part + 1) * len(todo) // parts]:
                ins = pe.matmul(self.out[:, lo:lo + 512], w[:, k * P:k * P + P], h[:, k, lo:lo + 512],
                                start=(k == 0), stop=(k == KD - 1))
        else:
            row = None if bias is None else self.core.brow[0:1, bass.ds(u * (bias[1] * P) + bias[0], P)]
            for c in range(part * NCH // parts, (part + 1) * NCH // parts):
                ins = project_chunk(pe, self.out, w, h, c, self.core.ones, row)
        if part == parts - 1:
            ins.then_inc(self.done, 1)

    def advance(self, pe, u, begin, end):
        for n in range(begin, end):
            self.multiply(pe, u, n // 16, n % 16, 16)

    def keep(self, act, u, i):
        s, (layout, func, bias) = i % self.ring, self.kinds[i]
        act.wait_ge(self.done, self.count(u, i))
        if i >= self.ring:
            act.wait_ge(self.stored[s], u * (16 * self.n // self.ring) + 16 * (i // self.ring))
        kw = {"bias": self.core.col_at(bias[0], u * bias[2] + bias[1])} if layout == "features" and bias is not None else {}
        act.activation(self.kept_sb[:, s, :], self.out, func, **kw).then_inc(self.kept, 1)
        park, first, stride = self.places[i]
        at = u * (stride * P) + first * P
        dst = park[at:at + P, :] if isinstance(u, int) else park[bass.ds(act.snap(at), P), :]
        act.wait_ge(self.kept, u * self.n + (i + 2))
        act.dma_start(dst, self.kept_sb[:, s, :]).then_inc(self.stored[s], 16)

    def begin(self, act):
        act.sem_inc(self.kept, 1)

    def end(self, act, u):
        for s in range(self.ring):
            act.wait_ge(self.stored[s], u * (16 * self.n // self.ring) + 16 * (self.n // self.ring))


def places(dram, n, first=0):
    return [(dram, first + i, n) for i in range(n)]


def load_input(core, x_dram):
    nc = core.nc
    with Stage(nc, "ldx") as st:
        xin = st.sb("xin", [P, 2, D])
        loaded = [st.sem("x_loaded0"), st.sem("x_loaded1")]
        turned, kept = st.sem("turned"), st.sem("kept")
        block = st.block()

        @block.sync
        def _(sp):
            for c in range(NCH):
                if c >= 2:
                    sp.wait_ge(turned, c - 1)
                sp.dma_start(xin[:, c % 2, :], x_dram[c * P:(c + 1) * P, :]).then_inc(loaded[c % 2], 16)

        @block.tensor
        def _(pe):
            for c in range(NCH):
                pe.wait_ge(loaded[c % 2], 16 * (c // 2 + 1))
                if c >= 2:
                    pe.wait_ge(kept, c - 1)
                for k in range(KD):
                    ins = pe.transpose(pair(core, c % 2)[:, k * P:(k + 1) * P],
                                       xin[:, c % 2, k * P:(k + 1) * P], core.ident[:, :])
                ins.then_inc(turned, 1)

        @block.vector
        def _(dve):
            for c in range(NCH):
                dve.wait_ge(turned, c + 1)
                dve.tensor_copy(core.xT[:, :, c * C:(c + 1) * C], chunks(pair(core, c % 2))).then_inc(kept, 1)


def spread_tokens(dve, diag, ident, values):
    return dve.tensor_tensor(diag, per_chunk(ident), values.unsqueeze(2).to_broadcast([P, NCH, C]), ALU.mult)


def rms_norm(core, name, src, gain, dst, eps=NORM_EPS, park=None, halves=None):
    with Stage(core.nc, name) as st:
        sq, acc = st.sb("sq", [P, 2, T]), st.sb("acc", [P, T])
        std, diag = st.sb("std", [P, NCH]), st.sb("diag", [P, NCH, C])
        (squared, added, summed, rooted, inverted, spread_ready, spread_done, normed, parked, rounded, cut) = (
            st.sem(n) for n in ("squared", "added", "summed", "rooted", "inverted", "spread_ready",
                                "spread_done", "normed", "parked", "rounded", "cut"))
        total, rstd = pair(core, 0)[:, 0:NCH], pair(core, 1)
        block = st.block()

        @block.sync
        def _(sp):
            if park is not None:
                for k in range(KD):
                    sp.dma_start(park[k * P:(k + 1) * P, :], src[:, k, :]).then_inc(parked, 16)
                sp.wait_ge(parked, 16 * KD)

        @block.scalar
        def _(act):
            act.activation(acc[:, :], src[:, 0, :], ACT.Square).then_inc(squared, 1)
            for k in range(1, KD):
                if k >= 3:
                    act.wait_ge(added, k - 2)
                act.activation(sq[:, k % 2, :], src[:, k, :], ACT.Square).then_inc(squared, 1)
            act.wait_ge(summed, 1)
            act.activation(std[:, :], total, ACT.Sqrt, bias=core.const(eps)).then_inc(rooted, 1)
            if halves:
                for k in range(KD):
                    act.wait_ge(normed, k + 1)
                    act.activation(halves[0][:, k, :], sq[:, k % 2, :], ACT.Copy).then_inc(rounded, 1)

        @block.tensor
        def _(pe):
            pe.wait_ge(added, KD - 1)
            for c in range(NCH):
                ins = pe.matmul(total[:, c:c + 1], acc[:, c * C:c * C + C], core.mean_d[:, 0:1], start=True, stop=True)
            ins.then_inc(summed, 1)
            pe.wait_ge(spread_ready, 1)
            for half in range(2):
                ins = pe.matmul(rstd[:, half * 512:half * 512 + 512], core.ones[:, :],
                                flat(diag[:, half * NCH // 2:(half + 1) * NCH // 2, :]), start=True, stop=True)
            ins.then_inc(spread_done, 1)

        @block.vector
        def _(dve):
            for k in range(1, KD):
                dve.wait_ge(squared, k + 1)
                if k >= 2:
                    dve.wait_ge(added, k - 1)
                dve.tensor_tensor(acc[:, :], acc[:, :], sq[:, k % 2, :], ALU.add).then_inc(added, 1)
            dve.wait_ge(rooted, 1)
            dve.reciprocal(std[:, :], std[:, :]).then_inc(inverted, 1)
            dve.wait_ge(inverted, 1)
            spread_tokens(dve, diag[:, :, :], core.ident[:, :], std[:, :]).then_inc(spread_ready, 1)
            dve.wait_ge(spread_done, 1)
            for k in range(KD + 1):
                if k < KD:
                    if halves and k >= 2:
                        dve.wait_ge(cut, k - 1)
                    dve.scalar_tensor_tensor(sq[:, k % 2, :] if halves else dst[:, k, :], src[:, k, :], core.col(gain, k),
                                             rstd, ALU.mult, ALU.mult).then_inc(normed, 1)
                if halves and k:
                    dve.wait_ge(rounded, k)
                    dve.tensor_tensor(halves[1][:, k - 1, :], sq[:, (k - 1) % 2, :], halves[0][:, k - 1, :],
                                      ALU.subtract).then_inc(cut, 1)


class SplitProjection:

    def __init__(self, st, y, nk, ring, halves=None):
        self.y, self.nk, self.ring = y, nk, ring
        self.y_hi, self.y_lo = halves or [st.sb(n, [P, nk, T], F32R) for n in ("y_hi", "y_lo")]
        self.w = st.sb("w", [P, ring, nk * P])
        self.w_hi, self.w_lo = (st.sb(n, [P, ring, nk * P], F32R) for n in ("w_hi", "w_lo"))
        self.loaded = [st.sem(f"w_loaded{s}") for s in range(ring)]
        self.w_rounded, self.w_cut, self.y_rounded, self.y_cut, self.done, self.passed = (
            st.sem(n) for n in ("w_rounded", "w_cut", "y_rounded", "y_cut", "projected", "cut_passed"))

    def load(self, sp, wt, first, count):
        for s in range(self.ring):
            sp.dma_start(self.w[:, s, :], wt[(first + s) * P:(first + s + 1) * P, :]).then_inc(self.loaded[s], 16)
        with sp.Fori(1, count // self.ring) as i:
            for s in range(self.ring):
                self.load_next(sp, wt, first, i, s)

    def load_next(self, sp, wt, first, i, s):
        at = sp.snap(i * (self.ring * P) + (first + s) * P)
        sp.wait_ge(self.w_cut, i * self.ring + (s + 1 - self.ring))
        sp.dma_start(self.w[:, s, :], wt[bass.ds(at, P), :]).then_inc(self.loaded[s], 16)

    def cut_weights(self, pool, count):
        def cut(i, s):
            w, hi, lo = self.w[:, s, :], self.w_hi[:, s, :], self.w_lo[:, s, :]
            wait_alone(pool, self.loaded[s], 16 * i + 16, self.passed)
            pool.tensor_copy(hi, w).then_inc(self.w_rounded, 1)
            pool.wait_ge(self.w_rounded, i * self.ring + (s + 1))
            pool.tensor_tensor(lo, w, hi, ALU.subtract).then_inc(self.w_cut, 1)
        for s in range(1, self.ring):
            pool.wait_ge(self.w_cut, s)
            cut(0, s)
        with pool.Fori(1, count // self.ring) as i:
            for s in range(self.ring):
                pool.wait_ge(self.done, i * self.ring + (s + 1 - self.ring))
                cut(i, s)

    def round_first(self, act):
        act.wait_ge(self.loaded[0], 16)
        act.activation(self.w_hi[:, 0, :], self.w[:, 0, :], ACT.Copy).then_inc(self.w_rounded, 1)

    def cut_first(self, dve):
        dve.wait_ge(self.w_rounded, 1)
        dve.tensor_tensor(self.w_lo[:, 0, :], self.w[:, 0, :], self.w_hi[:, 0, :], ALU.subtract).then_inc(self.w_cut, 1)

    def round_y(self, act):
        for k in range(self.nk):
            act.activation(self.y_hi[:, k, :], self.y[:, k, :], ACT.Copy).then_inc(self.y_rounded, 1)

    def cut_y(self, dve):
        for k in range(self.nk):
            dve.wait_ge(self.y_rounded, k + 1)
            dve.tensor_tensor(self.y_lo[:, k, :], self.y[:, k, :], self.y_hi[:, k, :], ALU.subtract).then_inc(self.y_cut, 1)

    def passes(self, s):
        for k in range(self.nk):
            for w, parts in ((self.w_hi, (self.y_hi, self.y_lo)), (self.w_lo, (self.y_hi,))):
                for half in range(2):
                    for y in parts:
                        t = slice(half * 512, half * 512 + 512)
                        yield k, w[:, s, k * P:k * P + P], y[:, k, t], t, \
                            k == 0 and w is self.w_hi and y is self.y_hi, k == self.nk - 1 and w is self.w_lo

    def multiply(self, pe, out, i, s):
        pe.wait_ge(self.w_cut, i * self.ring + (s + 1))
        seen = -1
        for k, w, y, t, start, stop in self.passes(s):
            if self.y is not None and k > seen:
                pe.wait_ge(self.y_cut, k + 1)
            seen = k
            ins = pe.matmul(out[:, t], w, y, start=start, stop=stop)
        ins.then_inc(self.done, 1)
        return ins


class OutProjection:

    def __init__(self, core, st, y, nk, wt, dst, pairs=(0, 1), halves=None):
        self.wt, self.dst, self.out = wt, dst, [pair(core, n) for n in pairs]
        self.proj, self.added = SplitProjection(st, y, nk, 2, halves), st.sem("added")

    def load(self, sp):
        self.proj.load(sp, self.wt, 0, KD)

    def cut_weights(self, pool):
        self.proj.cut_weights(pool, KD)

    def round(self, act):
        self.proj.round_first(act)
        self.proj.round_y(act)

    def cut(self, dve):
        dve.sem_inc(self.added, 2)
        self.proj.cut_first(dve)
        self.proj.cut_y(dve)

    def multiply(self, pe):
        with pe.Fori(0, KD // 2) as i:
            for s in range(2):
                pe.wait_ge(self.added, 2 * i + (s + 1))
                self.proj.multiply(pe, self.out[s], i, s)

    def add(self, dve):
        with dve.Fori(0, KD // 2) as i:
            for s in range(2):
                dve.wait_ge(self.proj.done, 2 * i + (s + 1))
                o = flat(self.dst[:, bass.ds(2 * i + s, 1), :])
                dve.tensor_tensor(o, self.out[s], o, ALU.add).then_inc(self.added, 1)


def out_projection(core, name, y, nk, wt, dst, halves=None):
    with Stage(core.nc, name) as st:
        out = OutProjection(core, st, y, nk, wt, dst, halves=halves)
        block = st.block()

        @block.sync
        def _(sp):
            out.load(sp)

        @block.gpsimd
        def _(pool):
            out.cut_weights(pool)

        @block.tensor
        def _(pe):
            out.multiply(pe)

        @block.scalar
        def _(act):
            out.round(act)

        @block.vector
        def _(dve):
            out.cut(dve)
            out.add(dve)


def store_output(core, src, out_dram):
    with Stage(core.nc, "out") as st:
        rows = st.sb("rows", [P, 2, D])
        stored = [st.sem("stored0"), st.sem("stored1")]
        turned, copied = st.sem("turned"), st.sem("copied")
        block = st.block()

        @block.tensor
        def _(pe):
            for c in range(NCH):
                if c >= 2:
                    pe.wait_ge(copied, c - 1)
                for k in range(KD):
                    ins = pe.transpose(pair(core, c % 2)[:, k * P:(k + 1) * P],
                                       src[:, k, c * C:(c + 1) * C], core.ident[:, :])
                ins.then_inc(turned, 1)

        @block.vector
        def _(dve):
            for c in range(NCH):
                dve.wait_ge(turned, c + 1)
                if c >= 2:
                    dve.wait_ge(stored[c % 2], 16 * (c // 2))
                dve.tensor_copy(rows[:, c % 2, :], pair(core, c % 2)).then_inc(copied, 1)

        @block.sync
        def _(sp):
            for c in range(NCH):
                sp.wait_ge(copied, c + 1)
                sp.dma_start(out_dram[c * P:(c + 1) * P, :], rows[:, c % 2, :]).then_inc(stored[c % 2], 16)
            for s in range(2):
                sp.wait_ge(stored[s], 16 * (NCH // 2))


GLA_A, ML_IF, GLA_FILL, ML_FILL = 16, 17, 18, 30
LEVELS = 7


def level_views(ap, lvl):
    v = ap.rearrange("p (n two m) -> p n two m", two=2, m=1 << lvl)
    return v[:, :, 0, :], v[:, :, 1, :]


def hg_lower_bound(core):
    with Stage(core.nc, "lb") as st:
        e, one = st.sb("e", [P, 4]), st.sb("one", [P, 4])
        dve_step, exped, shifted = st.sem("dve_step"), st.sem("exped"), st.sem("shifted")
        block = st.block()
        logits = core.cols[:, core.index["hg_lb"]:core.index["hg_lb"] + 4]
        lb = core.cols[:, core.index["lb"]:core.index["lb"] + 4]
        om = core.cols[:, core.index["one_minus_lb"]:core.index["one_minus_lb"] + 4]

        @block.vector
        def _(dve):
            step = Chain(dve, dve_step)
            dve.tensor_tensor(e[:, :], logits, logits, ALU.subtract).then_inc(shifted, 1)
            dve.wait_ge(exped, 1)
            step(dve.reciprocal(one[:, :], e[:, :]))
            step(dve.tensor_tensor(e[:, :], e[:, :], one[:, :], ALU.mult))
            step(dve.tensor_tensor(lb, e[:, :], e[:, :], ALU.subtract))
            step(dve.tensor_scalar(om, lb, -1.0, 1.0, ALU.mult, ALU.add))

        @block.scalar
        def _(act):
            act.wait_ge(shifted, 1)
            act.activation(e[:, :], e[:, :], ACT.Exp).then_inc(exped, 1)


def vector_decay_branch(core, name, nsub, units, wt, fill_first, fill_places, fill_kinds, parts, wcol, y, source=None, gl=None):
    hg = nsub == 1
    order = ["f", "q", "v0", "z0"] if hg else []
    nt = len(order)
    NE = LEVELS + 1
    places_of_parts = ["start"] + list(range(-1, LEVELS)) + ["keys", "update", "out"] + [f"mean{n}" for n in range(nsub)]
    ends = np.cumsum(parts).tolist()
    span = dict(zip(places_of_parts, zip([0] + ends, ends)))
    with Stage(core.nc, name) as st:
        if hg:
            w = st.sb("w", [P, nt, D])
            loaded = [st.sem(f"w_loaded{t}") for t in range(nt)]
        else:
            q_loaded, k_loaded, v_loaded, z_loaded = (st.sem(n + "_loaded") for n in "qkvz")
        fill = Filler(core, st, "fill", 3, wt, fill_first, fill_places, fill_kinds, ring=3 if hg else 2)
        assert ends[-1] == 16 * fill.n
        q, k, b = st.sb("q", [P, T]), st.sb("k", [P, T]), st.sb("b", [P, T])
        v = st.sb("v", [P, NCH, nsub, P])
        ex = st.sb("ex", [P, 2, T])
        qs, ks = st.sb("qs", [P, 2, T]), st.sb("ks", [P, 2, T])
        att = st.sb("att", [P, nsub, T])
        state = st.sb("state", [P, NCH, P])
        ktok, sq = qs[:, 0, :], qs[:, 1, :]
        S = {n: st.sem(n) for n in (
            "proj_done", "evacuated", "unit_free", "qk_ready", "gate_ready", "log_ready", "expo_ready", "expd",
            "factors", "level_done", "att_kept", "keys_turned", "keys_kept", "update_done", "state_ready",
            "out_done", "squared", "mean_done", "rooted", "dve_step", "passed")}
        A, B = [pair(core, 0), pair(core, 1)], pair(core, 2)
        into = (A[1], B)

        def rows(sub):
            return slice(sub * 64, sub * 64 + 64) if nsub == 2 else slice(0, P)

        block = st.block()

        @block.sync
        def _(sp):
            if hg:
                for n in range(nt):
                    sp.dma_start(w[:, n, :], wt[n * P:(n + 1) * P, :]).then_inc(loaded[n], 16)
                fill.load(sp, 0)
                with sp.Fori(1, units) as u:
                    for n in range(nt):
                        at = sp.snap(u * (nt * P) + n * P)
                        sp.wait_ge(S["proj_done"], u * nt + (n + 1 - nt))
                        sp.dma_start(w[:, n, :], wt[bass.ds(at, P), :]).then_inc(loaded[n], 16)
                    fill.load(sp, u)
            else:
                def inputs(q_at, k_at, v_at):
                    sp.dma_start(q[:, :], q_at).then_inc(q_loaded, 16)
                    sp.dma_start(k[:, :], k_at).then_inc(k_loaded, 16)
                    for sub in range(2):
                        sp.dma_start(v[:, :, sub, :], v_at[sub]).then_inc(v_loaded, 16)
                tiles = source.rearrange("(n p) t -> n p t", p=P)
                inputs(tiles[0], tiles[1], [chunks(tiles[4 + sub]) for sub in range(2)])
                fill.load(sp, 0)
                for n in range(2 * units):
                    sp.dma_start(y[:, n, :], tiles[8 + n]).then_inc(z_loaded, 16)
                with sp.Fori(1, units) as u:
                    at = [sp.snap(u * (2 * P) + n * P) for n in (0, 1, 4, 5)]
                    sp.wait_ge(S["unit_free"], u + 1)
                    q_at, k_at, *v_at = [source[bass.ds(a, P), :] for a in at]
                    inputs(q_at, k_at, [chunks(a) for a in v_at])
                    fill.load(sp, u)

        @block.tensor
        def _(pe):
            with pe.Fori(0, units) as u:
                pe.wait_ge(S["unit_free"], u + 1)
                for t, what in enumerate(order):
                    pe.wait_ge(loaded[t], 16 * u + 16)
                    if t >= 2:
                        pe.wait_ge(S["evacuated"], u * nt + (t - 1))
                    if what[0] == "v":
                        bias = core.brow[0:1, bass.ds(u * P, P)]
                        ins = project_tokens(pe, into[t % 2], w[:, t, :], core.hT, core.ones, bias)
                    else:
                        ins = project_features(pe, into[t % 2], w[:, t, :], core.hT)
                    ins.then_inc(S["proj_done"], 1)
                fill.advance(pe, u, *span["start"])
                pe.wait_ge(S["qk_ready"], u + 1)
                for l in range(-1, LEVELS):
                    if l >= 0:
                        pe.wait_ge(S["factors"], u * NE + (l + 1))
                        if not hg:
                            pe.wait_ge(S["att_kept"], u * (LEVELS + 1) + (l + 1))
                        elif l >= 1:
                            pe.wait_ge(S["att_kept"], u * (LEVELS + 1) + l)
                        else:
                            pe.wait_ge(S["evacuated"], u * nt + nt)
                    lhs, rhs = (k[:, :], q[:, :]) if l < 0 else (ks[:, l % 2, :], qs[:, l % 2, :])
                    for sub in range(nsub):
                        o = A[(l + 1) % 2] if hg else A[sub]
                        for c in range(NCH):
                            cs = slice(c * C, c * C + C)
                            ins = pe.matmul(o[:, cs], lhs[rows(sub), cs], rhs[rows(sub), cs], start=True, stop=True)
                    ins.then_inc(S["level_done"], 1)
                    fill.advance(pe, u, *span[l])
                pe.wait_ge(S["factors"], u * NE + NE)
                for c in range(NCH):
                    ins = pe.transpose(B[:, c * C:c * C + C], k[:, c * C:c * C + C], core.ident[:, :])
                ins.then_inc(S["keys_turned"], 1)
                fill.advance(pe, u, *span["keys"])
                pe.wait_ge(S["keys_kept"], u + 1)
                if not hg:
                    pe.wait_ge(v_loaded, u * 32 + 32)
                for c in range(NCH - 1):
                    for sub in range(nsub):
                        r = rows(sub)
                        ins = pe.matmul(B[r, c * P:c * P + P], ktok[:, c * C + r.start:c * C + r.stop], v[:, c, sub, :],
                                        start=True, stop=True)
                ins.then_inc(S["update_done"], 1)
                fill.advance(pe, u, *span["update"])
                pe.wait_ge(S["state_ready"], u + 1)
                pe.wait_ge(S["att_kept"], u * (LEVELS + 1) + (LEVELS + 1))
                for sub in range(nsub):
                    for c in range(NCH):
                        cs = slice(c * C, c * C + C)
                        ins = pe.matmul(A[sub][:, cs], v[:, c, sub, :], att[:, sub, cs], start=True, stop=(c == 0))
                        if c:
                            ins = pe.matmul(A[sub][:, cs], state[rows(sub), c, :],
                                            q[rows(sub), cs], start=False, stop=True)
                    ins.then_inc(S["out_done"], 1)
                fill.advance(pe, u, *span["out"])
                for sub in range(nsub):
                    pe.wait_ge(S["squared"], u * nsub + (sub + 1))
                    if sub:
                        pe.wait_ge(S["rooted"], u * nsub + sub)
                    for half in range(2):
                        ins = pe.matmul(B[:, half * 512:half * 512 + 512], core.mean_p[:, :],
                                        sq[:, half * 512:half * 512 + 512], start=True, stop=True)
                    ins.then_inc(S["mean_done"], 1)
                    fill.advance(pe, u, *span[f"mean{sub}"])

        @block.scalar
        def _(act):
            def keep_tiles(place):
                for n in range(span[place][0] // 16, span[place][1] // 16):
                    fill.keep(act, u, n)

            fill.begin(act)
            with act.Fori(0, units) as u:
                for t, what in enumerate(order):
                    act.wait_ge(S["proj_done"], u * nt + (t + 1))
                    src = into[t % 2]
                    if what == "f":
                        ins = act.activation(b[:, :], src, ACT.Sigmoid, bias=core.col_at("hg_f", u))
                    elif what == "q":
                        ins = act.activation(q[:, :], src, ACT.Silu, bias=core.col_at("hg_q", u))
                    elif what[0] == "v":
                        ins = act.activation(v[:, :, 0, :], chunks(src), ACT.Copy)
                    else:
                        ins = act.activation(flat(y[:, bass.ds(u, 1), :]), src, ACT.Silu, bias=core.col_at("hg_z", u))
                    ins.then_inc(S["evacuated"], 1)
                if hg:
                    act.wait_ge(S["gate_ready"], u + 1)
                    act.activation(b[:, :], b[:, :], ACT.Ln).then_inc(S["log_ready"], 1)
                for e in range(LEVELS):
                    act.wait_ge(S["expo_ready"], u * NE + (e + 1))
                    act.activation(ex[:, e % 2, :], ex[:, e % 2, :], ACT.Exp).then_inc(S["expd"], 1)
                    keep_tiles(e - 1)
                act.wait_ge(S["expo_ready"], u * NE + NE)
                act.activation(ex[:, 1, :], b[:, :], ACT.Exp)
                act.activation(ex[:, 0, :], ex[:, 0, :], ACT.Exp).then_inc(S["expd"], 1)
                keep_tiles(LEVELS - 1)
                act.wait_ge(S["keys_turned"], u + 1)
                act.activation(ktok, B, ACT.Copy).then_inc(S["keys_kept"], 1)
                keep_tiles("keys")
                for sub in range(nsub):
                    act.wait_ge(S["out_done"], u * nsub + (sub + 1))
                    if sub:
                        act.wait_ge(S["mean_done"], u * nsub + sub)
                    act.activation(sq, A[sub], ACT.Square).then_inc(S["squared"], 1)
                    if sub:
                        act.activation(ks[:, 0, :], B, ACT.Sqrt, bias=core.const(NORM_EPS)).then_inc(S["rooted"], 1)
                    else:
                        keep_tiles("out")
                act.wait_ge(S["mean_done"], u * nsub + nsub)
                act.activation(ks[:, nsub - 1, :], B, ACT.Sqrt, bias=core.const(NORM_EPS)).then_inc(S["rooted"], 1)
                for sub in range(nsub):
                    keep_tiles(f"mean{sub}")
                fill.end(act, u)

        @block.vector
        def _(dve):
            per = (2 if hg else 1) + (NCH - 3) + 1 + 3 * nsub - 1
            dve.memset(qs[:, :, :], 0.0)
            dve.memset(ks[:, :, :], 0.0).then_inc(S["unit_free"], 1)

            def exponents(l):
                be, bo = level_views(b[:, :], l)
                ee, eo = level_views(ex[:, l % 2, :], l)
                m = 1 << l
                ref = be[:, :, m - 1:m].to_broadcast([P, T // (2 * m), m])
                dve.tensor_tensor(ee, ref, be, ALU.subtract)
                dve.tensor_tensor(eo, bo, ref, ALU.subtract).then_inc(S["expo_ready"], 1)

            def keep(n, u):
                wait_alone(dve, S["level_done"], u * (LEVELS + 1) + (n + 1), S["passed"])
                for sub in range(nsub):
                    src = chunks(A[n % 2] if hg else A[sub])
                    dst = chunks(att[:, sub, :])
                    if n == 0:
                        ins = dve.tensor_tensor(dst, src, per_chunk(core.ident[:, :]), ALU.mult)
                    else:
                        ins = dve.copy_predicated(dst, bits(core.level_mask[:, n - 1, :]), src)
                ins.then_inc(S["att_kept"], 1)
                dve.wait_ge(S["att_kept"], u * (LEVELS + 1) + (n + 1))

            with dve.Fori(0, units) as u:
                step = Chain(dve, S["dve_step"], u * per)
                if hg:
                    dve.wait_ge(S["evacuated"], u * nt + 2)
                    step(dve.tensor_scalar(b[:, :], b[:, :], core.col_at("one_minus_lb", u), core.col_at("lb", u),
                                           ALU.mult, ALU.add))
                    dve.tensor_scalar(k[:, :], b[:, :], -1.0, 1.0, ALU.mult, ALU.add).then_inc(S["gate_ready"], 1)
                    dve.wait_ge(S["gate_ready"], u + 1)
                    dve.sem_inc(S["qk_ready"], 1)
                    dve.wait_ge(S["log_ready"], u + 1)
                    decay = b[:, :]
                else:
                    dve.wait_ge(k_loaded, u * 16 + 16)
                    dve.wait_ge(q_loaded, u * 16 + 16)
                    dve.tensor_scalar(q[:, :], q[:, :], 64 ** -0.5, None, ALU.mult).then_inc(S["qk_ready"], 1)
                    dve.wait_ge(S["qk_ready"], u + 1)
                    decay = flat(gl[:, bass.ds(u, 1), :])
                for c in range(NCH):
                    cs = slice(c * C, c * C + C)
                    ins = dve.tensor_tensor_scan(b[:, cs], decay[:, cs], decay[:, cs], 0.0, ALU.add, ALU.bypass)
                step(ins)
                exponents(0)
                for l in range(LEVELS):
                    if l + 1 < LEVELS:
                        exponents(l + 1)
                    dve.wait_ge(S["expd"], u * NE + (l + 1))
                    ee, eo = level_views(ex[:, l % 2, :], l)
                    dve.tensor_tensor(level_views(qs[:, l % 2, :], l)[1], level_views(q[:, :], l)[1], eo, ALU.mult)
                    dve.tensor_tensor(level_views(ks[:, l % 2, :], l)[0], level_views(k[:, :], l)[0], ee, ALU.mult) \
                        .then_inc(S["factors"], 1)
                    keep(l, u)
                keep(LEVELS, u)
                last = chunks(b[:, :])[:, :, C - 1:C].to_broadcast([P, NCH, C])
                dve.tensor_tensor(chunks(ex[:, 0, :]), last, chunks(b[:, :]), ALU.subtract).then_inc(S["expo_ready"], 1)
                dve.wait_ge(S["expd"], u * NE + NE)
                dve.tensor_tensor(q[:, :], q[:, :], ex[:, 1, :], ALU.mult)
                dve.tensor_tensor(k[:, :], k[:, :], ex[:, 0, :], ALU.mult).then_inc(S["factors"], 1)
                dve.wait_ge(S["update_done"], u + 1)
                step(dve.tensor_copy(state[:, 1, :], B[:, 0:P]))
                for c in range(1, NCH - 1):
                    ins = dve.scalar_tensor_tensor(state[:, c + 1, :], state[:, c, :],
                                                   ex[:, 1, c * C + C - 1:c * C + C],
                                                   B[:, c * P:(c + 1) * P], ALU.mult, ALU.add)
                    if c + 1 < NCH - 1:
                        step(ins)
                ins.then_inc(S["state_ready"], 1)
                if not hg:
                    dve.wait_ge(z_loaded, 16 * 2 * units)
                for sub in range(nsub):
                    dve.wait_ge(S["rooted"], u * nsub + (sub + 1))
                    yo = flat(y[:, bass.ds(u * nsub + sub, 1), :])
                    step(dve.reciprocal(ks[:, sub, :], ks[:, sub, :]))
                    step(dve.scalar_tensor_tensor(ks[:, sub, :], A[sub], core.col_at(wcol, u * nsub + sub),
                                                  ks[:, sub, :], ALU.mult, ALU.mult))
                    ins = dve.tensor_tensor(yo, yo, ks[:, sub, :], ALU.mult)
                    if sub + 1 < nsub:
                        step(ins)
                ins.then_inc(S["unit_free"], 1)
                step.ends(per)


def gates_and_projection(core, wt, w_a2, gl, rows_dram, cols, y, wo):
    H = 4
    with Stage(core.nc, "gates") as st:
        out = OutProjection(core, st, y, 4, wo, core.xT, pairs=(2, 3))
        w_if, w_a = st.sb("w_if", [P, D]), st.sb("w_a", [P, D])
        wa2, aT, gmag = st.sb("wa2", [16, 2 * P]), st.sb("aT", [16, T]), st.sb("gmag", [P, 2, T])
        ip, lf, mag, m, lam, b, ke, eb, em = (st.sb(n, [H, T]) for n in (
            "ip", "lf", "mag", "m", "lam", "b", "ke", "eb", "em"))
        (if_loaded, a_loaded, a2_loaded, if_done, a_done, a_kept, logit_done, mag_ready, softened, gmag_ready, gsoftened,
         b_ready, exped, turned, stored, copied, dve_step, act_step, gl_step) = (st.sem(n) for n in (
             "if_loaded", "a_loaded", "a2_loaded", "if_done", "a_done", "a_kept", "logit_done", "mag_ready", "softened",
             "gmag_ready", "gsoftened", "b_ready", "exped", "turned", "stored", "copied", "dve_step", "act_step", "gl_step"))
        block = st.block()

        @block.sync
        def _(sp):
            sp.dma_start(w_if[:, :], wt[ML_IF * P:(ML_IF + 1) * P, :]).then_inc(if_loaded, 16)
            sp.dma_start(w_a[:, :], wt[GLA_A * P:(GLA_A + 1) * P, :]).then_inc(a_loaded, 16)
            sp.dma_start(wa2[:, :], w_a2).then_inc(a2_loaded, 16)
            out.load(sp)
            sp.wait_ge(exped, 1)
            for n, r in enumerate((b, eb, em)):
                sp.dma_start(rows_dram[n * H:(n + 1) * H, :], r[:, :]).then_inc(stored, 16)
            sp.wait_ge(stored, 48)

        @block.gpsimd
        def _(pool):
            out.cut_weights(pool)

        @block.tensor
        def _(pe):
            pe.wait_ge(if_loaded, 16)
            project_features(pe, pair(core, 0), w_if, core.hT, m=H, c0=0)
            project_features(pe, pair(core, 1), w_if, core.hT, m=H, c0=H).then_inc(if_done, 1)
            pe.wait_ge(a_loaded, 16)
            project_features(pe, pair(core, 2), w_a, core.hT, m=16).then_inc(a_done, 1)
            pe.wait_ge(a2_loaded, 16)
            pe.wait_ge(a_kept, 1)
            pe.wait_ge(mag_ready, 1)
            for n in range(2):
                for half in range(2):
                    ins = pe.matmul(pair(core, n)[:, half * 512:half * 512 + 512],
                                    wa2[:, n * P:n * P + P], aT[:, half * 512:half * 512 + 512],
                                    start=True, stop=True)
                ins.then_inc(logit_done, 1)
            out.multiply(pe)
            pe.wait_ge(exped, 1)
            pe.wait_ge(gmag_ready, 2)
            for n, r in enumerate((b, ip, ke)):
                for c in range(NCH):
                    ins = pe.matmul(pair(core, 0)[:, (n * NCH + c) * H:(n * NCH + c + 1) * H],
                                    r[:, c * C:c * C + C], core.ident[0:H, 0:H], start=True, stop=True)
            ins.then_inc(turned, 1)

        @block.scalar
        def _(act):
            out.round(act)
            step = Chain(act, act_step)
            act.wait_ge(mag_ready, 1)
            step(act.activation(mag[:, :], mag[:, :], ACT.Exp, scale=-1.0))
            act.activation(mag[:, :], mag[:, :], ACT.Ln, bias=1.0).then_inc(softened, 1)
            act.wait_ge(a_done, 1)
            act.activation(aT[:, :], pair(core, 2)[0:16, :], ACT.Identity, bias=core.col("gla_a_b", 0)[0:16, :]) \
                .then_inc(a_kept, 1)
            act.wait_ge(b_ready, 1)
            act.activation(eb[:, :], b[:, :], ACT.Exp)
            act.activation(em[:, :], m[:, :], ACT.Exp, scale=-1.0)
            act.activation(ke[:, :], ke[:, :], ACT.Exp).then_inc(exped, 1)
            for n in range(2):
                act.wait_ge(gmag_ready, n + 1)
                step(act.activation(gmag[:, n, :], gmag[:, n, :], ACT.Exp, scale=-1.0))
                act.activation(gmag[:, n, :], gmag[:, n, :], ACT.Ln, bias=1.0).then_inc(gsoftened, 1)

        @block.vector
        def _(dve):
            out.cut(dve)
            step = Chain(dve, dve_step)
            dve.wait_ge(if_done, 1)
            dve.tensor_scalar(ip[:, :], pair(core, 0)[0:H, :], core.col("ml_i_b", 0)[0:H, :], None, ALU.add)
            bf = core.col("ml_f_b", 0)[0:H, :]
            dve.tensor_scalar(lf[:, :], pair(core, 1)[0:H, :], bf, 0.0, ALU.add, ALU.min)
            step(dve.tensor_scalar(mag[:, :], pair(core, 1)[0:H, :], bf, None, ALU.add))
            dve.scalar_tensor_tensor(mag[:, :], mag[:, :], -1.0, mag[:, :], ALU.mult, ALU.max).then_inc(mag_ready, 1)
            dve.wait_ge(softened, 1)
            step(dve.tensor_tensor(lf[:, :], lf[:, :], mag[:, :], ALU.subtract))
            step(dve.tensor_tensor_scan(m[:, :], lf[:, :], ip[:, :], 0.0, ALU.add, ALU.max))
            step(dve.tensor_tensor(lam[:, :], lf[:, :], m[:, :], ALU.subtract))
            dve.tensor_tensor(lam[:, 1:T], lam[:, 1:T], m[:, 0:T - 1], ALU.add)
            step(dve.tensor_tensor(ip[:, :], ip[:, :], m[:, :], ALU.subtract))
            for c in range(NCH):
                cs = slice(c * C, c * C + C)
                ins = dve.tensor_tensor_scan(b[:, cs], lam[:, cs], lam[:, cs], 0.0, ALU.add, ALU.bypass)
            step(ins)
            last = chunks(b[:, :])[:, :, C - 1:C].to_broadcast([H, NCH, C])
            step(dve.tensor_tensor(chunks(ke[:, :]), last, chunks(b[:, :]), ALU.subtract))
            dve.tensor_tensor(ke[:, :], ke[:, :], ip[:, :], ALU.add).then_inc(b_ready, 1)
            step = Chain(dve, gl_step)
            for n in range(2):
                dve.wait_ge(logit_done, n + 1)
                bias = core.col("gla_b_a2", n)
                dve.tensor_scalar(gl[:, n, :], pair(core, n), bias, 0.0, ALU.add, ALU.min)
                step(dve.tensor_scalar(gmag[:, n, :], pair(core, n), bias, None, ALU.add))
                dve.scalar_tensor_tensor(gmag[:, n, :], gmag[:, n, :], -1.0, gmag[:, n, :], ALU.mult, ALU.max) \
                    .then_inc(gmag_ready, 1)
            for n in range(2):
                dve.wait_ge(gsoftened, n + 1)
                step(dve.tensor_tensor(gl[:, n, :], gl[:, n, :], gmag[:, n, :], ALU.subtract))
                step(dve.tensor_scalar(gl[:, n, :], gl[:, n, :], 1.0 / 16.0, None, ALU.mult))
            out.add(dve)
            dve.wait_ge(turned, 1)
            dve.tensor_copy(cols[:, :], pair(core, 0)[:, 0:3 * NCH * H]).then_inc(copied, 1)


def mlstm_branch(core, source, rows_dram, cols, y):
    order = ["q", "k", "v0", "v1", "o0", "o1", "z0", "z1"]
    nt, units, nsub, H = len(order), 2, 2, 4
    colv = cols[:, :].rearrange("p (n c h) -> p n c h", n=3, c=NCH)
    with Stage(core.nc, "ml") as st:
        qk_loaded, v_loaded, oz_loaded = (st.sem(n + "_loaded") for n in ("qk", "v", "oz"))
        rows_loaded = st.sem("rows_loaded")
        pre = st.sb("pre", [P, 2, 3 + T])
        q, k = st.sb("q", [P, T]), st.sb("k", [P, T])
        v = st.sb("v", [P, NCH, nsub, P])
        og, ktok, sq = core.hT[:, 0:4, :], core.hT[:, 4, :], core.hT[:, 5:7, :]
        brep, em = st.sb("brep", [P, nsub, T]), st.sb("em", [P, nsub, T])
        qdec = st.sb("qdec", [P, T])
        att = st.sb("att", [P, nsub, T])
        state = st.sb("state", [P, NCH, nsub * P])
        nstate, nrep = st.sb("nstate", [P, NCH]), st.sb("nrep", [P, NCH, P])
        S = {n: st.sem(n) for n in (
            "unit_free", "conv_done", "silu_done", "qk_ready", "expo_ready", "expd",
            "prod_done", "att_ready", "keys_turned", "keys_kept", "update_done", "state_ready", "out_done",
            "h_ready", "squared", "mean_done", "rooted", "dve_step")}
        A, B = [pair(core, 0), pair(core, 1)], [pair(core, 2), pair(core, 3)]
        Bflat = core.ps[:, 4 * 512:8 * 512]
        N0 = (NCH - 1) * nsub * P

        def rows(sub):
            return slice(sub * 64, sub * 64 + 64)

        block = st.block()

        @block.sync
        def _(sp):
            def tile(u, n, head):
                at = n * P if head else sp.snap(u * (nt * P) + n * P)
                return source[at:at + P, :] if head else source[bass.ds(at, P), :]

            def unit(u, head):
                qk, vs = [tile(u, n, head) for n in range(2)], [chunks(tile(u, 2 + n, head)) for n in range(nsub)]
                if not head:
                    sp.wait_ge(S["conv_done"], u * 2)
                for n in range(2):
                    sp.dma_start(pre[:, n, 3:], qk[n]).then_inc(qk_loaded, 16)
                if not head:
                    sp.wait_ge(S["unit_free"], u + 1)
                for sub in range(nsub):
                    sp.dma_start(v[:, :, sub, :], vs[sub]).then_inc(v_loaded, 16)
                for sub in range(nsub):
                    def row(n):
                        h = n * H + sub
                        r = rows_dram[bass.ds(u * nsub + h, 1), :] if not head else rows_dram[h:h + 1, :]
                        return r
                    sp.dma_start(brep[:, sub, :], row(0).to_broadcast([P, T])).then_inc(rows_loaded, 16)
                    sp.dma_start(qdec[rows(sub), :], row(1).to_broadcast([64, T])).then_inc(rows_loaded, 16)
                    sp.dma_start(em[:, sub, :], row(2).to_broadcast([P, T])).then_inc(rows_loaded, 16)
            unit(0, True)
            for u in range(units):
                for n in range(nsub):
                    for dst, first in ((og, 4), (y, 6)):
                        at = (u * nt + first + n) * P
                        sp.dma_start(dst[:, u * nsub + n, :], source[at:at + P, :]).then_inc(oz_loaded, 16)
            with sp.Fori(1, units) as u:
                unit(u, False)

        @block.tensor
        def _(pe):
            with pe.Fori(0, units) as u:
                pe.wait_ge(S["unit_free"], u + 1)
                pe.wait_ge(S["qk_ready"], u + 1)
                for sub in range(nsub):
                    for c in range(NCH):
                        cs = slice(c * C, c * C + C)
                        ins = pe.matmul(A[sub][:, cs], k[rows(sub), cs], q[rows(sub), cs], start=True, stop=True)
                    ins.then_inc(S["prod_done"], 1)
                for c in range(NCH):
                    ins = pe.transpose(B[0][:, c * C:c * C + C], k[:, c * C:c * C + C], core.ident[:, :])
                ins.then_inc(S["keys_turned"], 1)
                pe.wait_ge(S["keys_kept"], u + 1)
                pe.wait_ge(v_loaded, u * 32 + 32)
                for c in range(NCH - 1):
                    pe.matmul(Bflat[:, c * nsub * P:(c + 1) * nsub * P], ktok[:, c * C:c * C + C],
                              v[:, c, :, :].rearrange("p n d -> p (n d)"), start=True, stop=True)
                    ins = pe.matmul(Bflat[:, N0 + c:N0 + c + 1], ktok[:, c * C:c * C + C], core.ones[:, 0:1],
                                    start=True, stop=True)
                ins.then_inc(S["update_done"], 1)
                pe.wait_ge(S["state_ready"], u + 1)
                pe.wait_ge(S["att_ready"], u * nsub + nsub)
                for sub in range(nsub):
                    for c in range(NCH):
                        cs = slice(c * C, c * C + C)
                        for o, lv, ls in ((A[sub], v[:, c, sub, :], state[rows(sub), c, sub * P:sub * P + P]),
                                          (B[sub], core.ones[:, :], nrep[rows(sub), c, :])):
                            ins = pe.matmul(o[:, cs], lv, att[:, sub, cs], start=True, stop=(c == 0))
                            if c:
                                ins = pe.matmul(o[:, cs], ls, q[rows(sub), cs], start=False, stop=True)
                    ins.then_inc(S["out_done"], 1)
                for sub in range(nsub):
                    pe.wait_ge(S["squared"], u * nsub + (sub + 1))
                    for half in range(2):
                        ins = pe.matmul(B[sub][:, half * 512:half * 512 + 512], core.mean_p[:, :],
                                        sq[:, sub, half * 512:half * 512 + 512], start=True, stop=True)
                    ins.then_inc(S["mean_done"], 1)

        @block.scalar
        def _(act):
            with act.Fori(0, units) as u:
                for n, dst in enumerate((q, k)):
                    act.wait_ge(S["conv_done"], u * 2 + (n + 1))
                    act.activation(dst[:, :], dst[:, :], ACT.Silu, bias=core.col_at("ml_cb", u + 2 * n)) \
                        .then_inc(S["silu_done"], 1)
                for sub in range(nsub):
                    act.wait_ge(S["expo_ready"], u * nsub + (sub + 1))
                    act.activation(att[:, sub, :], att[:, sub, :], ACT.Exp).then_inc(S["expd"], 1)
                for sub in range(nsub):
                    act.wait_ge(S["h_ready"], u * nsub + (sub + 1))
                    act.activation(sq[:, sub, :], flat(og[:, bass.ds(u * nsub + sub, 1), :]), ACT.Square).then_inc(S["squared"], 1)
                for sub in range(nsub):
                    act.wait_ge(S["mean_done"], u * nsub + (sub + 1))
                    act.activation(em[:, sub, :], B[sub], ACT.Sqrt, bias=core.const(NORM_EPS)).then_inc(S["rooted"], 1)

        @block.vector
        def _(dve):
            per = 2 * 3 + 3 * nsub + 1 + (NCH - 1) + 5 * nsub + (3 * nsub - 1)
            dve.memset(pre[:, :, 0:3], 0.0).then_inc(S["unit_free"], 1)
            dve.wait_ge(S["unit_free"], 1)
            with dve.Fori(0, units) as u:
                step = Chain(dve, S["dve_step"], u * per)
                dve.wait_ge(qk_loaded, u * 32 + 32)
                for n, dst in enumerate((q, k)):
                    step(dve.tensor_scalar(dst[:, :], pre[:, n, 0:T], core.col_at("ml_cw0", u + 2 * n), None, ALU.mult))
                    for j in range(1, 4):
                        ins = dve.scalar_tensor_tensor(dst[:, :], pre[:, n, j:j + T],
                                                       core.col_at(f"ml_cw{j}", u + 2 * n), dst[:, :],
                                                       ALU.mult, ALU.add)
                        if j < 3:
                            step(ins)
                    ins.then_inc(S["conv_done"], 1)
                dve.wait_ge(rows_loaded, u * (96) + 96)
                for sub in range(nsub):
                    def spread(n):
                        return colv[:, n, :, bass.ds(u * nsub + sub, 1)].to_broadcast([P, NCH, C])
                    a = chunks(att[:, sub, :])
                    step(dve.tensor_tensor(a, chunks(brep[:, sub, :]), spread(0), ALU.subtract))
                    step(dve.tensor_scalar(a, a, 0.0, None, ALU.min))
                    dve.tensor_tensor(a, a, spread(1), ALU.add).then_inc(S["expo_ready"], 1)
                dve.wait_ge(S["silu_done"], u * 2 + 2)
                dve.tensor_scalar(q[:, :], q[:, :], 64 ** -0.5, None, ALU.mult).then_inc(S["qk_ready"], 1)
                for sub in range(nsub):
                    a = chunks(att[:, sub, :])
                    dve.wait_ge(S["expd"], u * nsub + (sub + 1))
                    step(dve.tensor_tensor(a, a, per_chunk(core.tri[:, :]), ALU.mult))
                    dve.wait_ge(S["prod_done"], u * nsub + (sub + 1))
                    dve.tensor_tensor(a, a, chunks(A[sub]), ALU.mult).then_inc(S["att_ready"], 1)
                step(dve.tensor_tensor(q[:, :], q[:, :], qdec[:, :], ALU.mult))
                dve.wait_ge(S["keys_turned"], u + 1)
                for sub in range(nsub):
                    kd = colv[:, 2, :, bass.ds(u * nsub + sub, 1)].to_broadcast([P, NCH, 64])
                    ins = dve.tensor_tensor(chunks(ktok)[:, :, sub * 64:sub * 64 + 64],
                                            chunks(B[0])[:, :, sub * 64:sub * 64 + 64], kd, ALU.mult)
                ins.then_inc(S["keys_kept"], 1)
                dve.wait_ge(S["update_done"], u + 1)
                dve.tensor_copy(nstate[:, 1:2], Bflat[:, N0:N0 + 1])
                step(dve.tensor_copy(state[:, 1, :], Bflat[:, 0:nsub * P]))
                for c in range(1, NCH - 1):
                    g = qdec[:, c * C + C - 1:c * C + C]
                    dve.scalar_tensor_tensor(nstate[:, c + 1:c + 2], nstate[:, c:c + 1], g, Bflat[:, N0 + c:N0 + c + 1],
                                             ALU.mult, ALU.add)
                    step(dve.scalar_tensor_tensor(state[:, c + 1, :], state[:, c, :], g,
                                                  Bflat[:, c * nsub * P:(c + 1) * nsub * P], ALU.mult, ALU.add))
                dve.tensor_copy(nrep[:, 1:NCH, :], nstate[:, 1:NCH].unsqueeze(2).to_broadcast([P, NCH - 1, P])) \
                    .then_inc(S["state_ready"], 1)
                dve.wait_ge(oz_loaded, 16 * 2 * nsub * units)
                for sub in range(nsub):
                    gate = flat(og[:, bass.ds(u * nsub + sub, 1), :])
                    dve.wait_ge(S["out_done"], u * nsub + (sub + 1))
                    step(dve.tensor_scalar(att[:, sub, :], B[sub], -1.0, None, ALU.mult))
                    step(dve.tensor_tensor(att[:, sub, :], B[sub], att[:, sub, :], ALU.max))
                    step(dve.tensor_tensor(att[:, sub, :], att[:, sub, :], em[:, sub, :], ALU.max))
                    step(dve.reciprocal(att[:, sub, :], att[:, sub, :]))
                    step(dve.tensor_tensor(att[:, sub, :], A[sub], att[:, sub, :], ALU.mult))
                    dve.tensor_tensor(gate, gate, att[:, sub, :], ALU.mult).then_inc(S["h_ready"], 1)
                for sub in range(nsub):
                    dve.wait_ge(S["rooted"], u * nsub + (sub + 1))
                    yo = flat(y[:, bass.ds(u * nsub + sub, 1), :])
                    step(dve.reciprocal(em[:, sub, :], em[:, sub, :]))
                    gate = flat(og[:, bass.ds(u * nsub + sub, 1), :])
                    step(dve.scalar_tensor_tensor(em[:, sub, :], gate, core.col_at("ml_nw", u * nsub + sub),
                                                  em[:, sub, :], ALU.mult, ALU.mult))
                    ins = dve.tensor_tensor(yo, yo, em[:, sub, :], ALU.mult)
                    if sub + 1 < nsub:
                        step(ins)
                ins.then_inc(S["unit_free"], 1)
                step.ends(per)


def block_1(core, d):
    with Stage(core.nc, "b1") as st:
        core.hT = st.sb("hT", [P, KD, T])
        core.brow = st.sb("brow", [1, 3 * 512])
        y = st.sb("y", [P, 4, T])
        with Stage(core.nc, "b1row") as s2:
            got = s2.sem("brow_loaded")
            block = s2.block()

            @block.sync
            def _(sp):
                sp.dma_start(core.brow[:, :], d["b1_vrow"]).then_inc(got, 16)
                sp.wait_ge(got, 16)
        rms_norm(core, "rms1", core.xT, "norm_w", core.hT)
        hg_lower_bound(core)
        vector_decay_branch(core, "hg", 1, 4, d["w1"], GLA_FILL, [(d["gla_park"], 4 * n, 1) for n in range(3)],
                            [("features", ACT.Identity, ("gla_qk", 0, 1)), ("tokens", ACT.Copy, (512, 1)),
                             ("features", ACT.Silu, ("gla_z", 0, 1))],
                            [8] + [2] + [3] * 6 + [4] + [4, 4, 4] + [4], "hg_nw", y)
        cols = st.sb("cols", [P, 3 * NCH * 4])
        with Stage(core.nc, "glas") as s2:
            gl = s2.sb("gl", [P, 2, T])
            gates_and_projection(core, d["w1"], d["gla_w_a2"], gl, d["ml_rows"], cols, y, d["wo1a"])
            kinds = [("features", ACT.Identity, ("ml_q", 0, 1)), ("features", ACT.Identity, ("ml_k", 0, 1))]
            kinds += [("tokens", ACT.Copy, (1024 + n * P, 2)) for n in range(2)]
            kinds += [("features", f, (c, n, 2)) for c, f in (("ml_o", ACT.Sigmoid), ("ml_z", ACT.Silu)) for n in range(2)]
            vector_decay_branch(core, "gla", 2, 2, d["w1"], ML_FILL, places(d["ml_park"], 8), kinds,
                                [8] + [8] * 8 + [8, 8, 8] + [8, 24], "gla_nw", y, d["gla_park"], gl)
        out_projection(core, "o1b", y, 4, d["wo1b"], core.xT)
        mlstm_branch(core, d["ml_park"], d["ml_rows"], cols, y)
        out_projection(core, "o1c", y, 4, d["wo1c"], core.xT)
    rms_norm(core, "fin1", core.xT, "final_norm_w", core.xT)


RH, RDK, RDV = 4, 256, 512
CW = 31
SEG2 = segments([("val", D), ("glu", D), ("gate", D), ("q", RH * RDK), ("k", RH * RDK), ("v", RH * RDV),
                 ("rg", RH * RDV), ("ga", D), ("gb", D)])
CONV_TILE = RH * (12 + 4)


def tile_order_2():
    def tile(name, n):
        s = SEG2[name][0] + n * P
        return s, s + P
    gates = [tile(n, e) for n in ("gb", "ga") for e in range(KD)]
    out = []
    for h in range(RH):
        out += [tile("q", 2 * h), tile("q", 2 * h + 1), tile("k", 2 * h), tile("k", 2 * h + 1)]
        out += [tile(n, 4 * h + j) for n in ("v", "rg") for j in range(4)] + gates[4 * h:4 * h + 4]
    for e in range(KD):
        out += [tile("glu", e), tile("val", e), tile("gate", e)]
    return out


def columns_2(i):
    f = np.float32
    lg = np.log1p(-np.exp2(f(-5.0) - np.arange(RH, dtype=f))).astype(f)
    idx = np.arange(C, dtype=f)
    zeta = np.exp(lg[:, None] * (f(C - 1.0) - idx)).astype(f) * f(RDK ** -0.5)
    out = [("norm_gain_2", i["norm_gain_2"][0]), ("conv_b_2", i["conv_dw_b_2"][0]),
           ("ln_g_2", i["conv_ln_g_2"][0]), ("ln_b_2", i["conv_ln_b_2"][0]), ("ret_gn", i["ret_gn_g_2"][0]),
           ("final_gain_2", i["final_gain_2"]), ("zeta", zeta),
           ("gamma_chunk", np.repeat(np.exp(lg * f(C)).astype(f), P))]
    return out + [(f"cw{j}", i["conv_dw_w_2"][0, j]) for j in range(CW)]


def lay_out_2(i, d):
    f = np.float32
    d["w2"] = in_tiles(i["w_in_2"][0], tile_order_2())
    d["wret"] = out_tiles(i["w_ret_proj_2"][0])
    d["wconv"] = out_tiles(i["w_conv_proj_2"][0])
    d["wo2"] = out_tiles(i["w_out_2"][0])
    pos = np.arange(T, dtype=f)
    inv = np.power(f(10000.0), -np.arange(0, RDK, 2, dtype=f) / f(RDK)).astype(f)
    ang = (inv[:, None] * pos[None, :]).astype(f)
    d["c_rope"] = np.concatenate([np.cos(ang), np.sin(ang)], 1).astype(f)
    lg = np.log1p(-np.exp2(f(-5.0) - np.arange(RH, dtype=f))).astype(f)
    idx = np.arange(C, dtype=f)
    diff = idx[None, :] - idx[:, None]
    dec = np.where(diff >= 0, np.exp(lg[:, None, None] * np.maximum(diff, 0)), 0).astype(f) * f(RDK ** -0.5)
    xi = np.exp(lg[:, None] * (idx + 1)).astype(f)
    d["c_ret"] = np.concatenate([dec.transpose(1, 0, 2).reshape(P, RH * C),
                                 np.broadcast_to(xi.reshape(1, RH * C), (P, RH * C))], 1)


def weighted_projection(core, name, y, nk, wt, gates, first, dst, accumulate, back=None, halves=None):
    with Stage(core.nc, name) as st:
        proj = SplitProjection(st, y, nk, 2, halves)
        sg = st.sb("sg", [P, 2, T])
        g_loaded = [st.sem("g_loaded0"), st.sem("g_loaded1")]
        added, dve_step, back_loaded = (st.sem(n) for n in ("added", "dve_step", "back_loaded"))
        block = st.block()

        @block.sync
        def _(sp):
            for s in range(2):
                sp.dma_start(proj.w[:, s, :], wt[s * P:(s + 1) * P, :]).then_inc(proj.loaded[s], 16)
                sp.dma_start(sg[:, s, :], gates[(first + s) * P:(first + s + 1) * P, :]).then_inc(g_loaded[s], 16)
            if back is not None:
                for k in range(KD):
                    sp.wait_ge(proj.y_cut, k + 1)
                    sp.dma_start(back[0][:, k, :], back[1][k * P:(k + 1) * P, :]).then_inc(back_loaded, 16)
            with sp.Fori(1, KD // 2) as i:
                for s in range(2):
                    proj.load_next(sp, wt, 0, i, s)
                    sp.wait_ge(added, 2 * i + (s + 1))
                    sp.dma_start(sg[:, s, :], gates[bass.ds(i * (2 * P) + (first + s) * P, P), :]).then_inc(g_loaded[s], 16)
            if back is not None:
                sp.wait_ge(back_loaded, 16 * KD)

        @block.gpsimd
        def _(pool):
            proj.cut_weights(pool, KD)

        @block.tensor
        def _(pe):
            with pe.Fori(0, KD // 2) as i:
                for s in range(2):
                    pe.wait_ge(added, 2 * i + (s + 1))
                    proj.multiply(pe, pair(core, s), i, s)

        @block.scalar
        def _(act):
            proj.round_first(act)
            proj.round_y(act)

        @block.vector
        def _(dve):
            dve.sem_inc(added, 2)
            proj.cut_first(dve)
            proj.cut_y(dve)
            with dve.Fori(0, KD // 2) as i:
                step = Chain(dve, dve_step, i * 2)
                for s in range(2):
                    dve.wait_ge(g_loaded[s], 16 * i + 16)
                    dve.wait_ge(proj.done, 2 * i + (s + 1))
                    o = flat(dst[:, bass.ds(2 * i + s, 1), :])
                    if accumulate:
                        step(dve.tensor_tensor(sg[:, s, :], pair(core, s), sg[:, s, :], ALU.mult))
                        dve.tensor_tensor(o, o, sg[:, s, :], ALU.add).then_inc(added, 1)
                    else:
                        dve.tensor_tensor(o, pair(core, s), sg[:, s, :], ALU.mult).then_inc(added, 1)
                step.ends(2 if accumulate else 0)


def retention_branch(core, wt, d, halves):
    order = ["q0", "q1", "k0", "k1", "v0", "v1", "v2", "v3", "g0", "g1", "g2", "g3"]
    nt, units, NV = len(order), RH, RDV // P
    with Stage(core.nc, "ret") as st:
        proj = SplitProjection(st, None, KD, 2, halves)
        rope = st.sb("rope", [P, 2, T])
        tab = st.sb("tab", [P, 2, RH, C])
        q, k = core.xT[:, 0:2, :], core.xT[:, 2:4, :]
        v = core.xT[:, 4:8, :].rearrange("p a t -> p (a t)").rearrange("p (c n d) -> p c n d", c=NCH, n=NV)
        g, o = st.sb("g", [P, NV, T]), st.sb("o", [P, NV, T])
        att = st.sb("att", [P, T])
        ktok = st.sb("ktok", [P, NCH, RDK])
        R = st.sb("R", [P, 2, 2 * RDV])
        vT = R
        turn = ktok[:, :, :].rearrange("p c d -> p (c d)").rearrange("p (a t) -> p a t", a=2)
        sq = v[:, :, :, :].rearrange("p c n d -> p (c n d)").rearrange("p (n t) -> p n t", n=NV)
        S = {n: st.sem(n) for n in (
            "tables", "evacuated", "v_turned", "v_kept", "unit_free", "roped", "prod_done", "att_ready", "q_decayed",
            "keys_turned", "keys_kept", "update_done", "r_ready", "out_done", "o_kept", "mean_done", "centred",
            "squared", "var_done", "rooted", "o_ready", "stored", "dve_step", "passed")}
        A, B = pair(core, 0), [pair(core, 2), pair(core, 3)]
        fill = Filler(core, st, "gates", 1, None, None, places(d["gate_park"], 2 * KD // units),
                      [("features", ACT.Sigmoid, None)] * (2 * KD // units), proj=proj, before=nt)
        tiles = nt + fill.n
        cut = [8, 24]
        per_chunk_parts = (cut[1] - cut[0]) // NCH
        block = st.block()

        @block.sync
        def _(sp):
            sp.dma_start(rope[:, :, :].rearrange("p a t -> p (a t)"), d["c_rope"]).then_inc(S["tables"], 16)
            sp.dma_start(tab[:, :, :, :].rearrange("p a h t -> p (a h t)"), d["c_ret"]).then_inc(S["tables"], 16)
            proj.load(sp, wt, 0, units * tiles)

        @block.gpsimd
        def _(pool):
            proj.cut_weights(pool, units * tiles)

        @block.tensor
        def _(pe):
            with pe.Fori(0, units) as u:
                pe.wait_ge(S["unit_free"], u + 1)
                for t, what in enumerate(order):
                    if t >= 2:
                        pe.wait_ge(S["evacuated"], u * nt + (t - 1))
                    proj.multiply(pe, B[t % 2], u * (tiles // 2) + t // 2, t % 2)
                    if order[t - 1][0] == "v":
                        n = int(order[t - 1][1])
                        pe.wait_ge(S["evacuated"], u * nt + t)
                        if n:
                            pe.wait_ge(S["v_kept"], u * NV + n)
                        for c in range(NCH):
                            ins = pe.transpose(A[:, c * C:c * C + C], vT[:, n % 2, c * C:c * C + C], core.ident[:, :])
                        ins.then_inc(S["v_turned"], 1)
                pe.wait_ge(S["v_kept"], u * NV + NV)
                pe.wait_ge(S["roped"], u * 2 + 2)
                for c in range(NCH):
                    cs = slice(c * C, c * C + C)
                    for i in range(2):
                        ins = pe.matmul(A[:, cs], k[:, i, cs], q[:, i, cs], start=(i == 0), stop=(i == 1))
                ins.then_inc(S["prod_done"], 1)
                pe.wait_ge(S["evacuated"], u * nt + nt)
                for i in range(2):
                    for c in range(NCH):
                        cs = slice(c * C, c * C + C)
                        ins = pe.transpose(B[i][:, cs], k[:, i, cs], core.ident[:, :])
                    ins.then_inc(S["keys_turned"], 1)
                fill.advance(pe, u, 0, cut[0])
                pe.wait_ge(S["keys_kept"], u * 2 + 2)
                pe.wait_ge(S["att_ready"], u + 1)
                pe.wait_ge(S["q_decayed"], u + 1)
                for c in range(NCH):
                    cs = slice(c * C, c * C + C)
                    if c < NCH - 1:
                        if c >= 2:
                            pe.wait_ge(S["r_ready"], u * (NCH - 1) + (c - 1))
                        for i in range(2):
                            ins = pe.matmul(B[c % 2][:, i * RDV:(i + 1) * RDV], ktok[:, c, i * P:(i + 1) * P],
                                            v[:, c, :, :].rearrange("p n d -> p (n d)"), start=True, stop=True)
                        ins.then_inc(S["update_done"], 1)
                    fill.advance(pe, u, cut[0] + c * per_chunk_parts, cut[0] + (c + 1) * per_chunk_parts)
                    if c >= 2:
                        pe.wait_ge(S["o_kept"], u * NCH + (c - 1))
                    if c >= 1:
                        pe.wait_ge(S["r_ready"], u * (NCH - 1) + c)
                    for j in range(NV):
                        dst = A[:, (c % 2) * 512 + j * P:(c % 2) * 512 + (j + 1) * P]
                        ins = pe.matmul(dst, v[:, c, j, :], att[:, cs], start=True, stop=(c == 0))
                        if c >= 1:
                            for i in range(2):
                                ins = pe.matmul(dst, R[:, c % 2, i * RDV + j * P:i * RDV + (j + 1) * P],
                                                q[:, i, cs], start=False, stop=(i == 1))
                    ins.then_inc(S["out_done"], 1)
                for src, ready, n, done, end in ((o, "o_kept", NCH, "mean_done", 3 * 16), (sq, "squared", 1, "var_done", 4 * 16)):
                    pe.wait_ge(S[ready], u * n + n)
                    for half in range(2):
                        for j in range(NV):
                            ins = pe.matmul(A[:, half * 512:half * 512 + 512], core.mean_v[:, :],
                                            src[:, j, half * 512:half * 512 + 512],
                                            start=(j == 0), stop=(j == NV - 1))
                    ins.then_inc(S[done], 1)
                    fill.advance(pe, u, cut[1] if n > 1 else 3 * 16, end)

        @block.scalar
        def _(act):
            fill.begin(act)
            proj.round_first(act)
            with act.Fori(0, units) as u:
                for t, what in enumerate(order):
                    act.wait_ge(proj.done, u * tiles + (t + 1))
                    src, n = B[t % 2], int(what[1])
                    if what[0] == "v":
                        ins = act.activation(vT[:, n % 2, :], src, ACT.Copy)
                    elif what[0] == "g":
                        ins = act.activation(g[:, n, :], src, ACT.Silu)
                    else:
                        ins = act.activation((q if what[0] == "q" else k)[:, n, :], src, ACT.Copy)
                    ins.then_inc(S["evacuated"], 1)
                    if order[t - 1][0] == "v":
                        n = int(order[t - 1][1])
                        act.wait_ge(S["v_turned"], u * NV + (n + 1))
                        act.activation(v[:, :, n, :], chunks(A), ACT.Copy).then_inc(S["v_kept"], 1)
                for i in range(2):
                    wait_alone(act, S["keys_turned"], u * 2 + (i + 1), S["passed"])
                    act.activation(ktok[:, :, i * P:(i + 1) * P], chunks(B[i]), ACT.Copy,
                                   scale=core.col_at("zeta", u)).then_inc(S["keys_kept"], 1)
                for c in range(NCH):
                    if c == (16 - cut[0]) // per_chunk_parts - 1:
                        fill.keep(act, u, 0)
                    act.wait_ge(S["out_done"], u * NCH + (c + 1))
                    src = A[:, (c % 2) * 512:(c % 2) * 512 + 512].rearrange("p (n t) -> p n t", n=NV)
                    act.activation(o[:, :, c * C:c * C + C], src, ACT.Copy).then_inc(S["o_kept"], 1)
                fill.keep(act, u, 1)
                act.wait_ge(S["centred"], u + 1)
                act.activation(sq, o[:, :, :], ACT.Square).then_inc(S["squared"], 1)
                fill.keep(act, u, 2)
                act.wait_ge(S["var_done"], u + 1)
                act.activation(att[:, :], A, ACT.Sqrt, bias=core.const(LN_EPS)).then_inc(S["rooted"], 1)
                fill.keep(act, u, 3)
                fill.end(act, u)
                at = [act.snap(u * (NV * P) + j * P) for j in range(NV)]
                act.wait_ge(S["o_ready"], u + 1)
                for j in range(NV):
                    act.dma_start(d["o_park"][bass.ds(at[j], P), :], o[:, j, :]).then_inc(S["stored"], 16)
                act.wait_ge(S["stored"], u * (16 * NV) + 16 * NV)

        @block.vector
        def _(dve):
            per = 2 * 2 + 2
            dve.sem_inc(S["unit_free"], 1)
            proj.cut_first(dve)
            dve.wait_ge(S["tables"], 32)
            with dve.Fori(0, units) as u:
                step = Chain(dve, S["dve_step"], u * per)
                for n, x in enumerate((q, k)):
                    dve.wait_ge(S["evacuated"], u * nt + (2 * n + 2))
                    dve.tensor_tensor(turn[:, 0, :], x[:, 1, :], rope[:, 1, :], ALU.mult)
                    step(dve.tensor_tensor(turn[:, 1, :], x[:, 0, :], rope[:, 1, :], ALU.mult))
                    dve.tensor_tensor(x[:, 0, :], x[:, 0, :], rope[:, 0, :], ALU.mult)
                    step(dve.tensor_tensor(x[:, 1, :], x[:, 1, :], rope[:, 0, :], ALU.mult))
                    dve.tensor_tensor(x[:, 0, :], x[:, 0, :], turn[:, 0, :], ALU.subtract)
                    dve.tensor_tensor(x[:, 1, :], x[:, 1, :], turn[:, 1, :], ALU.add).then_inc(S["roped"], 1)
                    dve.wait_ge(S["roped"], u * 2 + (n + 1))
                dve.wait_ge(S["prod_done"], u + 1)
                dve.tensor_tensor(chunks(att[:, :]), chunks(A),
                                  tab[:, 0, bass.ds(u, 1), :].to_broadcast([P, NCH, C]), ALU.mult) \
                    .then_inc(S["att_ready"], 1)
                qc = q[:, :, :].rearrange("p a (c t) -> p (a c) t", t=C)
                dve.tensor_tensor(qc, qc, tab[:, 1, bass.ds(u, 1), :].to_broadcast([P, 2 * NCH, C]), ALU.mult) \
                    .then_inc(S["q_decayed"], 1)
                for c in range(NCH - 1):
                    dve.wait_ge(S["update_done"], u * (NCH - 1) + (c + 1))
                    if c == 0:
                        ins = dve.tensor_copy(R[:, 1, :], B[0])
                    else:
                        dve.wait_ge(S["out_done"], u * NCH + c)
                        ins = dve.scalar_tensor_tensor(R[:, (c + 1) % 2, :], R[:, c % 2, :],
                                                       core.col_at("gamma_chunk", u), B[c % 2], ALU.mult, ALU.add)
                    ins.then_inc(S["r_ready"], 1)
                    dve.wait_ge(S["r_ready"], u * (NCH - 1) + (c + 1))
                dve.wait_ge(S["mean_done"], u + 1)
                dve.tensor_tensor(o[:, :, :], o[:, :, :], A.unsqueeze(1).to_broadcast([P, NV, T]), ALU.subtract) \
                    .then_inc(S["centred"], 1)
                dve.wait_ge(S["rooted"], u + 1)
                step(dve.reciprocal(att[:, :], att[:, :]))
                for j in range(NV):
                    ins = dve.scalar_tensor_tensor(o[:, j, :], o[:, j, :], core.col_at("ret_gn", u * NV + j),
                                                   att[:, :], ALU.mult, ALU.mult)
                step(ins)
                dve.tensor_tensor(o[:, :, :], o[:, :, :], g[:, :, :], ALU.mult).then_inc(S["o_ready"], 1)
                dve.wait_ge(S["o_ready"], u + 1)
                dve.sem_inc(S["unit_free"], 1)
                step.ends(per)


def conv_branch(core, wt, first, halves, uT, gate):
    nt = 3
    with Stage(core.nc, "conv") as st:
        proj = SplitProjection(st, None, KD, nt, halves)
        sg, val = st.sb("sg", [P, T]), st.sb("val", [P, T])
        pad, odd = st.sb("pad", [P, CW - 1 + T]), st.sb("odd", [P, T])
        evacuated, consumed, dve_step = (st.sem(n) for n in ("evacuated", "consumed", "dve_step"))
        block = st.block()

        @block.sync
        def _(sp):
            proj.load(sp, wt, first, nt * KD)

        @block.gpsimd
        def _(pool):
            proj.cut_weights(pool, nt * KD)

        @block.tensor
        def _(pe):
            with pe.Fori(0, KD) as u:
                for t in range(nt):
                    pe.wait_ge(evacuated, u * nt + (t + 1))
                    proj.multiply(pe, pair(core, t), u, t)

        @block.scalar
        def _(act):
            act.sem_inc(evacuated, nt)
            proj.round_first(act)
            with act.Fori(0, KD) as u:
                act.wait_ge(consumed, u + 1)
                for t, (dst, fn) in enumerate(((sg[:, :], ACT.Sigmoid), (val[:, :], ACT.Copy),
                                               (flat(gate[:, bass.ds(u, 1), :]), ACT.Silu))):
                    act.wait_ge(proj.done, u * nt + (t + 1))
                    act.activation(dst, pair(core, t), fn).then_inc(evacuated, 1)

        @block.vector
        def _(dve):
            per = CW + 1
            proj.cut_first(dve)
            dve.memset(pad[:, 0:CW - 1], 0.0).then_inc(consumed, 1)
            with dve.Fori(0, KD) as u:
                dve.wait_ge(evacuated, u * nt + (nt + 2))
                dve.tensor_tensor(pad[:, CW - 1:], val[:, :], sg[:, :], ALU.mult).then_inc(consumed, 1)
                dve.wait_ge(consumed, u + 2)
                acc = (flat(uT[:, bass.ds(u, 1), :]), odd[:, :])
                for j in range(CW):
                    a, x, wj = acc[j % 2], pad[:, j:j + T], core.col_at(f"cw{j}", u)
                    if j >= 2:
                        dve.wait_ge(dve_step, u * per + (j - 1))
                        ins = dve.scalar_tensor_tensor(a, x, wj, a, ALU.mult, ALU.add)
                    elif j == 1:
                        ins = dve.tensor_scalar(a, x, wj, None, ALU.mult)
                    else:
                        ins = dve.tensor_scalar(a, x, wj, core.col_at("conv_b_2", u), ALU.mult, ALU.add)
                    ins.then_inc(dve_step, 1)
                dve.wait_ge(dve_step, u * per + CW)
                dve.tensor_tensor(acc[0], acc[0], acc[1], ALU.add).then_inc(dve_step, 1)
                dve.wait_ge(dve_step, u * per + per)


def conv_norm(core, uT, gate):
    with Stage(core.nc, "cnorm") as st:
        sq, rstd = st.sb("sq", [P, 2, T]), st.sb("rstd", [P, T])
        mean_done, centred, squared, summed, rooted, scaled, activated, dve_step = (
            st.sem(n) for n in ("mean_done", "centred", "squared", "summed", "rooted", "scaled", "activated", "dve_step"))
        block = st.block()

        @block.tensor
        def _(pe):
            for half in range(2):
                for k in range(KD):
                    ins = pe.matmul(pair(core, 0)[:, half * 512:half * 512 + 512], core.mean_d[:, :],
                                    uT[:, k, half * 512:half * 512 + 512], start=(k == 0), stop=(k == KD - 1))
            ins.then_inc(mean_done, 1)
            for k in range(KD):
                pe.wait_ge(squared, k + 1)
                for half in range(2):
                    ins = pe.matmul(pair(core, 1)[:, half * 512:half * 512 + 512], core.mean_d[:, :],
                                    sq[:, k % 2, half * 512:half * 512 + 512], start=(k == 0), stop=(k == KD - 1))
                ins.then_inc(summed, 1)

        @block.scalar
        def _(act):
            for k in range(KD):
                act.wait_ge(centred, k + 1)
                if k >= 2:
                    act.wait_ge(summed, k - 1)
                act.activation(sq[:, k % 2, :], uT[:, k, :], ACT.Square).then_inc(squared, 1)
            act.wait_ge(summed, KD)
            act.activation(rstd[:, :], pair(core, 1), ACT.Sqrt, bias=core.const(LN_EPS)).then_inc(rooted, 1)
            for k in range(KD):
                act.wait_ge(scaled, k + 1)
                act.activation(uT[:, k, :], uT[:, k, :], ACT.Silu, bias=core.col("ln_b_2", k)).then_inc(activated, 1)

        @block.vector
        def _(dve):
            step = Chain(dve, dve_step)
            dve.wait_ge(mean_done, 1)
            for k in range(KD):
                dve.tensor_tensor(uT[:, k, :], uT[:, k, :], pair(core, 0), ALU.subtract).then_inc(centred, 1)
            dve.wait_ge(rooted, 1)
            step(dve.reciprocal(rstd[:, :], rstd[:, :]))
            for k in range(KD):
                dve.scalar_tensor_tensor(uT[:, k, :], uT[:, k, :], core.col("ln_g_2", k), rstd[:, :],
                                         ALU.mult, ALU.mult).then_inc(scaled, 1)
            for k in range(KD):
                dve.wait_ge(activated, k + 1)
                dve.tensor_tensor(uT[:, k, :], uT[:, k, :], gate[:, k, :], ALU.mult)


def block_2(core, d):
    with Stage(core.nc, "b2") as st:
        halves = [st.sb(n, [P, KD, T], F32R) for n in ("hi", "lo")]
        rms_norm(core, "rms2", core.xT, "norm_gain_2", None, park=d["x_park"], halves=halves)
        retention_branch(core, d["w2"], d, halves)
        gate = st.sb("gate", [P, KD, T])
        uT, mixed = core.xT, gate
        conv_branch(core, d["w2"], CONV_TILE, halves, uT, gate)
        conv_norm(core, uT, gate)
        weighted_projection(core, "ya", uT, KD, d["wconv"], d["gate_park"], KD, mixed, False,
                            back=(core.xT, d["o_park"][0:D, :]), halves=halves)
        weighted_projection(core, "yb1", core.xT, KD, d["wret"][:, 0:D], d["gate_park"], 0, mixed, True,
                            back=(core.xT, d["o_park"][D:2 * D, :]), halves=halves)
        weighted_projection(core, "yb2", core.xT, KD, d["wret"][:, D:2 * D], d["gate_park"], 0, mixed, True,
                            back=(core.xT, d["x_park"]), halves=halves)
        out_projection(core, "o2", mixed, KD, d["wo2"], core.xT, halves)
    rms_norm(core, "fin2", core.xT, "final_gain_2", core.xT)


SBW, SSH, RWW = 512, 16, 512
SEG3 = segments([("sb_q", SBW), ("sb_k", SBW), ("sb_v", SBW), ("sb_g", SBW), ("z", D), ("xs", D), ("bm", P), ("cm", P),
                 ("dt", SSH), ("r", RWW), ("k", RWW), ("v", RWW), ("rw_g", RWW), ("lo", P),
                 ("g_sb", D), ("g_ssd", D), ("g_rw", D)])
RW_LO, RW_TILE, RW_FILL, SSD_TILE, SSD_UNIT, SSD_GATE = 0, 1, 17, 49, 52, 68


def tile_order_3():
    def tile(name, n):
        s = SEG3[name][0] + n * P
        return s, min(s + P, SEG3[name][1])
    gates = [tile(n, e) for n in ("g_sb", "g_rw") for e in range(KD)]
    out = [tile("lo", 0)]
    for u in range(4):
        out += [tile(n, u) for n in ("r", "k", "v", "rw_g")]
    for u in range(4):
        out += gates[4 * u:4 * u + 4] + [tile(n, u) for n in ("sb_q", "sb_k", "sb_v", "sb_g")]
    out += [tile("bm", 0), tile("cm", 0), tile("dt", 0)]
    for u in range(8):
        out += [tile("xs", u), tile("z", u)]
    return out + [tile("g_ssd", e) for e in range(KD)]


def columns_3(i):
    cw, cb, mu = i["conv_w_3"][0], i["conv_b_3"][0], i["rw_mu_3"][0]
    out = [("norm_g_3", i["norm_g_3"][0]), ("final_g_3", i["final_g_3"]), ("ssd_ng", i["ssd_norm_g_3"][0]),
           ("ssd_cb", cb), ("dt_bias", i["dt_bias_3"][0]), ("a_log", i["a_log_3"][0]),
           ("a_head", np.zeros(SSH, np.float32)),
           ("d_skip", np.repeat(i["d_skip_3"][0], D // SSH)),
           ("w0", i["rw_w0_3"][0]), ("a0", i["rw_a0_3"][0]), ("k_k", i["rw_k_k_3"][0]), ("k_a", i["rw_k_a_3"][0]),
           ("r_k", i["rw_r_k_3"][0]), ("rw_ln_g", i["rw_ln_g_3"][0]), ("rw_ln_b", i["rw_ln_b_3"][0])]
    for n, name in enumerate(("r", "k", "v", "g")):
        out.append(("mu_" + name, mu[n * RWW:(n + 1) * RWW]))
    out.append(("mu_lo", mu[4 * RWW:]))
    return out + [(f"ssd_cw{j}", cw[j]) for j in range(4)]


def lay_out_3(i, d):
    d["w3"] = in_tiles(i["w_in_3"][0], tile_order_3())
    for n, name in (("wsb", "w_out_sb_3"), ("wssd", "w_out_ssd_3"), ("wrw", "w_out_rw_3"), ("wo3", "w_o_3")):
        d[n] = out_tiles(i[name][0])
    up = np.concatenate([i["rw_w_up_3"][0], i["rw_a_up_3"][0]], 0)
    d["w_up"] = up.reshape(P, 4, P).transpose(1, 0, 2).reshape(4 * P, P)
    s, t = np.arange(P)[:, None], np.arange(P)[None, :]
    same = s // 64 == t // 64
    d["c_mat3"] = np.concatenate([same, same / 64.0, s >= t], 1).astype(np.float32)
    level0 = level_masks()[:, 0, :]
    d["c_mask3"] = np.concatenate([s < t, s <= t, level0.T], 1).astype(np.float32)


def spans(lo):
    return [(max(lo, h * 512), h * 512 + 512) for h in range(2) if lo < h * 512 + 512]


def stick_breaking_branch(core, wt, y, sb_park, xz_park):
    units, nt = 4, 4
    steps = [(b, sub) for b in reversed(range(NCH)) for sub in range(2)]
    NS = len(steps)
    with Stage(core.nc, "sb") as st:
        q_loaded, k_loaded, v_loaded, y_loaded = (st.sem(n + "_loaded") for n in "qkvy")
        q, k = st.sb("q", [P, T]), st.sb("k", [P, T])
        v = st.sb("v", [P, NCH, P])
        neg, soft, keep, later, att = (st.sb(n, [P, 2, T]) for n in ("neg", "soft", "keep", "later", "att"))
        diag = st.sb("diag", [P, 2, C])
        zeros = st.sb("zeros", [P, 512])
        S = {n: st.sem(n) for n in (
            "unit_free", "q_scaled", "z_done", "mag_ready", "softened", "keep_ready",
            "sum_done", "att_expd", "att_ready", "out_done", "dve_step", "act_step")}
        Z, O = [pair(core, 0), pair(core, 1)], pair(core, 2)
        fill = Filler(core, st, "xz", 3, wt, SSD_UNIT, places(xz_park, 4),
                      [("features", ACT.Copy, None)] * 4)
        parts = NS // fill.n

        def rows(sub):
            return slice(sub * 64, sub * 64 + 64)

        block = st.block()

        @block.sync
        def _(sp):
            def load(dst, sem, at):
                src = sb_park[at:at + P, :] if isinstance(at, int) else sb_park[bass.ds(at, P), :]
                sp.dma_start(dst, src).then_inc(sem, 16)
            vf = v[:, :, :].rearrange("p c d -> p (c d)")
            for n, (dst, sem) in enumerate(((q[:, :], q_loaded), (k[:, :], k_loaded), (vf, v_loaded))):
                load(dst, sem, n * P)
            fill.load(sp, 0)
            for u in range(units):
                load(y[:, u, :], y_loaded, (u * nt + 3) * P)
            with sp.Fori(1, units) as u:
                at = [sp.snap(u * (nt * P) + n * P) for n in range(nt)]
                sp.wait_ge(S["z_done"], u * NS)
                load(q[:, :], q_loaded, at[0])
                load(k[:, :], k_loaded, at[1])
                sp.wait_ge(S["out_done"], u * NS)
                load(vf, v_loaded, at[2])
                fill.load(sp, u)

        @block.tensor
        def _(pe):
            with pe.Fori(0, units) as u:
                pe.wait_ge(S["unit_free"], u + 1)
                pe.wait_ge(k_loaded, u * 16 + 16)
                pe.wait_ge(S["q_scaled"], u + 1)
                for n in range(NS + 2):
                    if n < NS:
                        b, sub = steps[n]
                        if n >= 2:
                            pe.wait_ge(S["att_expd"], u * NS + (n - 1))
                        for lo, hi in spans(b * C):
                            ins = pe.matmul(Z[sub][:, lo:hi], k[rows(sub), b * C:b * C + C], q[rows(sub), lo:hi],
                                            start=True, stop=True)
                        ins.then_inc(S["z_done"], 1)
                        fill.multiply(pe, u, n // parts, n % parts, parts)
                    if 1 <= n <= NS:
                        b, sub = steps[n - 1]
                        pe.wait_ge(S["keep_ready"], u * NS + n)
                        for lo, hi in spans(b * C):
                            ins = pe.matmul(Z[sub][:, lo:hi], core.triangle[:, :], keep[:, sub, lo:hi],
                                            start=False, stop=True, skip_group_check=True)
                        for lo, hi in spans((b + 1) * C):
                            ins = pe.matmul(Z[sub][:, lo:hi], core.ones[:, :], later[:, sub, lo:hi],
                                            start=False, stop=True, skip_group_check=True)
                        ins.then_inc(S["sum_done"], 1)
                    if n >= 2:
                        b, sub = steps[n - 2]
                        pe.wait_ge(S["att_ready"], u * NS + (n - 1))
                        if n == 2:
                            pe.wait_ge(v_loaded, u * 16 + 16)
                        vb = v[:, b, sub * 64:sub * 64 + 64]
                        if b == NCH - 1:
                            for lo, hi in spans(0):
                                pe.matmul(O[rows(sub), lo:hi], vb, zeros[:, :], start=True, stop=True)
                        ins = pe.matmul(O[rows(sub), b * C:b * C + C], vb, diag[:, sub, :], start=False, stop=True,
                                        skip_group_check=True)
                        for lo, hi in spans((b + 1) * C):
                            ins = pe.matmul(O[rows(sub), lo:hi], vb, att[:, sub, lo:hi], start=False, stop=True,
                                            skip_group_check=True)
                        ins.then_inc(S["out_done"], 1)

        @block.scalar
        def _(act):
            act.preload_act_table_set("natural_log_exp_and_others")
            fill.begin(act)
            with act.Fori(0, units) as u:
                step = Chain(act, S["act_step"], u * NS)
                for n in range(NS + 1):
                    if n < NS:
                        b, sub = steps[n]
                        act.wait_ge(S["mag_ready"], u * NS + (n + 1))
                        a = soft[:, sub, b * C:T]
                        step(act.activation(a, a, ACT.Exp))
                        act.activation(a, a, ACT.Ln, bias=1.0).then_inc(S["softened"], 1)
                    if n >= 1:
                        b, sub = steps[n - 1]
                        act.wait_ge(S["sum_done"], u * NS + n)
                        if n >= 3:
                            act.wait_ge(S["out_done"], u * NS + (n - 2))
                        act.activation(att[:, sub, b * C:T], Z[sub][:, b * C:T], ACT.Exp).then_inc(S["att_expd"], 1)
                    if n % parts == parts - 1:
                        fill.keep(act, u, n // parts)
                step.ends(NS)
                fill.end(act, u)

        @block.vector
        def _(dve):
            dve.memset(zeros[:, :], 0.0)
            dve.memset(diag[:, :, :], 0.0).then_inc(S["unit_free"], 1)
            per = 2 * NS
            with dve.Fori(0, units) as u:
                step = Chain(dve, S["dve_step"], u * per)
                dve.wait_ge(q_loaded, u * 16 + 16)
                dve.tensor_scalar(q[:, :], q[:, :], 64 ** -0.5, None, ALU.mult).then_inc(S["q_scaled"], 1)
                for n in range(NS + 1):
                    if n < NS:
                        b, sub = steps[n]
                        lo = b * C
                        dve.wait_ge(S["z_done"], u * NS + (n + 1))
                        step(dve.tensor_scalar(neg[:, sub, lo:T], Z[sub][:, lo:T], -1.0, None, ALU.mult))
                        dve.tensor_tensor(soft[:, sub, lo:T], Z[sub][:, lo:T], neg[:, sub, lo:T], ALU.min) \
                            .then_inc(S["mag_ready"], 1)
                        dve.wait_ge(S["softened"], u * NS + (n + 1))
                        step(dve.scalar_tensor_tensor(keep[:, sub, lo:T], neg[:, sub, lo:T], 0.0, soft[:, sub, lo:T],
                                                      ALU.min, ALU.subtract))
                        dve.tensor_tensor(keep[:, sub, lo:lo + C], keep[:, sub, lo:lo + C], core.strict[:, :], ALU.mult) \
                            .then_inc(S["keep_ready"], 1)
                    if n >= 1:
                        b, sub = steps[n - 1]
                        lo = b * C
                        dve.wait_ge(S["att_expd"], u * NS + n)
                        if b < NCH - 1:
                            dve.wait_ge(S["out_done"], u * NS + (n - 2))
                            dve.tensor_tensor(later[:, sub, lo + C:T], later[:, sub, lo + C:T], keep[:, sub, lo + C:T],
                                              ALU.add)
                        dve.tensor_copy(later[:, sub, lo:lo + C], keep[:, sub, lo:lo + C])
                        dve.copy_predicated(diag[:, sub, :], core.strict[:, :].bitcast(U32), att[:, sub, lo:lo + C]) \
                            .then_inc(S["att_ready"], 1)
                        dve.wait_ge(S["att_ready"], u * NS + n)
                dve.wait_ge(S["out_done"], u * NS + NS)
                dve.wait_ge(y_loaded, 16 * units)
                yo = flat(y[:, bass.ds(u, 1), :])
                dve.tensor_tensor(yo, yo, O, ALU.mult).then_inc(S["unit_free"], 1)
                step.ends(per)


def ssd_gates(core, wt, rows_dram, cols, ct, btok, cb):
    H = SSH
    with Stage(core.nc, "ssdgate") as st:
        w = st.sb("w", [P, 3, D])
        pre, bt = st.sb("pre", [P, 2, 3 + T]), st.sb("bt", [P, T])
        raw, mag, dt, cs, ec, de = (st.sb(n, [H, T]) for n in ("raw", "mag", "dt", "cs", "ec", "de"))
        (w_loaded, proj_done, evacuated, conv_done, activated, mag_ready, softened, a_ready, cs_ready, exped, turned,
         prod_done, b_turned, b_kept, dve_step, act_step, stored) = (st.sem(n) for n in (
             "w_loaded", "proj_done", "evacuated", "conv_done", "activated", "mag_ready", "softened", "a_ready", "cs_ready",
             "exped", "turned", "prod_done", "b_turned", "b_kept", "dve_step", "act_step", "stored"))
        a_head = core.col("a_head", 0)[0:H, :]
        block = st.block()

        @block.sync
        def _(sp):
            for n in range(3):
                sp.dma_start(w[:, n, :], wt[(SSD_TILE + n) * P:(SSD_TILE + n + 1) * P, :]).then_inc(w_loaded, 16)
            sp.wait_ge(exped, 1)
            sp.dma_start(rows_dram[0:H, :], cs[:, :]).then_inc(stored, 16)
            sp.dma_start(rows_dram[H:2 * H, :], ec[:, :]).then_inc(stored, 16)
            sp.wait_ge(stored, 32)

        @block.tensor
        def _(pe):
            pe.wait_ge(w_loaded, 48)
            project_features(pe, pair(core, 2), w[:, 2, :], core.hT, m=H).then_inc(proj_done, 1)
            for n in range(2):
                project_features(pe, pair(core, n), w[:, n, :], core.hT).then_inc(proj_done, 1)
            pe.wait_ge(exped, 1)
            for n, r in enumerate((cs, dt, de)):
                for c in range(NCH):
                    ins = pe.matmul(pair(core, 3)[:, (n * NCH + c) * H:(n * NCH + c + 1) * H],
                                    r[:, c * C:c * C + C], core.ident[0:H, 0:H], start=True, stop=True)
            ins.then_inc(turned, 1)
            pe.wait_ge(activated, 2)
            for g in range(2):
                for c in range(NCH):
                    s = slice(c * C, c * C + C)
                    ins = pe.matmul(pair(core, g)[:, s], bt[g * 64:g * 64 + 64, s], ct[g * 64:g * 64 + 64, s],
                                    start=True, stop=True)
                ins.then_inc(prod_done, 1)
            for c in range(NCH):
                s = slice(c * C, c * C + C)
                ins = pe.transpose(pair(core, 2)[:, s], bt[:, s], core.ident[:, :])
            ins.then_inc(b_turned, 1)

        @block.scalar
        def _(act):
            step = Chain(act, act_step)
            act.activation(a_head, core.col("a_log", 0)[0:H, :], ACT.Exp).then_inc(a_ready, 1)
            act.wait_ge(mag_ready, 1)
            step(act.activation(mag[:, :], mag[:, :], ACT.Exp, scale=-1.0))
            act.activation(mag[:, :], mag[:, :], ACT.Ln, bias=1.0).then_inc(softened, 1)
            for n in range(2):
                act.wait_ge(proj_done, n + 2)
                act.activation(pre[:, n, 3:3 + T], pair(core, n), ACT.Copy).then_inc(evacuated, 1)
            act.wait_ge(cs_ready, 1)
            act.activation(ec[:, :], cs[:, :], ACT.Exp)
            act.activation(de[:, :], de[:, :], ACT.Exp).then_inc(exped, 1)
            for n, dst in enumerate((bt, ct)):
                act.wait_ge(conv_done, n + 1)
                act.activation(dst[:, :], dst[:, :], ACT.Silu, bias=core.col("ssd_cb", KD + n)).then_inc(activated, 1)
            act.wait_ge(b_turned, 1)
            act.activation(btok[:, :, :], chunks(pair(core, 2)), ACT.Copy).then_inc(b_kept, 1)

        @block.vector
        def _(dve):
            step = Chain(dve, dve_step)
            dve.wait_ge(proj_done, 1)
            step(dve.tensor_scalar(raw[:, :], pair(core, 2)[0:H, :], core.col("dt_bias", 0)[0:H, :], None, ALU.add))
            dve.scalar_tensor_tensor(mag[:, :], raw[:, :], -1.0, raw[:, :], ALU.mult, ALU.max).then_inc(mag_ready, 1)
            dve.wait_ge(softened, 1)
            step(dve.scalar_tensor_tensor(dt[:, :], raw[:, :], 0.0, mag[:, :], ALU.max, ALU.add))
            dve.wait_ge(a_ready, 1)
            step(dve.tensor_scalar(raw[:, :], dt[:, :], a_head, -1.0, ALU.mult, ALU.mult))
            for c in range(NCH):
                s = slice(c * C, c * C + C)
                ins = dve.tensor_tensor_scan(cs[:, s], raw[:, s], raw[:, s], 0.0, ALU.add, ALU.bypass)
            step(ins)
            last = chunks(cs[:, :])[:, :, C - 1:C].to_broadcast([H, NCH, C])
            dve.tensor_tensor(chunks(de[:, :]), last, chunks(cs[:, :]), ALU.subtract).then_inc(cs_ready, 1)
            dve.wait_ge(evacuated, 2)
            step(dve.memset(pre[:, :, 0:3], 0.0))
            for n, dst in enumerate((bt, ct)):
                step(dve.tensor_scalar(dst[:, :], pre[:, n, 0:T], core.col("ssd_cw0", KD + n), None, ALU.mult))
                for j in range(1, 4):
                    ins = dve.scalar_tensor_tensor(dst[:, :], pre[:, n, j:j + T], core.col(f"ssd_cw{j}", KD + n),
                                                   dst[:, :], ALU.mult, ALU.add)
                    if j < 3:
                        step(ins)
                ins.then_inc(conv_done, 1)
            dve.wait_ge(turned, 1)
            dve.tensor_copy(cols[:, :], pair(core, 3)[:, 0:3 * NCH * H])
            for g in range(2):
                dve.wait_ge(prod_done, g + 1)
                dve.tensor_tensor(chunks(cb[:, g, :]), chunks(pair(core, g)),
                                  per_chunk(core.tri[:, :]), ALU.mult)


def ssd_branch(core, wt, gate_park, xz_park, rows_dram, cols, ct, btok, cb, y):
    units, per_group, H = 8, 4, SSH
    colv = cols[:, :].rearrange("p (n c h) -> p n c h", n=3, c=NCH)
    with Stage(core.nc, "ssd") as st:
        pre = st.sb("pre", [P, 2, 3 + T])
        xs = st.sb("xs", [P, 2, T])
        xdt, xend = st.sb("xdt", [P, NCH, P]), st.sb("xend", [P, NCH, P])
        crep, erep, cdec = (st.sb(n, [P, 2, T]) for n in ("crep", "erep", "cdec"))
        att = st.sb("att", [P, 2, 2, T])
        state = st.sb("state", [P, NCH, P])
        S = {n: st.sem(n) for n in (
            "unit_done", "out_free", "conv_done", "activated", "expo_ready", "expd", "att_ready",
            "x_turned", "x_ready", "update_done", "state_ready", "out_done", "z_ready", "conv_step", "expo_step", "dve_step")}
        c_loaded, e_loaded = st.sem("c_loaded"), st.sem("e_loaded")
        loaded, z_loaded = [st.sem("loaded0"), st.sem("loaded1")], [st.sem("z_loaded0"), st.sem("z_loaded1")]
        A, X, U = (pair(core, n) for n in (0, 2, 3))
        fill = Filler(core, st, "gates", 1, wt, SSD_GATE, places(gate_park, 1, 2 * KD), [("features", ACT.Sigmoid, None)], ring=1)

        def g_rows(g):
            return slice(g * 64, g * 64 + 64)

        def in_pairs(eng, unit):
            for g in range(2):
                with eng.Fori(g * per_group // 2, (g + 1) * per_group // 2 - g) as two:
                    for par in range(2):
                        unit(g, two, par)
            for par in range(2):
                unit(1, units // 2 - 1, par, last=par == 1)

        block = st.block()

        @block.sync
        def _(sp):
            def tile(n):
                return xz_park[n * P:(n + 1) * P, :] if isinstance(n, int) else xz_park[bass.ds(sp.snap(n * P), P), :]

            def load_pre(u, par):
                src = tile(u * 2)
                if not isinstance(u, int):
                    sp.wait_ge(S["conv_done"], u - 1)
                sp.dma_start(pre[:, par, 3:], src).then_inc(loaded[par], 16)

            def load_z(u, par):
                dst = y[:, u, :] if isinstance(u, int) else flat(y[:, bass.ds(u, 1), :])
                src = tile(u * 2 + 1)
                if not isinstance(u, int):
                    sp.wait_ge(S["z_ready"], u - 1)
                sp.dma_start(dst, src).then_inc(z_loaded[par], 16)

            def load_rows(u, n, dst, sem, used, count):
                def row(r):
                    return rows_dram[r:r + 1, :] if isinstance(r, int) else rows_dram[bass.ds(sp.snap(r), 1), :]
                src = [row(u * 2 + (n * H + sub)).to_broadcast([P, T]) for sub in range(2)]
                if not isinstance(u, int) or u:
                    sp.wait_ge(used, u * count)
                for sub in range(2):
                    sp.dma_start(dst[:, sub, :], src[sub]).then_inc(sem, 16)

            def load_c(u):
                load_rows(u, 0, crep, c_loaded, S["expo_ready"], 2)

            def load_e(u):
                load_rows(u, 1, erep, e_loaded, S["state_ready"], 1)

            load_pre(0, 0)
            load_c(0)
            load_pre(1, 1)
            load_e(0)
            load_c(1)
            for u in range(2):
                load_z(u, u)
            fill.load(sp, 0)
            with sp.Fori(0, units // 2 - 1) as two:
                for par in range(2):
                    u = two * 2 + (par + 1)
                    load_pre(u + 1, par)
                    load_e(u)
                    load_c(u + 1)
                    load_z(u + 1, par)
                    fill.load(sp, u)
            load_e(units - 1)
            fill.load(sp, units - 1)

        @block.tensor
        def _(pe):
            def turn(u, par):
                pe.wait_ge(S["activated"], u + 1)
                for c in range(NCH):
                    s = slice(c * C, c * C + C)
                    ins = pe.transpose(X[:, s], xs[:, par, s], core.ident[:, :])
                ins.then_inc(S["x_turned"], 1)

            def unit(g, two, par, last=False):
                u = two * 2 + par
                pe.wait_ge(S["x_ready"], u + 1)
                for c in range(NCH - 1):
                    ins = pe.matmul(U[g_rows(g), c * P:c * P + P], btok[:, c, g * 64:g * 64 + 64], xend[:, c, :],
                                    start=True, stop=True)
                ins.then_inc(S["update_done"], 1)
                fill.advance(pe, u, 0, 6)
                pe.wait_ge(S["state_ready"], u + 1)
                pe.wait_ge(S["att_ready"], u * 2 + 2)
                pe.wait_ge(S["out_free"], u + 1)
                for sub in range(2):
                    h = slice(sub * 64, sub * 64 + 64)
                    for c in range(NCH):
                        s = slice(c * C, c * C + C)
                        ins = pe.matmul(A[h, s], xdt[:, c, h], att[:, par, sub, s], start=True, stop=(c == 0))
                        if c:
                            ins = pe.matmul(A[h, s], state[g_rows(g), c, h], cdec[g_rows(g), sub, s],
                                            start=False, stop=True)
                ins.then_inc(S["out_done"], 1)
                fill.advance(pe, u, 6, 10)
                if not last:
                    turn(u + 1, 1 - par)
                fill.advance(pe, u, 10, 16)

            turn(0, 0)
            in_pairs(pe, unit)

        @block.scalar
        def _(act):
            fill.begin(act)
            def silu(u, par):
                act.wait_ge(S["conv_done"], u + 1)
                x = xs[:, par, :]
                act.activation(x, x, ACT.Silu, bias=core.col_at("ssd_cb", u)).then_inc(S["activated"], 1)

            def decays(u, par):
                for sub in range(2):
                    act.wait_ge(S["expo_ready"], u * 2 + (sub + 1))
                    a = att[:, par, sub, :]
                    act.activation(a, a, ACT.Exp).then_inc(S["expd"], 1)

            def unit(g, two, par, last=False):
                u = two * 2 + par
                if not last:
                    silu(u + 1, 1 - par)
                act.wait_ge(z_loaded[par], two * 16 + 16)
                z = flat(y[:, bass.ds(u, 1), :])
                act.activation(z, z, ACT.Silu).then_inc(S["z_ready"], 1)
                if not last:
                    decays(u + 1, 1 - par)
                fill.keep(act, u, 0)
                fill.end(act, u)

            silu(0, 0)
            decays(0, 0)
            in_pairs(act, unit)

        @block.vector
        def _(dve):
            per = 1 + 1 + (NCH - 3) + 1

            def convolve(u, par, load):
                x = xs[:, par, :]
                step = Chain(dve, S["conv_step"], u * 3)
                dve.wait_ge(loaded[par], load * 16 + 16)
                step(dve.tensor_scalar(x, pre[:, par, 0:T], core.col_at("ssd_cw0", u), None, ALU.mult))
                for j in range(1, 4):
                    ins = dve.scalar_tensor_tensor(x, pre[:, par, j:j + T], core.col_at(f"ssd_cw{j}", u), x,
                                                   ALU.mult, ALU.add)
                    if j < 3:
                        step(ins)
                ins.then_inc(S["conv_done"], 1)

            def spread(u, n, h, width):
                return colv[:, n, :, bass.ds(u * 2 + h, 1)].to_broadcast([P, NCH, width])

            def exponents(u, par):
                dve.wait_ge(c_loaded, u * 32 + 32)
                for sub in range(2):
                    a = chunks(att[:, par, sub, :])
                    dve.tensor_tensor(a, chunks(crep[:, sub, :]), spread(u, 0, sub, C), ALU.subtract).then_inc(S["expo_step"], 1)
                for sub in range(2):
                    a = chunks(att[:, par, sub, :])
                    dve.wait_ge(S["expo_step"], u * 2 + (sub + 1))
                    dve.tensor_scalar(a, a, 0.0, None, ALU.min).then_inc(S["expo_ready"], 1)

            def unit(g, two, par, last=False):
                u, r = two * 2 + par, g_rows(g)
                step = Chain(dve, S["dve_step"], u * per)
                heads = [slice(sub * 64, sub * 64 + 64) for sub in range(2)]
                dve.wait_ge(S["x_turned"], u + 1)
                for sub, h in enumerate(heads):
                    ins = dve.tensor_tensor(xdt[:, :, h], chunks(X)[:, :, h], spread(u, 1, sub, 64), ALU.mult)
                step(ins)
                for sub, h in enumerate(heads):
                    ins = dve.tensor_tensor(xend[:, :, h], xdt[:, :, h], spread(u, 2, sub, 64), ALU.mult)
                ins.then_inc(S["x_ready"], 1)
                dve.wait_ge(e_loaded, u * 32 + 32)
                for sub in range(2):
                    dve.tensor_tensor(cdec[r, sub, :], ct[r, :], erep[r, sub, :], ALU.mult)
                for sub in range(2):
                    dve.wait_ge(S["expd"], u * 2 + (sub + 1))
                    a = att[:, par, sub, :]
                    dve.tensor_tensor(a, a, cb[:, g, :], ALU.mult).then_inc(S["att_ready"], 1)
                dve.wait_ge(S["update_done"], u + 1)
                step(dve.tensor_copy(state[r, 1, :], U[r, 0:P]))
                for c in range(1, NCH - 1):
                    for sub, h in enumerate(heads):
                        ins = dve.scalar_tensor_tensor(state[r, c + 1, h], state[r, c, h],
                                                       erep[r, sub, c * C + C - 1:c * C + C],
                                                       U[r, c * P + sub * 64:c * P + sub * 64 + 64], ALU.mult, ALU.add)
                    if c < NCH - 2:
                        step(ins)
                ins.then_inc(S["state_ready"], 1)
                if not last:
                    convolve(u + 1, 1 - par, two + par)
                    exponents(u + 1, 1 - par)
                dve.wait_ge(S["out_done"], u + 1)
                step(dve.scalar_tensor_tensor(xs[:, par, :], xs[:, par, :], core.col_at("d_skip", u), A, ALU.mult, ALU.add))
                dve.sem_inc(S["out_free"], 1)
                dve.wait_ge(S["z_ready"], u + 1)
                yo = flat(y[:, bass.ds(u, 1), :])
                dve.tensor_tensor(yo, yo, xs[:, par, :], ALU.mult).then_inc(S["unit_done"], 1)
                dve.wait_ge(S["unit_done"], u + 1)
                step.ends(per)

            dve.memset(pre[:, :, 0:3], 0.0).then_inc(S["out_free"], 1)
            dve.wait_ge(S["out_free"], 1)
            convolve(0, 0, 0)
            exponents(0, 0)
            in_pairs(dve, unit)


def rwkv_low_rank(core, wt, lo):
    with Stage(core.nc, "rwlo") as st:
        w = st.sb("w", [P, D])
        raw, delta = st.sb("raw", [P, 1 + T]), st.sb("delta", [P, T])
        w_loaded, done, kept, mixed, step_sem, out = (st.sem(n) for n in ("w_loaded", "done", "kept", "mixed", "dve_step", "out"))
        block = st.block()

        @block.sync
        def _(sp):
            sp.dma_start(w[:, :], wt[RW_LO * P:(RW_LO + 1) * P, :]).then_inc(w_loaded, 16)

        @block.tensor
        def _(pe):
            pe.wait_ge(w_loaded, 16)
            project_features(pe, pair(core, 0), w, core.hT).then_inc(done, 1)

        @block.scalar
        def _(act):
            act.wait_ge(done, 1)
            act.activation(raw[:, 1:], pair(core, 0), ACT.Copy).then_inc(kept, 1)
            act.wait_ge(mixed, 1)
            act.activation(lo[0:64, :], lo[0:64, :], ACT.Tanh).then_inc(out, 1)

        @block.vector
        def _(dve):
            step = Chain(dve, step_sem)
            step(dve.memset(raw[:, 0:1], 0.0))
            dve.wait_ge(kept, 1)
            step(dve.tensor_tensor(delta[:, :], raw[:, 0:T], raw[:, 1:], ALU.subtract))
            dve.scalar_tensor_tensor(lo[:, :], delta[:, :], core.col("mu_lo", 0), raw[:, 1:], ALU.mult, ALU.add) \
                .then_inc(mixed, 1)


def rwkv_branch(core, wt, w_up, lo, F, y, gate_park, sb_park):
    order = ["r", "k", "v", "g"]
    nt, units = 4, 4
    r, k, v, kk, b, lw, cum, bonus = (F[:, n, :] for n in range(8))
    NL = LEVELS - 1
    with Stage(core.nc, "rw") as st:
        w = st.sb("w", [P, nt, D])
        up = st.sb("up", [P, P])
        loaded = [st.sem(f"w_loaded{t}") for t in range(nt)]
        raw = st.sb("raw", [P, 1 + T])
        tmp = st.sb("tmp", [P, T])
        tok = st.sb("tok", [P, 4, NCH, P])
        at, ak = (st.sb(n, [P, T]) for n in ("at", "ak"))
        ab, ar = (st.sb(n, [P, 2, T]) for n in ("ab", "ar"))
        X, XT, al1 = (st.sb(n, [P, T]) for n in ("X", "XT", "al1"))
        Y, al = v, (cum, al1)
        WT = st.sb("WT", [P, T])
        G = st.sb("G", [P, NCH, 64])
        U0, sa = (st.sb(n, [P, NCH, 2, 64]) for n in ("U0", "sa"))
        M = st.sb("M", [P, NCH, 64])
        gc = st.sb("gc", [P, NCH])
        S = {n: st.sem(n) for n in (
            "up_loaded", "proj_done", "evacuated", "unit_free", "raw_free", "mixed", "silu_done", "low_done", "low_kept",
            "kk_raw", "squared", "normed", "rooted", "bonus_in", "bonus_done", "cum_ready", "expd", "factors", "turned", "tok_ready",
            "prods", "prods2", "kept", "level_a", "y_done", "y_kept", "xyx", "x_ready", "w_done", "w_kept",
            "u_done", "u_kept", "sa_done", "sa_ready", "m_done", "m_ready", "out_done", "out_kept",
            "mean_done", "centred", "sq2", "var_done", "rooted2", "dve_step", "passed")}
        PA, PB, PC = (pair(core, n) for n in range(3))
        ng = 2 * KD // units
        fill = Filler(core, st, "fill", 3, wt, RW_FILL, places(gate_park, ng) + places(sb_park, 4),
                      [("features", ACT.Sigmoid, None)] * ng +
                      [(layout, func, None) for layout, func in (("features", ACT.Copy), ("features", ACT.Copy),
                                                                 ("tokens", ACT.Copy), ("features", ACT.Silu))])
        EARLY, HEAD, LEVEL, CHUNK = 4 * 16, 4, 1, 2
        PER_HEAD = HEAD + LEVEL * 2 * NL
        TAIL = EARLY + 2 * PER_HEAD + NCH * CHUNK
        assert TAIL == 16 * (fill.n - 1)

        def rows(sub):
            return slice(sub * 64, sub * 64 + 64)

        def cs(c):
            return slice(c * C, c * C + C)

        block = st.block()

        @block.sync
        def _(sp):
            def unit(u, head):
                for t in range(nt):
                    at = (RW_TILE + t) * P if head else sp.snap(u * (nt * P) + (RW_TILE + t) * P)
                    if not head:
                        sp.wait_ge(S["proj_done"], u * nt + (t + 1 - nt))
                    src = wt[at:at + P, :] if head else wt[bass.ds(at, P), :]
                    sp.dma_start(w[:, t, :], src).then_inc(loaded[t], 16)
                at = 0 if head else sp.snap(u * P)
                if not head:
                    sp.wait_ge(S["low_done"], u)
                sp.dma_start(up[:, :], w_up[0:P, :] if head else w_up[bass.ds(at, P), :]).then_inc(S["up_loaded"], 16)
                fill.load(sp, u)
            unit(0, True)
            with sp.Fori(1, units) as u:
                unit(u, False)

        @block.tensor
        def _(pe):
            def block_sum(mat, src, dst):
                for half in range(2):
                    h = slice(half * 512, half * 512 + 512)
                    ins = pe.matmul(dst[:, h], mat, src[:, h], start=True, stop=True)
                return ins

            def products(dst, lhs, rhs, sub):
                for c in range(NCH):
                    ins = pe.matmul(dst[:, cs(c)], lhs[rows(sub), cs(c)], rhs[rows(sub), cs(c)], start=True, stop=True)
                return ins

            def by_chunk(dst, lhs, rhs):
                for c in range(NCH):
                    ins = pe.matmul(dst[:, cs(c)], lhs[:, cs(c)], rhs[:, cs(c)], start=True, stop=True)
                return ins

            with pe.Fori(0, units) as u:
                pe.wait_ge(S["unit_free"], u + 1)
                for t in range(nt):
                    pe.wait_ge(loaded[t], 16 * u + 16)
                    if t >= 2:
                        pe.wait_ge(S["evacuated"], u * nt + (t - 1))
                    project_features(pe, (PA, PB)[t % 2], w[:, t, :], core.hT).then_inc(S["proj_done"], 1)
                pe.wait_ge(S["up_loaded"], 16 * u + 16)
                pe.wait_ge(S["evacuated"], u * nt + (nt - 1))
                for half in range(2):
                    h = slice(half * 512, half * 512 + 512)
                    pe.matmul(PC[:, h], up[0:64, :], lo[0:64, h], start=True, stop=True)
                    ins = pe.matmul(PA[:, h], up[64:128, :], lo[64:128, h], start=True, stop=True)
                ins.then_inc(S["low_done"], 1)
                fill.advance(pe, u, 0, 16)
                pe.wait_ge(S["evacuated"], u * nt + nt)
                pe.wait_ge(S["squared"], u + 1)
                block_sum(core.same_head[:, :], tmp, PB).then_inc(S["normed"], 1)
                fill.advance(pe, u, 16, 32)
                pe.wait_ge(S["low_kept"], u + 1)
                pe.wait_ge(S["bonus_in"], u + 1)
                block_sum(core.same_head[:, :], bonus, PC).then_inc(S["bonus_done"], 1)
                fill.advance(pe, u, 32, EARLY)
                pe.wait_ge(S["factors"], u + 1)
                for n, src in enumerate((v, b, k, kk)):
                    dst = (PA, PC, PB, PA)[n]
                    if n == 3:
                        pe.wait_ge(S["tok_ready"], u * 4 + 1)
                    for c in range(NCH):
                        ins = pe.transpose(dst[:, cs(c)], src[:, cs(c)], core.ident[:, :])
                    ins.then_inc(S["turned"], 1)
                pe.wait_ge(S["tok_ready"], u * 4 + 4)
                for sub in range(2):
                    e = u * 2 + sub
                    if sub:
                        pe.wait_ge(S["u_kept"], u * 2 + 1)
                    products(PA, b, kk, sub)
                    products(PB, kk, b, sub)
                    products(PC, k, kk, sub).then_inc(S["prods"], 1)
                    at = EARLY + sub * PER_HEAD
                    fill.advance(pe, u, at, at + HEAD)
                    at += HEAD
                    pe.wait_ge(S["kept"], e * 2 + 1)
                    products(PC, b, r, sub)
                    products(PA, k, r, sub).then_inc(S["prods2"], 1)
                    for l in range(1, LEVELS):
                        n = e * NL + (l - 1)
                        pe.wait_ge(S["level_a"], n + 1)
                        for hf in range(2):
                            if l > 1:
                                pe.wait_ge(S["x_ready"], n * 2 + (hf - 1))
                            elif hf == 0:
                                pe.wait_ge(S["kept"], e * 2 + 2)
                            for c in range(hf * NCH // 2, (hf + 1) * NCH // 2):
                                ins = pe.matmul(PC[:, cs(c)], al[l % 2][:, cs(c)], X[:, cs(c)], start=True, stop=True)
                            ins.then_inc(S["y_done"], 1)
                            fill.advance(pe, u, at, at + LEVEL)
                            at += LEVEL
                        for hf in range(2):
                            pe.wait_ge(S["y_kept"], n * 2 + (hf + 1))
                            for c in range(hf * NCH // 2, (hf + 1) * NCH // 2):
                                if l < NL:
                                    pe.matmul(level_views(PA[:, cs(c)], l)[0], XT[:, cs(c)],
                                              level_views(Y[:, cs(c)], l)[0], start=True, stop=True)
                                ins = pe.matmul(level_views(PB[:, cs(c)], l)[1], Y[:, cs(c)],
                                                level_views(XT[:, cs(c)], l)[1], start=True, stop=True)
                            ins.then_inc(S["xyx"], 1)
                    pe.wait_ge(S["x_ready"], (e * NL + NL) * 2)
                    for c in range(NCH):
                        pe.matmul(PC[rows(sub), cs(c)], tok[:, 3, c, rows(sub)], XT[:, cs(c)], start=True, stop=True)
                        ins = pe.matmul(PB[:, c * 64:c * 64 + 64], ak[:, cs(c)], tok[:, 0, c, rows(sub)], start=True, stop=True)
                    ins.then_inc(S["w_done"], 1)
                    pe.wait_ge(S["w_kept"], e + 1)
                    for c in range(NCH):
                        ins = pe.matmul(PA[:, c * 64:c * 64 + 64], XT[:, cs(c)], G[:, c, :], start=True, stop=True)
                    ins.then_inc(S["u_done"], 1)
                pe.wait_ge(S["u_kept"], u * 2 + 2)
                for c in range(NCH):
                    if c:
                        pe.wait_ge(S["m_ready"], u * (NCH - 1) + c)
                        for sub in range(2):
                            ins = pe.matmul(PB[:, sub * 512 + c * 64:sub * 512 + c * 64 + 64], WT[rows(sub), cs(c)],
                                            M[rows(sub), c, :], start=True, stop=True)
                        ins.then_inc(S["sa_done"], 1)
                    if c < NCH - 1:
                        mc = slice(c * 64, c * 64 + 64)
                        for sub in range(2):
                            pe.matmul(PC[rows(sub), mc], tok[:, 2, c, rows(sub)], tok[:, 0, c, rows(sub)],
                                      start=True, stop=False)
                            if c:
                                pe.matmul(PC[rows(sub), mc], core.ident[rows(sub), rows(sub)], M[rows(sub), c, :],
                                          start=False, stop=False)
                    at = EARLY + 2 * PER_HEAD + c * CHUNK
                    fill.advance(pe, u, at, at + CHUNK)
                    pe.wait_ge(S["sa_ready"], u * NCH + (c + 1))
                    if c < NCH - 1:
                        for sub in range(2):
                            ins = pe.matmul(PC[rows(sub), mc], tok[:, 1, c, rows(sub)], sa[:, c, sub, :],
                                            start=False, stop=True)
                        ins.then_inc(S["m_done"], 1)
                for sub in range(2):
                    for c in range(NCH):
                        o = PA[rows(sub), cs(c)]
                        pe.matmul(o, tok[:, 0, c, rows(sub)], ar[:, sub, cs(c)], start=True, stop=False)
                        ins = pe.matmul(o, sa[:, c, sub, :], ab[:, sub, cs(c)], start=False, stop=(c == 0))
                        if c:
                            ins = pe.matmul(o, M[rows(sub), c, :], r[rows(sub), cs(c)], start=False, stop=True)
                ins.then_inc(S["out_done"], 1)
                pe.wait_ge(S["out_kept"], u + 1)
                block_sum(core.mean_head[:, :], lw, PB).then_inc(S["mean_done"], 1)
                fill.advance(pe, u, TAIL, TAIL + 8)
                pe.wait_ge(S["sq2"], u + 1)
                block_sum(core.mean_head[:, :], cum, PC).then_inc(S["var_done"], 1)
                fill.advance(pe, u, TAIL + 8, 16 * fill.n)

        @block.scalar
        def _(act):
            fill.begin(act)
            with act.Fori(0, units) as u:
                for t in range(nt):
                    act.wait_ge(S["proj_done"], u * nt + (t + 1))
                    act.wait_ge(S["raw_free"], u * nt + (t + 1))
                    act.activation(raw[:, 1:], (PA, PB)[t % 2], ACT.Copy).then_inc(S["evacuated"], 1)
                act.wait_ge(S["low_done"], u + 1)
                act.activation(lw, PC, ACT.Sigmoid, bias=core.col_at("w0", u))
                act.activation(b, PA, ACT.Sigmoid, bias=core.col_at("a0", u)).then_inc(S["low_kept"], 1)
                act.wait_ge(S["mixed"], u * nt + nt)
                yo = flat(y[:, bass.ds(u, 1), :])
                act.activation(yo, yo, ACT.Silu).then_inc(S["silu_done"], 1)
                act.wait_ge(S["kk_raw"], u + 1)
                act.activation(tmp[:, :], kk, ACT.Square).then_inc(S["squared"], 1)
                fill.keep(act, u, 0)
                act.wait_ge(S["normed"], u + 1)
                act.activation(tmp[:, :], PB, ACT.Sqrt).then_inc(S["rooted"], 1)
                fill.keep(act, u, 1)
                act.wait_ge(S["cum_ready"], u + 1)
                act.activation(gc[:, 0:NCH - 1], gc[:, 0:NCH - 1], ACT.Exp)
                act.activation(lw, lw, ACT.Exp)
                act.activation(tmp[:, :], cum, ACT.Exp, scale=-1.0).then_inc(S["expd"], 1)
                act.wait_ge(S["expd"], u * 2 + 1)
                act.activation(cum, cum, ACT.Exp).then_inc(S["expd"], 1)
                for n in range(2, EARLY // 16):
                    fill.keep(act, u, n)
                for n in range(4):
                    act.wait_ge(S["turned"], u * 4 + (n + 1))
                    act.activation(tok[:, n, :, :], chunks((PA, PC, PB, PA)[n]), ACT.Copy).then_inc(S["tok_ready"], 1)
                for sub in range(2):
                    e = u * 2 + sub
                    at = EARLY + sub * PER_HEAD + HEAD
                    for l in range(1, LEVELS):
                        for hf in range(2):
                            h = slice(hf * 512, hf * 512 + 512)
                            act.wait_ge(S["y_done"], (e * NL + (l - 1)) * 2 + (hf + 1))
                            act.activation(Y[:, h], PC[:, h], ACT.Copy).then_inc(S["y_kept"], 1)
                            at += LEVEL
                            if at % 16 == 0:
                                fill.keep(act, u, at // 16 - 1)
                    act.wait_ge(S["w_done"], e + 1)
                    act.activation(WT[rows(sub), :], PC[rows(sub), :], ACT.Copy)
                    act.activation(G[:, :, :], PB[:, 0:NCH * 64].rearrange("p (c i) -> p c i", c=NCH), ACT.Copy) \
                        .then_inc(S["w_kept"], 1)
                fill.keep(act, u, fill.n - 2)
                act.wait_ge(S["out_done"], u + 1)
                act.activation(lw, PA, ACT.Copy).then_inc(S["out_kept"], 1)
                act.wait_ge(S["centred"], u + 1)
                act.activation(cum, lw, ACT.Square).then_inc(S["sq2"], 1)
                act.wait_ge(S["var_done"], u + 1)
                act.activation(tmp[:, :], PC, ACT.Sqrt, bias=core.const(GN_EPS)).then_inc(S["rooted2"], 1)
                fill.keep(act, u, fill.n - 1)
                fill.end(act, u)

        @block.gpsimd
        def _(pool):
            with pool.Fori(0, 2 * units) as e:
                pool.wait_ge(S["kept"], e * 2 + 1)
                for l in range(1, LEVELS):
                    if l >= 3:
                        pool.wait_ge(S["y_done"], (e * NL + (l - 2)) * 2)
                    pool.tensor_tensor(chunks(al[l % 2][:, :]), chunks(at[:, :]), per_chunk(core.level_mask[:, l, :]),
                                       ALU.mult).then_inc(S["level_a"], 1)

        @block.vector
        def _(dve):
            for a in (at[:, :], ak[:, :], ab[:, :, :], ar[:, :, :]):
                dve.memset(a, 0.0)
            dve.memset(raw[:, 0:1], 0.0).then_inc(S["unit_free"], 1)
            dve.sem_inc(S["raw_free"], 1)
            per = 4 + 3 + 2 + 7 + 2 + 3
            with dve.Fori(0, units) as u:
                step = Chain(dve, S["dve_step"], u * per)
                yo = flat(y[:, bass.ds(u, 1), :])
                for t, (dst, what) in enumerate(((r, "r"), (k, "k"), (v, "v"), (yo, "g"))):
                    dve.wait_ge(S["evacuated"], u * nt + (t + 1))
                    step(dve.tensor_tensor(bonus, raw[:, 0:T], raw[:, 1:], ALU.subtract))
                    dve.scalar_tensor_tensor(dst, bonus, core.col_at("mu_" + what, u), raw[:, 1:], ALU.mult, ALU.add) \
                        .then_inc(S["mixed"], 1)
                    dve.wait_ge(S["mixed"], u * nt + (t + 1))
                    dve.sem_inc(S["raw_free"], 1)
                dve.tensor_scalar(kk, k, core.col_at("k_k", u), None, ALU.mult).then_inc(S["kk_raw"], 1)
                dve.wait_ge(S["rooted"], u + 1)
                step(dve.tensor_scalar(tmp[:, :], tmp[:, :], 1e-12, None, ALU.max))
                step(dve.reciprocal(tmp[:, :], tmp[:, :]))
                step(dve.tensor_tensor(kk, kk, tmp[:, :], ALU.mult))
                dve.wait_ge(S["low_kept"], u + 1)
                step(dve.tensor_scalar(tmp[:, :], b, -1.0, core.col_at("k_a", u), ALU.add, ALU.mult))
                step(dve.scalar_tensor_tensor(k, tmp[:, :], 1.0, k, ALU.add, ALU.mult))
                dve.scalar_tensor_tensor(bonus, r, core.col_at("r_k", u), k, ALU.mult, ALU.mult).then_inc(S["bonus_in"], 1)
                dve.tensor_tensor(b, kk, b, ALU.mult)
                step(dve.tensor_scalar(lw, lw, -float(np.exp(-0.5)), None, ALU.mult))
                for c in range(NCH):
                    ins = dve.tensor_tensor_scan(cum[:, cs(c)], lw[:, cs(c)], lw[:, cs(c)], 0.0, ALU.add, ALU.bypass)
                step(ins)
                cc = chunks(cum)
                last, mid = cc[:, :, C - 1:C], cc[:, :, C // 2 - 1:C // 2]
                gv = gc[:, :].unsqueeze(2)
                step(dve.tensor_tensor(gv[:, 0:NCH - 1, :], last[:, 0:NCH - 1, :], mid[:, 0:NCH - 1, :], ALU.subtract))
                step(dve.tensor_tensor(gv[:, 0:NCH - 1, :], gv[:, 0:NCH - 1, :], mid[:, 1:NCH, :], ALU.add))
                step(dve.tensor_tensor(chunks(WT[:, :]), cc, mid.to_broadcast([P, NCH, C]), ALU.subtract))
                step(dve.tensor_tensor(lw, WT[:, :], lw, ALU.subtract))
                dve.tensor_copy(cum, WT[:, :]).then_inc(S["cum_ready"], 1)
                dve.wait_ge(S["bonus_done"], u + 1)
                step(dve.tensor_tensor(bonus, PC, v, ALU.mult))
                dve.wait_ge(S["expd"], u * 2 + 2)
                dve.tensor_tensor(r, r, cum, ALU.mult)
                dve.tensor_tensor(kk, kk, lw, ALU.mult)
                dve.scalar_tensor_tensor(b, b, -1.0, tmp[:, :], ALU.mult, ALU.mult)
                dve.tensor_tensor(k, k, tmp[:, :], ALU.mult).then_inc(S["factors"], 1)
                for sub in range(2):
                    e = u * 2 + sub
                    eye = per_chunk(core.ident[:, :])
                    dve.tensor_copy(chunks(X[:, :]), eye)
                    step(dve.tensor_copy(chunks(XT[:, :]), eye))
                    wait_alone(dve, S["prods"], e + 1, S["passed"])
                    dve.copy_predicated(chunks(at[:, :]), bits(core.strict[:, :]), chunks(PA))
                    dve.copy_predicated(chunks(XT[:, :]), bits(core.level_mask[:, 0, :]), chunks(PA))
                    dve.copy_predicated(chunks(X[:, :]), bits(core.level0_T[:, :]), chunks(PB))
                    dve.copy_predicated(chunks(ak[:, :]), bits(core.strict[:, :]), chunks(PC)).then_inc(S["kept"], 1)
                    wait_alone(dve, S["prods2"], e + 1, S["passed"])
                    dve.copy_predicated(chunks(ab[:, sub, :]), bits(core.upto[:, :]), chunks(PC))
                    dve.copy_predicated(chunks(ar[:, sub, :]), bits(core.upto[:, :]), chunks(PA)).then_inc(S["kept"], 1)
                    for l in range(1, LEVELS):
                        for hf in range(2):
                            n = (e * NL + (l - 1)) * 2 + (hf + 1)
                            h = slice(hf * 512, hf * 512 + 512)
                            dve.wait_ge(S["xyx"], n)
                            if l < NL:
                                xe = level_views(X[:, h], l)[0]
                                dve.tensor_tensor(xe, xe, level_views(PA[:, h], l)[0], ALU.add)
                            xo = level_views(XT[:, h], l)[1]
                            dve.tensor_tensor(xo, xo, level_views(PB[:, h], l)[1], ALU.add).then_inc(S["x_ready"], 1)
                    dve.wait_ge(S["u_done"], e + 1)
                    uc = PA[:, 0:NCH * 64].rearrange("p (c i) -> p c i", c=NCH)
                    dve.tensor_copy(sa[:, 0, sub, :], uc[:, 0, :])
                    dve.tensor_copy(U0[:, 1:, sub, :], uc[:, 1:, :]).then_inc(S["u_kept"], 1)
                dve.wait_ge(S["u_kept"], u * 2 + 2)
                dve.sem_inc(S["sa_ready"], 1)
                for c in range(NCH):
                    if c:
                        dve.wait_ge(S["sa_done"], u * (NCH - 1) + c)
                        dve.tensor_tensor(sa[:, c, :, :], PB.rearrange("p (a n) -> p a n", a=2)[:, :, c * 64:c * 64 + 64],
                                          U0[:, c, :, :], ALU.add).then_inc(S["sa_ready"], 1)
                    if c < NCH - 1:
                        dve.wait_ge(S["m_done"], u * (NCH - 1) + (c + 1))
                        dve.tensor_scalar(M[:, c + 1, :], PC[:, c * 64:c * 64 + 64], gc[:, c:c + 1], None, ALU.mult) \
                            .then_inc(S["m_ready"], 1)
                dve.wait_ge(S["mean_done"], u + 1)
                dve.tensor_tensor(lw, lw, PB, ALU.subtract).then_inc(S["centred"], 1)
                dve.wait_ge(S["rooted2"], u + 1)
                step(dve.reciprocal(tmp[:, :], tmp[:, :]))
                step(dve.scalar_tensor_tensor(lw, lw, core.col_at("rw_ln_g", u), tmp[:, :], ALU.mult, ALU.mult))
                step(dve.scalar_tensor_tensor(lw, lw, core.col_at("rw_ln_b", u), bonus, ALU.add, ALU.add))
                dve.wait_ge(S["silu_done"], u + 1)
                dve.tensor_tensor(yo, yo, lw, ALU.mult).then_inc(S["unit_free"], 1)
                step.ends(per)


def block_3(core, d):
    nc = core.nc
    with Stage(nc, "b3") as st:
        core.hT = st.sb("hT", [P, KD, T])
        mats, masks = st.sb("mats", [P, 3, P]), st.sb("masks", [P, 3, P])
        core.same_head, core.mean_head, core.triangle = (mats[:, n, :] for n in range(3))
        core.strict, core.upto, core.level0_T = (masks[:, n, :] for n in range(3))
        with Stage(nc, "consts3") as s2:
            got = s2.sem("consts_loaded")
            block = s2.block()

            @block.sync
            def _(sp):
                sp.dma_start(mats[:, :, :].rearrange("p a b -> p (a b)"), d["c_mat3"]).then_inc(got, 16)
                sp.dma_start(masks[:, :, :].rearrange("p a b -> p (a b)"), d["c_mask3"]).then_inc(got, 16)
                sp.wait_ge(got, 32)
        rms_norm(core, "rms3", core.xT, "norm_g_3", core.hT, park=d["x_park"])
        with Stage(nc, "rws") as s2:
            y, lo = s2.sb("y", [P, 4, T]), s2.sb("lo", [P, T])
            rwkv_low_rank(core, d["w3"], lo)
            rwkv_branch(core, d["w3"], d["w_up"], lo, core.xT, y, d["gate_park"], d["sb_park"])
            weighted_projection(core, "yrw", y, 4, d["wrw"], d["gate_park"], KD, core.xT, False)
        with Stage(nc, "sbs") as s2:
            y = s2.sb("y", [P, 4, T])
            stick_breaking_branch(core, d["w3"], y, d["sb_park"], d["xz_park"])
            weighted_projection(core, "ysb", y, 4, d["wsb"], d["gate_park"], 0, core.xT, True)
        with Stage(nc, "ssds") as s2:
            y = s2.sb("y", [P, KD, T])
            with Stage(nc, "ssdp") as s3:
                cols = s3.sb("cols", [P, 3 * NCH * SSH])
                ct, btok, cb = s3.sb("ct", [P, T]), s3.sb("btok", [P, NCH, P]), s3.sb("cb", [P, 2, T])
                ssd_gates(core, d["w3"], d["ssd_rows"], cols, ct, btok, cb)
                ssd_branch(core, d["w3"], d["gate_park"], d["xz_park"], d["ssd_rows"], cols, ct, btok, cb, y)
            rms_norm(core, "rms_ssd", y, "ssd_ng", y)
            weighted_projection(core, "yssd", y, KD, d["wssd"], d["gate_park"], 2 * KD, core.xT, True,
                                back=(core.hT, d["x_park"]))
        out_projection(core, "o3", core.xT, KD, d["wo3"], core.hT)
        rms_norm(core, "fin3", core.hT, "final_g_3", core.xT)


SEG1 = segments([("hg_q", 512), ("hg_f", 512), ("hg_i", 512), ("hg_z", 512), ("gla_q", 256), ("gla_k", 256),
                 ("gla_v", 512), ("gla_a", 16), ("gla_z", 512), ("ml_q", 256), ("ml_k", 256), ("ml_v", 512),
                 ("ml_i", 4), ("ml_f", 4), ("ml_o", 512), ("ml_z", 512)])


def tile_order_1():
    def tile(name, n):
        s = SEG1[name][0] + n * P
        return s, min(s + P, SEG1[name][1])
    out = []
    for h in range(4):
        out += [tile("hg_f", h), tile("hg_q", h), tile("hg_i", h), tile("hg_z", h)]
    out += [tile("gla_a", 0), (SEG1["ml_i"][0], SEG1["ml_f"][1])]
    for u in range(4):
        out += [tile("gla_" + "qk"[u % 2], u // 2), tile("gla_v", u), tile("gla_z", u)]
    for u in range(2):
        out += [tile("ml_q", u), tile("ml_k", u)]
        out += [tile(n, 2 * u + s) for n in ("ml_v", "ml_o", "ml_z") for s in range(2)]
    return out


def in_tiles(w, ranges):
    k = w.shape[0] // P
    out = np.zeros((len(ranges), P, k, P), np.float32)
    v = w.reshape(k, P, -1)
    for n, (a, b) in enumerate(ranges):
        out[n, :, :, :b - a] = v[:, :, a:b].transpose(1, 0, 2)
    return out.reshape(len(ranges) * P, k * P)


def out_tiles(w):
    return in_tiles(w, [(e * P, e * P + P) for e in range(w.shape[1] // P)])


def columns(i):
    b = i["b_in"][0]
    out = [("norm_w", i["norm_w"][0])]
    g = b[SEG1["gla_q"][0]:SEG1["gla_k"][1]].reshape(2, 2, P)
    out.append(("gla_qk", g.transpose(1, 0, 2).reshape(-1)))
    for n in ("hg_q", "hg_f", "hg_z", "gla_z", "ml_q", "ml_k", "ml_o", "ml_z"):
        out.append((n, b[slice(*SEG1[n])]))
    out += [("gla_a_b", b[slice(*SEG1["gla_a"])]), ("ml_i_b", b[slice(*SEG1["ml_i"])]),
            ("ml_f_b", b[slice(*SEG1["ml_f"])]), ("hg_lb", i["hg_lb_logits"][0]),
            ("lb", np.zeros(512, np.float32)), ("one_minus_lb", np.zeros(512, np.float32)),
            ("hg_nw", i["hg_norm_w"][0]), ("gla_b_a2", i["gla_b_a2"][0]), ("gla_nw", i["gla_norm_w"][0]),
            ("ml_cb", i["ml_conv_b"][0]), ("ml_nw", i["ml_norm_w"][0]), ("final_norm_w", i["final_norm_w"])]
    out += [(f"ml_cw{j}", i["ml_conv_w"][0, j]) for j in range(4)]
    return out + columns_2(i) + columns_3(i)


CONSTS = (NORM_EPS, LN_EPS, GN_EPS, -0.5)


def pack_columns(i):
    index, parts, at = {}, [], 0
    for name, vec in columns(i):
        n = -(-vec.size // P)
        col = np.zeros(n * P, np.float32)
        col[:vec.size] = vec.reshape(-1)
        parts.append(col.reshape(n, P).T)
        index[name] = at
        at += n
    for v in CONSTS:
        parts.append(np.full((P, 1), v, np.float32))
        index[v] = at
        at += 1
    return np.ascontiguousarray(np.concatenate(parts, 1)), index


def level_masks():
    s, t = np.arange(P)[:, None], np.arange(P)[None, :]
    top = np.floor(np.log2(np.maximum(s ^ t, 1))).astype(int)
    return np.stack([((s < t) & (top == l)) for l in range(LEVELS)], 1).astype(np.float32)


def shape_constants():
    s, t = np.arange(P)[:, None], np.arange(P)[None, :]
    mats = {"ident": np.eye(P), "ones": np.ones((P, P)), "mean_d": np.full((P, P), 1.0 / D),
            "mean_p": np.full((P, P), 1.0 / P),
            "mean_v": np.full((P, P), 1.0 / RDV), "tri": (t >= s)}
    return {n: m.astype(np.float32) for n, m in mats.items()}


def lay_out(i):
    i = {n: np.asarray(a) for n, a in i.items()}
    d = {"x": i["x"][0]}
    w1 = i["w_in"][0]
    d["w1"] = in_tiles(w1, tile_order_1())
    b = i["b_in"][0]
    d["b1_vrow"] = np.concatenate([b[slice(*SEG1[n])] for n in ("hg_i", "gla_v", "ml_v")])[None, :]
    d["gla_w_a2"] = i["gla_w_a2"][0]
    for n, name in enumerate(("wo1a", "wo1b", "wo1c")):
        d[name] = out_tiles(i["w_out"][0, n * 512:(n + 1) * 512])
    d["cols"], index = pack_columns(i)
    for n, m in shape_constants().items():
        d["c_" + n] = m
    d["c_level_mask"] = level_masks().reshape(P, LEVELS * P)
    lay_out_2(i, d)
    lay_out_3(i, d)
    return {n: np.ascontiguousarray(a) for n, a in d.items()}, index


def build(nc, d, out, index, blocks=(1, 2, 3)):
    core = Core()
    core.nc, core.index = nc, index
    Stage.ended = []
    with ExitStack() as ctx:
        core.ps = ctx.enter_context(nc.psum_tensor("ps", [P, 8 * 512], F32))
        core.xT = ctx.enter_context(nc.sbuf_tensor("xT", [P, KD, T], F32))
        core.cols = ctx.enter_context(nc.sbuf_tensor("cols_sb", list(d["cols"].shape), F32))
        core.col = lambda name, n: core.cols[:, index[name] + n:index[name] + n + 1]
        core.col_at = lambda name, n: core.cols[:, bass.ds(n + index[name], 1)]
        core.const = lambda v: core.col(v, 0)
        names = ["ident", "ones", "mean_d", "mean_p", "mean_v", "tri"]
        tiles = {n: ctx.enter_context(nc.sbuf_tensor("c_" + n + "_sb", [P, P], F32)) for n in names}
        core.ident, core.ones, core.mean_d, core.mean_p, core.mean_v, core.tri = (tiles[n] for n in names)
        core.level_mask = ctx.enter_context(nc.sbuf_tensor("level_mask", [P, LEVELS, P], F32))
        with Stage(nc, "consts") as st:
            got = st.sem("consts_loaded")
            block = st.block()

            @block.sync
            def _(sp):
                for n in names:
                    sp.dma_start(tiles[n][:, :], d["c_" + n]).then_inc(got, 16)
                sp.dma_start(core.level_mask[:, :, :].rearrange("p l t -> p (l t)"), d["c_level_mask"]).then_inc(got, 16)
                sp.dma_start(core.cols[:, :], d["cols"]).then_inc(got, 16)
                sp.wait_ge(got, 16 * (len(names) + 2))
        load_input(core, d["x"])
        if 1 in blocks:
            block_1(core, d)
        if 2 in blocks:
            block_2(core, d)
        if 3 in blocks:
            block_3(core, d)
        store_output(core, core.xT, out)


SCRATCH = {"gla_park": (12 * P, T), "ml_park": (16 * P, T), "ml_rows": (12, T), "o_park": (RH * RDV, T), "x_park": (D, T), "gate_park": (3 * D, T), "xz_park": (2 * D, T), "sb_park": (4 * SBW, T), "ssd_rows": (2 * SSH, T)}


def kernel(**inputs):
    from concourse import bacc
    from concourse.bass_utils import run_bass_kernel_spmd

    arrays, index = lay_out(inputs)
    nc = bacc.Bacc("TRN2", target_bir_lowering=False, num_devices=1)
    d = {n: nc.dram_tensor("in_" + n, a.shape, mybir.dt.from_np(a.dtype), kind="ExternalInput").ap()
         for n, a in arrays.items()}
    for n, shape in SCRATCH.items():
        d[n] = nc.dram_tensor("scratch_" + n, shape, F32, kind="Internal").ap()
    out = nc.dram_tensor("out_0", (T, D), F32, kind="ExternalOutput").ap()
    build(nc, d, out, index)
    r = run_bass_kernel_spmd(nc, [{"in_" + n: a for n, a in arrays.items()}], core_ids=[0])
    return r.results[0]["out_0"].reshape(1, T, D)
```
